# Optimizing a Trainium2 kernel written in Bass

```python
import jax, jax.numpy as jnp
from jax import lax
import numpy as np

D_MODEL = 1024
BATCH = 1
SEQ = 256
DEPTH = 2

RWKV_HEADS = 8
RWKV_HEAD_DIM = 64
RWKV_WIDTH = RWKV_HEADS * RWKV_HEAD_DIM
DECAY_LORA = 64
AAA_LORA = 64
GATE_LORA = 128
RWKV_GN_EPS = 64e-5
RWKV_COLS = 3 * RWKV_WIDTH + DECAY_LORA + AAA_LORA + GATE_LORA
CONF_WIDTH = 256
CONF_CONV_WIDTH = 31
CONF_COLS = 2 * CONF_WIDTH
SHORT_WIDTH = 256
SHORT_CONV_WIDTH = 3
SHORT_COLS = 3 * SHORT_WIDTH
N_BRANCHES = 3
GATE_COLS = N_BRANCHES * D_MODEL
IN_COLS = RWKV_COLS + CONF_COLS + SHORT_COLS + GATE_COLS
D_FF = 2816
N_EXPERTS = 8
TOP_K = 2
EXPERT_FF = 2816
MOE_BLOCK = 256
LN_EPS = 1e-5


def _layernorm(x, g, b, eps=LN_EPS):
    xf = x.astype(jnp.float32)
    mu = jnp.mean(xf, axis=-1, keepdims=True)
    var = jnp.mean(jnp.square(xf - mu), axis=-1, keepdims=True)
    return ((xf - mu) * lax.rsqrt(var + eps) * g + b).astype(x.dtype)

def _causal_depthwise_conv(x, w):
    width, ch = w.shape
    return lax.conv_general_dilated(
        x, w[:, None, :].astype(x.dtype), window_strides=(1,), padding=[(width - 1, 0)],
        dimension_numbers=("NWC", "WIO", "NWC"), feature_group_count=ch)

def _rwkv7_scan(r, decay, k, v, kk, a):
    bn, _, h, n = r.shape

    def step(state, inp):
        r_t, w_t, k_t, v_t, kk_t, a_t = inp
        sa = jnp.einsum("bhvk,bhk->bhv", state, -kk_t)
        state = (state * w_t[:, :, None, :]
                 + sa[..., None] * (kk_t * a_t)[:, :, None, :]
                 + v_t[..., None] * k_t[:, :, None, :])
        out = jnp.einsum("bhvk,bhk->bhv", state, r_t)
        return state, out

    xs = tuple(jnp.moveaxis(t, 1, 0) for t in (r, decay, k, v, kk, a))
    s0 = jnp.zeros((bn, h, n, n), jnp.float32)
    _, out = lax.scan(step, s0, xs)
    return jnp.moveaxis(out, 0, 1)

def _rwkv7_branch(p, mu, w0, w2, a0, a2, g2, k_k, k_a, r_k, ln_g, ln_b, w_o):
    bn, s, _ = p.shape
    H, N, W = RWKV_HEADS, RWKV_HEAD_DIM, RWKV_WIDTH
    f32 = jnp.float32
    p_prev = jnp.pad(p, ((0, 0), (1, 0), (0, 0)))[:, :-1]
    p = p + (p_prev - p) * mu
    cuts = [W, 2 * W, 3 * W, 3 * W + DECAY_LORA, 3 * W + DECAY_LORA + AAA_LORA]
    r, k, v, pw, pa, pg = jnp.split(p, cuts, axis=-1)
    w = -jax.nn.softplus(-(w0 + jnp.tanh(pw) @ w2).astype(f32)) - 0.5
    decay = jnp.exp(-jnp.exp(w))
    a = jax.nn.sigmoid((a0 + pa @ a2).astype(f32))
    g = jax.nn.sigmoid(pg) @ g2
    heads = lambda t: t.reshape(bn, s, H, N)
    k = k.astype(f32)
    kk = heads(k * k_k)
    kk = kk / jnp.maximum(jnp.sqrt(jnp.sum(kk * kk, axis=-1, keepdims=True)), 1e-12)
    k = k * (1.0 + (a - 1.0) * k_a)
    r4, k4, v4 = heads(r.astype(f32)), heads(k), heads(v.astype(f32))
    o = _rwkv7_scan(r4, heads(decay), k4, v4, kk, heads(a))
    mean = jnp.mean(o, axis=-1, keepdims=True)
    var = jnp.mean(jnp.square(o - mean), axis=-1, keepdims=True)
    o = (o - mean) * lax.rsqrt(var + RWKV_GN_EPS) * ln_g.reshape(H, N) + ln_b.reshape(H, N)
    o = o + jnp.sum(r4 * k4 * r_k, axis=-1, keepdims=True) * v4
    o = (o.reshape(bn, s, W) * g).astype(p.dtype)
    return o @ w_o

def _conformer_conv_branch(p, dw, dw_b, ln_g, ln_b, w_o):
    u = p[..., :CONF_WIDTH] * jax.nn.sigmoid(p[..., CONF_WIDTH:])
    u = _causal_depthwise_conv(u, dw) + dw_b
    u = jax.nn.silu(_layernorm(u, ln_g, ln_b))
    return u @ w_o

def _short_conv_branch(p, dw, w_o):
    gb, gc, h = jnp.split(p, 3, axis=-1)
    return (gb * _causal_depthwise_conv(gc * h, dw)) @ w_o

def _hybrid_mixer(x, w_in, rwkv_mu, rwkv_w0, rwkv_w2, rwkv_a0, rwkv_a2, rwkv_g2, rwkv_k_k,
                  rwkv_k_a, rwkv_r_k, rwkv_ln_g, rwkv_ln_b, rwkv_w_o, conf_dw, conf_dw_b,
                  conf_ln_g, conf_ln_b, conf_w_o, short_dw, short_w_o, w_out):
    p = x @ w_in
    c1 = RWKV_COLS
    c2 = c1 + CONF_COLS
    c3 = c2 + SHORT_COLS
    p_rwkv, p_conf, p_short, p_gate = jnp.split(p, [c1, c2, c3], axis=-1)
    y_a = _rwkv7_branch(p_rwkv, rwkv_mu, rwkv_w0, rwkv_w2, rwkv_a0, rwkv_a2, rwkv_g2,
                        rwkv_k_k, rwkv_k_a, rwkv_r_k, rwkv_ln_g, rwkv_ln_b, rwkv_w_o)
    y_b = _conformer_conv_branch(p_conf, conf_dw, conf_dw_b, conf_ln_g, conf_ln_b, conf_w_o)
    y_c = _short_conv_branch(p_short, short_dw, short_w_o)
    g_a, g_b, g_c = jnp.split(jax.nn.sigmoid(p_gate), N_BRANCHES, axis=-1)
    return (g_a * y_a.astype(x.dtype) + g_b * y_b + g_c * y_c) @ w_out

def _swiglu(x, w_gate, w_up, w_down):
    return (jax.nn.silu(x @ w_gate) * (x @ w_up)) @ w_down

def _moe_swiglu(x, w_router, w_gate, w_up, w_down):
    bn, s, d = x.shape
    xf = x.reshape(-1, d)
    n_tok = xf.shape[0]
    logits = (xf @ w_router).astype(jnp.float32)
    top_logit, top_idx = lax.top_k(logits, TOP_K)
    top_w = jax.nn.softmax(top_logit, axis=-1)
    n_assign = n_tok * TOP_K
    expert = top_idx.reshape(-1).astype(jnp.int32)
    token = jnp.repeat(jnp.arange(n_tok, dtype=jnp.int32), TOP_K)
    weight = top_w.reshape(-1)
    order = jnp.argsort(expert)
    s_expert, s_token, s_weight = expert[order], token[order], weight[order]
    counts = jnp.bincount(expert, length=N_EXPERTS).astype(jnp.int32)
    starts = jnp.cumsum(counts) - counts
    padded = ((counts + MOE_BLOCK - 1) // MOE_BLOCK) * MOE_BLOCK
    pad_ends = jnp.cumsum(padded)
    pad_starts = pad_ends - padded
    rank = jnp.arange(n_assign, dtype=jnp.int32) - starts[s_expert]
    dest = pad_starts[s_expert] + rank
    n_rows = (-(-n_assign // MOE_BLOCK) + N_EXPERTS) * MOE_BLOCK
    n_blocks = n_rows // MOE_BLOCK
    row_token = jnp.zeros((n_rows,), jnp.int32).at[dest].set(s_token)
    row_weight = jnp.zeros((n_rows,), jnp.float32).at[dest].set(s_weight)
    block_start = jnp.arange(n_blocks, dtype=jnp.int32) * MOE_BLOCK
    block_expert = jnp.minimum(jnp.searchsorted(pad_ends, block_start, side="right"),
                               N_EXPERTS - 1)
    xb = xf[row_token].reshape(n_blocks, MOE_BLOCK, d)

    def expert_block(args):
        xs, e = args
        return (jax.nn.silu(xs @ w_gate[e]) * (xs @ w_up[e])) @ w_down[e]

    yb = lax.map(expert_block, (xb, block_expert))
    y_rows = yb.reshape(n_rows, d) * row_weight[:, None].astype(x.dtype)
    out = jnp.zeros_like(xf).at[row_token].add(y_rows)
    return out.reshape(bn, s, d)

def first_inputs(seed: int = 0) -> dict:
    key = jax.random.key(seed)
    ks = jax.random.split(key, 40)
    L = DEPTH
    n_dense = (DEPTH + 1) // 2
    n_moe = DEPTH // 2
    beta = (8.0 * DEPTH) ** -0.25
    D, W = D_MODEL, RWKV_WIDTH

    def nrm(k, shape, scale):
        return jax.random.normal(k, shape, jnp.float32) * scale

    w0_base = -6.0 + 5.0 * (jnp.arange(W, dtype=jnp.float32) / (W - 1)) ** 0.9
    return {
        "x": nrm(ks[0], (BATCH, SEQ, D), 1.0),
        "w_in": nrm(ks[1], (L, D, IN_COLS), D ** -0.5),
        "rwkv_mu": jax.random.uniform(ks[2], (L, RWKV_COLS), jnp.float32),
        "rwkv_w0": w0_base + nrm(ks[3], (L, W), 0.1),
        "rwkv_w2": nrm(ks[4], (L, DECAY_LORA, W), 0.1 * DECAY_LORA ** -0.5),
        "rwkv_a0": nrm(ks[5], (L, W), 0.1),
        "rwkv_a2": nrm(ks[6], (L, AAA_LORA, W), AAA_LORA ** -0.5),
        "rwkv_g2": nrm(ks[7], (L, GATE_LORA, W), GATE_LORA ** -0.5),
        "rwkv_k_k": 0.85 + nrm(ks[8], (L, W), 0.02),
        "rwkv_k_a": 1.0 + nrm(ks[9], (L, W), 0.02),
        "rwkv_r_k": nrm(ks[10], (L, RWKV_HEADS, RWKV_HEAD_DIM), 0.1),
        "rwkv_ln_g": 1.0 + nrm(ks[11], (L, W), 0.02),
        "rwkv_ln_b": nrm(ks[12], (L, W), 0.02),
        "rwkv_w_o": nrm(ks[13], (L, W, D), W ** -0.5),
        "conf_dw": nrm(ks[14], (L, CONF_CONV_WIDTH, CONF_WIDTH), CONF_CONV_WIDTH ** -0.5),
        "conf_dw_b": nrm(ks[15], (L, CONF_WIDTH), 0.02),
        "conf_ln_g": 1.0 + nrm(ks[16], (L, CONF_WIDTH), 0.02),
        "conf_ln_b": nrm(ks[17], (L, CONF_WIDTH), 0.02),
        "conf_w_o": nrm(ks[18], (L, CONF_WIDTH, D), CONF_WIDTH ** -0.5),
        "short_dw": nrm(ks[19], (L, SHORT_CONV_WIDTH, SHORT_WIDTH), SHORT_CONV_WIDTH ** -0.5),
        "short_w_o": nrm(ks[20], (L, SHORT_WIDTH, D), SHORT_WIDTH ** -0.5),
        "w_out": nrm(ks[21], (L, D, D), beta * D ** -0.5),
        "ln1_g": 1.0 + nrm(ks[22], (L, D), 0.02),
        "ln1_b": nrm(ks[23], (L, D), 0.02),
        "ffn_w_gate": nrm(ks[24], (n_dense, D, D_FF), D ** -0.5),
        "ffn_w_up": nrm(ks[25], (n_dense, D, D_FF), D ** -0.5),
        "ffn_w_down": nrm(ks[26], (n_dense, D_FF, D), beta * D_FF ** -0.5),
        "moe_router": nrm(ks[27], (n_moe, D, N_EXPERTS), D ** -0.5),
        "moe_w_gate": nrm(ks[28], (n_moe, N_EXPERTS, D, EXPERT_FF), D ** -0.5),
        "moe_w_up": nrm(ks[29], (n_moe, N_EXPERTS, D, EXPERT_FF), D ** -0.5),
        "moe_w_down": nrm(ks[30], (n_moe, N_EXPERTS, EXPERT_FF, D), beta * EXPERT_FF ** -0.5),
        "ln2_g": 1.0 + nrm(ks[31], (L, D), 0.02),
        "ln2_b": nrm(ks[32], (L, D), 0.02),
    }

def first_block(x, w_in, rwkv_mu, rwkv_w0, rwkv_w2, rwkv_a0, rwkv_a2, rwkv_g2, rwkv_k_k,
              rwkv_k_a, rwkv_r_k, rwkv_ln_g, rwkv_ln_b, rwkv_w_o, conf_dw, conf_dw_b,
              conf_ln_g, conf_ln_b, conf_w_o, short_dw, short_w_o, w_out, ln1_g, ln1_b,
              ffn_w_gate, ffn_w_up, ffn_w_down, moe_router, moe_w_gate, moe_w_up,
              moe_w_down, ln2_g, ln2_b):
    alpha = (2.0 * DEPTH) ** 0.25
    for i in range(DEPTH):
        mix = _hybrid_mixer(x, w_in[i], rwkv_mu[i], rwkv_w0[i], rwkv_w2[i], rwkv_a0[i],
                            rwkv_a2[i], rwkv_g2[i], rwkv_k_k[i], rwkv_k_a[i], rwkv_r_k[i],
                            rwkv_ln_g[i], rwkv_ln_b[i], rwkv_w_o[i], conf_dw[i], conf_dw_b[i],
                            conf_ln_g[i], conf_ln_b[i], conf_w_o[i], short_dw[i],
                            short_w_o[i], w_out[i])
        x = _layernorm(alpha * x + mix, ln1_g[i], ln1_b[i])
        j = i // 2
        if i % 2 == 0:
            f = _swiglu(x, ffn_w_gate[j], ffn_w_up[j], ffn_w_down[j])
        else:
            f = _moe_swiglu(x, moe_router[j], moe_w_gate[j], moe_w_up[j], moe_w_down[j])
        x = _layernorm(alpha * x + f, ln2_g[i], ln2_b[i])
    return x


HEAD_DIM = 64
ROPE_THETA = 10000.0
EPS = 1e-6
NEG = -1e30
D_FF_2 = 4 * D_MODEL
N_MEM = 256
MEM_HEADS = 4
NSA_HEADS = 12
NSA_KV_HEADS = 3
NSA_GQA = NSA_HEADS // NSA_KV_HEADS
CMP_BLOCK = 32
CMP_STRIDE = 16
CMP_HIDDEN = 256
SEL_BLOCK = 64
SEL_TOPK = 16
WINDOW = 512
NSA_Q_BLOCK = 32
SEL_FORCE = 1e9
DIL_PATTERNS = ((128, 1), (512, 4), (2048, 16))
N_DIL_GROUPS = 3
DIL_SLOTS = 8
DIL_Q_BLOCK = 64
N_A_LAYERS = DEPTH // 2
N_B_LAYERS = DEPTH - N_A_LAYERS
MEM_W = MEM_HEADS * HEAD_DIM
A_Q = NSA_HEADS * HEAD_DIM
A_KV = NSA_KV_HEADS * HEAD_DIM
A_GATES = 3 * NSA_HEADS
A_IN = A_Q + 6 * A_KV + MEM_W + A_GATES
A_OUT = A_Q + MEM_W
A_SPLITS = (A_Q, A_Q + A_KV, A_Q + 2 * A_KV, A_Q + 3 * A_KV, A_Q + 4 * A_KV, A_Q + 5 * A_KV, A_Q + 6 * A_KV, A_Q + 6 * A_KV + MEM_W)
B_Q = N_DIL_GROUPS * DIL_SLOTS * HEAD_DIM
B_IN = B_Q + MEM_W
B_OUT = DIL_SLOTS * HEAD_DIM + MEM_W
SHARED_KV = 2 * DIL_SLOTS * HEAD_DIM


def rmsnorm(x, g):
    x32 = x.astype(jnp.float32)
    y = x32 * lax.rsqrt(jnp.mean(x32 * x32, axis=-1, keepdims=True) + EPS)
    return (y * g.astype(jnp.float32)).astype(x.dtype)

def rope(x, pos):
    half = x.shape[-1] // 2
    inv_freq = ROPE_THETA ** (-jnp.arange(half, dtype=jnp.float32) / half)
    ang = jnp.asarray(pos, jnp.float32)[:, None] * inv_freq[None, :]
    cos = jnp.cos(ang).astype(x.dtype)
    sin = jnp.sin(ang).astype(x.dtype)
    x1, x2 = x[..., :half], x[..., half:]
    return jnp.concatenate([x1 * cos - x2 * sin, x1 * sin + x2 * cos], axis=-1)

def split_heads(x, n):
    b, s, _ = x.shape
    return x.reshape(b, s, n, HEAD_DIM).transpose(0, 2, 1, 3)

def merge_heads(x):
    b, h, s, d = x.shape
    return x.transpose(0, 2, 1, 3).reshape(b, s, h * d)

def chunk_seq(x, axis, size):
    shp = x.shape
    x = x.reshape(shp[:axis] + (shp[axis] // size, size) + shp[axis + 1:])
    return jnp.moveaxis(x, axis, 0)

def unchunk_seq(y, axis):
    y = jnp.moveaxis(y, 0, axis)
    shp = y.shape
    return y.reshape(shp[:axis] + (shp[axis] * shp[axis + 1],) + shp[axis + 2:])

def masked_softmax(s, mask):
    return jax.nn.softmax(jnp.where(mask, s.astype(jnp.float32), NEG), axis=-1)

def nsa_attention(q, k_cmp, v_cmp, k_sel, v_sel, k_win, v_win, gate_logits,
                  q_norm, k_norm, cmp_pos, cmp_w1, cmp_b1, cmp_w2, cmp_b2):
    B, S, _ = q.shape
    G, R, D, QB = NSA_KV_HEADS, NSA_GQA, HEAD_DIM, NSA_Q_BLOCK
    scale = D ** -0.5
    pos = jnp.arange(S)
    q = rope(rmsnorm(split_heads(q, NSA_HEADS), q_norm), pos).reshape(B, G, R, S, D)
    k_sel = rope(rmsnorm(split_heads(k_sel, G), k_norm[1]), pos)
    v_sel = split_heads(v_sel, G)
    k_win = rope(rmsnorm(split_heads(k_win, G), k_norm[2]), pos)
    v_win = split_heads(v_win, G)

    n_cmp = (S - CMP_BLOCK) // CMP_STRIDE + 1
    blk_tok = np.arange(n_cmp)[:, None] * CMP_STRIDE + np.arange(CMP_BLOCK)[None, :]
    cmp_end = jnp.asarray(blk_tok[:, -1], jnp.int32)

    def compress(t, i):
        tb = (t[:, :, blk_tok] + cmp_pos[i]).reshape(B, G, n_cmp, CMP_BLOCK * D)
        return jax.nn.gelu(tb @ cmp_w1[i] + cmp_b1[i]) @ cmp_w2[i] + cmp_b2[i]

    k_c = rope(rmsnorm(compress(split_heads(k_cmp, G), 0), k_norm[0]), cmp_end)
    v_c = compress(split_heads(v_cmp, G), 1)

    n_blk = S // SEL_BLOCK
    n_sel = min(SEL_TOPK, n_blk)
    c_start = np.arange(n_cmp)[:, None] * CMP_STRIDE
    b_start = np.arange(n_blk)[None, :] * SEL_BLOCK
    overlap = jnp.asarray((c_start < b_start + SEL_BLOCK) & (c_start + CMP_BLOCK > b_start), jnp.float32)
    k_sel_blk = k_sel.reshape(B, G, n_blk, SEL_BLOCK, D)
    v_sel_blk = v_sel.reshape(B, G, n_blk, SEL_BLOCK, D)
    k_win_pad = jnp.pad(k_win, ((0, 0), (0, 0), (WINDOW, 0), (0, 0)))
    v_win_pad = jnp.pad(v_win, ((0, 0), (0, 0), (WINDOW, 0), (0, 0)))
    b_ix = jnp.arange(B)[:, None, None, None]
    g_ix = jnp.arange(G)[None, :, None, None]
    blk_ids = jnp.arange(n_blk)

    gates = jax.nn.sigmoid(gate_logits).reshape(B, S, NSA_HEADS, 3)
    gates = gates.transpose(0, 2, 1, 3).reshape(B, G, R, S, 3)

    def block(args):
        c, q_b, g_b = args
        t = c * QB + jnp.arange(QB)
        m_c = cmp_end[None, :] <= t[:, None]
        p_c = masked_softmax(jnp.einsum('bgrqd,bgcd->bgrqc', q_b, k_c) * scale, m_c)
        o_c = jnp.einsum('bgrqc,bgcd->bgrqd', p_c.astype(v_c.dtype), v_c)
        o_c = jnp.where(m_c.any(-1)[:, None], o_c, 0)
        imp = jnp.einsum('bgqc,cj->bgqj', p_c.sum(axis=2), overlap)
        cur = (t // SEL_BLOCK)[:, None]
        forced = (blk_ids == 0) | (blk_ids == cur) | (blk_ids == cur - 1)
        imp = jnp.where(forced, SEL_FORCE, jnp.where(blk_ids <= cur, imp, NEG))
        top_v, top_i = lax.top_k(imp, n_sel)
        k_g = k_sel_blk[b_ix, g_ix, top_i].reshape(B, G, QB, n_sel * SEL_BLOCK, D)
        v_g = v_sel_blk[b_ix, g_ix, top_i].reshape(B, G, QB, n_sel * SEL_BLOCK, D)
        key_pos = top_i[..., None] * SEL_BLOCK + jnp.arange(SEL_BLOCK)
        m_s = (key_pos <= t[:, None, None]) & (top_v > NEG / 2)[..., None]
        m_s = m_s.reshape(B, G, 1, QB, n_sel * SEL_BLOCK)
        p_s = masked_softmax(jnp.einsum('bgrqd,bgqkd->bgrqk', q_b, k_g) * scale, m_s)
        o_s = jnp.einsum('bgrqk,bgqkd->bgrqd', p_s.astype(v_g.dtype), v_g)
        k_b = lax.dynamic_slice_in_dim(k_win_pad, c * QB, QB + WINDOW, axis=2)
        v_b = lax.dynamic_slice_in_dim(v_win_pad, c * QB, QB + WINDOW, axis=2)
        kpos = c * QB - WINDOW + jnp.arange(QB + WINDOW)
        dist = t[:, None] - kpos[None, :]
        m_w = (kpos[None, :] >= 0) & (dist >= 0) & (dist < WINDOW)
        p_w = masked_softmax(jnp.einsum('bgrqd,bgkd->bgrqk', q_b, k_b) * scale, m_w)
        o_w = jnp.einsum('bgrqk,bgkd->bgrqd', p_w.astype(v_b.dtype), v_b)
        return g_b[..., 0:1] * o_c + g_b[..., 1:2] * o_s + g_b[..., 2:3] * o_w

    n_chunks = S // QB
    out = lax.map(block, (jnp.arange(n_chunks), chunk_seq(q, 3, QB), chunk_seq(gates, 3, QB)))
    out = unchunk_seq(out, 3).reshape(B, NSA_HEADS, S, D)
    return merge_heads(out)

def dilated_attention(q, k, v, q_norm):
    B, S, _ = q.shape
    H, D, QB = DIL_SLOTS, HEAD_DIM, DIL_Q_BLOCK
    scale = D ** -0.5
    q = q.reshape(B, S, N_DIL_GROUPS, H, D).transpose(0, 2, 3, 1, 4)
    q = rope(rmsnorm(q, q_norm[:, None, None, :]), jnp.arange(S))

    def block(args):
        c, q_b = args
        t = c * QB + jnp.arange(QB)
        outs, lses = [], []
        for gi, (window, dil) in enumerate(DIL_PATTERNS):
            n_k = window // dil + 1
            idx = t[:, None] - dil * jnp.arange(n_k)[None, :]
            valid = idx >= 0
            idx = jnp.maximum(idx, 0)
            k_g = jnp.take(k, idx, axis=2)
            v_g = jnp.take(v, idx, axis=2)
            s = jnp.einsum('bhqd,bhqkd->bhqk', q_b[:, gi], k_g).astype(jnp.float32) * scale
            s = jnp.where(valid, s, NEG)
            lse = jax.nn.logsumexp(s, axis=-1, keepdims=True)
            p = jnp.exp(s - lse)
            outs.append(jnp.einsum('bhqk,bhqkd->bhqd', p.astype(v.dtype), v_g))
            lses.append(lse)
        wts = jax.nn.softmax(jnp.stack(lses), axis=0).astype(v.dtype)
        return jnp.sum(jnp.stack(outs) * wts, axis=0)

    out = lax.map(block, (jnp.arange(S // QB), chunk_seq(q, 3, QB)))
    return merge_heads(unchunk_seq(out, 2))

def memory_attention(q, mem_kv, q_norm, k_norm):
    scale = HEAD_DIM ** -0.5
    q = rmsnorm(split_heads(q, MEM_HEADS), q_norm)
    k, v = jnp.split(mem_kv, 2, axis=-1)
    k = rmsnorm(split_heads(k, MEM_HEADS), k_norm)
    v = split_heads(v, MEM_HEADS)
    p = jax.nn.softmax(jnp.einsum('bhqd,bhmd->bhqm', q, k).astype(jnp.float32) * scale, axis=-1)
    return merge_heads(jnp.einsum('bhqm,bhmd->bhqd', p.astype(v.dtype), v))

def squared_relu_mlp(h, w_up, w_down):
    return jnp.square(jax.nn.relu(h @ w_up)) @ w_down

def second_inputs(seed: int = 0) -> dict:
    key = jax.random.key(seed)
    keys = jax.random.split(key, 25)
    cnt = [0]

    def nk():
        k = keys[cnt[0]]
        cnt[0] += 1
        return k

    def normal(shape, scale):
        return scale * jax.random.normal(nk(), shape, jnp.float32)

    def gain(shape):
        return 1.0 + 0.05 * jax.random.normal(nk(), shape, jnp.float32)

    NA, NB = N_A_LAYERS, N_B_LAYERS
    return {
        "x": normal((BATCH, SEQ, D_MODEL), 1.0),
        "mem": normal((BATCH, N_MEM, D_MODEL), 1.0),
        "attn_norm": gain((DEPTH, D_MODEL)),
        "mlp_norm": gain((DEPTH, D_MODEL)),
        "w_up": normal((DEPTH, D_MODEL, D_FF_2), D_MODEL ** -0.5),
        "w_down": normal((DEPTH, D_FF_2, D_MODEL), D_FF_2 ** -0.5),
        "mem_norm": gain((DEPTH, D_MODEL)),
        "w_mem_kv": normal((DEPTH, D_MODEL, 2 * MEM_W), D_MODEL ** -0.5),
        "mem_q_norm": gain((DEPTH, HEAD_DIM)),
        "mem_k_norm": gain((DEPTH, HEAD_DIM)),
        "a_w_in": normal((NA, D_MODEL, A_IN), D_MODEL ** -0.5),
        "a_w_out": normal((NA, A_OUT, D_MODEL), A_OUT ** -0.5),
        "a_q_norm": gain((NA, HEAD_DIM)),
        "a_k_norm": gain((NA, 3, HEAD_DIM)),
        "a_cmp_pos": normal((NA, 2, CMP_BLOCK, HEAD_DIM), 0.1),
        "a_cmp_w1": normal((NA, 2, CMP_BLOCK * HEAD_DIM, CMP_HIDDEN), (CMP_BLOCK * HEAD_DIM) ** -0.5),
        "a_cmp_b1": normal((NA, 2, CMP_HIDDEN), 0.01),
        "a_cmp_w2": normal((NA, 2, CMP_HIDDEN, HEAD_DIM), CMP_HIDDEN ** -0.5),
        "a_cmp_b2": normal((NA, 2, HEAD_DIM), 0.01),
        "kv_norm": gain((D_MODEL,)),
        "w_kv_shared": normal((D_MODEL, SHARED_KV), D_MODEL ** -0.5),
        "kv_k_norm": gain((HEAD_DIM,)),
        "b_w_in": normal((NB, D_MODEL, B_IN), D_MODEL ** -0.5),
        "b_w_out": normal((NB, B_OUT, D_MODEL), B_OUT ** -0.5),
        "b_q_norm": gain((NB, N_DIL_GROUPS, HEAD_DIM)),
    }

def second_block(x, mem, attn_norm, mlp_norm, w_up, w_down, mem_norm, w_mem_kv, mem_q_norm, mem_k_norm,
              a_w_in, a_w_out, a_q_norm, a_k_norm, a_cmp_pos, a_cmp_w1, a_cmp_b1, a_cmp_w2, a_cmp_b2,
              kv_norm, w_kv_shared, kv_k_norm, b_w_in, b_w_out, b_q_norm):
    pos = jnp.arange(x.shape[1])
    k_shared = None
    v_shared = None
    for layer in range(DEPTH):
        h = rmsnorm(x, attn_norm[layer])
        mem_kv = rmsnorm(mem, mem_norm[layer]) @ w_mem_kv[layer]
        if layer < N_A_LAYERS:
            i = layer
            q, kc, vc, ks, vs, kw, vw, q_mem, gl = jnp.split(h @ a_w_in[i], A_SPLITS, axis=-1)
            o_main = nsa_attention(q, kc, vc, ks, vs, kw, vw, gl, a_q_norm[i], a_k_norm[i],
                                   a_cmp_pos[i], a_cmp_w1[i], a_cmp_b1[i], a_cmp_w2[i], a_cmp_b2[i])
            o_mem = memory_attention(q_mem, mem_kv, mem_q_norm[layer], mem_k_norm[layer])
            x = x + jnp.concatenate([o_main, o_mem], axis=-1) @ a_w_out[i]
        else:
            i = layer - N_A_LAYERS
            if i == 0:
                k_s, v_s = jnp.split(rmsnorm(x, kv_norm) @ w_kv_shared, 2, axis=-1)
                k_shared = rope(rmsnorm(split_heads(k_s, DIL_SLOTS), kv_k_norm), pos)
                v_shared = split_heads(v_s, DIL_SLOTS)
            q, q_mem = jnp.split(h @ b_w_in[i], [B_Q], axis=-1)
            o_main = dilated_attention(q, k_shared, v_shared, b_q_norm[i])
            o_mem = memory_attention(q_mem, mem_kv, mem_q_norm[layer], mem_k_norm[layer])
            x = x + jnp.concatenate([o_main, o_mem], axis=-1) @ b_w_out[i]
        x = x + squared_relu_mlp(rmsnorm(x, mlp_norm[layer]), w_up[layer], w_down[layer])
    return x


def setup_inputs(seed=0):
    out = dict(first_inputs(seed))
    for name, value in second_inputs(seed + 1).items():
        if name != "x":
            out[name + "_2"] = value
    return out


def reference(
    x, w_in, rwkv_mu, rwkv_w0, rwkv_w2, rwkv_a0, rwkv_a2, rwkv_g2, rwkv_k_k, rwkv_k_a, rwkv_r_k,
    rwkv_ln_g, rwkv_ln_b, rwkv_w_o, conf_dw, conf_dw_b, conf_ln_g, conf_ln_b, conf_w_o,
    short_dw, short_w_o, w_out, ln1_g, ln1_b, ffn_w_gate, ffn_w_up, ffn_w_down, moe_router,
    moe_w_gate, moe_w_up, moe_w_down, ln2_g, ln2_b, mem_2, attn_norm_2, mlp_norm_2, w_up_2,
    w_down_2, mem_norm_2, w_mem_kv_2, mem_q_norm_2, mem_k_norm_2, a_w_in_2, a_w_out_2,
    a_q_norm_2, a_k_norm_2, a_cmp_pos_2, a_cmp_w1_2, a_cmp_b1_2, a_cmp_w2_2, a_cmp_b2_2,
    kv_norm_2, w_kv_shared_2, kv_k_norm_2, b_w_in_2, b_w_out_2, b_q_norm_2,
):
    x = first_block(
        x, w_in, rwkv_mu, rwkv_w0, rwkv_w2, rwkv_a0, rwkv_a2, rwkv_g2, rwkv_k_k, rwkv_k_a,
        rwkv_r_k, rwkv_ln_g, rwkv_ln_b, rwkv_w_o, conf_dw, conf_dw_b, conf_ln_g, conf_ln_b,
        conf_w_o, short_dw, short_w_o, w_out, ln1_g, ln1_b, ffn_w_gate, ffn_w_up, ffn_w_down,
        moe_router, moe_w_gate, moe_w_up, moe_w_down, ln2_g, ln2_b,
    )
    return second_block(
        x, mem_2, attn_norm_2, mlp_norm_2, w_up_2, w_down_2, mem_norm_2, w_mem_kv_2,
        mem_q_norm_2, mem_k_norm_2, a_w_in_2, a_w_out_2, a_q_norm_2, a_k_norm_2, a_cmp_pos_2,
        a_cmp_w1_2, a_cmp_b1_2, a_cmp_w2_2, a_cmp_b2_2, kv_norm_2, w_kv_shared_2, kv_k_norm_2,
        b_w_in_2, b_w_out_2, b_q_norm_2,
    )


_drawn_inputs = setup_inputs


def setup_inputs(seed=0):
    import zlib

    import numpy as np

    out = dict(_drawn_inputs(seed))
    spreads = {}
    factors = {'rwkv_w2': 8.0,
     'rwkv_a0': 3.416,
     'rwkv_k_k': 8.0,
     'rwkv_k_a': 7.968,
     'rwkv_ln_g': 5.531,
     'rwkv_ln_b': 8.0,
     'conf_dw_b': 3.36,
     'conf_ln_g': 8.0,
     'conf_ln_b': 4.34,
     'attn_norm_2': 3.041,
     'mem_norm_2': 8.0,
     'mem_q_norm_2': 8.0,
     'mem_k_norm_2': 8.0,
     'a_q_norm_2': 6.576,
     'a_k_norm_2': 7.262,
     'a_cmp_b1_2': 8.0,
     'a_cmp_b2_2': 8.0,
     'kv_norm_2': 4.416,
     'kv_k_norm_2': 8.0,
     'b_q_norm_2': 8.0}
    for name, (base, spread) in spreads.items():
        noise = np.random.default_rng([zlib.crc32(name.encode()), seed]).standard_normal(out[name].shape)
        drawn = base * np.exp(spread * noise) if base else spread * noise
        out[name] = __import__('jax').numpy.asarray(drawn.astype(out[name].dtype))
    for name, factor in factors.items():
        out[name] = (out[name] * factor).astype(out[name].dtype)
    return out
```

```python
from contextlib import ExitStack

import concourse.bass as bass
from concourse import mybir
import numpy as np

F32 = mybir.dt.float32
ALU = mybir.AluOpType
ACT = mybir.ActivationFunctionType
AX = mybir.AxisListType

P = 128
D = 1024
T = 256
TT = T // P
KB = D // P
DEPTH = 2
ALPHA = (2.0 * DEPTH) ** 0.25
HEAD = 64

W = 512
RH = W // HEAD
NC = W // P
KAPPA = float(np.exp(-0.5))
CHUNK = 64
CONF = 256
CONF_TAPS = 31
SHORT = 256
SHORT_TAPS = 3
RWKV_BLOCKS = 14
N_EXPERTS = 8
D_FF = 2816
D_FF_2 = 4096
FCH = 256
LN_EPS = 1e-5
GN_EPS = 64e-5
RMS_EPS = 1e-6

NSA_HEADS = 12
NSA_G = 3
NSA_R = NSA_HEADS // NSA_G
MEM_HEADS = 4
N_CMP = 15
CMP_BLOCK = 32
CMP_STRIDE = 16
CMP_HIDDEN = 256
DIL = ((128, 1), (512, 4), (2048, 16))
SLOTS = 8
SCALE = HEAD ** -0.5
NEG = -1e30
ROPE_THETA = 10000.0

PANEL = 2048
RING = 3
PC = PANEL // KB
PR = PANEL // D


class Fields:

    def __init__(self, *sizes):
        self.at, self.n = {}, 0
        for name, n in sizes:
            self.at[name] = (self.n, n)
            self.n += n

    def __getitem__(self, name):
        a, n = self.at[name]
        return slice(a, a + n)


COLS = Fields(*[(f"{name}{l}", n) for l in range(DEPTH) for name, n in (
    ("mu", RWKV_BLOCKS), ("a0", NC), ("k_k", NC), ("k_a", NC), ("r_k", NC), ("gn_g", NC), ("gn_b", NC),
    ("conf_dw", 2 * CONF_TAPS), ("conf_dw_b", 2), ("conf_ln_g", 2), ("conf_ln_b", 2),
    ("short_dw", 2 * SHORT_TAPS), ("attn_norm", KB), ("mlp_norm", KB), ("mem_norm", KB))],
    ("kv_norm", KB), ("cmp_b1", 4), ("cmp_pos", 2 * CMP_BLOCK // 2))
MIDS = Fields(*[(f"{name}{l}", W) for l in range(DEPTH) for name in ("w2a2", "g2")],
              ("router", KB * N_EXPERTS), ("cmp_w2", 2 * 2 * HEAD))
ROWS = Fields(("w00", W), ("w01", W), ("a_q", HEAD), ("a_k", 3 * HEAD), ("mem_q0", HEAD), ("mem_q1", HEAD),
              ("mem_k0", HEAD), ("mem_k1", HEAD), ("cmp_b2", 2 * HEAD), ("kv_k", HEAD), ("b_q", 3 * HEAD))
CONST = Fields(("ident", P), ("ones", P), ("heads", P), ("tri", 2 * P), ("unit_mask", 4 * P), ("inv_mask", 3 * P),
               ("earlier", N_EXPERTS * N_EXPERTS), ("ln_eps", 1), ("gn_eps", 1), ("rms_eps", 1))
ATTN = Fields(("causal", 3 * P), ("dil0", 3 * P), ("dil1", 3 * T), ("cmp", TT * 16), ("cmp_ok", TT),
              ("cos", TT * 32), ("sin", TT * 32), ("cmp_cos", 32), ("cmp_sin", 32))


def shape_constants():
    c = np.zeros((P, CONST.n), np.float32)
    i, j = np.arange(P)[:, None], np.arange(P)[None, :]

    def same(n):
        return i // n == j // n

    c[:, CONST["ident"]] = i == j
    c[:, CONST["ones"]] = 1
    c[:, CONST["heads"]] = same(HEAD)
    up, up_eq, low = same(CHUNK) & (i < j), same(CHUNK) & (i <= j), same(CHUNK) & (i > j)
    c[:, CONST["tri"]] = np.concatenate([up_eq, up], 1)
    c[:, CONST["unit_mask"]] = np.concatenate([up & same(16), up_eq, up, up_eq], 1)
    c[:, CONST["inv_mask"]] = np.concatenate([low & same(16), low & same(32) & ~same(16), low & ~same(32)], 1)
    e = np.arange(N_EXPERTS)
    c[:, CONST["earlier"]] = (e[None, :] < e[:, None]).reshape(1, -1)
    c[:, CONST["ln_eps"]], c[:, CONST["gn_eps"]], c[:, CONST["rms_eps"]] = LN_EPS, GN_EPS, RMS_EPS

    a = np.zeros((P, ATTN.n), np.float32)
    causal = np.where(j <= i, 0, NEG)
    a[:, ATTN["causal"]] = np.concatenate([causal, np.zeros((P, P)), causal], 1)
    t, s = np.arange(T)[:, None], np.arange(T)[None, :]
    dil = [np.where((s <= t) & ((t - s) % d == 0) & (t - s <= w), 0, NEG) for w, d in DIL]
    a[:, ATTN["dil0"]] = np.concatenate([m[:P, :P] for m in dil], 1)
    a[:, ATTN["dil1"]] = np.concatenate([m[P:] for m in dil], 1)
    end = np.arange(N_CMP) * CMP_STRIDE + CMP_BLOCK - 1
    ok = np.zeros((T, 16), bool)
    ok[:, :N_CMP] = end[None, :] <= t
    a[:, ATTN["cmp"]] = np.where(ok, 0, NEG).reshape(TT, P, 16).transpose(1, 0, 2).reshape(P, -1)
    a[:, ATTN["cmp_ok"]] = ok.any(1).reshape(TT, P).T
    freq = ROPE_THETA ** (-np.arange(32, dtype=np.float32) / 32)

    def turns(pos):
        return np.asarray(pos, np.float32)[:, None] * freq.astype(np.float32)[None, :]

    for name, f in (("cos", np.cos), ("sin", np.sin)):
        a[:, ATTN[name]] = f(turns(np.arange(T))).reshape(TT, P, 32).transpose(1, 0, 2).reshape(P, -1)
        a[:N_CMP, ATTN["cmp_" + name]] = f(turns(end))
    return c, a


def chunk_panels(n, parts):
    order = []
    for step in range(n + 1):
        if step < n:
            order += [(p, step) for p in parts[:-1]]
        if step:
            order.append((parts[-1], step - 1))
    return order


def panel_order():
    order = []
    for l in range(DEPTH):
        order += [("w_in", l, n) for n in range(24)] + [("mix", l, n) for n in range(4)]
        order += [("w_out", l, n) for n in range(4)]
        if l == 0:
            order += [(p, 0, n) for p, n in chunk_panels(D_FF // FCH, ("gate", "up", "down"))]
        else:
            order += [(p, 1, n) for p, n in chunk_panels(N_EXPERTS * D_FF // FCH, ("gate", "up", "down"))]
    for l in range(DEPTH):
        order += [("mem_kv", l, n) for n in range(2)]
        if l == 0:
            order += [("a_in", 0, n) for n in range(9)] + [("cmp", 0, n) for n in range(4)]
            order += [("a_out", 0, n) for n in range(4)]
        else:
            order += [("kv", 1, n) for n in range(4)] + [("b_in", 1, n) for n in range(7)]
            order += [("b_out", 1, n) for n in range(3)]
        order += [(p, l, n) for p, n in chunk_panels(D_FF_2 // FCH, ("mlp_up", "mlp_down"))]
    return order


ORDER = panel_order()
N_PANELS = len(ORDER)
N_CHUNKS = (1 + N_EXPERTS) * (D_FF // FCH) + DEPTH * (D_FF_2 // FCH)


class Made:

    def __init__(self):
        self.count = {}

    def next(self, name):
        self.count[name] = self.count.get(name, 0) + 1
        return self.count[name]


class PanelReader:

    def __init__(self, pe, ring, landed, used):
        self.pe, self.ring, self.landed, self.used = pe, ring, landed, used
        self.n, self.give_back = 0, False

    def take(self, turn=0, per_turn=0):
        slot, fill = self.n % RING, self.n // RING + 1
        self.pe.wait_ge(self.landed[slot], (turn * (per_turn // RING) + fill) * 16)
        self.give_back = self.n > 0
        self.n += 1
        return self.ring[:, slot, :]

    def skip(self, n):
        assert n % RING == 0
        self.n += n

    def mm(self, out, lhsT, rhs, start, stop):
        ins = self.pe.matmul(out, lhsT, rhs, start=start, stop=stop)
        if self.give_back:
            ins.then_inc(self.used, 1)
            self.give_back = False
        return ins


SIGNALS = """
consts_in params_in ln_rows_in mem_in x_in out_stored panel_used cleared
dve_step act_step 
x_turned xT_dve xT_act
proj_out proj_read shifted 
lora_in lora_z lora_a lora_g decay_in aaa gate_lora
cum_mm decays kk_sq kk_mm kk_norm features bonus_in bonus_mm
turn_mm turned_dve turned_act unit_mm masks inv_mm inv_dve inv_act rhs_mm rhs u_mm u state_mm state o_mm o_read
gn_mean_mm gn_sq gn_var_mm gn_std branch_a conf_conv conf_mean_mm conf_sq conf_var_mm conf_std branch_b conf_silu branch_c
mix_mm mixed wout_mm ln_x ln_std ln_x_done
router_mm router_w router_exp gu_full act_out h_ready y_full y_read
rms_ss rms_std rms_x attn_proj attn_read qk_std qk_ready turnq_mm turnq_dve turnq_act
cmp_h_mm cmp_h cmp_o_mm cmp_tb cmp_kv cmp_k_std cmp_k_ready cmp_kT_mm cmp_kT cmp_s_mm cmp_s cmp_e cmp_p cmp_pT_mm cmp_pT cmp_pv_mm cmp_done
score_mm score_max score_exp pT_mm pT pv_mm pv_read proj2_mm x_done nsa_gates
""".split()


def program(nc, weights, consts, attn_consts, cols, mids, rows, ln_rows, x, mem, out):
    ctx = ExitStack()
    with ctx:
        def sb(name, *shape, stack=ctx):
            return stack.enter_context(nc.sbuf_tensor(name, [P, *shape], F32))

        S = {name: ctx.enter_context(nc.semaphore(name)) for name in SIGNALS}
        landed = [ctx.enter_context(nc.semaphore(f"panel_landed{i}")) for i in range(RING)]
        bank = [ctx.enter_context(nc.psum_tensor(f"bank{i}", [P, 512], F32)) for i in range(8)]

        ring = sb("ring", RING, PANEL)
        x_tm = sb("x_tm", TT, D)
        xT = sb("xT", KB, T)
        cst = sb("cst", CONST.n)
        col = sb("col", COLS.n)
        mid = sb("mid", MIDS.n)
        row = sb("row", ROWS.n)
        ln_row = sb("ln_row", 2, D)
        stat = sb("stat", 64)
        ident = cst[:, CONST["ident"]]
        ones = cst[:, CONST["ones"]]
        head_sum = cst[:, CONST["heads"]]
        tri = cst[:, CONST["tri"]]
        inv_mask = cst[:, CONST["inv_mask"]].rearrange("p (m s) -> p m s", m=3)
        unit_mask = cst[:, CONST["unit_mask"]]

        def c1(name, n=0):
            a = COLS[name].start + n
            return col[:, a:a + 1]

        def eps(name):
            return cst[:, CONST[name]]

        mixer = ExitStack()
        gates = sb("gates", 24, T, stack=mixer)
        pz = sb("pz", 2, 2, T + 1, stack=mixer)
        sh = sb("sh", RWKV_BLOCKS, T, stack=mixer)
        u_pad = sb("u_pad", 2, T + CONF_TAPS - 1, stack=mixer)
        s_pad = sb("s_pad", 2, T + SHORT_TAPS - 1, stack=mixer)
        conf_s = sb("conf_s", 2, T, stack=mixer)
        conv = sb("conv", 2, T, stack=mixer)
        gb = sb("gb", 2, T, stack=mixer)
        conv_c = sb("conv_c", 2, T, stack=mixer)
        a_ = sb("a_", NC, T, stack=mixer)
        kk = sb("kk", NC, T, stack=mixer)
        tmp = sb("tmp", NC, T, stack=mixer)
        p_in = sb("p_in", NC, T, stack=mixer)
        p_inv = sb("p_inv", NC, T, stack=mixer)
        p_ex = sb("p_ex", NC, T, stack=mixer)
        ar = sb("ar", NC, TT, 2, P, stack=mixer)
        vt = sb("vt", TT, W, stack=mixer)
        bt = sb("bt", TT, W, stack=mixer)
        kt = sb("kt", TT, W, stack=mixer)
        g_ = sb("g_", NC, T, stack=mixer)
        unit = sb("unit", RH, 4, P, stack=mixer)
        inv = sb("inv", RH, P, stack=mixer)
        rhs_sb = sb("rhs_sb", RH, HEAD, stack=mixer)
        u_sb = sb("u_sb", RH, HEAD, stack=mixer)
        state = sb("state", NC, 2, HEAD, stack=mixer)
        sh_flat = sh[:].rearrange("p b t -> p (b t)")
        a3 = sh_flat[:, 0:12 * P].rearrange("p (i m s) -> p i m s", i=4, m=3)
        pw = sh_flat[:, 12 * P:28 * P].rearrange("p (m s) -> p m s", m=4)
        xa = sb("xa", 4 * P, stack=mixer)
        xb = sb("xb", 4 * P, stack=mixer)
        loras = sb("loras", 2, T, stack=mixer)
        r_, k_, v_ = (sh[:, n * NC:(n + 1) * NC, :] for n in range(3))
        oT = p_ex
        sg_tok = kt
        yT = p_in
        mixT = sh[:, 0:KB, :]
        conv_sq = gb
        mixer.close()

        mlp = ExitStack()
        gate_s = sb("gate_s", 3, 2, T, stack=mlp)
        hT = sb("hT", 3, 2, T, stack=mlp)
        moe_w = sb("moe_w", TT, N_EXPERTS, stack=mlp)
        moe_cols = sb("moe_cols", TT, N_EXPERTS, D_FF // FCH, stack=mlp)
        rt = sb("rt", 6, N_EXPERTS * N_EXPERTS, stack=mlp)

        attn = ExitStack()
        atc = sb("atc", ATTN.n, stack=attn)
        xn = sb("xn", TT, D, stack=attn)
        proj = sb("proj", TT, 11 * PC, stack=attn)
        mem_kv = sb("mem_kv", TT, 2 * MEM_HEADS * HEAD, stack=attn)
        scr = sb("scr", 2, 24 * HEAD, stack=attn)
        qkT = sb("qkT", 22, T, stack=attn)
        o_tm = sb("o_tm", TT, D, stack=attn)
        p_sb = sb("p_sb", 4, 3 * T, stack=attn)
        pT_sb = sb("pT_sb", 2, 512, stack=attn)
        cmp_in = sb("cmp_in", 2, CMP_BLOCK // 2, NSA_G, N_CMP, stack=attn)
        cmp_h = sb("cmp_h", 2, 2, NSA_G * N_CMP, stack=attn)
        cmp_kv = sb("cmp_kv", 2, NSA_G, HEAD, stack=attn)
        cmp_dup = sb("cmp_dup", NSA_G, 2, HEAD, stack=attn)
        cmp_kT = sb("cmp_kT", NSA_G, 16, stack=attn)
        cmp_s = sb("cmp_s", NSA_HEADS, TT, 16, stack=attn)
        cmp_pT = sb("cmp_pT", 4, P, stack=attn)
        rs = sb("rs", 160, stack=attn)
        coef = sb("coef", 3, NSA_HEADS, TT, stack=attn)
        s_sb, e_sb = p_sb[:, 0:2, :], p_sb[:, 2:4, :]
        twice = p_sb[:].rearrange("p a b -> p (a b)").rearrange("p (t k d e) -> p t k d e", t=TT, d=2, e=HEAD)
        attn.close()
        mlp.close()
        causal = atc[:, ATTN["causal"]]
        MEM_Q = {0: 1920, 1: 1536 + 2 * SLOTS * HEAD}
        B_Q0 = 2 * SLOTS * HEAD

        def head_sets(l):
            mq = proj[:, :, MEM_Q[l]:MEM_Q[l] + MEM_HEADS * HEAD]
            mk = mem_kv[:, :, 0:MEM_HEADS * HEAD]
            rq, rk = ROWS[f"mem_q{l}"].start, ROWS[f"mem_k{l}"].start
            if l == 0:
                k0, q0 = ROWS["a_k"].start, ROWS["a_q"].start
                return [(proj[:, :, 0:768], 12, q0, True, None), (proj[:, :, 1152:1344], 3, k0 + HEAD, True, 0),
                        (proj[:, :, 1536:1728], 3, k0 + 2 * HEAD, True, 3), (mq, 4, rq, False, None), (mk, 4, rk, False, None)]
            sets = [(proj[:, :, B_Q0 + g * 512:B_Q0 + (g + 1) * 512], SLOTS, ROWS["b_q"].start + g * HEAD, True, None) for g in range(3)]
            return sets + [(proj[:, :, 0:512], SLOTS, ROWS["kv_k"].start, True, None), (mq, 4, rq, False, None), (mk, 4, rk, False, None)]

        def turn_items(l, tt):
            def pairs(t, a, n):
                return [t[:, tt, a + i * P:a + (i + 1) * P] for i in range(n)]

            if l == 0:
                dup = [twice[:, tt, k, :, :].rearrange("p d e -> p (d e)") for k in range(12)]
                return pairs(proj, 0, 6) + dup + pairs(proj, MEM_Q[0], 2) + pairs(mem_kv, 0, 2)
            return pairs(proj, B_Q0, 12) + pairs(proj, 0, 4) + pairs(proj, MEM_Q[1], 2) + pairs(mem_kv, 0, 2)

        N_ITEMS = (22, 20)
        BANKS_T = (11, 10)
        MEM_ITEM = (18, 16)

        def units(l):
            if l == 0:
                u = [(kind, h, None) for h in range(NSA_HEADS) for kind in ("sel", "win")]
            else:
                u = [("dil", s, tt) for s in range(SLOTS) for tt in range(TT)]
            return u + [("mem", h, None) for h in range(MEM_HEADS)]

        def blocks_of(kind, tt):
            if kind == "dil":
                n = tt + 1
                return [([g * n * P + k * P for g in range(3)], tt, k) for k in range(n)]
            if kind == "mem":
                return [([(2 * t + k) * P], t, k) for t in range(TT) for k in range(TT)]
            return [([0], 0, 0), ([P], 1, 0), ([2 * P], 1, 1)]

        def values(l, kind, h, k):
            if kind == "mem":
                return mem_kv[:, k, (MEM_HEADS + h) * HEAD:(MEM_HEADS + h + 1) * HEAD]
            a = 512 + h * HEAD if kind == "dil" else {"sel": 1344, "win": 1728}[kind] + h // NSA_R * HEAD
            return proj[:, k, a:a + HEAD]

        block = ctx.enter_context(nc.Block())

        @block.sync
        def _(sp):
            sp.dma_start(x_tm[:], x.rearrange("(t p) d -> p t d", p=P)).then_inc(S["x_in"], 16)
            sp.dma_start(cst[:], consts).then_inc(S["consts_in"], 16)
            for i in range(RING):
                sp.dma_start(ring[:, i, :], weights[i]).then_inc(landed[i], 16)
            rounds = N_PANELS // RING - 1
            with sp.Fori(0, rounds) as turn:
                for i in range(RING):
                    sp.wait_ge(S["panel_used"], turn * RING + (i + 1))
                    sp.dma_start(ring[:, i, :], weights[bass.ds(turn * RING + (RING + i), 1)].rearrange("a p n -> p (a n)")
                                 ).then_inc(landed[i], 16)
            for n in range((rounds + 1) * RING, N_PANELS):
                sp.wait_ge(S["panel_used"], n - RING + 1)
                sp.dma_start(ring[:, n % RING, :], weights[n]).then_inc(landed[n % RING], 16)
            sp.wait_ge(S["y_read"], N_CHUNKS)
            sp.dma_start(out.rearrange("(t p) d -> p t d", p=P), x_tm[:]).then_inc(S["out_stored"], 16)
            sp.wait_ge(S["out_stored"], 16)

        @block.tensor
        def _(pe):
            panels = PanelReader(pe, ring, landed, S["panel_used"])
            mm = panels.mm

            def turn_x(n, src):
                for b in range(4):
                    for kk_ in range(2):
                        for tt in range(TT):
                            f = (2 * b + kk_) * P
                            ins = pe.transpose(bank[b][:, (kk_ * TT + tt) * P:][:, 0:P], src[:, tt, f:f + P], ident)
                    ins.then_inc(S["x_turned"], 1)

            def wait_xT(n):
                pe.wait_ge(S["xT_dve"], 2 * (n + 1))
                pe.wait_ge(S["xT_act"], 2 * (n + 1))

            def project(l, j):
                n = 24 * l + j
                w = panels.take()
                if n >= 2:
                    pe.wait_ge(S["proj_read"], n - 1)
                for m in range(2):
                    for kb in range(KB):
                        ins = mm(bank[n % 2][:, m * T:(m + 1) * T], w[:, kb * PC + m * P:][:, 0:P], xT[:, kb, :],
                                 start=(kb == 0), stop=(kb == KB - 1))
                ins.then_inc(S["proj_out"], 1)

            def mixer_pe(l):
                def project_gate():
                    project(l, gate.pop(0))

                gate = list(range(12, 24))
                wait_xT(2 * l)
                for j in range(12):
                    project(l, j)
                w2a2 = mid[:, MIDS[f"w2a2{l}"]]
                g2 = mid[:, MIDS[f"g2{l}"]]
                pe.wait_ge(S["lora_in"], l + 1)
                for tt in range(TT):
                    pe.matmul(bank[2 + tt][:], loras[0:HEAD, 0, tt * P:(tt + 1) * P], w2a2[0:HEAD, :], start=True, stop=False)
                    ins = pe.matmul(bank[2 + tt][:], ones[0:1, :], row[0:1, ROWS[f"w0{l}"]], start=False, stop=True)
                ins.then_inc(S["lora_z"], 1)
                for c in range(NC):
                    ins = pe.matmul(bank[4 + c // 2][:, (c % 2) * T:][:, 0:T], w2a2[HEAD:P, c * P:(c + 1) * P], sh[HEAD:P, 12, :],
                                    start=True, stop=True)
                ins.then_inc(S["lora_a"], 1)
                for c in range(NC):
                    ins = pe.matmul(bank[6 + c // 2][:, (c % 2) * T:][:, 0:T], g2[:, c * P:(c + 1) * P], loras[:, 1, :],
                                    start=True, stop=True)
                ins.then_inc(S["lora_g"], 1)
                project_gate()
                pe.wait_ge(S["decay_in"], l + 1)
                pe.wait_ge(S["aaa"], l + 1)
                for c in range(NC):
                    for tt in range(TT):
                        ins = pe.matmul(bank[2 + c][:, tt * T:(tt + 1) * T], sg_tok[:, tt, c * P:(c + 1) * P], tri,
                                        start=True, stop=True)
                ins.then_inc(S["cum_mm"], 1)
                pe.wait_ge(S["kk_sq"], l + 1)
                pe.wait_ge(S["gate_lora"], l + 1)
                for c in range(NC):
                    ins = pe.matmul(bank[6 + c // 2][:, (c % 2) * T:][:, 0:T], head_sum, tmp[:, c, :], start=True, stop=True)
                ins.then_inc(S["kk_mm"], 1)
                project_gate()
                project_gate()
                pe.wait_ge(S["bonus_in"], l + 1)
                for c in range(NC):
                    ins = pe.matmul(bank[6 + c // 2][:, (c % 2) * T:][:, 0:T], head_sum, tmp[:, c, :], start=True, stop=True)
                ins.then_inc(S["bonus_mm"], 1)
                pe.wait_ge(S["features"], l + 1)
                pe.wait_ge(S["decays"], l + 1)
                for n, src in enumerate((v_, a_, kk)):
                    for tt in range(TT):
                        b = 2 + (2 * n + tt) % 4
                        if n == 2:
                            pe.wait_ge((S["turned_dve"], S["turned_act"])[tt], 3 * l + 1)
                        for c in range(NC):
                            ins = pe.transpose(bank[b][:, c * P:(c + 1) * P], src[:, c, tt * P:(tt + 1) * P], ident)
                        ins.then_inc(S["turn_mm"], 1)
                pe.wait_ge(S["turned_dve"], 3 * (l + 1))
                pe.wait_ge(S["turned_act"], 3 * (l + 1))
                for tt in range(TT):
                    tok = slice(tt * P, (tt + 1) * P)
                    for hg in range(2):
                        group = 4 * l + 2 * tt + hg
                        if group % 4:
                            pe.wait_ge(S["inv_dve"], 8 * group)
                            pe.wait_ge(S["inv_act"], 6 * group)
                        if tt and not hg:
                            pe.wait_ge(S["state"], 3 * l + 2)
                            pe.wait_ge(S["o_read"], 4 * l + 2)
                        for i in range(4):
                            c, lo = (4 * hg + i) // 2, HEAD * (i % 2)
                            hd = slice(lo, lo + HEAD)
                            pe.matmul(bank[2 + i][:, 0:T], a_[hd, c, tok], ar[hd, c, tt, :, :], start=True, stop=True)
                            pe.matmul(bank[2 + i][:, T:2 * T], kk[hd, c, tok], ar[hd, c, tt, :, :], start=True, stop=True)
                            ins = pe.matmul(bank[6 + i % 2][:, i // 2 * P:][:, 0:P], ar[hd, c, tt, 0, :], a_[hd, c, tok],
                                            start=True, stop=True)
                        ins.then_inc(S["unit_mm"], 1)
                        if gate:
                            project_gate()

                        def four(b, lhs, rhs, turn=False):
                            for i in range(4):
                                o = bank[b][:, i * P:(i + 1) * P]
                                if turn:
                                    ins = pe.transpose(o, lhs(i), ident)
                                else:
                                    ins = pe.matmul(o, lhs(i), rhs(i), start=True, stop=True)
                            ins.then_inc(S["inv_mm"], 1)

                        def part(t):
                            return lambda i: t[:, i * P:(i + 1) * P]

                        def n_1(i):
                            return unit[:, 4 * hg + i, 0, :]

                        def a_1(i):
                            return a3[:, i, 0, :]

                        n_2, a_2, n_4, a_4 = (part(pw[:, m, :]) for m in range(4))
                        a_8, x_odd, x_even = part(pw[:, 0, :]), part(xa), part(xb)
                        turned, g_of = a_2, n_4
                        pe.wait_ge(S["masks"], group + 1)
                        four(2, a_1, n_1)
                        four(3, n_1, a_1)
                        dve, act = 8 * group, 6 * group
                        pe.wait_ge(S["inv_dve"], dve + 1)
                        pe.wait_ge(S["inv_act"], act + 1)
                        four(4, a_2, x_odd)
                        four(5, a_2, n_2)
                        four(6, n_2, a_2)
                        if gate:
                            project_gate()
                        pe.wait_ge(S["inv_dve"], dve + 2)
                        pe.wait_ge(S["inv_act"], act + 3)
                        four(2, a_4, x_even)
                        four(3, n_4, a_4)
                        pe.wait_ge(S["inv_dve"], dve + 3)
                        pe.wait_ge(S["inv_act"], act + 4)
                        four(4, a_8, x_odd)
                        if gate:
                            project_gate()
                        pe.wait_ge(S["inv_dve"], dve + 4)
                        four(2, x_even, None, turn=True)
                        four(3, lambda i: a3[:, i, 1, :], x_even)
                        pe.wait_ge(S["inv_dve"], dve + 5)
                        pe.wait_ge(S["inv_act"], act + 5)
                        four(6, turned, g_of)
                        pe.wait_ge(S["inv_dve"], dve + 6)
                        four(4, x_odd, None, turn=True)
                        four(5, lambda i: a3[:, i, 2, :], x_odd)
                        pe.wait_ge(S["inv_dve"], dve + 7)
                        pe.wait_ge(S["inv_act"], act + 6)
                        four(2, turned, g_of)
                    pe.wait_ge(S["inv_dve"], 8 * (4 * l + 2 * tt + 2))
                    for half in range(2):
                        q = 4 * l + 2 * tt + half
                        hs = slice(half * CHUNK, (half + 1) * CHUNK)
                        if q % 4 == 0:
                            pe.wait_ge(S["cleared"], l + 2)
                        else:
                            pe.wait_ge(S["state"], q - l)
                        for c in range(NC):
                            pe.matmul(bank[2][hs, c * P:(c + 1) * P], ar[:, c, tt, 0, hs], state[:, c, :, :], start=True, stop=False)
                            for h in (2 * c, 2 * c + 1):
                                hv = slice(h * HEAD, (h + 1) * HEAD)
                                ins = pe.matmul(bank[2][hs, hv], unit[:, h, 2, hs], vt[:, tt, hv], start=False, stop=(h % 2 == 1))
                        ins.then_inc(S["rhs_mm"], 1)
                        pe.wait_ge(S["rhs"], q + 1)
                        for h in range(RH):
                            hv = slice(h * HEAD, (h + 1) * HEAD)
                            ins = pe.matmul(bank[3][hs, hv], inv[hs, h, hs], rhs_sb[hs, h, :], start=True, stop=True)
                        ins.then_inc(S["u_mm"], 1)
                        if q:
                            pe.wait_ge(S["o_read"], q)
                        for h in range(RH):
                            c, lo = h // 2, HEAD * (h % 2)
                            hd, hv = slice(lo, lo + HEAD), slice(h * HEAD, (h + 1) * HEAD)
                            o = bank[5][hd, c * CHUNK:(c + 1) * CHUNK]
                            pe.matmul(o, state[:, c, h % 2, :], ar[:, c, tt, 1, hs], start=True, stop=False)
                            pe.matmul(o, vt[:, tt, hv], unit[:, h, 3, hs], start=False, stop=False)
                            if h == 0:
                                pe.wait_ge(S["u"], q + 1)
                            ins = pe.matmul(o, u_sb[:, h, :], unit[:, h, 1, hs], start=False, stop=True)
                        ins.then_inc(S["o_mm"], 1)
                        if q % 4 < 3:
                            for h in range(RH):
                                c, lo = h // 2, HEAD * (h % 2)
                                hv = slice(h * HEAD, (h + 1) * HEAD)
                                o = bank[4][lo:lo + HEAD, c * HEAD:(c + 1) * HEAD]
                                pe.matmul(o, bt[hs, tt, hv], u_sb[hs, h, :], start=True, stop=False)
                                ins = pe.matmul(o, kt[hs, tt, hv], vt[hs, tt, hv], start=False, stop=True)
                            ins.then_inc(S["state_mm"], 1)
                while gate:
                    project_gate()
                pe.wait_ge(S["o_read"], 4 * (l + 1))
                for c in range(NC):
                    ins = pe.matmul(bank[2 + c // 2][:, (c % 2) * T:][:, 0:T], head_sum, oT[:, c, :], start=True, stop=True)
                ins.then_inc(S["gn_mean_mm"], 1)
                pe.wait_ge(S["conf_conv"], l + 1)
                for n in range(2):
                    ins = pe.matmul(bank[6][:, 0:T], ones, conv[:, n, :], start=(n == 0), stop=(n == 1))
                ins.then_inc(S["conf_mean_mm"], 1)
                pe.wait_ge(S["gn_sq"], l + 1)
                for c in range(NC):
                    ins = pe.matmul(bank[4 + c // 2][:, (c % 2) * T:][:, 0:T], head_sum, ar[:, c, :, 0, :], start=True, stop=True)
                ins.then_inc(S["gn_var_mm"], 1)
                pe.wait_ge(S["conf_sq"], l + 1)
                for n in range(2):
                    ins = pe.matmul(bank[7][:, 0:T], ones, conv_sq[:, n, :], start=(n == 0), stop=(n == 1))
                ins.then_inc(S["conf_var_mm"], 1)
                for n in range(4):
                    w = panels.take()
                    b = 2 + 3 * (n % 2)
                    if n == 0:
                        pe.wait_ge(S["branch_c"], l + 1)
                        pe.wait_ge(S["conf_silu"], l + 1)
                        pe.wait_ge(S["branch_a"], l + 1)
                    elif n >= 2:
                        pe.wait_ge(S["mixed"], 4 * l + n - 1)
                    for part_, (k0, k1, src) in enumerate(((0, 4, yT), (4, 6, conf_s), (6, 8, conv_c))):
                        for m in range(2):
                            for kb in range(k0, k1):
                                ins = mm(bank[b + part_][:, m * T:(m + 1) * T], w[:, kb * PC + m * P:][:, 0:P], src[:, kb - k0, :],
                                         start=(kb == k0), stop=(kb == k1 - 1))
                    ins.then_inc(S["mix_mm"], 1)
                pe.wait_ge(S["mixed"], 4 * (l + 1))
                rows_out(4, lambda kb, tt: mixT[:, kb, tt * P:(tt + 1) * P], S["wout_mm"])

            def rows_out(n_panels, lhs, done):
                for n in range(n_panels):
                    w = panels.take()
                    for i in range(PR):
                        kb = n * PR + i
                        for tt in range(TT):
                            for h in range(2):
                                ins = mm(bank[2 * tt + h][:], lhs(kb, tt), w[:, i * D + h * 512:][:, 0:512],
                                         start=(kb == 0), stop=(kb == n_panels * PR - 1))
                ins.then_inc(done, 1)

            def mlp_pe(kind, n_chunks, base, per_step):
                gated = kind != "mlp"
                nb = 2 if gated else 3

                def first(i, slot, turn=0, per_turn=0):
                    for g in range(2 if gated else 1):
                        w = panels.take(turn, per_turn)
                        b = bank[(2 * slot + g) if gated else slot]
                        for m in range(2):
                            for kb in range(KB):
                                ins = mm(b[:, m * T:(m + 1) * T], w[:, kb * PC + m * P:][:, 0:P], xT[:, kb, :],
                                         start=(kb == 0), stop=(kb == KB - 1))
                    ins.then_inc(S["gu_full"], 1)

                def last(i, slot, turn=0, per_turn=0):
                    w = panels.take(turn, per_turn)
                    pe.wait_ge(S["h_ready"], i + 1)
                    if not (isinstance(i, int) and i == 0):
                        pe.wait_ge(S["y_read"], i)
                    for m in range(2):
                        for tt in range(TT):
                            for h in range(2):
                                ins = mm(bank[4 + 2 * tt + h][:], hT[:, slot, m, tt * P:(tt + 1) * P],
                                         w[:, m * D + h * 512:][:, 0:512], start=(m == 0), stop=(m == 1))
                    ins.then_inc(S["y_full"], 1)

                first(base, 0)
                lead = 2 + (n_chunks - 2) % per_step
                for s in range(1, lead):
                    first(base + s, s % nb)
                    last(base + s - 1, (s - 1) % nb)
                per_turn = per_step * (3 if gated else 2)
                turns = (n_chunks - lead) // per_step
                with pe.Fori(0, turns) as turn:
                    for s in range(lead, lead + per_step):
                        first(turn * per_step + (base + s), s % nb, turn, per_turn)
                        last(turn * per_step + (base + s - 1), (s - 1) % nb, turn, per_turn)
                panels.skip((turns - 1) * per_turn)
                last(base + n_chunks - 1, (n_chunks - 1) % nb)

            def project_tokens(n_panels, n0):
                for n in range(n0, n0 + n_panels):
                    w = panels.take()
                    if n >= 2:
                        pe.wait_ge(S["attn_read"], n - 1)
                    for tt in range(TT):
                        for kb in range(KB):
                            ins = mm(bank[4 + n % 2][:, tt * PC:(tt + 1) * PC], xT[:, kb, tt * P:(tt + 1) * P],
                                     w[:, kb * PC:(kb + 1) * PC], start=(kb == 0), stop=(kb == KB - 1))
                    ins.then_inc(S["attn_proj"], 1)

            def turn_heads(l):
                n0 = 0 if l == 0 else BANKS_T[0]
                items = [turn_items(l, tt) for tt in range(TT)]
                pe.wait_ge(S["qk_ready"], l + 1)
                for n in range(BANKS_T[l]):
                    if n >= 4:
                        m = n0 + n - 4
                        pe.wait_ge(S["turnq_dve"] if m % 2 == 0 else S["turnq_act"], m // 2 + 1)
                    for i in range(2):
                        for tt in range(TT):
                            ins = pe.transpose(bank[n % 4][:, (2 * i + tt) * P:][:, 0:P], items[tt][2 * n + i], ident)
                    ins.then_inc(S["turnq_mm"], 1)

            def wait_heads(l):
                n = sum(BANKS_T[:l + 1])
                pe.wait_ge(S["turnq_dve"], (n + 1) // 2)
                pe.wait_ge(S["turnq_act"], n // 2)

            def compress():
                pe.wait_ge(S["cmp_tb"], 1)
                for kv in range(2):
                    for half in range(2):
                        w = panels.take()
                        for kb in range(KB):
                            for hb in range(2):
                                ins = mm(bank[4 + 2 * kv + hb][:, 0:NSA_G * N_CMP], w[:, kb * CMP_HIDDEN + hb * P:][:, 0:P],
                                         cmp_in[:, kv, half * KB + kb, :, :].rearrange("p g i -> p (g i)"),
                                         start=(half == 0 and kb == 0), stop=(half == 1 and kb == KB - 1))
                    ins.then_inc(S["cmp_h_mm"], 1)
                w2 = mid[:, MIDS["cmp_w2"]].rearrange("p (k h e) -> p k h e", k=2, h=2)
                pe.wait_ge(S["cmp_h"], 2)
                for kv in range(2):
                    for g in range(NSA_G):
                        for hb in range(2):
                            ins = pe.matmul(bank[0][0:N_CMP, (kv * NSA_G + g) * HEAD:][:, 0:HEAD], cmp_h[:, kv, hb, g * N_CMP:(g + 1) * N_CMP],
                                            w2[:, kv, hb, :], start=(hb == 0), stop=(hb == 1))
                ins.then_inc(S["cmp_o_mm"], 1)
                pe.wait_ge(S["cmp_k_ready"], 1)
                for g in range(NSA_G):
                    ins = pe.transpose(bank[1][:, g * 16:g * 16 + N_CMP], cmp_dup[0:N_CMP, g, :, :].rearrange("p d e -> p (d e)"),
                                       ident[0:N_CMP, 0:N_CMP])
                ins.then_inc(S["cmp_kT_mm"], 1)
                pe.wait_ge(S["cmp_kT"], 1)
                for h in range(NSA_HEADS):
                    hd = slice(HEAD * (h % 2), HEAD * (h % 2) + HEAD)
                    for tt in range(TT):
                        ins = pe.matmul(bank[2 + h % 2][:, (h // 2 * TT + tt) * 16:][:, 0:N_CMP], qkT[hd, h // 2, tt * P:(tt + 1) * P],
                                        cmp_kT[hd, h // NSA_R, 0:N_CMP], start=True, stop=True)
                ins.then_inc(S["cmp_s_mm"], 1)
                pe.wait_ge(S["cmp_p"], 1)
                for h in range(NSA_HEADS):
                    b = h % 2
                    if h >= 2:
                        pe.wait_ge(S["cmp_pT"], h - 1)
                        pe.wait_ge(S["cmp_done"], h - 1)
                    for tt in range(TT):
                        ins = pe.transpose(bank[4 + b][0:N_CMP, tt * P:(tt + 1) * P], cmp_s[:, h, tt, 0:N_CMP], ident)
                    ins.then_inc(S["cmp_pT_mm"], 1)
                    pe.wait_ge(S["cmp_pT"], h + 1)
                    for tt in range(TT):
                        ins = pe.matmul(bank[6 + b][:, tt * HEAD:(tt + 1) * HEAD], cmp_pT[0:N_CMP, 2 * b + tt, :],
                                        cmp_kv[0:N_CMP, 1, h // NSA_R, :], start=True, stop=True)
                    ins.then_inc(S["cmp_pv_mm"], 1)
                pe.wait_ge(S["cmp_done"], NSA_HEADS)

            def attend(l):
                n0 = 0 if l == 0 else len(units(0))
                todo = units(l)

                def scores(n):
                    kind, h, tile = todo[n]
                    u = n0 + n
                    if u >= 2:
                        pe.wait_ge(S["score_exp"], u - 1)
                    hd = slice(HEAD * (h % 2), HEAD * (h % 2) + HEAD)
                    for tt in (range(TT) if tile is None else (tile,)):
                        tok, n_k = slice(tt * P, (tt + 1) * P), (tt + 1) * P
                        b = 2 * (u % 2)
                        if kind == "dil":
                            for g in range(3):
                                o = bank[b + (g * n_k) // 512][:, g * n_k % 512:][:, 0:n_k]
                                ins = pe.matmul(o, qkT[hd, 4 * g + h // 2, tok], qkT[hd, 12 + h // 2, 0:n_k], start=True, stop=True)
                        elif kind == "mem":
                            ins = pe.matmul(bank[b][:, tt * T:(tt + 1) * T], qkT[hd, MEM_ITEM[l] + h // 2, tok],
                                            qkT[hd, MEM_ITEM[l] + 2 + h // 2, :], start=True, stop=True)
                        else:
                            item = 6 + (0 if kind == "sel" else 3) + h // NSA_R
                            ins = pe.matmul(bank[b][:, tt * P:tt * P + n_k], qkT[hd, h // 2, tok], qkT[hd, item, 0:n_k], start=True, stop=True)
                    ins.then_inc(S["score_mm"], 1)

                def finish(n):
                    kind, h, tile = todo[n]
                    u = n0 + n
                    s = u % 2
                    pe.wait_ge(S["score_exp"], u + 1)
                    if u >= 2:
                        pe.wait_ge(S["pT"], u - 1)
                    parts = blocks_of(kind, tile)
                    for i, (starts, _, _) in enumerate(parts):
                        for m, a in enumerate(starts):
                            o = bank[4 + s][:, i * P:(i + 1) * P]
                            if len(starts) == 1:
                                ins = pe.transpose(o, e_sb[:, s, a:a + P], ident)
                            else:
                                ins = pe.matmul(o, e_sb[:, s, a:a + P], ident, start=(m == 0), stop=(m == len(starts) - 1))
                    ins.then_inc(S["pT_mm"], 1)
                    pe.wait_ge(S["pT"], u + 1)
                    if u >= 2:
                        pe.wait_ge(S["pv_read"], u - 1)
                    for i, (_, tt, k) in enumerate(parts):
                        at = 0 if tile is not None else tt * HEAD
                        first = i == 0 or parts[i - 1][1] != tt
                        last = i == len(parts) - 1 or parts[i + 1][1] != tt
                        ins = pe.matmul(bank[6 + s][:, at:at + HEAD], pT_sb[:, s, i * P:(i + 1) * P], values(l, kind, h, k), start=first, stop=last)
                    ins.then_inc(S["pv_mm"], 1)

                scores(0)
                for n in range(len(todo)):
                    if n + 1 < len(todo):
                        scores(n + 1)
                    finish(n)

            def attention_pe(l):
                n_turn = 4 + 4 * l
                rms = 3 * l
                n_proj = 11 * l
                pe.wait_ge(S["rms_x"], rms + 1)
                turn_x(n_turn, xn)
                wait_xT(n_turn)
                project_tokens(2, n_proj)
                pe.wait_ge(S["rms_x"], rms + 2)
                turn_x(n_turn + 1, xn)
                wait_xT(n_turn + 1)
                if l == 0:
                    project_tokens(9, 2)
                else:
                    project_tokens(4, n_proj + 2)
                    turn_x(n_turn + 2, xn)
                    wait_xT(n_turn + 2)
                    project_tokens(7, n_proj + 6)
                turn_heads(l)
                wait_heads(l)
                if l == 0:
                    compress()
                attend(l)
                n_turn = 6 if l == 0 else 11
                pe.wait_ge(S["pv_read"], sum(len(units(i)) for i in range(l + 1)))
                turn_x(n_turn, o_tm)
                wait_xT(n_turn)
                rows_out((4, 3)[l], lambda kb, tt: xT[:, kb, tt * P:(tt + 1) * P], S["proj2_mm"])
                pe.wait_ge(S["rms_x"], rms + 3)
                turn_x(n_turn + 1, xn)
                wait_xT(n_turn + 1)
                mlp_pe("mlp", D_FF_2 // FCH, chunks + l * (D_FF_2 // FCH), 3)

            pe.wait_ge(S["consts_in"], 16)
            pe.wait_ge(S["params_in"], 16 * 3)
            pe.wait_ge(S["x_in"], 16)
            chunks = 0
            for l in range(DEPTH):
                if l:
                    pe.wait_ge(S["ln_x_done"], 2 * l)
                turn_x(2 * l, x_tm)
                mixer_pe(l)
                pe.wait_ge(S["ln_x_done"], 2 * l + 1)
                turn_x(2 * l + 1, x_tm)
                wait_xT(2 * l + 1)
                if l == 0:
                    mlp_pe("ffn", D_FF // FCH, 0, 2)
                    chunks = D_FF // FCH
                else:
                    router = mid[:, MIDS["router"]]
                    for tt in range(TT):
                        for kb in range(KB):
                            ins = pe.matmul(bank[0][:, tt * N_EXPERTS:(tt + 1) * N_EXPERTS], xT[:, kb, tt * P:(tt + 1) * P],
                                            router[:, kb * N_EXPERTS:(kb + 1) * N_EXPERTS], start=(kb == 0), stop=(kb == KB - 1))
                    ins.then_inc(S["router_mm"], 1)
                    pe.wait_ge(S["router_w"], 1)
                    mlp_pe("moe", N_EXPERTS * D_FF // FCH, chunks, 2)
                    chunks += N_EXPERTS * D_FF // FCH
            for l in range(DEPTH):
                attention_pe(l)

        @block.scalar
        def _(act):
            made = Made()

            def copy_xT(n, gain=None):
                for i, b in enumerate((1, 3)):
                    act.wait_ge(S["x_turned"], 4 * n + b + 1)
                    for kk_ in range(2):
                        ins = act.activation(xT[:, 2 * b + kk_, :], bank[b][:, kk_ * T:(kk_ + 1) * T], ACT.Copy,
                                             scale=1.0 if gain is None else c1(gain, 2 * b + kk_))
                    ins.then_inc(S["xT_act"], 1)
                    act.wait_ge(S["xT_act"], made.next("xT_act"))

            def proj_copy(l, j):
                n = 24 * l + j
                act.wait_ge(S["proj_out"], n + 1)
                src = bank[n % 2][:].rearrange("p (m t) -> p m t", m=2)
                if j < 7:
                    if 7 * l + j >= 2:
                        act.wait_ge(S["shifted"], 7 * l + j - 1)
                    else:
                        act.wait_ge(S["cleared"], 1)
                    act.activation(pz[:, j % 2, :, 1:], src, ACT.Copy).then_inc(S["proj_read"], 1)
                    act.wait_ge(S["proj_read"], made.next("proj_read"))
                elif j == 7:
                    act.activation(u_pad[:, :, CONF_TAPS - 1:], src, ACT.Copy).then_inc(S["proj_read"], 1)
                    act.wait_ge(S["proj_read"], made.next("proj_read"))
                elif j == 8:
                    act.activation(conf_s[:], src, ACT.Sigmoid).then_inc(S["proj_read"], 1)
                    act.wait_ge(S["proj_read"], made.next("proj_read"))
                elif j == 9:
                    act.activation(gb[:], src, ACT.Copy).then_inc(S["proj_read"], 1)
                    act.wait_ge(S["proj_read"], made.next("proj_read"))
                elif j == 10:
                    act.activation(s_pad[:, :, SHORT_TAPS - 1:], src, ACT.Copy).then_inc(S["proj_read"], 1)
                    act.wait_ge(S["proj_read"], made.next("proj_read"))
                elif j == 11:
                    act.activation(conv_c[:], src, ACT.Copy).then_inc(S["proj_read"], 1)
                    act.wait_ge(S["proj_read"], made.next("proj_read"))
                else:
                    m = 2 * (j - 12)
                    act.activation(gates[:, m:m + 2, :], src, ACT.Sigmoid).then_inc(S["proj_read"], 1)
                    act.wait_ge(S["proj_read"], made.next("proj_read"))

            def mixer_act(l):
                gate = list(range(12, 24))

                def gate_copy():
                    proj_copy(l, gate.pop(0))

                copy_xT(2 * l)
                for j in range(12):
                    proj_copy(l, j)
                act.wait_ge(S["shifted"], 7 * (l + 1))
                act.activation(loras[0:HEAD, 0, :], sh[0:HEAD, 12, :], ACT.Tanh)
                act.activation(loras[:, 1, :], sh[:, 13, :], ACT.Sigmoid).then_inc(S["lora_in"], 1)
                act.wait_ge(S["lora_in"], made.next("lora_in"))
                act.wait_ge(S["lora_z"], l + 1)
                for tt in range(TT):
                    ins = act.activation(sg_tok[:, tt, :], bank[2 + tt][:], ACT.Sigmoid)
                ins.then_inc(S["decay_in"], 1)
                act.wait_ge(S["decay_in"], made.next("decay_in"))
                act.wait_ge(S["lora_a"], l + 1)
                for c in range(NC):
                    ins = act.activation(a_[:, c, :], bank[4 + c // 2][:, (c % 2) * T:][:, 0:T], ACT.Sigmoid, bias=c1(f"a0{l}", c))
                ins.then_inc(S["aaa"], 1)
                act.wait_ge(S["aaa"], made.next("aaa"))
                act.wait_ge(S["lora_g"], l + 1)
                for n in range(2):
                    ins = act.activation(g_[:, 2 * n:2 * n + 2, :], bank[6 + n][:].rearrange("p (m t) -> p m t", m=2), ACT.Copy)
                ins.then_inc(S["gate_lora"], 1)
                act.wait_ge(S["gate_lora"], made.next("gate_lora"))
                gate_copy()
                act.wait_ge(S["cum_mm"], l + 1)
                for c in range(NC):
                    s = bank[2 + c][:].rearrange("p (t m k) -> p m t k", t=TT, m=2)
                    for dst, m, sign in ((p_in, 0, -KAPPA), (p_inv, 0, KAPPA), (p_ex, 1, -KAPPA)):
                        ins = act.activation(dst[:, c, :].rearrange("p (t k) -> p t k", t=TT), s[:, m], ACT.Exp, scale=sign)
                ins.then_inc(S["decays"], 1)
                act.wait_ge(S["decays"], made.next("decays"))
                act.wait_ge(S["kk_mm"], l + 1)
                for n in range(2):
                    ins = act.activation(vt[:, n, :], bank[6 + n][:], ACT.Sqrt)
                ins.then_inc(S["kk_norm"], 1)
                act.wait_ge(S["kk_norm"], made.next("kk_norm"))
                gate_copy()
                gate_copy()
                for n, dst in enumerate((vt, bt, kt)):
                    act.wait_ge(S["turn_mm"], 6 * l + 2 * n + 2)
                    act.activation(dst[:, 1, :], bank[2 + (2 * n + 1) % 4][:], ACT.Copy).then_inc(S["turned_act"], 1)
                    act.wait_ge(S["turned_act"], made.next("turned_act"))
                for tt in range(TT):
                    for hg in range(2):
                        group = 4 * l + 2 * tt + hg
                        if gate:
                            gate_copy()
                        n = 14 * group
                        for count, b, dst in ((2, 3, 1), (4, 5, 2), (5, 6, 3), (7, 3, 0), (9, 2, 1), (12, 4, 1)):
                            act.wait_ge(S["inv_mm"], n + count)
                            if count == 12:
                                act.wait_ge(S["inv_mm"], n + 12)
                            act.activation(pw[:, dst, :], bank[b][:], ACT.Copy).then_inc(S["inv_act"], 1)
                            act.wait_ge(S["inv_act"], made.next("inv_act"))
                            if count in (5, 7) and gate:
                                gate_copy()
                    for half in range(2):
                        q = 4 * l + 2 * tt + half
                        act.wait_ge(S["o_mm"], q + 1)
                        lo = (2 * tt + half) * CHUNK
                        act.activation(oT[:, :, lo:lo + CHUNK], bank[5][:, 0:NC * CHUNK].rearrange("p (c t) -> p c t", c=NC),
                                       ACT.Copy).then_inc(S["o_read"], 1)
                        act.wait_ge(S["o_read"], made.next("o_read"))
                while gate:
                    gate_copy()
                act.wait_ge(S["gn_var_mm"], l + 1)
                for n in range(2):
                    ins = act.activation(kk[:, 2 * n:2 * n + 2, :], bank[4 + n][:].rearrange("p (m t) -> p m t", m=2), ACT.Sqrt,
                                         scale=1.0 / HEAD, bias=eps("gn_eps"))
                ins.then_inc(S["gn_std"], 1)
                act.wait_ge(S["gn_std"], made.next("gn_std"))
                act.wait_ge(S["conf_var_mm"], l + 1)
                act.activation(conf_s[:, 0, :], bank[7][:, 0:T], ACT.Sqrt, scale=1.0 / CONF, bias=eps("ln_eps")).then_inc(S["conf_std"], 1)
                act.wait_ge(S["conf_std"], made.next("conf_std"))
                act.wait_ge(S["branch_b"], l + 1)
                for n in range(2):
                    ins = act.activation(conf_s[:, n, :], conv[:, n, :], ACT.Silu, scale=c1(f"conf_ln_g{l}", n), bias=c1(f"conf_ln_b{l}", n))
                ins.then_inc(S["conf_silu"], 1)
                act.wait_ge(S["conf_silu"], made.next("conf_silu"))

            def ln_std(n):
                act.wait_ge(S["ln_x"], n + 1)
                act.activation(stat[:, 32:32 + TT], stat[:, 26:26 + 2 * TT].rearrange("p (t s) -> p s t", s=2)[:, 1, :], ACT.Sqrt,
                               bias=eps("ln_eps")).then_inc(S["ln_std"], 1)
                act.wait_ge(S["ln_std"], made.next("ln_std"))

            def mlp_act(kind, n_chunks, base, per_step):
                gated = kind != "mlp"
                nb = 2 if gated else 3
                func = ACT.Silu if gated else ACT.Relu

                def chunk(i, slot, early):
                    act.wait_ge(S["gu_full"], i + 1)
                    if not early:
                        act.wait_ge(S["h_ready"], i - nb + 1)
                    b = bank[2 * slot if gated else slot]
                    act.activation(gate_s[:, slot, :, :], b[:].rearrange("p (m t) -> p m t", m=2), func).then_inc(S["act_out"], 1)

                lead = nb + (n_chunks - nb) % per_step
                for s in range(lead):
                    chunk(base + s, s % nb, s < nb)
                with act.Fori(0, (n_chunks - lead) // per_step) as turn:
                    for s in range(lead, lead + per_step):
                        chunk(turn * per_step + (base + s), s % nb, False)

            def rms(n, src):
                if n in (0, 3):
                    act.wait_ge(S["mem_in"], 16 * (1 + n // 3))
                elif n == 1:
                    act.wait_ge(S["ln_x_done"], 2 * DEPTH)
                elif n == 4:
                    act.wait_ge(S["y_read"], chunks + D_FF_2 // FCH)
                else:
                    act.wait_ge(S["x_done"], 1 + n // 3)
                for tt in range(TT):
                    ins = act.activation(scr[:, tt, 0:D], src[:, tt, :], ACT.Square, accum_out=rs[:, tt:tt + 1])
                ins.then_inc(S["act_step"], 1)
                act.wait_ge(S["act_step"], made.next("act_step"))
                act.activation(rs[:, 2:2 + TT], rs[:, 0:TT], ACT.Sqrt, scale=1.0 / D, bias=eps("rms_eps")).then_inc(S["rms_std"], 1)
                act.wait_ge(S["rms_std"], made.next("rms_std"))

            def copy_tokens(dst, n_panels, n0):
                for j in range(n_panels):
                    n = n0 + j
                    act.wait_ge(S["attn_proj"], n + 1)
                    act.activation(dst[:, :, j * PC:(j + 1) * PC], bank[4 + n % 2][:].rearrange("p (t c) -> p t c", t=TT), ACT.Copy).then_inc(S["attn_read"], 1)
                    act.wait_ge(S["attn_read"], made.next("attn_read"))

            def attention_act(l):
                n_turn = 4 + 4 * l
                rms(3 * l, o_tm)
                copy_xT(n_turn, f"mem_norm{l}")
                copy_tokens(mem_kv, 2, 11 * l)
                act.wait_ge(S["rms_x"], 3 * l + 1)
                rms(3 * l + 1, x_tm)
                if l == 0:
                    copy_xT(n_turn + 1, "attn_norm0")
                    copy_tokens(proj, 9, 2)
                    act.activation(coef[:], proj[:, :, 2176:2212].rearrange("p t (h b) -> p b h t", b=3), ACT.Sigmoid).then_inc(S["nsa_gates"], 1)
                    act.wait_ge(S["nsa_gates"], made.next("nsa_gates"))
                else:
                    copy_xT(n_turn + 1, "kv_norm")
                    copy_tokens(proj, 4, 13)
                    copy_xT(n_turn + 2, "attn_norm1")
                    copy_tokens(proj[:, :, 4 * PC:], 7, 17)
                n_heads = sum(s[1] for s in head_sets(l)) * TT
                act.wait_ge(S["rms_ss"], l + 1)
                act.activation(rs[:, 8:8 + n_heads], rs[:, 8:8 + n_heads], ACT.Sqrt, scale=1.0 / HEAD, bias=eps("rms_eps")).then_inc(S["qk_std"], 1)
                act.wait_ge(S["qk_std"], made.next("qk_std"))
                n0 = 0 if l == 0 else BANKS_T[0]
                for n in range(BANKS_T[l]):
                    if (n0 + n) % 2:
                        act.wait_ge(S["turnq_mm"], n0 + n + 1)
                        act.activation(qkT[:, 2 * n:2 * n + 2, :], bank[n % 4][:].rearrange("p (i t) -> p i t", i=2), ACT.Copy).then_inc(S["turnq_act"], 1)
                        act.wait_ge(S["turnq_act"], made.next("turnq_act"))
                if l == 0:
                    for kv in range(2):
                        act.wait_ge(S["cmp_h_mm"], kv + 1)
                        for hb in range(2):
                            ins = act.activation(cmp_h[:, kv, hb, :], bank[4 + 2 * kv + hb][:, 0:NSA_G * N_CMP], ACT.Gelu_apprx_tanh,
                                                 bias=c1("cmp_b1", 2 * kv + hb))
                        ins.then_inc(S["cmp_h"], 1)
                        act.wait_ge(S["cmp_h"], made.next("cmp_h"))
                    act.wait_ge(S["cmp_kv"], 1)
                    act.activation(rs[0:N_CMP, 4:4 + NSA_G], rs[0:N_CMP, 4:4 + NSA_G], ACT.Sqrt, scale=1.0 / HEAD,
                                   bias=eps("rms_eps")[0:N_CMP]).then_inc(S["cmp_k_std"], 1)
                    act.wait_ge(S["cmp_k_std"], made.next("cmp_k_std"))
                    act.wait_ge(S["cmp_s"], 1)
                    act.activation(cmp_s[:, :, :, 0:N_CMP], cmp_s[:, :, :, 0:N_CMP], ACT.Exp, scale=SCALE).then_inc(S["cmp_e"], 1)
                    act.wait_ge(S["cmp_e"], made.next("cmp_e"))
                    for h in range(NSA_HEADS):
                        act.wait_ge(S["cmp_pT_mm"], h + 1)
                        if h >= 2:
                            act.wait_ge(S["cmp_pv_mm"], h - 1)
                        b = h % 2
                        act.activation(cmp_pT[0:N_CMP, 2 * b:2 * b + 2, :], bank[4 + b][0:N_CMP, 0:T].rearrange("p (t q) -> p t q", t=TT),
                                       ACT.Copy).then_inc(S["cmp_pT"], 1)
                        act.wait_ge(S["cmp_pT"], made.next("cmp_pT"))
                n0 = 0 if l == 0 else len(units(0))
                todo = units(l)

                def exps(n):
                    kind, h, tile = todo[n]
                    u = n0 + n
                    s = u % 2
                    act.wait_ge(S["score_max"], u + 1)
                    if u >= 2:
                        act.wait_ge(S["pT_mm"], u - 1)
                        act.wait_ge(S["pv_read"], u - 1)
                    for tt in range(TT):
                        if kind == "dil":
                            a, w, at = 0, 3 * P * (tile + 1), 0
                        elif kind == "mem":
                            a, w, at = tt * T, T, tt
                        else:
                            a, w, at = tt * P, P * (tt + 1), tt
                        if kind == "dil" and tt:
                            break
                        src = bank[2 * s][:, a:a + w] if kind == "mem" else s_sb[:, s, a:a + w]
                        ins = act.activation(e_sb[:, s, a:a + w], src, ACT.Exp, scale=SCALE, bias=rs[:, 140 + 2 * s + at:141 + 2 * s + at],
                                             accum_out=rs[:, 144 + 2 * s + at:145 + 2 * s + at])
                    ins.then_inc(S["score_exp"], 1)
                    act.wait_ge(S["score_exp"], made.next("score_exp"))

                def turned(n):
                    kind, h, tile = todo[n]
                    u = n0 + n
                    s = u % 2
                    act.wait_ge(S["pT_mm"], u + 1)
                    if u >= 2:
                        act.wait_ge(S["pv_mm"], u - 1)
                    w = len(blocks_of(kind, tile)) * P
                    act.activation(pT_sb[:, s, 0:w], bank[4 + s][:, 0:w], ACT.Copy).then_inc(S["pT"], 1)
                    act.wait_ge(S["pT"], made.next("pT"))

                exps(0)
                for n in range(len(todo)):
                    if n + 1 < len(todo):
                        exps(n + 1)
                    turned(n)
                n_turn = 6 if l == 0 else 11
                copy_xT(n_turn)
                rms(3 * l + 2, x_tm)
                copy_xT(n_turn + 1, f"mlp_norm{l}")
                mlp_act("mlp", D_FF_2 // FCH, chunks + l * (D_FF_2 // FCH), 3)

            act.wait_ge(S["consts_in"], 16)
            act.wait_ge(S["params_in"], 16 * 3)
            chunks = 0
            for l in range(DEPTH):
                mixer_act(l)
                ln_std(2 * l)
                copy_xT(2 * l + 1)
                if l == 0:
                    mlp_act("ffn", D_FF // FCH, 0, 2)
                    chunks = D_FF // FCH
                else:
                    act.wait_ge(S["router_w"], 1)
                    p = rt[:, 2, 0:TT * N_EXPERTS]
                    act.activation(p, p, ACT.Exp).then_inc(S["router_exp"], 1)
                    act.wait_ge(S["router_exp"], made.next("router_exp"))
                    mlp_act("moe", N_EXPERTS * D_FF // FCH, chunks, 2)
                    chunks += N_EXPERTS * D_FF // FCH
                ln_std(2 * l + 1)
            for l in range(DEPTH):
                attention_act(l)

        @block.vector
        def _(dve):
            made = Made()
            tt_, ts_, stt, copy = dve.tensor_tensor, dve.tensor_scalar, dve.scalar_tensor_tensor, dve.tensor_copy

            def pair(b):
                return bank[b][:].rearrange("p (m t) -> p m t", m=2)

            def copy_xT(n, gain=None):
                for i, b in enumerate((0, 2)):
                    dve.wait_ge(S["x_turned"], 4 * n + b + 1)
                    if gain is None:
                        ins = copy(xT[:, 2 * b:2 * b + 2, :], pair(b))
                    else:
                        for kk_ in range(2):
                            ins = ts_(xT[:, 2 * b + kk_, :], bank[b][:, kk_ * T:(kk_ + 1) * T], c1(gain, 2 * b + kk_), None, ALU.mult)
                    ins.then_inc(S["xT_dve"], 1)
                    dve.wait_ge(S["xT_dve"], made.next("xT_dve"))

            def depthwise(out, src, name, taps):
                for j in range(taps):
                    for n in range(2):
                        ins = stt(out[:, n, :], src[:, n, j:j + T], c1(name, n * taps + j), out[:, n, :], ALU.mult, ALU.add) if j else \
                            ts_(out[:, n, :], src[:, n, 0:T], c1(name, n * taps), None, ALU.mult)
                    if j < taps - 1:
                        ins.then_inc(S["dve_step"], 1)
                        dve.wait_ge(S["dve_step"], made.next("dve_step"))
                return ins

            def mixer_dve(l):
                dve.memset(state[:], 0.0).then_inc(S["cleared"], 1)
                dve.wait_ge(S["cleared"], made.next("cleared"))
                copy_xT(2 * l)
                for j in range(7):
                    dve.wait_ge(S["proj_read"], 24 * l + j + 1)
                    z = pz[:, j % 2]
                    tt_(tmp[:, 0:2, :], z[:, :, 0:T], z[:, :, 1:], ALU.subtract).then_inc(S["dve_step"], 1)
                    dve.wait_ge(S["dve_step"], made.next("dve_step"))
                    for m in range(2):
                        ins = stt(sh[:, 2 * j + m, :], tmp[:, m, :], c1(f"mu{l}", 2 * j + m), z[:, m, 1:], ALU.mult, ALU.add)
                    ins.then_inc(S["shifted"], 1)
                    dve.wait_ge(S["shifted"], made.next("shifted"))
                for c in range(NC):
                    ins = ts_(kk[:, c, :], k_[:, c, :], c1(f"k_k{l}", c), None, ALU.mult)
                ins.then_inc(S["dve_step"], 1)
                dve.wait_ge(S["dve_step"], made.next("dve_step"))
                tt_(tmp[:], kk[:], kk[:], ALU.mult).then_inc(S["kk_sq"], 1)
                dve.wait_ge(S["kk_sq"], made.next("kk_sq"))
                dve.wait_ge(S["proj_read"], 24 * l + 12)
                tt_(u_pad[:, :, CONF_TAPS - 1:], u_pad[:, :, CONF_TAPS - 1:], conf_s[:], ALU.mult).then_inc(S["dve_step"], 1)
                dve.wait_ge(S["dve_step"], made.next("dve_step"))
                tt_(s_pad[:, :, SHORT_TAPS - 1:], s_pad[:, :, SHORT_TAPS - 1:], conv_c[:], ALU.mult).then_inc(S["dve_step"], 1)
                dve.wait_ge(S["dve_step"], made.next("dve_step"))
                dve.wait_ge(S["aaa"], l + 1)
                dve.wait_ge(S["kk_mm"], l + 1)
                for c in range(NC):
                    ins = ts_(tmp[:, c, :], a_[:, c, :], 1.0, c1(f"k_a{l}", c), ALU.subtract, ALU.mult)
                ins.then_inc(S["dve_step"], 1)
                dve.wait_ge(S["dve_step"], made.next("dve_step"))
                stt(k_, tmp[:], 1.0, k_, ALU.add, ALU.mult).then_inc(S["dve_step"], 1)
                dve.wait_ge(S["dve_step"], made.next("dve_step"))
                for c in range(NC):
                    ins = stt(tmp[:, c, :], r_[:, c, :], c1(f"r_k{l}", c), k_[:, c, :], ALU.mult, ALU.mult)
                dve.wait_ge(S["kk_norm"], l + 1)
                norm = vt[:].rearrange("p a (b t) -> p (a b) t", t=T)
                ts_(norm, norm, 1e-12, None, ALU.max).then_inc(S["dve_step"], 1)
                dve.wait_ge(S["dve_step"], made.next("dve_step"))
                dve.reciprocal(norm, norm).then_inc(S["bonus_in"], 1)
                dve.wait_ge(S["bonus_in"], made.next("bonus_in"))
                tt_(kk[:], kk[:], norm, ALU.mult).then_inc(S["dve_step"], 1)
                dve.wait_ge(S["dve_step"], made.next("dve_step"))
                tt_(a_[:], kk[:], a_[:], ALU.mult).then_inc(S["dve_step"], 1)
                dve.wait_ge(S["dve_step"], made.next("dve_step"))
                dve.wait_ge(S["decays"], l + 1)
                for c in range(NC):
                    stt(ar[:, c, :, 0, :], kk[:, c, :].rearrange("p (t k) -> p t k", t=TT), -1.0,
                        p_ex[:, c, :].rearrange("p (t k) -> p t k", t=TT), ALU.mult, ALU.mult)
                    ins = tt_(ar[:, c, :, 1, :], r_[:, c, :].rearrange("p (t k) -> p t k", t=TT),
                              p_in[:, c, :].rearrange("p (t k) -> p t k", t=TT), ALU.mult)
                ins.then_inc(S["dve_step"], 1)
                dve.wait_ge(S["dve_step"], made.next("dve_step"))
                tt_(a_[:], a_[:], p_inv[:], ALU.mult)
                tt_(kk[:], k_, p_inv[:], ALU.mult).then_inc(S["dve_step"], 1)
                dve.wait_ge(S["dve_step"], made.next("dve_step"))
                dve.wait_ge(S["bonus_mm"], l + 1)
                for n in range(2):
                    ins = tt_(tmp[:, 2 * n:2 * n + 2, :], pair(6 + n), v_[:, 2 * n:2 * n + 2, :], ALU.mult)
                ins.then_inc(S["features"], 1)
                dve.wait_ge(S["features"], made.next("features"))
                for n, dst in enumerate((vt, bt, kt)):
                    dve.wait_ge(S["turn_mm"], 6 * l + 2 * n + 1)
                    copy(dst[:, 0, :], bank[2 + 2 * n % 4][:]).then_inc(S["turned_dve"], 1)
                    dve.wait_ge(S["turned_dve"], made.next("turned_dve"))

                for tt in range(TT):
                    for hg in range(2):
                        group = 4 * l + 2 * tt + hg
                        dve.wait_ge(S["unit_mm"], group + 1)
                        if tt and not hg:
                            dve.wait_ge(S["o_mm"], 4 * l + 2)
                        for i in range(4):
                            tt_(unit[:, 4 * hg + i, :, :].rearrange("p m t -> p (m t)"), bank[2 + i][:], unit_mask, ALU.mult)
                        for j in range(2):
                            ins = tt_(a3[:, j::2], bank[6 + j][:, 0:2 * P].rearrange("p (i s) -> p i s", i=2).unsqueeze(2).to_broadcast([P, 2, 3, P]),
                                      inv_mask.unsqueeze(1).to_broadcast([P, 2, 3, P]), ALU.mult)
                        ins.then_inc(S["dve_step"], 1)
                        dve.wait_ge(S["dve_step"], made.next("dve_step"))
                        tt_(xa[:].rearrange("p (i s) -> p i s", i=4), unit[:, 4 * hg:4 * hg + 4, 0, :],
                            ident.unsqueeze(1).to_broadcast([P, 4, P]), ALU.add).then_inc(S["masks"], 1)
                        dve.wait_ge(S["masks"], made.next("masks"))
                        n = 14 * group
                        fin = inv[:, 4 * hg:4 * hg + 4, :].rearrange("p i s -> p (i s)")
                        for count, b, dst, add in ((1, 2, pw[:, 0, :], None), (3, 4, xb[:], xa[:]), (6, 2, xa[:], xb[:]),
                                                   (8, 4, xb[:], xa[:]), (10, 3, pw[:, 2, :], None), (11, 6, xa[:], xb[:]),
                                                   (13, 5, pw[:, 2, :], None), (14, 2, fin, xa[:])):
                            dve.wait_ge(S["inv_mm"], n + count)
                            ins = copy(dst, bank[b][:]) if add is None else tt_(dst, bank[b][:], add, ALU.add)
                            ins.then_inc(S["inv_dve"], 1)
                            dve.wait_ge(S["inv_dve"], made.next("inv_dve"))
                    for half in range(2):
                        q = 4 * l + 2 * tt + half
                        hs = slice(half * CHUNK, (half + 1) * CHUNK)
                        dve.wait_ge(S["rhs_mm"], q + 1)
                        copy(rhs_sb[hs].rearrange("p h v -> p (h v)"), bank[2][hs, :]).then_inc(S["rhs"], 1)
                        dve.wait_ge(S["rhs"], made.next("rhs"))
                        dve.wait_ge(S["u_mm"], q + 1)
                        copy(u_sb[hs].rearrange("p h v -> p (h v)"), bank[3][hs, :]).then_inc(S["u"], 1)
                        dve.wait_ge(S["u"], made.next("u"))
                        if q % 4 < 3:
                            dve.wait_ge(S["state_mm"], q - l + 1)
                            end = (2 * tt + half) * CHUNK + CHUNK - 1
                            for j, hd in enumerate((slice(0, HEAD), slice(HEAD, P))):
                                ins = tt_(state[hd, :, j, :], bank[4][hd, 0:NC * HEAD].rearrange("p (c v) -> p c v", c=NC), state[hd, :, j, :], ALU.add)
                            ins.then_inc(S["dve_step"], 1)
                            dve.wait_ge(S["dve_step"], made.next("dve_step"))
                            for j, hd in enumerate((slice(0, HEAD), slice(HEAD, P))):
                                ins = tt_(state[hd, :, j, :], state[hd, :, j, :], p_in[hd, :, end:end + 1].to_broadcast([HEAD, NC, HEAD]), ALU.mult)
                            ins.then_inc(S["state"], 1)
                            dve.wait_ge(S["state"], made.next("state"))

                ins = depthwise(conv, u_pad, f"conf_dw{l}", CONF_TAPS)
                ins.then_inc(S["dve_step"], 1)
                dve.wait_ge(S["dve_step"], made.next("dve_step"))
                for n in range(2):
                    ins = ts_(conv[:, n, :], conv[:, n, :], c1(f"conf_dw_b{l}", n), None, ALU.add)
                ins.then_inc(S["conf_conv"], 1)
                dve.wait_ge(S["conf_conv"], made.next("conf_conv"))
                depthwise(conv_c, s_pad, f"short_dw{l}", SHORT_TAPS).then_inc(S["dve_step"], 1)
                dve.wait_ge(S["dve_step"], made.next("dve_step"))
                tt_(conv_c[:], conv_c[:], gb[:], ALU.mult).then_inc(S["branch_c"], 1)
                dve.wait_ge(S["branch_c"], made.next("branch_c"))
                dve.wait_ge(S["gn_mean_mm"], l + 1)
                for n in range(2):
                    ins = stt(oT[:, 2 * n:2 * n + 2, :], pair(2 + n), -1.0 / HEAD, oT[:, 2 * n:2 * n + 2, :], ALU.mult, ALU.add)
                ins.then_inc(S["dve_step"], 1)
                dve.wait_ge(S["dve_step"], made.next("dve_step"))
                ot4 = oT[:].rearrange("p c (t k) -> p c t k", t=TT)
                for c in range(NC):
                    ins = tt_(ar[:, c, :, 0, :], ot4[:, c], ot4[:, c], ALU.mult)
                ins.then_inc(S["gn_sq"], 1)
                dve.wait_ge(S["gn_sq"], made.next("gn_sq"))
                dve.wait_ge(S["conf_mean_mm"], l + 1)
                for n in range(2):
                    ins = stt(conv[:, n, :], bank[6][:, 0:T], -1.0 / CONF, conv[:, n, :], ALU.mult, ALU.add)
                ins.then_inc(S["dve_step"], 1)
                dve.wait_ge(S["dve_step"], made.next("dve_step"))
                tt_(conv_sq[:], conv[:], conv[:], ALU.mult).then_inc(S["conf_sq"], 1)
                dve.wait_ge(S["conf_sq"], made.next("conf_sq"))
                dve.wait_ge(S["gn_std"], l + 1)
                dve.reciprocal(kk[:], kk[:]).then_inc(S["dve_step"], 1)
                dve.wait_ge(S["dve_step"], made.next("dve_step"))
                tt_(oT[:], oT[:], kk[:], ALU.mult).then_inc(S["dve_step"], 1)
                dve.wait_ge(S["dve_step"], made.next("dve_step"))
                for c in range(NC):
                    ins = ts_(yT[:, c, :], oT[:, c, :], c1(f"gn_g{l}", c), c1(f"gn_b{l}", c), ALU.mult, ALU.add)
                ins.then_inc(S["dve_step"], 1)
                dve.wait_ge(S["dve_step"], made.next("dve_step"))
                tt_(yT[:], yT[:], tmp[:], ALU.add).then_inc(S["dve_step"], 1)
                dve.wait_ge(S["dve_step"], made.next("dve_step"))
                tt_(yT[:], yT[:], g_[:], ALU.mult).then_inc(S["branch_a"], 1)
                dve.wait_ge(S["branch_a"], made.next("branch_a"))
                dve.wait_ge(S["conf_std"], l + 1)
                dve.reciprocal(conf_s[:, 0, :], conf_s[:, 0, :]).then_inc(S["dve_step"], 1)
                dve.wait_ge(S["dve_step"], made.next("dve_step"))
                for n in range(2):
                    ins = tt_(conv[:, n, :], conv[:, n, :], conf_s[:, 0, :], ALU.mult)
                ins.then_inc(S["branch_b"], 1)
                dve.wait_ge(S["branch_b"], made.next("branch_b"))
                dve.wait_ge(S["proj_read"], 24 * (l + 1))
                for n in range(4):
                    b = 2 + 3 * (n % 2)
                    m = slice(2 * n, 2 * n + 2)
                    dve.wait_ge(S["mix_mm"], 4 * l + n + 1)
                    for part_ in range(3):
                        g = gates[:, 8 * part_ + 2 * n:8 * part_ + 2 * n + 2, :]
                        ins = tt_(g, pair(b + part_), g, ALU.mult)
                    ins.then_inc(S["dve_step"], 1)
                    dve.wait_ge(S["dve_step"], made.next("dve_step"))
                    tt_(mixT[:, m, :], gates[:, m, :], gates[:, 8 + 2 * n:10 + 2 * n, :], ALU.add).then_inc(S["dve_step"], 1)
                    dve.wait_ge(S["dve_step"], made.next("dve_step"))
                    tt_(mixT[:, m, :], mixT[:, m, :], gates[:, 16 + 2 * n:18 + 2 * n, :], ALU.add).then_inc(S["mixed"], 1)
                    dve.wait_ge(S["mixed"], made.next("mixed"))
                dve.wait_ge(S["wout_mm"], l + 1)
                for tt in range(TT):
                    for h in range(2):
                        xs = x_tm[:, tt, h * 512:(h + 1) * 512]
                        ins = stt(xs, xs, ALPHA, bank[2 * tt + h][:], ALU.mult, ALU.add)
                ins.then_inc(S["dve_step"], 1)
                dve.wait_ge(S["dve_step"], made.next("dve_step"))

            def layer_norm(n):
                for tt in range(TT):
                    for h in range(2):
                        s = 12 * tt + 6 * h
                        ins = dve.bn_stats(stat[:, s:s + 6], x_tm[:, tt, h * 512:(h + 1) * 512])
                ins.then_inc(S["dve_step"], 1)
                dve.wait_ge(S["dve_step"], made.next("dve_step"))
                for tt in range(TT):
                    ins = dve.bn_aggr(stat[:, 26 + 2 * tt:28 + 2 * tt], stat[:, 12 * tt:12 * tt + 12])
                ins.then_inc(S["ln_x"], 1)
                dve.wait_ge(S["ln_x"], made.next("ln_x"))
                dve.wait_ge(S["ln_std"], n + 1)
                dve.reciprocal(stat[:, 34:34 + TT], stat[:, 32:32 + TT]).then_inc(S["dve_step"], 1)
                dve.wait_ge(S["dve_step"], made.next("dve_step"))
                for tt in range(TT):
                    ins = ts_(x_tm[:, tt, :], x_tm[:, tt, :], stat[:, 26 + 2 * tt:27 + 2 * tt], stat[:, 34 + tt:35 + tt], ALU.subtract, ALU.mult)
                ins.then_inc(S["dve_step"], 1)
                dve.wait_ge(S["dve_step"], made.next("dve_step"))
                dve.wait_ge(S["ln_rows_in"], 16 * (n + 1))
                tt_(x_tm[:], x_tm[:], ln_row[:, 0, :].unsqueeze(1).to_broadcast([P, TT, D]), ALU.mult).then_inc(S["dve_step"], 1)
                dve.wait_ge(S["dve_step"], made.next("dve_step"))
                tt_(x_tm[:], x_tm[:], ln_row[:, 1, :].unsqueeze(1).to_broadcast([P, TT, D]), ALU.add).then_inc(S["ln_x_done"], 1)
                dve.wait_ge(S["ln_x_done"], made.next("ln_x_done"))

            def scale_x(n):
                dve.wait_ge(S["x_turned"], 4 * (n + 1))
                ts_(x_tm[:], x_tm[:], ALPHA, None, ALU.mult).then_inc(S["dve_step"], 1)
                dve.wait_ge(S["dve_step"], made.next("dve_step"))

            def route():
                dve.wait_ge(S["router_mm"], 1)
                E = N_EXPERTS
                lg, rank, p, mx, sq = rt[:, 0, 0:TT * E], rt[:, 1, 0:TT * E], rt[:, 2, 0:TT * E], rt[:, 3, 0:TT], rt[:, 4:6, :]
                l3, p3 = (t.rearrange("p (t e) -> p t e", t=TT) for t in (lg, p))
                copy(lg, bank[0][:, 0:TT * E]).then_inc(S["dve_step"], 1)
                dve.wait_ge(S["dve_step"], made.next("dve_step"))
                dve.tensor_reduce(mx, l3, AX.X, ALU.max).then_inc(S["dve_step"], 1)
                dve.wait_ge(S["dve_step"], made.next("dve_step"))
                tt_(p3, l3, mx.unsqueeze(2).to_broadcast([P, TT, E]), ALU.subtract).then_inc(S["dve_step"], 1)
                dve.wait_ge(S["dve_step"], made.next("dve_step"))
                earlier = cst[:, CONST["earlier"]].rearrange("p (e f) -> p e f", e=E)
                for tt in range(TT):
                    this = l3[:, tt, :].unsqueeze(2).to_broadcast([P, E, E])
                    other = l3[:, tt, :].unsqueeze(1).to_broadcast([P, E, E])
                    s0, s1 = (sq[:, i, :].rearrange("p (e f) -> p e f", e=E) for i in range(2))
                    tt_(s0, other, this, ALU.is_gt)
                    tt_(s1, other, this, ALU.is_equal).then_inc(S["dve_step"], 1)
                    dve.wait_ge(S["dve_step"], made.next("dve_step"))
                    tt_(s1, s1, earlier, ALU.mult).then_inc(S["dve_step"], 1)
                    dve.wait_ge(S["dve_step"], made.next("dve_step"))
                    tt_(s0, s0, s1, ALU.add).then_inc(S["dve_step"], 1)
                    dve.wait_ge(S["dve_step"], made.next("dve_step"))
                    dve.tensor_reduce(rank[:, tt * E:(tt + 1) * E], s0, AX.X, ALU.add).then_inc(S["dve_step"], 1)
                    dve.wait_ge(S["dve_step"], made.next("dve_step"))
                ts_(rank, rank, 1.5, None, ALU.is_lt).then_inc(S["router_w"], 1)
                dve.wait_ge(S["router_w"], made.next("router_w"))
                dve.wait_ge(S["router_exp"], 1)
                tt_(p, p, rank, ALU.mult).then_inc(S["dve_step"], 1)
                dve.wait_ge(S["dve_step"], made.next("dve_step"))
                dve.tensor_reduce(mx, p3, AX.X, ALU.add).then_inc(S["dve_step"], 1)
                dve.wait_ge(S["dve_step"], made.next("dve_step"))
                dve.reciprocal(mx, mx).then_inc(S["dve_step"], 1)
                dve.wait_ge(S["dve_step"], made.next("dve_step"))
                tt_(moe_w[:], p3, mx.unsqueeze(2).to_broadcast([P, TT, E]), ALU.mult).then_inc(S["dve_step"], 1)
                dve.wait_ge(S["dve_step"], made.next("dve_step"))
                for tt in range(TT):
                    ins = copy(moe_cols[:, tt, :, :], moe_w[:, tt, :].unsqueeze(2).to_broadcast([P, E, D_FF // FCH]))
                ins.then_inc(S["dve_step"], 1)
                dve.wait_ge(S["dve_step"], made.next("dve_step"))

            def mlp_dve(kind, n_chunks, base, per_step):
                gated = kind != "mlp"
                nb = 2 if gated else 3
                scales = moe_cols[:].rearrange("p t e f -> p t (e f)")

                def hidden(i, slot, early):
                    dve.wait_ge(S["act_out"], i + 1)
                    if not early:
                        dve.wait_ge(S["y_full"], i - nb + 1)
                    b = bank[(2 * slot + 1) if gated else slot]
                    tt_(hT[:, slot, :, :], gate_s[:, slot, :, :], b[:].rearrange("p (m t) -> p m t", m=2), ALU.mult).then_inc(S["h_ready"], 1)

                def add(i, j):
                    dve.wait_ge(S["y_full"], i + 1)
                    if not (isinstance(i, int) and i == 0):
                        dve.wait_ge(S["y_read"], i)
                    for tt in range(TT):
                        for h in range(2):
                            xs = x_tm[:, tt, h * 512:(h + 1) * 512]
                            s = scales[:, tt, j] if kind == "moe" else 1.0
                            ins = stt(xs, bank[4 + 2 * tt + h][:], s, xs, ALU.mult, ALU.add)
                    ins.then_inc(S["y_read"], 1)

                hidden(base, 0, True)
                lead = nb + (n_chunks - nb) % per_step
                for s in range(1, lead):
                    hidden(base + s, s % nb, s < nb)
                    add(base + s - 1, slice(s - 1, s))
                with dve.Fori(0, (n_chunks - lead) // per_step) as turn:
                    for s in range(lead, lead + per_step):
                        hidden(turn * per_step + (base + s), s % nb, False)
                        add(turn * per_step + (base + s - 1), bass.ds(turn * per_step + (s - 1), 1))
                add(base + n_chunks - 1, slice(n_chunks - 1, n_chunks))
                dve.wait_ge(S["y_read"], base + n_chunks)

            def rms_x(n, src):
                dve.wait_ge(S["rms_std"], n + 1)
                if n:
                    dve.wait_ge(S["x_turned"], 4 * (4, 5, 6, 8, 9, 11)[n])
                dve.reciprocal(rs[:, 4:4 + TT], rs[:, 2:2 + TT]).then_inc(S["dve_step"], 1)
                dve.wait_ge(S["dve_step"], made.next("dve_step"))
                for tt in range(TT):
                    ins = ts_(xn[:, tt, :], src[:, tt, :], rs[:, 4 + tt:5 + tt], None, ALU.mult)
                ins.then_inc(S["rms_x"], 1)
                dve.wait_ge(S["rms_x"], made.next("rms_x"))

            def rotate(dst1, dst2, src, n, cos, sin, parts=slice(0, P)):
                a, b = (scr[parts, i, 0:n * HEAD] for i in range(2))
                w = a.shape[0]
                for t, f in ((a, cos), (b, sin)):
                    ins = tt_(t.rearrange("p (n d e) -> p n d e", d=2, e=32), src.rearrange("p n (d e) -> p n d e", d=2),
                              f.unsqueeze(1).unsqueeze(1).to_broadcast([w, n, 2, 32]), ALU.mult)
                ins.then_inc(S["dve_step"], 1)
                dve.wait_ge(S["dve_step"], made.next("dve_step"))
                a, b = (t.rearrange("p (n e) -> p n e", e=HEAD) for t in (a, b))
                for d, x0, x1, op in ((dst1, a[:, :, 0:32], b[:, :, 32:], ALU.subtract), (dst2, b[:, :, 0:32], a[:, :, 32:], ALU.add)):
                    for dst in d:
                        ins = tt_(dst, x0, x1, op)
                return ins

            def norm_heads(l):
                sets = head_sets(l)
                at = 8
                for src, n, _, _, _ in sets:
                    for tt in range(TT):
                        sq = scr[:, tt, 0:n * HEAD]
                        tt_(sq, src[:, tt, :], src[:, tt, :], ALU.mult).then_inc(S["dve_step"], 1)
                        dve.wait_ge(S["dve_step"], made.next("dve_step"))
                        ins = dve.tensor_reduce(rs[:, at:at + n], sq.rearrange("p (n e) -> p n e", e=HEAD), AX.X, ALU.add)
                        last = at + n == 8 + TT * sum(s[1] for s in sets)
                        sem = "rms_ss" if last else "dve_step"
                        ins.then_inc(S[sem], 1)
                        dve.wait_ge(S[sem], made.next(sem))
                        at += n
                dve.wait_ge(S["qk_std"], l + 1)
                dve.reciprocal(rs[:, 8:at], rs[:, 8:at]).then_inc(S["dve_step"], 1)
                dve.wait_ge(S["dve_step"], made.next("dve_step"))
                at, end = 8, at
                for src, n, gain, rotary, place in sets:
                    for tt in range(TT):
                        x3 = src[:, tt, :].rearrange("p (n e) -> p n e", e=HEAD)
                        tt_(x3, x3, rs[:, at:at + n].unsqueeze(2).to_broadcast([P, n, HEAD]), ALU.mult).then_inc(S["dve_step"], 1)
                        dve.wait_ge(S["dve_step"], made.next("dve_step"))
                        ins = tt_(x3, x3, row[:, gain:gain + HEAD].unsqueeze(1).to_broadcast([P, n, HEAD]), ALU.mult)
                        at += n
                        if l and at == end:
                            ins.then_inc(S["qk_ready"], 1)
                            dve.wait_ge(S["qk_ready"], made.next("qk_ready"))
                        else:
                            ins.then_inc(S["dve_step"], 1)
                            dve.wait_ge(S["dve_step"], made.next("dve_step"))
                        if rotary:
                            cos, sin = (atc[:, ATTN[f]].rearrange("p (t e) -> p t e", t=TT)[:, tt, :] for f in ("cos", "sin"))
                            if place is None:
                                d1, d2 = [x3[:, :, 0:32]], [x3[:, :, 32:]]
                            else:
                                d1, d2 = ([twice[:, tt, place:place + n, i, e:e + 32] for i in range(2)] for e in (0, 32))
                            rotate(d1, d2, x3, n, cos, sin).then_inc(S["dve_step"], 1)
                            dve.wait_ge(S["dve_step"], made.next("dve_step"))
                if l == 0:
                    for tt in range(TT):
                        for i in range(2):
                            ins = copy(twice[:, tt, 6:12, i, :], proj[:, tt, 768:1152].rearrange("p (n e) -> p n e", e=HEAD))
                    ins.then_inc(S["qk_ready"], 1)
                    dve.wait_ge(S["qk_ready"], made.next("qk_ready"))

            def compress():
                pos = col[:, COLS["cmp_pos"]].rearrange("p (k l) -> p k l", k=2)
                dve.wait_ge(S["turnq_act"], BANKS_T[0] // 2)
                for kv in range(2):
                    for g in range(NSA_G):
                        item = qkT[:, 12 + 3 * kv + g, :].rearrange("p (a s) -> p a s", s=CMP_STRIDE)
                        for odd in range(2):
                            hd = slice(HEAD * odd, HEAD * (odd + 1))
                            for hi in range(2):
                                ins = tt_(cmp_in[hd, kv, 8 * hi:8 * hi + 8, g, :].rearrange("p l i -> p i l"), item[hd, hi:hi + N_CMP, odd::2],
                                          pos[hd, kv, 8 * hi:8 * hi + 8].unsqueeze(1).to_broadcast([HEAD, N_CMP, 8]), ALU.add)
                ins.then_inc(S["cmp_tb"], 1)
                dve.wait_ge(S["cmp_tb"], made.next("cmp_tb"))
                dve.wait_ge(S["cmp_o_mm"], 1)
                blk = slice(0, N_CMP)
                for kv in range(2):
                    b2 = row[blk, ROWS["cmp_b2"]][:, kv * HEAD:(kv + 1) * HEAD].unsqueeze(1).to_broadcast([N_CMP, NSA_G, HEAD])
                    ins = tt_(cmp_kv[blk, kv, :, :], bank[0][blk, kv * NSA_G * HEAD:(kv + 1) * NSA_G * HEAD].rearrange("p (g e) -> p g e", e=HEAD), b2, ALU.add)
                ins.then_inc(S["dve_step"], 1)
                dve.wait_ge(S["dve_step"], made.next("dve_step"))
                k = cmp_kv[blk, 0, :, :]
                tt_(cmp_dup[blk, :, 0, :], k, k, ALU.mult).then_inc(S["dve_step"], 1)
                dve.wait_ge(S["dve_step"], made.next("dve_step"))
                dve.tensor_reduce(rs[blk, 4:4 + NSA_G], cmp_dup[blk, :, 0, :], AX.X, ALU.add).then_inc(S["cmp_kv"], 1)
                dve.wait_ge(S["cmp_kv"], made.next("cmp_kv"))
                dve.wait_ge(S["cmp_k_std"], 1)
                dve.reciprocal(rs[blk, 4:4 + NSA_G], rs[blk, 4:4 + NSA_G]).then_inc(S["dve_step"], 1)
                dve.wait_ge(S["dve_step"], made.next("dve_step"))
                tt_(k, k, rs[blk, 4:4 + NSA_G].unsqueeze(2).to_broadcast([N_CMP, NSA_G, HEAD]), ALU.mult).then_inc(S["dve_step"], 1)
                dve.wait_ge(S["dve_step"], made.next("dve_step"))
                tt_(k, k, row[blk, ROWS["a_k"]][:, 0:HEAD].unsqueeze(1).to_broadcast([N_CMP, NSA_G, HEAD]), ALU.mult).then_inc(S["dve_step"], 1)
                dve.wait_ge(S["dve_step"], made.next("dve_step"))
                d1, d2 = ([cmp_dup[blk, :, i, e:e + 32] for i in range(2)] for e in (0, 32))
                rotate(d1, d2, k, NSA_G, atc[blk, ATTN["cmp_cos"]], atc[blk, ATTN["cmp_sin"]], blk).then_inc(S["cmp_k_ready"], 1)
                dve.wait_ge(S["cmp_k_ready"], made.next("cmp_k_ready"))
                dve.wait_ge(S["cmp_kT_mm"], 1)
                copy(cmp_kT[:, :, 0:N_CMP], bank[1][:, 0:NSA_G * 16].rearrange("p (g i) -> p g i", g=NSA_G)[:, :, 0:N_CMP]).then_inc(S["cmp_kT"], 1)
                dve.wait_ge(S["cmp_kT"], made.next("cmp_kT"))
                dve.wait_ge(S["cmp_s_mm"], 1)
                s3 = cmp_s[:].rearrange("p h t i -> p (h t) i")[:, :, 0:N_CMP]
                mask = atc[:, ATTN["cmp"]].rearrange("p (t i) -> p t i", t=TT)[:, :, 0:N_CMP]
                for odd in range(2):
                    ins = tt_(cmp_s[:, odd::2, :, 0:N_CMP], bank[2 + odd][:, 0:6 * TT * 16].rearrange("p (h t i) -> p h t i", h=6, t=TT)[:, :, :, 0:N_CMP],
                              mask.unsqueeze(1).to_broadcast([P, 6, TT, N_CMP]), ALU.add)
                ins.then_inc(S["dve_step"], 1)
                dve.wait_ge(S["dve_step"], made.next("dve_step"))
                n = NSA_HEADS * TT
                mx = rs[:, 8:8 + n]
                dve.tensor_reduce(mx, s3, AX.X, ALU.max).then_inc(S["dve_step"], 1)
                dve.wait_ge(S["dve_step"], made.next("dve_step"))
                tt_(s3, s3, mx.unsqueeze(2).to_broadcast([P, n, N_CMP]), ALU.subtract).then_inc(S["cmp_s"], 1)
                dve.wait_ge(S["cmp_s"], made.next("cmp_s"))
                dve.wait_ge(S["cmp_e"], 1)
                dve.wait_ge(S["nsa_gates"], 1)
                dve.tensor_reduce(mx, s3, AX.X, ALU.add).then_inc(S["dve_step"], 1)
                dve.wait_ge(S["dve_step"], made.next("dve_step"))
                dve.reciprocal(mx, mx).then_inc(S["dve_step"], 1)
                dve.wait_ge(S["dve_step"], made.next("dve_step"))
                tt_(mx, mx, coef[:, 0].rearrange("p h t -> p (h t)"), ALU.mult).then_inc(S["dve_step"], 1)
                dve.wait_ge(S["dve_step"], made.next("dve_step"))
                m3 = mx.rearrange("p (h t) -> p h t", t=TT)
                tt_(m3, m3, atc[:, ATTN["cmp_ok"]].unsqueeze(1).to_broadcast([P, NSA_HEADS, TT]), ALU.mult).then_inc(S["dve_step"], 1)
                dve.wait_ge(S["dve_step"], made.next("dve_step"))
                tt_(s3, s3, mx.unsqueeze(2).to_broadcast([P, n, N_CMP]), ALU.mult).then_inc(S["cmp_p"], 1)
                dve.wait_ge(S["cmp_p"], made.next("cmp_p"))
                for h in range(NSA_HEADS):
                    dve.wait_ge(S["cmp_pv_mm"], h + 1)
                    copy(o_tm[:, :, h * HEAD:(h + 1) * HEAD], bank[6 + h % 2][:, 0:TT * HEAD].rearrange("p (t e) -> p t e", t=TT)).then_inc(S["cmp_done"], 1)
                    dve.wait_ge(S["cmp_done"], made.next("cmp_done"))

            def attend(l):
                n0 = 0 if l == 0 else len(units(0))
                todo = units(l)

                def maxima(n):
                    kind, h, tile = todo[n]
                    u = n0 + n
                    s = u % 2
                    mx, neg = rs[:, 136 + 2 * s:138 + 2 * s], rs[:, 140 + 2 * s:142 + 2 * s]
                    dve.wait_ge(S["score_mm"], u + 1)
                    if u >= 2:
                        dve.wait_ge(S["score_exp"], u - 1)
                    k = TT
                    if kind == "dil":
                        k, w = 1, 3 * P * (tile + 1)
                        mask = atc[:, ATTN[f"dil{tile}"]]
                        for a in range(0, w, 512):
                            e = min(a + 512, w)
                            ins = tt_(s_sb[:, s, a:e], bank[2 * s + a // 512][:, 0:e - a], mask[:, a:e], ALU.add)
                        ins.then_inc(S["dve_step"], 1)
                        dve.wait_ge(S["dve_step"], made.next("dve_step"))
                        ins = dve.tensor_reduce(mx[:, 0:1], s_sb[:, s, 0:w], AX.X, ALU.max)
                    elif kind == "mem":
                        ins = dve.tensor_reduce(mx, bank[2 * s][:].rearrange("p (t k) -> p t k", t=TT), AX.X, ALU.max)
                    else:
                        tt_(s_sb[:, s, 0:3 * P], bank[2 * s][:, 0:3 * P], causal, ALU.add).then_inc(S["dve_step"], 1)
                        dve.wait_ge(S["dve_step"], made.next("dve_step"))
                        dve.tensor_reduce(mx[:, 0:1], s_sb[:, s, 0:P], AX.X, ALU.max)
                        ins = dve.tensor_reduce(mx[:, 1:2], s_sb[:, s, P:3 * P], AX.X, ALU.max)
                    ins.then_inc(S["dve_step"], 1)
                    dve.wait_ge(S["dve_step"], made.next("dve_step"))
                    ts_(neg[:, 0:k], mx[:, 0:k], -SCALE, None, ALU.mult).then_inc(S["score_max"], 1)
                    dve.wait_ge(S["score_max"], made.next("score_max"))

                def finish(n):
                    kind, h, tile = todo[n]
                    u = n0 + n
                    s = u % 2
                    k = 1 if kind == "dil" else TT
                    inv_, scale_ = rs[:, 148 + 2 * s:148 + 2 * s + k], rs[:, 152 + 2 * s:152 + 2 * s + k]
                    dve.wait_ge(S["pv_mm"], u + 1)
                    dve.reciprocal(inv_, rs[:, 144 + 2 * s:144 + 2 * s + k]).then_inc(S["dve_step"], 1)
                    dve.wait_ge(S["dve_step"], made.next("dve_step"))
                    if kind == "dil":
                        ins = ts_(o_tm[:, tile, h * HEAD:(h + 1) * HEAD], bank[6 + s][:, 0:HEAD], inv_, None, ALU.mult)
                    else:
                        pv = bank[6 + s][:, 0:TT * HEAD].rearrange("p (t e) -> p t e", t=TT)
                        base = {"mem": NSA_HEADS * HEAD if l == 0 else SLOTS * HEAD}.get(kind, 0)
                        o = o_tm[:, :, base + h * HEAD:base + (h + 1) * HEAD]
                        if kind == "mem":
                            ins = tt_(o, pv, inv_.unsqueeze(2).to_broadcast([P, TT, HEAD]), ALU.mult)
                        else:
                            tt_(scale_, inv_, coef[:, 1 if kind == "sel" else 2, h, :], ALU.mult).then_inc(S["dve_step"], 1)
                            dve.wait_ge(S["dve_step"], made.next("dve_step"))
                            part_ = scr[:, 0, 0:TT * HEAD].rearrange("p (t e) -> p t e", t=TT)
                            tt_(part_, pv, scale_.unsqueeze(2).to_broadcast([P, TT, HEAD]), ALU.mult).then_inc(S["dve_step"], 1)
                            dve.wait_ge(S["dve_step"], made.next("dve_step"))
                            ins = tt_(o, o, part_, ALU.add)
                    ins.then_inc(S["pv_read"], 1)
                    dve.wait_ge(S["pv_read"], made.next("pv_read"))

                maxima(0)
                for n in range(len(todo)):
                    if n + 1 < len(todo):
                        maxima(n + 1)
                    finish(n)

            def attention_dve(l):
                n_turn = 4 + 4 * l
                dve.wait_ge(S["params_in"], 16 * 4)
                rms_x(3 * l, o_tm)
                copy_xT(n_turn, f"mem_norm{l}")
                rms_x(3 * l + 1, x_tm)
                if l == 0:
                    copy_xT(n_turn + 1, "attn_norm0")
                else:
                    copy_xT(n_turn + 1, "kv_norm")
                    copy_xT(n_turn + 2, "attn_norm1")
                dve.wait_ge(S["attn_read"], (11, 24)[l])
                norm_heads(l)
                n0 = 0 if l == 0 else BANKS_T[0]
                for n in range(BANKS_T[l]):
                    if (n0 + n) % 2 == 0:
                        dve.wait_ge(S["turnq_mm"], n0 + n + 1)
                        copy(qkT[:, 2 * n:2 * n + 2, :], bank[n % 4][:].rearrange("p (i t) -> p i t", i=2)).then_inc(S["turnq_dve"], 1)
                        dve.wait_ge(S["turnq_dve"], made.next("turnq_dve"))
                if l == 0:
                    compress()
                else:
                    dve.memset(o_tm[:, :, (SLOTS + MEM_HEADS) * HEAD:], 0.0).then_inc(S["dve_step"], 1)
                    dve.wait_ge(S["dve_step"], made.next("dve_step"))
                attend(l)
                n_turn = 6 if l == 0 else 11
                copy_xT(n_turn)
                dve.wait_ge(S["proj2_mm"], l + 1)
                for tt in range(TT):
                    for h in range(2):
                        xs = x_tm[:, tt, h * 512:(h + 1) * 512]
                        ins = tt_(xs, xs, bank[2 * tt + h][:], ALU.add)
                ins.then_inc(S["x_done"], 1)
                dve.wait_ge(S["x_done"], made.next("x_done"))
                rms_x(3 * l + 2, x_tm)
                copy_xT(n_turn + 1, f"mlp_norm{l}")
                mlp_dve("mlp", D_FF_2 // FCH, chunks + l * (D_FF_2 // FCH), 3)

            dve.memset(u_pad[:, :, 0:CONF_TAPS - 1], 0.0)
            dve.memset(s_pad[:, :, 0:SHORT_TAPS - 1], 0.0)
            dve.memset(u_sb[:], 0.0)
            dve.memset(pz[:, :, :, 0:1], 0.0).then_inc(S["cleared"], 1)
            dve.wait_ge(S["cleared"], made.next("cleared"))
            dve.wait_ge(S["consts_in"], 16)
            dve.wait_ge(S["params_in"], 16 * 3)
            chunks = 0
            for l in range(DEPTH):
                mixer_dve(l)
                layer_norm(2 * l)
                copy_xT(2 * l + 1)
                scale_x(2 * l + 1)
                if l == 0:
                    mlp_dve("ffn", D_FF // FCH, 0, 2)
                    chunks = D_FF // FCH
                else:
                    route()
                    mlp_dve("moe", N_EXPERTS * D_FF // FCH, chunks, 2)
                    chunks += N_EXPERTS * D_FF // FCH
                layer_norm(2 * l + 1)
            for l in range(DEPTH):
                attention_dve(l)

        @block.gpsimd
        def _(pool):
            for dst, src in ((col, cols), (mid, mids)):
                pool.dma_start(dst[:], src).then_inc(S["params_in"], 16)
            pool.dma_start(row[:], rows.partition_broadcast(P)).then_inc(S["params_in"], 16)
            for n in range(2 * DEPTH):
                if n:
                    pool.wait_ge(S["ln_x_done"], n)
                pool.dma_start(ln_row[:], ln_rows[n].partition_broadcast(P)).then_inc(S["ln_rows_in"], 16)
            pool.wait_ge(S["ln_x_done"], 2 * DEPTH)
            pool.dma_start(atc[:], attn_consts).then_inc(S["params_in"], 16)
            for l in range(DEPTH):
                if l:
                    pool.wait_ge(S["proj2_mm"], l)
                pool.dma_start(o_tm[:], mem.rearrange("(t p) d -> p t d", p=P)).then_inc(S["mem_in"], 16)


def lay_out(i):
    def f(name):
        return np.asarray(i[name], np.float32)

    def blocks(v):
        return v.reshape(-1, P).T

    def col_panel(w, n):
        c = w[:, n * PC:(n + 1) * PC]
        if c.shape[1] < PC:
            c = np.pad(c, ((0, 0), (0, PC - c.shape[1])))
        return c.reshape(KB, P, PC).transpose(1, 0, 2)

    def row_panel(w, n):
        return w[n * PR * P:(n + 1) * PR * P].reshape(PR, P, D).transpose(1, 0, 2)

    per = D_FF // FCH
    branch_out = [np.concatenate([f(n)[l] for n in ("rwkv_w_o", "conf_w_o", "short_w_o")]) for l in range(DEPTH)]
    w_in, w_out, mem_kv = f("w_in"), f("w_out"), f("w_mem_kv_2")
    ffn = [f("ffn_w_gate"), f("ffn_w_up"), f("ffn_w_down")]
    moe = [f("moe_w_gate")[0], f("moe_w_up")[0], f("moe_w_down")[0]]
    a_in, a_out, kv, b_in, b_out = f("a_w_in_2")[0], f("a_w_out_2")[0], f("w_kv_shared_2"), f("b_w_in_2")[0], f("b_w_out_2")[0]
    cmp_w1, up, down = f("a_cmp_w1_2")[0], f("w_up_2"), f("w_down_2")

    def panel(kind, l, n):
        if kind == "w_in":
            return col_panel(w_in[l], n)
        if kind == "mix":
            return col_panel(branch_out[l], n)
        if kind == "w_out":
            return row_panel(w_out[l], n)
        if kind in ("gate", "up", "down"):
            m = ("gate", "up", "down").index(kind)
            w = (moe if l else ffn)[m][n // per]
            return row_panel(w, n % per) if kind == "down" else col_panel(w, n % per)
        if kind == "mem_kv":
            return col_panel(mem_kv[l], n)
        if kind == "cmp":
            return cmp_w1[n // 2].reshape(2, KB, P, CMP_HIDDEN)[n % 2].transpose(1, 0, 2)
        if kind in ("mlp_up", "mlp_down"):
            return col_panel(up[l], n) if kind == "mlp_up" else row_panel(down[l], n)
        w = {"a_in": a_in, "kv": kv, "b_in": b_in, "a_out": a_out, "b_out": b_out}[kind]
        return row_panel(w, n) if kind.endswith("out") else col_panel(w, n)

    weights = np.empty((N_PANELS, P, PANEL), np.float32)
    for n, (kind, l, m) in enumerate(ORDER):
        weights[n] = panel(kind, l, m).reshape(P, PANEL)

    cols = np.zeros((P, COLS.n), np.float32)
    for l in range(DEPTH):
        for name, src in (("mu", "rwkv_mu"), ("a0", "rwkv_a0"), ("k_k", "rwkv_k_k"), ("k_a", "rwkv_k_a"), ("r_k", "rwkv_r_k"),
                          ("gn_g", "rwkv_ln_g"), ("gn_b", "rwkv_ln_b"), ("conf_dw_b", "conf_dw_b"), ("conf_ln_g", "conf_ln_g"),
                          ("conf_ln_b", "conf_ln_b"), ("attn_norm", "attn_norm_2"), ("mlp_norm", "mlp_norm_2"),
                          ("mem_norm", "mem_norm_2")):
            cols[:, COLS[f"{name}{l}"]] = blocks(f(src)[l].reshape(-1))
        for name in ("conf_dw", "short_dw"):
            w = f(name)[l]
            cols[:, COLS[f"{name}{l}"]] = w.T.reshape(2, P, -1).transpose(1, 0, 2).reshape(P, -1)
    cols[:, COLS["kv_norm"]] = blocks(f("kv_norm_2"))
    cols[:, COLS["cmp_b1"]] = blocks(f("a_cmp_b1_2").reshape(-1))
    cols[:, COLS["cmp_pos"]] = f("a_cmp_pos_2")[0].reshape(2, CMP_BLOCK // 2, P).transpose(2, 0, 1).reshape(P, -1)

    mids = np.zeros((P, MIDS.n), np.float32)
    for l in range(DEPTH):
        mids[:, MIDS[f"w2a2{l}"]] = np.concatenate([f("rwkv_w2")[l], f("rwkv_a2")[l]])
        mids[:, MIDS[f"g2{l}"]] = f("rwkv_g2")[l]
    mids[:, MIDS["router"]] = f("moe_router")[0].reshape(KB, P, N_EXPERTS).transpose(1, 0, 2).reshape(P, -1)
    mids[:, MIDS["cmp_w2"]] = f("a_cmp_w2_2")[0].reshape(2, 2, P, HEAD).transpose(2, 0, 1, 3).reshape(P, -1)

    rows = np.concatenate([f("rwkv_w0").reshape(-1), f("a_q_norm_2").reshape(-1), f("a_k_norm_2").reshape(-1),
                           f("mem_q_norm_2").reshape(-1), f("mem_k_norm_2").reshape(-1), f("a_cmp_b2_2").reshape(-1),
                           f("kv_k_norm_2").reshape(-1), f("b_q_norm_2").reshape(-1)])
    ln_rows = np.stack([np.stack([f(g)[l], f(b)[l]]) for l in range(DEPTH)
                        for g, b in (("ln1_g", "ln1_b"), ("ln2_g", "ln2_b"))])
    consts, attn_consts = shape_constants()
    return {"weights": weights, "consts": consts, "attn_consts": attn_consts, "cols": cols, "mids": mids, "rows": rows,
            "ln_rows": ln_rows, "x": f("x")[0], "mem": f("mem_2")[0]}


def kernel(**inputs):
    import concourse.bacc as bacc
    from concourse.bass_utils import run_bass_kernel_spmd

    arrays = {name: np.ascontiguousarray(a) for name, a in lay_out(inputs).items()}
    nc = bacc.Bacc("TRN2", target_bir_lowering=False, num_devices=1)
    aps = {name: nc.dram_tensor(f"in_{name}", a.shape, F32, kind="ExternalInput").ap() for name, a in arrays.items()}
    out = nc.dram_tensor("out", (T, D), F32, kind="ExternalOutput").ap()
    program(nc, out=out, **aps)
    r = run_bass_kernel_spmd(nc, [{f"in_{name}": a for name, a in arrays.items()}], core_ids=[0])
    return r.results[0]["out"].reshape(1, T, D)
```

```python
from contextlib import ExitStack

import concourse.bass as bass
from concourse import mybir
import numpy as np

F32 = mybir.dt.float32
ALU = mybir.AluOpType
ACT = mybir.ActivationFunctionType
AX = mybir.AxisListType

P = 128
D = 1024
T = 256
TT = T // P
KB = D // P
DEPTH = 2
ALPHA = (2.0 * DEPTH) ** 0.25
HEAD = 64

W = 512
RH = W // HEAD
NC = W // P
KAPPA = float(np.exp(-0.5))
CHUNK = 64
CONF = 256
CONF_TAPS = 31
SHORT = 256
SHORT_TAPS = 3
RWKV_BLOCKS = 14
N_EXPERTS = 8
TOP_K = 2
D_FF = 2816
D_FF_2 = 4096
FCH = 256
CAP = 128
ITEMS = N_EXPERTS + (TOP_K * T) // (CAP + 1)
LN_EPS = 1e-5
GN_EPS = 64e-5
RMS_EPS = 1e-6

NSA_HEADS = 12
NSA_G = 3
NSA_R = NSA_HEADS // NSA_G
MEM_HEADS = 4
N_CMP = 15
CMP_BLOCK = 32
CMP_STRIDE = 16
CMP_HIDDEN = 256
DIL = ((128, 1), (512, 4), (2048, 16))
SLOTS = 8
SCALE = HEAD ** -0.5
NEG = -1e30
ROPE_THETA = 10000.0

PANEL = 2048
RING = 3
PC = PANEL // KB
PR = PANEL // D


class Fields:

    def __init__(self, *sizes):
        self.at, self.n = {}, 0
        for name, n in sizes:
            self.at[name] = (self.n, n)
            self.n += n

    def __getitem__(self, name):
        a, n = self.at[name]
        return slice(a, a + n)


COLS = Fields(*[(f"{name}{l}", n) for l in range(DEPTH) for name, n in (
    ("mu", RWKV_BLOCKS), ("a0", NC), ("k_k", NC), ("k_a", NC), ("r_k", NC), ("gn_g", NC), ("gn_b", NC),
    ("conf_dw", 2 * CONF_TAPS), ("conf_dw_b", 2), ("conf_ln_g", 2), ("conf_ln_b", 2),
    ("short_dw", 2 * SHORT_TAPS), ("ln1_g", KB), ("ln1_b", KB), ("ln2_g", KB), ("ln2_b", KB),
    ("attn_norm", KB), ("mlp_norm", KB), ("mem_norm", KB))],
    ("kv_norm", KB), ("cmp_b1", 4), ("cmp_pos", 2 * CMP_BLOCK // 2))
MIDS = Fields(*[(f"{name}{l}", W) for l in range(DEPTH) for name in ("w2a2", "g2")],
              ("router", KB * N_EXPERTS), ("cmp_w2", 2 * 2 * HEAD))
ROWS = Fields(("w00", W), ("w01", W), ("a_q", HEAD), ("a_k", 3 * HEAD), ("mem_q0", HEAD), ("mem_q1", HEAD),
              ("mem_k0", HEAD), ("mem_k1", HEAD), ("cmp_b2", 2 * HEAD), ("kv_k", HEAD), ("b_q", 3 * HEAD))
CONST = Fields(("ident", P), ("ones", P), ("heads", P), ("tri", 2 * P), ("unit_mask", 4 * P), ("inv_mask", 3 * P),
               ("earlier", N_EXPERTS * N_EXPERTS),
               ("before", P), ("count", CAP), ("ln_eps", 1), ("gn_eps", 1), ("rms_eps", 1))
ATTN = Fields(("causal", 3 * P), ("dil0", 3 * P), ("dil1", 3 * T), ("cmp", TT * 16), ("cmp_ok", TT),
              ("cos", TT * 32), ("sin", TT * 32), ("cmp_cos", 32), ("cmp_sin", 32))


def shape_constants():
    c = np.zeros((P, CONST.n), np.float32)
    i, j = np.arange(P)[:, None], np.arange(P)[None, :]

    def same(n):
        return i // n == j // n

    c[:, CONST["ident"]] = i == j
    c[:, CONST["ones"]] = 1
    c[:, CONST["heads"]] = same(HEAD)
    up, up_eq, low = same(CHUNK) & (i < j), same(CHUNK) & (i <= j), same(CHUNK) & (i > j)
    c[:, CONST["tri"]] = np.concatenate([up_eq, up], 1)
    c[:, CONST["unit_mask"]] = np.concatenate([up & same(16), up_eq, up, up_eq], 1)
    c[:, CONST["inv_mask"]] = np.concatenate([low & same(16), low & same(32) & ~same(16), low & ~same(32)], 1)
    e = np.arange(N_EXPERTS)
    c[:, CONST["earlier"]] = (e[None, :] < e[:, None]).reshape(1, -1)
    c[:, CONST["before"]] = i < j
    c[:, CONST["count"]] = np.arange(CAP)
    c[:, CONST["ln_eps"]], c[:, CONST["gn_eps"]], c[:, CONST["rms_eps"]] = LN_EPS, GN_EPS, RMS_EPS

    a = np.zeros((P, ATTN.n), np.float32)
    causal = np.where(j <= i, 0, NEG)
    a[:, ATTN["causal"]] = np.concatenate([causal, np.zeros((P, P)), causal], 1)
    t, s = np.arange(T)[:, None], np.arange(T)[None, :]
    dil = [np.where((s <= t) & ((t - s) % d == 0) & (t - s <= w), 0, NEG) for w, d in DIL]
    a[:, ATTN["dil0"]] = np.concatenate([m[:P, :P] for m in dil], 1)
    a[:, ATTN["dil1"]] = np.concatenate([m[P:] for m in dil], 1)
    end = np.arange(N_CMP) * CMP_STRIDE + CMP_BLOCK - 1
    ok = np.zeros((T, 16), bool)
    ok[:, :N_CMP] = end[None, :] <= t
    a[:, ATTN["cmp"]] = np.where(ok, 0, NEG).reshape(TT, P, 16).transpose(1, 0, 2).reshape(P, -1)
    a[:, ATTN["cmp_ok"]] = ok.any(1).reshape(TT, P).T
    freq = ROPE_THETA ** (-np.arange(32, dtype=np.float32) / 32)

    def turns(pos):
        return np.asarray(pos, np.float32)[:, None] * freq.astype(np.float32)[None, :]

    for name, f in (("cos", np.cos), ("sin", np.sin)):
        a[:, ATTN[name]] = f(turns(np.arange(T))).reshape(TT, P, 32).transpose(1, 0, 2).reshape(P, -1)
        a[:N_CMP, ATTN["cmp_" + name]] = f(turns(end))
    return c, a


def chunk_panels(n, parts):
    order = []
    for step in range(n + 1):
        if step < n:
            order += [(p, step) for p in parts[:-1]]
        if step:
            order.append((parts[-1], step - 1))
    return order


IN_ORDER = [*range(7, 12), *range(7), *range(12, 24)]
CONV_PANELS = 5


def panel_order():
    order = []
    for l in range(DEPTH):
        order += [("w_in", l, n) for n in IN_ORDER] + [("mix", l, n) for n in range(4)]
        order += [("w_out", l, n) for n in range(4)]
        for e in range(N_EXPERTS if l else 1):
            order += [(p, l, e * (D_FF // FCH) + n) for p, n in chunk_panels(D_FF // FCH, ("gate", "up", "down"))]
    for l in range(DEPTH):
        order += [("mem_kv", l, n) for n in range(2)]
        if l == 0:
            order += [("a_in", 0, n) for n in range(9)] + [("cmp", 0, n) for n in range(4)]
            order += [("a_out", 0, n) for n in range(4)]
        else:
            order += [("kv", 1, n) for n in range(4)] + [("b_in", 1, n) for n in range(7)]
            order += [("b_out", 1, n) for n in range(3)]
        order += [(p, l, n) for p, n in chunk_panels(D_FF_2 // FCH, ("mlp_up", "mlp_down"))]
    return order


ORDER = panel_order()
N_PANELS = len(ORDER)
FF_CHUNKS = D_FF // FCH
PER_ITEM = 3 * FF_CHUNKS
BEFORE_MOE = ORDER.index(("gate", 1, 0))
AFTER_MOE = BEFORE_MOE + N_EXPERTS * PER_ITEM


class Made:

    def __init__(self):
        self.count = {}

    def next(self, name):
        self.count[name] = self.count.get(name, 0) + 1
        return self.count[name]


class PanelReader:

    def __init__(self, pe, ring, landed, used):
        self.pe, self.ring, self.landed, self.used = pe, ring, landed, used
        self.n, self.first, self.give_back = 0, 0, False

    def take(self, turn=0, per_turn=0):
        slot, fill = (self.first + self.n) % RING, self.n // RING + 1
        self.pe.wait_ge(self.landed[slot], (turn * (per_turn // RING) + fill) * 16)
        self.give_back = self.n > 0
        self.n += 1
        return self.ring[:, slot, :]

    def skip(self, n):
        assert n % RING == 0
        self.n += n

    def restart(self, landed, used, ins):
        ins.then_inc(self.used, 1)
        self.first, self.landed, self.used = (self.n + self.first) % RING, landed, used
        self.n, self.give_back = 0, False

    def mm(self, out, lhsT, rhs, start, stop):
        ins = self.pe.matmul(out, lhsT, rhs, start=start, stop=stop)
        if self.give_back:
            ins.then_inc(self.used, 1)
            self.give_back = False
        return ins


SIGNALS = """
panel_used_2 consts_in params_in ln_rows_in mem_in x_in out_stored panel_used cleared
dve_step act_step 
x_turned xT_dve xT_act
proj_out proj_read shifted 
lora_in lora_z lora_a lora_g decay_in aaa gate_lora
cum_mm decays kk_sq kk_mm kk_norm features bonus_in bonus_mm
turn_mm turned_dve turned_act unit_mm masks inv_mm inv_dve inv_act rhs_mm rhs u_mm u state_mm state o_mm o_read
gn_mean_mm gn_sq gn_var_mm gn_std branch_a conf_conv conf_mean_mm conf_sq conf_var_mm conf_std branch_b conf_silu branch_c
mix_mm mixed wout_mm ln_x ln_std ln_z ln_x_done
router_mm router_w router_exp gu_full act_out h_ready y_full y_read up_full relu_out h_ready_2 y_full_2 y_read_2
counts_mm items_ready one_hot routed_mm xe_dve xe_act spread y_half y_sb scatter_mm acc_read
rms_ss rms_std rms_x attn_proj attn_read qk_std qk_ready turnq_mm turnq_dve turnq_act
cmp_h_mm cmp_h cmp_o_mm cmp_tb cmp_kv cmp_k_std cmp_k_ready cmp_kT_mm cmp_kT cmp_s_mm cmp_s cmp_e cmp_p cmp_pT_mm cmp_pT cmp_pv_mm cmp_done
score_mm score_max score_exp pT_mm pT pv_mm pv_read proj2_mm x_done nsa_gates
""".split()


def program(nc, weights, consts, attn_consts, cols, mids, rows, ln_rows, x, mem, out):
    ctx = ExitStack()
    with ctx:
        def sb(name, *shape, stack=ctx):
            return stack.enter_context(nc.sbuf_tensor(name, [P, *shape], F32))

        S = {name: ctx.enter_context(nc.semaphore(name)) for name in SIGNALS}
        landed = [ctx.enter_context(nc.semaphore(f"panel_landed{i}")) for i in range(RING)]
        landed_2 = [ctx.enter_context(nc.semaphore(f"panel_landed_2_{i}")) for i in range(RING)]
        bank = [ctx.enter_context(nc.psum_tensor(f"bank{i}", [P, 512], F32)) for i in range(8)]

        ring = sb("ring", RING, PANEL)
        x_tm = sb("x_tm", TT, D)
        xT = sb("xT", KB, T)
        cst = sb("cst", CONST.n)
        col = sb("col", COLS.n)
        mid = sb("mid", MIDS.n)
        row = sb("row", ROWS.n)
        ln_row = sb("ln_row", 2, D)
        stat = sb("stat", 64)
        ident = cst[:, CONST["ident"]]
        ones = cst[:, CONST["ones"]]
        head_sum = cst[:, CONST["heads"]]
        tri = cst[:, CONST["tri"]]
        inv_mask = cst[:, CONST["inv_mask"]].rearrange("p (m s) -> p m s", m=3)
        unit_mask = cst[:, CONST["unit_mask"]]

        def c1(name, n=0):
            a = COLS[name].start + n
            return col[:, a:a + 1]

        def eps(name):
            return cst[:, CONST[name]]

        mixer = ExitStack()
        gates = sb("gates", 24, T, stack=mixer)
        pz = sb("pz", 2, 2, T + 1, stack=mixer)
        sh = sb("sh", RWKV_BLOCKS, T, stack=mixer)
        u_pad = sb("u_pad", 2, T + CONF_TAPS - 1, stack=mixer)
        s_pad = sb("s_pad", 2, T + SHORT_TAPS - 1, stack=mixer)
        conf_s = sb("conf_s", 2, T, stack=mixer)
        conv = sb("conv", 2, T, stack=mixer)
        gb = sb("gb", 2, T, stack=mixer)
        conv_c = sb("conv_c", 2, T, stack=mixer)
        a_ = sb("a_", NC, T, stack=mixer)
        kk = sb("kk", NC, T, stack=mixer)
        tmp = sb("tmp", NC, T, stack=mixer)
        p_in = sb("p_in", NC, T, stack=mixer)
        p_inv = sb("p_inv", NC, T, stack=mixer)
        p_ex = sb("p_ex", NC, T, stack=mixer)
        ar = sb("ar", NC, TT, 2, P, stack=mixer)
        vt = sb("vt", TT, W, stack=mixer)
        bt = sb("bt", TT, W, stack=mixer)
        kt = sb("kt", TT, W, stack=mixer)
        g_ = sb("g_", NC, T, stack=mixer)
        unit = sb("unit", RH, 4, P, stack=mixer)
        inv = sb("inv", RH, P, stack=mixer)
        rhs_sb = sb("rhs_sb", RH, HEAD, stack=mixer)
        u_sb = sb("u_sb", RH, HEAD, stack=mixer)
        state = sb("state", NC, 2, HEAD, stack=mixer)
        sh_flat = sh[:].rearrange("p b t -> p (b t)")
        a3 = sh_flat[:, 0:12 * P].rearrange("p (i m s) -> p i m s", i=4, m=3)
        pw = sh_flat[:, 12 * P:28 * P].rearrange("p (m s) -> p m s", m=4)
        xa = sb("xa", 4 * P, stack=mixer)
        xb = sb("xb", 4 * P, stack=mixer)
        loras = unit[:].rearrange("p h m s -> p (h m s)")[:, 0:2 * T].rearrange("p (a t) -> p a t", a=2)
        r_, k_, v_ = (sh[:, n * NC:(n + 1) * NC, :] for n in range(3))
        oT = p_ex
        sg_tok = kt
        yT = p_in
        mixT = sh[:, 0:KB, :]
        conv_sq = gb
        mixer.close()

        mlp = ExitStack()
        gate_s = sb("gate_s", 3, 2, T, stack=mlp)
        hT = sb("hT", 3, 2, T, stack=mlp)
        moe = ExitStack()
        E = N_EXPERTS
        rt = sb("rt", 6, E * E, stack=moe)
        moe_w = sb("moe_w", TT, E, stack=moe)
        moe_pos = sb("moe_pos", TT, E, stack=moe)
        tiles = sb("tiles", 4, E, stack=moe)
        in_item = sb("in_item", 4, (ITEMS + 1) * E, stack=moe)
        item_pos = sb("item_pos", TT, ITEMS + 1, stack=moe)
        item_w = sb("item_w", TT, ITEMS + 1, stack=moe)
        table = sb("table", ITEMS + 2, stack=moe)
        table_i = moe.enter_context(nc.sbuf_tensor("table_i", [P, ITEMS + 2], mybir.dt.int32))
        one_hot = sb("one_hot", TT, CAP, stack=moe)
        weighted = sb("weighted", TT, CAP, stack=moe)
        spread = sb("spread", TT, P, stack=moe)
        xeT = sb("xeT", KB, CAP, stack=moe)
        y_sb = sb("y_sb", D, stack=moe)
        acc = sb("acc", TT, D, stack=moe)
        moe.close()

        attn = ExitStack()
        atc = sb("atc", ATTN.n, stack=attn)
        xn = sb("xn", TT, D, stack=attn)
        proj = sb("proj", TT, 11 * PC, stack=attn)
        mem_kv = sb("mem_kv", TT, 2 * MEM_HEADS * HEAD, stack=attn)
        scr = sb("scr", 2, 24 * HEAD, stack=attn)
        qkT = sb("qkT", 22, T, stack=attn)
        o_tm = sb("o_tm", TT, D, stack=attn)
        p_sb = sb("p_sb", 4, 3 * T, stack=attn)
        pT_sb = sb("pT_sb", 2, 512, stack=attn)
        cmp_in = sb("cmp_in", 2, CMP_BLOCK // 2, NSA_G, N_CMP, stack=attn)
        cmp_h = sb("cmp_h", 2, 2, NSA_G * N_CMP, stack=attn)
        cmp_kv = sb("cmp_kv", 2, NSA_G, HEAD, stack=attn)
        cmp_dup = sb("cmp_dup", NSA_G, 2, HEAD, stack=attn)
        cmp_kT = sb("cmp_kT", NSA_G, 16, stack=attn)
        cmp_s = sb("cmp_s", NSA_HEADS, TT, 16, stack=attn)
        cmp_pT = sb("cmp_pT", 4, P, stack=attn)
        rs = sb("rs", 192, stack=attn)
        coef = sb("coef", 3, NSA_HEADS, TT, stack=attn)
        twice = p_sb[:].rearrange("p a b -> p (a b)").rearrange("p (t k d e) -> p t k d e", t=TT, d=2, e=HEAD)
        attn.close()
        mlp.close()
        causal = atc[:, ATTN["causal"]]
        MEM_Q = {0: 1920, 1: 1536 + 2 * SLOTS * HEAD}
        B_Q0 = 2 * SLOTS * HEAD

        def head_sets(l):
            mq = proj[:, :, MEM_Q[l]:MEM_Q[l] + MEM_HEADS * HEAD]
            mk = mem_kv[:, :, 0:MEM_HEADS * HEAD]
            rq, rk = ROWS[f"mem_q{l}"].start, ROWS[f"mem_k{l}"].start
            if l == 0:
                k0, q0 = ROWS["a_k"].start, ROWS["a_q"].start
                return [(mk, 4, rk, False, None, 1), (proj[:, :, 0:768], 12, q0, True, None, 5),
                        (proj[:, :, 1152:1344], 3, k0 + HEAD, True, 0, 8), (proj[:, :, 1536:1728], 3, k0 + 2 * HEAD, True, 3, 9),
                        (mq, 4, rq, False, None, 11)]
            sets = [(proj[:, :, B_Q0 + g * 512:B_Q0 + (g + 1) * 512], SLOTS, ROWS["b_q"].start + g * HEAD, True, None, 8 + 2 * g) for g in range(3)]
            return [(mk, 4, rk, False, None, 1), (proj[:, :, 0:512], SLOTS, ROWS["kv_k"].start, True, None, 4)] + sets + \
                [(mq, 4, rq, False, None, 13)]

        PANELS_ATTN = (11, 13)
        N_SETS = (5, 6)

        def set_stats(l, n):
            sizes = [TT * h[1] for h in head_sets(l)]
            return 8 + sum(sizes[:n]), sizes[n]

        def turn_items(l, tt):
            def pairs(t, a, n):
                return [t[:, tt, a + i * P:a + (i + 1) * P] for i in range(n)]

            if l == 0:
                dup = [twice[:, tt, k, :, :].rearrange("p d e -> p (d e)") for k in range(12)]
                return pairs(proj, 0, 6) + dup + pairs(proj, MEM_Q[0], 2) + pairs(mem_kv, 0, 2)
            return pairs(proj, B_Q0, 12) + pairs(proj, 0, 4) + pairs(proj, MEM_Q[1], 2) + pairs(mem_kv, 0, 2)

        N_ITEMS = (22, 20)
        BANKS_T = (11, 10)
        MEM_ITEM = (18, 16)

        def units(l):
            if l == 0:
                u = [(kind, h, None) for h in range(NSA_HEADS) for kind in ("sel", "win")]
            else:
                u = [("dil", s, tt) for s in range(SLOTS) for tt in range(TT)]
            return u + [("mem", h, None) for h in range(MEM_HEADS)]

        def unit_stat(u, name):
            a = 96 + 16 * ("max", "neg", "sum", "inv", "scale").index(name) + 2 * (u % 8)
            return rs[:, a:a + TT]

        def blocks_of(kind, tt):
            if kind == "dil":
                n = tt + 1
                return [([g * n * P + k * P for g in range(3)], tt, k) for k in range(n)]
            if kind == "mem":
                return [([(2 * t + k) * P], t, k) for t in range(TT) for k in range(TT)]
            return [([0], 0, 0), ([P], 1, 0), ([2 * P], 1, 1)]

        def values(l, kind, h, k):
            if kind == "mem":
                return mem_kv[:, k, (MEM_HEADS + h) * HEAD:(MEM_HEADS + h + 1) * HEAD]
            a = 512 + h * HEAD if kind == "dil" else {"sel": 1344, "win": 1728}[kind] + h // NSA_R * HEAD
            return proj[:, k, a:a + HEAD]

        def mlp_signals(kind):
            names = ("gu_full", "act_out", "h_ready", "y_full", "y_read") if kind == "ffn" else \
                ("up_full", "relu_out", "h_ready_2", "y_full_2", "y_read_2")
            return dict(zip(("up", "out", "h", "y", "read"), (S[n] for n in names)))

        block = ctx.enter_context(nc.Block())

        @block.sync
        def _(sp):
            sp.dma_start(x_tm[:], x.rearrange("(t p) d -> p t d", p=P)).then_inc(S["x_in"], 16)
            sp.dma_start(cst[:], consts).then_inc(S["consts_in"], 16)
            for i in range(RING):
                sp.dma_start(ring[:, i, :], weights[i]).then_inc(landed[i], 16)
            rounds = BEFORE_MOE // RING - 1
            with sp.Fori(0, rounds) as turn:
                for i in range(RING):
                    sp.wait_ge(S["panel_used"], turn * RING + (i + 1))
                    sp.dma_start(ring[:, i, :], weights[bass.ds(turn * RING + (RING + i), 1)].rearrange("a p n -> p (a n)")
                                 ).then_inc(landed[i], 16)
            for n in range((rounds + 1) * RING, BEFORE_MOE):
                sp.wait_ge(S["panel_used"], n - RING + 1)
                sp.dma_start(ring[:, n % RING, :], weights[n]).then_inc(landed[n % RING], 16)
            sp.wait_ge(S["items_ready"], 1)
            n_items = sp.value_load(table_i[0:1, 0:1], min_val=N_EXPERTS, max_val=ITEMS)
            with sp.Fori(0, n_items) as item:
                expert = sp.value_load(table_i[0:1, bass.ds(item + 1, 1)], min_val=0, max_val=N_EXPERTS - 1)
                with sp.Fori(0, PER_ITEM // RING) as turn:
                    for i in range(RING):
                        slot = (BEFORE_MOE + i) % RING
                        sp.wait_ge(S["panel_used"], item * PER_ITEM + turn * RING + (BEFORE_MOE + i - RING + 1))
                        sp.dma_start(ring[:, slot, :], weights[bass.ds(expert * PER_ITEM + turn * RING + (BEFORE_MOE + i), 1)]
                                     .rearrange("a p n -> p (a n)")).then_inc(landed[slot], 16)
            for i in range(RING):
                slot = (BEFORE_MOE + i) % RING
                sp.wait_ge(S["panel_used"], n_items * PER_ITEM + (BEFORE_MOE + i - RING + 1))
                sp.dma_start(ring[:, slot, :], weights[AFTER_MOE + i]).then_inc(landed_2[slot], 16)
            rounds = (N_PANELS - AFTER_MOE) // RING - 1
            with sp.Fori(0, rounds) as turn:
                for i in range(RING):
                    slot = (BEFORE_MOE + i) % RING
                    sp.wait_ge(S["panel_used_2"], turn * RING + (i + 1))
                    sp.dma_start(ring[:, slot, :], weights[bass.ds(turn * RING + (AFTER_MOE + RING + i), 1)]
                                 .rearrange("a p n -> p (a n)")).then_inc(landed_2[slot], 16)
            for n in range((rounds + 1) * RING, N_PANELS - AFTER_MOE):
                slot = (BEFORE_MOE + n) % RING
                sp.wait_ge(S["panel_used_2"], n - RING + 1)
                sp.dma_start(ring[:, slot, :], weights[AFTER_MOE + n]).then_inc(landed_2[slot], 16)
            sp.wait_ge(S["y_read_2"], DEPTH * (D_FF_2 // FCH))
            sp.dma_start(out.rearrange("(t p) d -> p t d", p=P), x_tm[:]).then_inc(S["out_stored"], 16)
            sp.wait_ge(S["out_stored"], 16)

        @block.tensor
        def _(pe):
            panels = PanelReader(pe, ring, landed, S["panel_used"])
            mm = panels.mm

            def turn_x(n, src):
                for b in range(4):
                    for kk_ in range(2):
                        for tt in range(TT):
                            f = (2 * b + kk_) * P
                            ins = pe.transpose(bank[b][:, (kk_ * TT + tt) * P:][:, 0:P], src[:, tt, f:f + P], ident)
                    ins.then_inc(S["x_turned"], 1)

            def wait_xT(n):
                pe.wait_ge(S["xT_dve"], 2 * (n + 1))
                pe.wait_ge(S["xT_act"], 2 * (n + 1))

            def project(l, j):
                n = 24 * l + j
                w = panels.take()
                if n >= 2:
                    pe.wait_ge(S["proj_read"], n - 1)
                for m in range(2):
                    for kb in range(KB):
                        ins = mm(bank[n % 2][:, m * T:(m + 1) * T], w[:, kb * PC + m * P:][:, 0:P], xT[:, kb, :],
                                 start=(kb == 0), stop=(kb == KB - 1))
                ins.then_inc(S["proj_out"], 1)

            def mixer_pe(l):
                def project_gate():
                    project(l, gate.pop(0))

                gate = list(range(12, 24))
                wait_xT(2 * l)
                for j in range(12):
                    project(l, j)
                w2a2 = mid[:, MIDS[f"w2a2{l}"]]
                g2 = mid[:, MIDS[f"g2{l}"]]
                if l == 0:
                    pe.wait_ge(S["params_in"], 16 * 3)
                pe.wait_ge(S["lora_in"], l + 1)
                for tt in range(TT):
                    pe.matmul(bank[2 + tt][:], loras[0:HEAD, 0, tt * P:(tt + 1) * P], w2a2[0:HEAD, :], start=True, stop=False)
                    ins = pe.matmul(bank[2 + tt][:], ones[0:1, :], row[0:1, ROWS[f"w0{l}"]], start=False, stop=True)
                ins.then_inc(S["lora_z"], 1)
                for c in range(NC):
                    ins = pe.matmul(bank[4 + c // 2][:, (c % 2) * T:][:, 0:T], w2a2[HEAD:P, c * P:(c + 1) * P], sh[HEAD:P, 12, :],
                                    start=True, stop=True)
                ins.then_inc(S["lora_a"], 1)
                for c in range(NC):
                    ins = pe.matmul(bank[6 + c // 2][:, (c % 2) * T:][:, 0:T], g2[:, c * P:(c + 1) * P], loras[:, 1, :],
                                    start=True, stop=True)
                ins.then_inc(S["lora_g"], 1)
                project_gate()
                pe.wait_ge(S["decay_in"], l + 1)
                pe.wait_ge(S["aaa"], l + 1)
                for c in range(NC):
                    for tt in range(TT):
                        ins = pe.matmul(bank[2 + c][:, tt * T:(tt + 1) * T], sg_tok[:, tt, c * P:(c + 1) * P], tri,
                                        start=True, stop=True)
                ins.then_inc(S["cum_mm"], 1)
                pe.wait_ge(S["kk_sq"], l + 1)
                pe.wait_ge(S["gate_lora"], l + 1)
                for c in range(NC):
                    ins = pe.matmul(bank[6 + c // 2][:, (c % 2) * T:][:, 0:T], head_sum, tmp[:, c, :], start=True, stop=True)
                ins.then_inc(S["kk_mm"], 1)
                project_gate()
                project_gate()
                pe.wait_ge(S["bonus_in"], l + 1)
                for c in range(NC):
                    ins = pe.matmul(bank[6 + c // 2][:, (c % 2) * T:][:, 0:T], head_sum, tmp[:, c, :], start=True, stop=True)
                ins.then_inc(S["bonus_mm"], 1)
                pe.wait_ge(S["features"], l + 1)
                pe.wait_ge(S["decays"], l + 1)
                for n, src in enumerate((v_, a_, kk)):
                    for tt in range(TT):
                        b = 2 + (2 * n + tt) % 4
                        if n == 2:
                            pe.wait_ge((S["turned_dve"], S["turned_act"])[tt], 3 * l + 1)
                        for c in range(NC):
                            ins = pe.transpose(bank[b][:, c * P:(c + 1) * P], src[:, c, tt * P:(tt + 1) * P], ident)
                        ins.then_inc(S["turn_mm"], 1)
                pe.wait_ge(S["turned_dve"], 3 * (l + 1))
                pe.wait_ge(S["turned_act"], 3 * (l + 1))
                for tt in range(TT):
                    tok = slice(tt * P, (tt + 1) * P)
                    for hg in range(2):
                        group = 4 * l + 2 * tt + hg
                        if group % 4:
                            pe.wait_ge(S["inv_dve"], 8 * group)
                            pe.wait_ge(S["inv_act"], 6 * group)
                        if tt and not hg:
                            pe.wait_ge(S["state"], 3 * l + 2)
                            pe.wait_ge(S["o_read"], 4 * l + 2)
                        for i in range(4):
                            c, lo = (4 * hg + i) // 2, HEAD * (i % 2)
                            hd = slice(lo, lo + HEAD)
                            pe.matmul(bank[2 + i][:, 0:T], a_[hd, c, tok], ar[hd, c, tt, :, :], start=True, stop=True)
                            pe.matmul(bank[2 + i][:, T:2 * T], kk[hd, c, tok], ar[hd, c, tt, :, :], start=True, stop=True)
                            ins = pe.matmul(bank[6 + i % 2][:, i // 2 * P:][:, 0:P], ar[hd, c, tt, 0, :], a_[hd, c, tok],
                                            start=True, stop=True)
                        ins.then_inc(S["unit_mm"], 1)
                        if gate:
                            project_gate()

                        def four(b, lhs, rhs, turn=False):
                            for i in range(4):
                                o = bank[b][:, i * P:(i + 1) * P]
                                if turn:
                                    ins = pe.transpose(o, lhs(i), ident)
                                else:
                                    ins = pe.matmul(o, lhs(i), rhs(i), start=True, stop=True)
                            ins.then_inc(S["inv_mm"], 1)

                        def part(t):
                            return lambda i: t[:, i * P:(i + 1) * P]

                        def n_1(i):
                            return unit[:, 4 * hg + i, 0, :]

                        def a_1(i):
                            return a3[:, i, 0, :]

                        n_2, a_2, n_4, a_4 = (part(pw[:, m, :]) for m in range(4))
                        a_8, x_odd, x_even = part(pw[:, 0, :]), part(xa), part(xb)
                        turned, g_of = a_2, n_4
                        pe.wait_ge(S["masks"], group + 1)
                        four(2, a_1, n_1)
                        four(3, n_1, a_1)
                        dve, act = 8 * group, 6 * group
                        pe.wait_ge(S["inv_dve"], dve + 1)
                        pe.wait_ge(S["inv_act"], act + 1)
                        four(4, a_2, x_odd)
                        four(5, a_2, n_2)
                        four(6, n_2, a_2)
                        if gate:
                            project_gate()
                        pe.wait_ge(S["inv_dve"], dve + 2)
                        pe.wait_ge(S["inv_act"], act + 3)
                        four(2, a_4, x_even)
                        four(3, n_4, a_4)
                        pe.wait_ge(S["inv_dve"], dve + 3)
                        pe.wait_ge(S["inv_act"], act + 4)
                        four(4, a_8, x_odd)
                        if gate:
                            project_gate()
                        pe.wait_ge(S["inv_dve"], dve + 4)
                        four(2, x_even, None, turn=True)
                        four(3, lambda i: a3[:, i, 1, :], x_even)
                        pe.wait_ge(S["inv_dve"], dve + 5)
                        pe.wait_ge(S["inv_act"], act + 5)
                        four(6, turned, g_of)
                        pe.wait_ge(S["inv_dve"], dve + 6)
                        four(4, x_odd, None, turn=True)
                        four(5, lambda i: a3[:, i, 2, :], x_odd)
                        pe.wait_ge(S["inv_dve"], dve + 7)
                        pe.wait_ge(S["inv_act"], act + 6)
                        four(2, turned, g_of)
                    pe.wait_ge(S["inv_dve"], 8 * (4 * l + 2 * tt + 2))
                    for half in range(2):
                        q = 4 * l + 2 * tt + half
                        hs = slice(half * CHUNK, (half + 1) * CHUNK)
                        if q % 4 == 0:
                            pe.wait_ge(S["cleared"], l + 2)
                        else:
                            pe.wait_ge(S["state"], q - l)
                        for c in range(NC):
                            pe.matmul(bank[2][hs, c * P:(c + 1) * P], ar[:, c, tt, 0, hs], state[:, c, :, :], start=True, stop=False)
                            for h in (2 * c, 2 * c + 1):
                                hv = slice(h * HEAD, (h + 1) * HEAD)
                                ins = pe.matmul(bank[2][hs, hv], unit[:, h, 2, hs], vt[:, tt, hv], start=False, stop=(h % 2 == 1))
                        ins.then_inc(S["rhs_mm"], 1)
                        pe.wait_ge(S["rhs"], q + 1)
                        for h in range(RH):
                            hv = slice(h * HEAD, (h + 1) * HEAD)
                            ins = pe.matmul(bank[3][hs, hv], inv[hs, h, hs], rhs_sb[hs, h, :], start=True, stop=True)
                        ins.then_inc(S["u_mm"], 1)
                        if q:
                            pe.wait_ge(S["o_read"], q)
                        for h in range(RH):
                            c, lo = h // 2, HEAD * (h % 2)
                            hd, hv = slice(lo, lo + HEAD), slice(h * HEAD, (h + 1) * HEAD)
                            o = bank[5][hd, c * CHUNK:(c + 1) * CHUNK]
                            pe.matmul(o, state[:, c, h % 2, :], ar[:, c, tt, 1, hs], start=True, stop=False)
                            pe.matmul(o, vt[:, tt, hv], unit[:, h, 3, hs], start=False, stop=False)
                            if h == 0:
                                pe.wait_ge(S["u"], q + 1)
                            ins = pe.matmul(o, u_sb[:, h, :], unit[:, h, 1, hs], start=False, stop=True)
                        ins.then_inc(S["o_mm"], 1)
                        if q % 4 < 3:
                            for h in range(RH):
                                c, lo = h // 2, HEAD * (h % 2)
                                hv = slice(h * HEAD, (h + 1) * HEAD)
                                o = bank[4][lo:lo + HEAD, c * HEAD:(c + 1) * HEAD]
                                pe.matmul(o, bt[hs, tt, hv], u_sb[hs, h, :], start=True, stop=False)
                                ins = pe.matmul(o, kt[hs, tt, hv], vt[hs, tt, hv], start=False, stop=True)
                            ins.then_inc(S["state_mm"], 1)
                while gate:
                    project_gate()
                pe.wait_ge(S["o_read"], 4 * (l + 1))
                for c in range(NC):
                    ins = pe.matmul(bank[2 + c // 2][:, (c % 2) * T:][:, 0:T], head_sum, oT[:, c, :], start=True, stop=True)
                ins.then_inc(S["gn_mean_mm"], 1)
                pe.wait_ge(S["conf_conv"], l + 1)
                for n in range(2):
                    ins = pe.matmul(bank[6][:, 0:T], ones, conv[:, n, :], start=(n == 0), stop=(n == 1))
                ins.then_inc(S["conf_mean_mm"], 1)
                pe.wait_ge(S["gn_sq"], l + 1)
                for c in range(NC):
                    ins = pe.matmul(bank[4 + c // 2][:, (c % 2) * T:][:, 0:T], head_sum, ar[:, c, :, 0, :], start=True, stop=True)
                ins.then_inc(S["gn_var_mm"], 1)
                pe.wait_ge(S["conf_sq"], l + 1)
                for n in range(2):
                    ins = pe.matmul(bank[7][:, 0:T], ones, conv_sq[:, n, :], start=(n == 0), stop=(n == 1))
                ins.then_inc(S["conf_var_mm"], 1)
                for n in range(4):
                    w = panels.take()
                    b = 2 + 3 * (n % 2)
                    if n == 0:
                        pe.wait_ge(S["branch_c"], l + 1)
                        pe.wait_ge(S["conf_silu"], l + 1)
                        pe.wait_ge(S["branch_a"], l + 1)
                    elif n >= 2:
                        pe.wait_ge(S["mixed"], 4 * l + n - 1)
                    for part_, (k0, k1, src) in enumerate(((0, 4, yT), (4, 6, conf_s), (6, 8, conv_c))):
                        for m in range(2):
                            for kb in range(k0, k1):
                                ins = mm(bank[b + part_][:, m * T:(m + 1) * T], w[:, kb * PC + m * P:][:, 0:P], src[:, kb - k0, :],
                                         start=(kb == k0), stop=(kb == k1 - 1))
                    ins.then_inc(S["mix_mm"], 1)
                pe.wait_ge(S["mixed"], 4 * (l + 1))
                rows_out(4, lambda kb, tt: mixT[:, kb, tt * P:(tt + 1) * P], S["wout_mm"])

            def rows_out(n_panels, lhs, done):
                for n in range(n_panels):
                    w = panels.take()
                    for i in range(PR):
                        kb = n * PR + i
                        for tt in range(TT):
                            for h in range(2):
                                ins = mm(bank[2 * tt + h][:], lhs(kb, tt), w[:, i * D + h * 512:][:, 0:512],
                                         start=(kb == 0), stop=(kb == n_panels * PR - 1))
                ins.then_inc(done, 1)

            def mlp_pe(kind, n_chunks, base, per_step):
                gated, sems = kind == "ffn", mlp_signals(kind)
                nb = 2 if gated else 3

                def first(i, slot, turn=0, per_turn=0):
                    for g in range(2 if gated else 1):
                        w = panels.take(turn, per_turn)
                        b = bank[(2 * slot + g) if gated else slot]
                        for m in range(2):
                            for kb in range(KB):
                                ins = mm(b[:, m * T:(m + 1) * T], w[:, kb * PC + m * P:][:, 0:P], xT[:, kb, :],
                                         start=(kb == 0), stop=(kb == KB - 1))
                    ins.then_inc(sems["up"], 1)

                def last(i, slot, turn=0, per_turn=0):
                    w = panels.take(turn, per_turn)
                    pe.wait_ge(sems["h"], i + 1)
                    if not (isinstance(i, int) and i == 0):
                        pe.wait_ge(sems["read"], i)
                    for m in range(2):
                        for tt in range(TT):
                            for h in range(2):
                                ins = mm(bank[4 + 2 * tt + h][:], hT[:, slot, m, tt * P:(tt + 1) * P],
                                         w[:, m * D + h * 512:][:, 0:512], start=(m == 0), stop=(m == 1))
                    ins.then_inc(sems["y"], 1)

                first(base, 0)
                lead = 2 + (n_chunks - 2) % per_step
                for s in range(1, lead):
                    first(base + s, s % nb)
                    last(base + s - 1, (s - 1) % nb)
                per_turn = per_step * (3 if gated else 2)
                turns = (n_chunks - lead) // per_step
                with pe.Fori(0, turns) as turn:
                    for s in range(lead, lead + per_step):
                        first(turn * per_step + (base + s), s % nb, turn, per_turn)
                        last(turn * per_step + (base + s - 1), (s - 1) % nb, turn, per_turn)
                panels.skip((turns - 1) * per_turn)
                last(base + n_chunks - 1, (n_chunks - 1) % nb)

            def moe_pe():
                def first(s, item):
                    for g in range(2):
                        w = panels.take(item, PER_ITEM)
                        for m in range(2):
                            o = bank[s % 2][:, (2 * g + m) * CAP:][:, 0:CAP]
                            for kb in range(KB):
                                ins = mm(o, w[:, kb * PC + m * P:][:, 0:P], xeT[:, kb, :], start=(kb == 0), stop=(kb == KB - 1))
                    ins.then_inc(S["gu_full"], 1)

                def last(s, item):
                    w = panels.take(item, PER_ITEM)
                    pe.wait_ge(S["h_ready"], item * FF_CHUNKS + (FF_CHUNKS + s + 1))
                    for h in range(2):
                        for m in range(2):
                            ins = mm(bank[2 + h][:], hT[:, s % 2, m, 0:CAP], w[:, m * D + h * 512:][:, 0:512],
                                     start=(s == 0 and m == 0), stop=(s == FF_CHUNKS - 1 and m == 1))
                        if s == FF_CHUNKS - 1 and h == 0:
                            ins.then_inc(S["y_half"], 1)
                    ins.then_inc(S["y_full"], 1)

                def gather():
                    for kb in range(KB):
                        for tt in range(TT):
                            ins = pe.matmul(bank[4 + kb // 4][:, kb % 4 * CAP:][:, 0:CAP], x_tm[:, tt, kb * P:(kb + 1) * P], one_hot[:, tt, :],
                                            start=(tt == 0), stop=(tt == TT - 1))
                    return ins

                pe.wait_ge(S["items_ready"], 1)
                n_items = pe.value_load(table_i[0:1, 0:1], min_val=N_EXPERTS, max_val=ITEMS)
                pe.wait_ge(S["one_hot"], 1)
                pe.wait_ge(S["ln_x_done"], 2 * DEPTH - 1)
                gather().then_inc(S["routed_mm"], 1)
                with pe.Fori(0, n_items) as item:
                    pe.wait_ge(S["xe_dve"], item + 1)
                    pe.wait_ge(S["xe_act"], item + 1)
                    first(0, item)
                    for s in range(1, FF_CHUNKS):
                        first(s, item)
                        last(s - 1, item)
                    pe.wait_ge(S["one_hot"], item + 2)
                    pe.wait_ge(S["acc_read"], item + 1)
                    gather()
                    for tt in range(TT):
                        ins = pe.transpose(bank[6][:, tt * P:(tt + 1) * P], weighted[:, tt, :], ident)
                    ins.then_inc(S["routed_mm"], 1)
                    last(FF_CHUNKS - 1, item)
                    pe.wait_ge(S["xe_dve"], item + 2)
                    pe.wait_ge(S["xe_act"], item + 2)
                    pe.wait_ge(S["spread"], item + 1)
                    for h in range(2):
                        pe.wait_ge(S["y_sb"], 2 * item + (h + 1))
                        for tt in range(TT):
                            ins = pe.matmul(bank[4 + 2 * h + tt][:], spread[:, tt, :], y_sb[:, h * 512:(h + 1) * 512], start=True, stop=True)
                        ins.then_inc(S["scatter_mm"], 1)

            def project_tokens(n_panels, n0):
                for n in range(n0, n0 + n_panels):
                    w = panels.take()
                    if n >= 2:
                        pe.wait_ge(S["attn_read"], n - 1)
                    for tt in range(TT):
                        for kb in range(KB):
                            ins = mm(bank[4 + n % 2][:, tt * PC:(tt + 1) * PC], xT[:, kb, tt * P:(tt + 1) * P],
                                     w[:, kb * PC:(kb + 1) * PC], start=(kb == 0), stop=(kb == KB - 1))
                    ins.then_inc(S["attn_proj"], 1)

            def turn_heads(l):
                n0 = 0 if l == 0 else BANKS_T[0]
                items = [turn_items(l, tt) for tt in range(TT)]
                pe.wait_ge(S["qk_ready"], l + 1)
                for n in range(BANKS_T[l]):
                    if n >= 4:
                        m = n0 + n - 4
                        pe.wait_ge(S["turnq_dve"] if m % 2 == 0 else S["turnq_act"], m // 2 + 1)
                    for i in range(2):
                        for tt in range(TT):
                            ins = pe.transpose(bank[n % 4][:, (2 * i + tt) * P:][:, 0:P], items[tt][2 * n + i], ident)
                    ins.then_inc(S["turnq_mm"], 1)

            def wait_heads(l):
                n = sum(BANKS_T[:l + 1])
                pe.wait_ge(S["turnq_dve"], (n + 1) // 2)
                pe.wait_ge(S["turnq_act"], n // 2)

            def compress():
                pe.wait_ge(S["cmp_tb"], 1)
                for kv in range(2):
                    for half in range(2):
                        w = panels.take()
                        for kb in range(KB):
                            for hb in range(2):
                                ins = mm(bank[4 + 2 * kv + hb][:, 0:NSA_G * N_CMP], w[:, kb * CMP_HIDDEN + hb * P:][:, 0:P],
                                         cmp_in[:, kv, half * KB + kb, :, :].rearrange("p g i -> p (g i)"),
                                         start=(half == 0 and kb == 0), stop=(half == 1 and kb == KB - 1))
                    ins.then_inc(S["cmp_h_mm"], 1)
                w2 = mid[:, MIDS["cmp_w2"]].rearrange("p (k h e) -> p k h e", k=2, h=2)
                pe.wait_ge(S["cmp_h"], 2)
                for kv in range(2):
                    for g in range(NSA_G):
                        for hb in range(2):
                            ins = pe.matmul(bank[0][0:N_CMP, (kv * NSA_G + g) * HEAD:][:, 0:HEAD], cmp_h[:, kv, hb, g * N_CMP:(g + 1) * N_CMP],
                                            w2[:, kv, hb, :], start=(hb == 0), stop=(hb == 1))
                ins.then_inc(S["cmp_o_mm"], 1)
                pe.wait_ge(S["cmp_k_ready"], 1)
                for g in range(NSA_G):
                    ins = pe.transpose(bank[1][:, g * 16:g * 16 + N_CMP], cmp_dup[0:N_CMP, g, :, :].rearrange("p d e -> p (d e)"),
                                       ident[0:N_CMP, 0:N_CMP])
                ins.then_inc(S["cmp_kT_mm"], 1)
                pe.wait_ge(S["cmp_kT"], 1)
                for h in range(NSA_HEADS):
                    hd = slice(HEAD * (h % 2), HEAD * (h % 2) + HEAD)
                    for tt in range(TT):
                        ins = pe.matmul(bank[2 + h % 2][:, (h // 2 * TT + tt) * 16:][:, 0:N_CMP], qkT[hd, h // 2, tt * P:(tt + 1) * P],
                                        cmp_kT[hd, h // NSA_R, 0:N_CMP], start=True, stop=True)
                ins.then_inc(S["cmp_s_mm"], 1)
                pe.wait_ge(S["cmp_p"], 1)
                for h in range(NSA_HEADS):
                    b = h % 2
                    if h >= 2:
                        pe.wait_ge(S["cmp_pT"], h - 1)
                        pe.wait_ge(S["cmp_done"], h - 1)
                    for tt in range(TT):
                        ins = pe.transpose(bank[4 + b][0:N_CMP, tt * P:(tt + 1) * P], cmp_s[:, h, tt, 0:N_CMP], ident)
                    ins.then_inc(S["cmp_pT_mm"], 1)
                    pe.wait_ge(S["cmp_pT"], h + 1)
                    for tt in range(TT):
                        ins = pe.matmul(bank[6 + b][:, tt * HEAD:(tt + 1) * HEAD], cmp_pT[0:N_CMP, 2 * b + tt, :],
                                        cmp_kv[0:N_CMP, 1, h // NSA_R, :], start=True, stop=True)
                    ins.then_inc(S["cmp_pv_mm"], 1)
                pe.wait_ge(S["cmp_done"], NSA_HEADS)

            def attend(l):
                n0 = 0 if l == 0 else len(units(0))
                todo = units(l)

                def scores(n):
                    kind, h, tile = todo[n]
                    u = n0 + n
                    if u >= 2:
                        pe.wait_ge(S["score_exp"], u - 1)
                    hd = slice(HEAD * (h % 2), HEAD * (h % 2) + HEAD)
                    for tt in (range(TT) if tile is None else (tile,)):
                        tok, n_k = slice(tt * P, (tt + 1) * P), (tt + 1) * P
                        b = 2 * (u % 2)
                        if kind == "dil":
                            for g in range(3):
                                o = bank[b + (g * n_k) // 512][:, g * n_k % 512:][:, 0:n_k]
                                ins = pe.matmul(o, qkT[hd, 4 * g + h // 2, tok], qkT[hd, 12 + h // 2, 0:n_k], start=True, stop=True)
                        elif kind == "mem":
                            ins = pe.matmul(bank[b][:, tt * T:(tt + 1) * T], qkT[hd, MEM_ITEM[l] + h // 2, tok],
                                            qkT[hd, MEM_ITEM[l] + 2 + h // 2, :], start=True, stop=True)
                        else:
                            item = 6 + (0 if kind == "sel" else 3) + h // NSA_R
                            ins = pe.matmul(bank[b][:, tt * P:tt * P + n_k], qkT[hd, h // 2, tok], qkT[hd, item, 0:n_k], start=True, stop=True)
                    ins.then_inc(S["score_mm"], 1)

                def transposed(n):
                    kind, h, tile = todo[n]
                    u = n0 + n
                    pe.wait_ge(S["score_exp"], u + 1)
                    if u >= 2:
                        pe.wait_ge(S["pT"], u - 1)
                    for i, (starts, _, _) in enumerate(blocks_of(kind, tile)):
                        for m, a in enumerate(starts):
                            o = bank[4 + u % 2][:, i * P:(i + 1) * P]
                            if len(starts) == 1:
                                ins = pe.transpose(o, p_sb[:, u % 4, a:a + P], ident)
                            else:
                                ins = pe.matmul(o, p_sb[:, u % 4, a:a + P], ident, start=(m == 0), stop=(m == len(starts) - 1))
                    ins.then_inc(S["pT_mm"], 1)

                def with_values(n):
                    kind, h, tile = todo[n]
                    u = n0 + n
                    pe.wait_ge(S["pT"], u + 1)
                    if u >= 2:
                        pe.wait_ge(S["pv_read"], u - 1)
                    parts = blocks_of(kind, tile)
                    for i, (_, tt, k) in enumerate(parts):
                        at = 0 if tile is not None else tt * HEAD
                        first = i == 0 or parts[i - 1][1] != tt
                        last = i == len(parts) - 1 or parts[i + 1][1] != tt
                        ins = pe.matmul(bank[6 + u % 2][:, at:at + HEAD], pT_sb[:, u % 2, i * P:(i + 1) * P], values(l, kind, h, k), start=first, stop=last)
                    ins.then_inc(S["pv_mm"], 1)

                for n in range(len(todo) + 3):
                    if n < len(todo):
                        scores(n)
                    if 0 <= n - 2 < len(todo):
                        transposed(n - 2)
                    if n >= 3:
                        with_values(n - 3)

            def attention_pe(l):
                n_turn = 4 + 4 * l
                rms = 3 * l
                n_proj = 11 * l
                pe.wait_ge(S["rms_x"], rms + 1)
                turn_x(n_turn, xn)
                wait_xT(n_turn)
                project_tokens(2, n_proj)
                pe.wait_ge(S["rms_x"], rms + 2)
                turn_x(n_turn + 1, xn)
                wait_xT(n_turn + 1)
                if l == 0:
                    project_tokens(9, 2)
                else:
                    project_tokens(4, n_proj + 2)
                    turn_x(n_turn + 2, xn)
                    wait_xT(n_turn + 2)
                    project_tokens(7, n_proj + 6)
                turn_heads(l)
                wait_heads(l)
                if l == 0:
                    compress()
                attend(l)
                n_turn = 6 if l == 0 else 11
                pe.wait_ge(S["pv_read"], sum(len(units(i)) for i in range(l + 1)))
                turn_x(n_turn, o_tm)
                wait_xT(n_turn)
                rows_out((4, 3)[l], lambda kb, tt: xT[:, kb, tt * P:(tt + 1) * P], S["proj2_mm"])
                pe.wait_ge(S["rms_x"], rms + 3)
                turn_x(n_turn + 1, xn)
                wait_xT(n_turn + 1)
                mlp_pe("mlp", D_FF_2 // FCH, l * (D_FF_2 // FCH), 3)

            pe.wait_ge(S["consts_in"], 16)
            pe.wait_ge(S["x_in"], 16)
            for l in range(DEPTH):
                if l:
                    pe.wait_ge(S["ln_z"], 2 * l)
                turn_x(2 * l, x_tm)
                mixer_pe(l)
                pe.wait_ge(S["ln_z"], 2 * l + 1)
                turn_x(2 * l + 1, x_tm)
                wait_xT(2 * l + 1)
                if l == 0:
                    mlp_pe("ffn", FF_CHUNKS, 0, 2)
                else:
                    router = mid[:, MIDS["router"]]
                    for tt in range(TT):
                        for kb in range(KB):
                            ins = pe.matmul(bank[0][:, tt * N_EXPERTS:(tt + 1) * N_EXPERTS], xT[:, kb, tt * P:(tt + 1) * P],
                                            router[:, kb * N_EXPERTS:(kb + 1) * N_EXPERTS], start=(kb == 0), stop=(kb == KB - 1))
                    ins.then_inc(S["router_mm"], 1)
                    pe.wait_ge(S["router_w"], 1)
                    chosen = [rt[:, 1, tt * N_EXPERTS:(tt + 1) * N_EXPERTS] for tt in range(TT)]
                    before = cst[:, CONST["before"]]
                    e = N_EXPERTS
                    pe.matmul(bank[1][:, 0:e], before, chosen[0], start=True, stop=True)
                    pe.matmul(bank[1][:, e:2 * e], ones, chosen[0], start=True, stop=False)
                    pe.matmul(bank[1][:, e:2 * e], before, chosen[1], start=False, stop=True)
                    pe.matmul(bank[1][:, 2 * e:3 * e], ones, chosen[0], start=True, stop=False)
                    ins = pe.matmul(bank[1][:, 2 * e:3 * e], ones, chosen[1], start=False, stop=True)
                    ins.then_inc(S["counts_mm"], 1)
                    moe_pe()
            pe.wait_ge(S["ln_x_done"], 2 * DEPTH)
            panels.restart(landed_2, S["panel_used_2"], pe.transpose(bank[0][:, 0:P], ident, ident))
            for l in range(DEPTH):
                attention_pe(l)

        @block.scalar
        def _(act):
            made = Made()

            def copy_xT(n, gain=None, bias=None):
                for i, b in enumerate((1, 3)):
                    act.wait_ge(S["x_turned"], 4 * n + b + 1)
                    for kk_ in range(2):
                        f = 2 * b + kk_
                        ins = act.activation(xT[:, f, :], bank[b][:, kk_ * T:(kk_ + 1) * T], ACT.Copy if bias is None else ACT.Identity,
                                             scale=1.0 if gain is None else c1(gain, f), bias=0.0 if bias is None else c1(bias, f))
                    ins.then_inc(S["xT_act"], 1)
                    act.wait_ge(S["xT_act"], made.next("xT_act"))

            def proj_copy(l, j):
                n = 24 * l + IN_ORDER.index(j)
                act.wait_ge(S["proj_out"], n + 1)
                src = bank[n % 2][:].rearrange("p (m t) -> p m t", m=2)
                if j < 7:
                    if 7 * l + j >= 2:
                        act.wait_ge(S["shifted"], 7 * l + j - 1)
                    else:
                        act.wait_ge(S["cleared"], 1)
                    act.activation(pz[:, j % 2, :, 1:], src, ACT.Copy).then_inc(S["proj_read"], 1)
                    act.wait_ge(S["proj_read"], made.next("proj_read"))
                elif j == 7:
                    act.activation(u_pad[:, :, CONF_TAPS - 1:], src, ACT.Copy).then_inc(S["proj_read"], 1)
                    act.wait_ge(S["proj_read"], made.next("proj_read"))
                elif j == 8:
                    act.activation(conf_s[:], src, ACT.Sigmoid).then_inc(S["proj_read"], 1)
                    act.wait_ge(S["proj_read"], made.next("proj_read"))
                elif j == 9:
                    act.activation(gb[:], src, ACT.Copy).then_inc(S["proj_read"], 1)
                    act.wait_ge(S["proj_read"], made.next("proj_read"))
                elif j == 10:
                    act.activation(s_pad[:, :, SHORT_TAPS - 1:], src, ACT.Copy).then_inc(S["proj_read"], 1)
                    act.wait_ge(S["proj_read"], made.next("proj_read"))
                elif j == 11:
                    act.activation(conv_c[:], src, ACT.Copy).then_inc(S["proj_read"], 1)
                    act.wait_ge(S["proj_read"], made.next("proj_read"))
                else:
                    m = 2 * (j - 12)
                    act.activation(gates[:, m:m + 2, :], src, ACT.Sigmoid).then_inc(S["proj_read"], 1)
                    act.wait_ge(S["proj_read"], made.next("proj_read"))

            def mixer_act(l):
                gate = list(range(12, 24))

                def gate_copy():
                    proj_copy(l, gate.pop(0))

                copy_xT(2 * l, *((f"ln2_g{l - 1}", f"ln2_b{l - 1}") if l else ()))
                for j in IN_ORDER[:12]:
                    proj_copy(l, j)
                act.wait_ge(S["shifted"], 7 * (l + 1))
                act.activation(loras[0:HEAD, 0, :], sh[0:HEAD, 12, :], ACT.Tanh)
                act.activation(loras[:, 1, :], sh[:, 13, :], ACT.Sigmoid).then_inc(S["lora_in"], 1)
                act.wait_ge(S["lora_in"], made.next("lora_in"))
                act.wait_ge(S["lora_z"], l + 1)
                for tt in range(TT):
                    ins = act.activation(sg_tok[:, tt, :], bank[2 + tt][:], ACT.Sigmoid)
                ins.then_inc(S["decay_in"], 1)
                act.wait_ge(S["decay_in"], made.next("decay_in"))
                if l == 0:
                    act.wait_ge(S["params_in"], 16 * 3)
                act.wait_ge(S["lora_a"], l + 1)
                for c in range(NC):
                    ins = act.activation(a_[:, c, :], bank[4 + c // 2][:, (c % 2) * T:][:, 0:T], ACT.Sigmoid, bias=c1(f"a0{l}", c))
                ins.then_inc(S["aaa"], 1)
                act.wait_ge(S["aaa"], made.next("aaa"))
                act.wait_ge(S["lora_g"], l + 1)
                for n in range(2):
                    ins = act.activation(g_[:, 2 * n:2 * n + 2, :], bank[6 + n][:].rearrange("p (m t) -> p m t", m=2), ACT.Copy)
                ins.then_inc(S["gate_lora"], 1)
                act.wait_ge(S["gate_lora"], made.next("gate_lora"))
                gate_copy()
                act.wait_ge(S["cum_mm"], l + 1)
                for c in range(NC):
                    s = bank[2 + c][:].rearrange("p (t m k) -> p m t k", t=TT, m=2)
                    for dst, m, sign in ((p_in, 0, -KAPPA), (p_inv, 0, KAPPA), (p_ex, 1, -KAPPA)):
                        ins = act.activation(dst[:, c, :].rearrange("p (t k) -> p t k", t=TT), s[:, m], ACT.Exp, scale=sign)
                ins.then_inc(S["decays"], 1)
                act.wait_ge(S["decays"], made.next("decays"))
                act.wait_ge(S["kk_mm"], l + 1)
                for n in range(2):
                    ins = act.activation(vt[:, n, :], bank[6 + n][:], ACT.Sqrt)
                ins.then_inc(S["kk_norm"], 1)
                act.wait_ge(S["kk_norm"], made.next("kk_norm"))
                gate_copy()
                gate_copy()
                for n, dst in enumerate((vt, bt, kt)):
                    act.wait_ge(S["turn_mm"], 6 * l + 2 * n + 2)
                    act.activation(dst[:, 1, :], bank[2 + (2 * n + 1) % 4][:], ACT.Copy).then_inc(S["turned_act"], 1)
                    act.wait_ge(S["turned_act"], made.next("turned_act"))
                for tt in range(TT):
                    for hg in range(2):
                        group = 4 * l + 2 * tt + hg
                        if gate:
                            gate_copy()
                        n = 14 * group
                        for count, b, dst in ((2, 3, 1), (4, 5, 2), (5, 6, 3), (7, 3, 0), (9, 2, 1), (12, 4, 1)):
                            act.wait_ge(S["inv_mm"], n + count)
                            if count == 12:
                                act.wait_ge(S["inv_mm"], n + 12)
                            act.activation(pw[:, dst, :], bank[b][:], ACT.Copy).then_inc(S["inv_act"], 1)
                            act.wait_ge(S["inv_act"], made.next("inv_act"))
                            if count in (5, 7) and gate:
                                gate_copy()
                    for half in range(2):
                        q = 4 * l + 2 * tt + half
                        act.wait_ge(S["o_mm"], q + 1)
                        lo = (2 * tt + half) * CHUNK
                        act.activation(oT[:, :, lo:lo + CHUNK], bank[5][:, 0:NC * CHUNK].rearrange("p (c t) -> p c t", c=NC),
                                       ACT.Copy).then_inc(S["o_read"], 1)
                        act.wait_ge(S["o_read"], made.next("o_read"))
                while gate:
                    gate_copy()
                act.wait_ge(S["gn_var_mm"], l + 1)
                for n in range(2):
                    ins = act.activation(kk[:, 2 * n:2 * n + 2, :], bank[4 + n][:].rearrange("p (m t) -> p m t", m=2), ACT.Sqrt,
                                         scale=1.0 / HEAD, bias=eps("gn_eps"))
                ins.then_inc(S["gn_std"], 1)
                act.wait_ge(S["gn_std"], made.next("gn_std"))
                act.wait_ge(S["conf_var_mm"], l + 1)
                act.activation(conf_s[:, 0, :], bank[7][:, 0:T], ACT.Sqrt, scale=1.0 / CONF, bias=eps("ln_eps")).then_inc(S["conf_std"], 1)
                act.wait_ge(S["conf_std"], made.next("conf_std"))
                act.wait_ge(S["branch_b"], l + 1)
                for n in range(2):
                    ins = act.activation(conf_s[:, n, :], conv[:, n, :], ACT.Silu, scale=c1(f"conf_ln_g{l}", n), bias=c1(f"conf_ln_b{l}", n))
                ins.then_inc(S["conf_silu"], 1)
                act.wait_ge(S["conf_silu"], made.next("conf_silu"))

            def ln_std(n):
                act.wait_ge(S["ln_x"], n + 1)
                act.activation(stat[:, 32:32 + TT], stat[:, 26:26 + 2 * TT].rearrange("p (t s) -> p s t", s=2)[:, 1, :], ACT.Sqrt,
                               bias=eps("ln_eps")).then_inc(S["ln_std"], 1)
                act.wait_ge(S["ln_std"], made.next("ln_std"))

            def mlp_act(kind, n_chunks, base, per_step):
                gated, sems = kind == "ffn", mlp_signals(kind)
                nb = 2 if gated else 3
                func = ACT.Silu if gated else ACT.Relu

                def chunk(i, slot, early):
                    act.wait_ge(sems["up"], i + 1)
                    if not early:
                        act.wait_ge(sems["h"], i - nb + 1)
                    b = bank[2 * slot if gated else slot]
                    act.activation(gate_s[:, slot, :, :], b[:].rearrange("p (m t) -> p m t", m=2), func).then_inc(sems["out"], 1)

                lead = nb + (n_chunks - nb) % per_step
                for s in range(lead):
                    chunk(base + s, s % nb, s < nb)
                with act.Fori(0, (n_chunks - lead) // per_step) as turn:
                    for s in range(lead, lead + per_step):
                        chunk(turn * per_step + (base + s), s % nb, False)

            def moe_act():
                act.wait_ge(S["items_ready"], 1)
                n_items = act.value_load(table_i[0:1, 0:1], min_val=N_EXPERTS, max_val=ITEMS)

                def tokens():
                    return act.activation(xeT[:, 4:8, :], bank[5][:].rearrange("p (k c) -> p k c", k=4), ACT.Copy)

                act.wait_ge(S["routed_mm"], 1)
                tokens().then_inc(S["xe_act"], 1)
                with act.Fori(0, n_items) as item:
                    for s in range(FF_CHUNKS):
                        act.wait_ge(S["gu_full"], item * FF_CHUNKS + (FF_CHUNKS + s + 1))
                        act.wait_ge(S["h_ready"], item * FF_CHUNKS + (FF_CHUNKS + max(s - 1, 0)))
                        act.activation(gate_s[:, s % 2, :, 0:CAP], bank[s % 2][:, 0:2 * CAP].rearrange("p (m c) -> p m c", m=2), ACT.Silu
                                       ).then_inc(S["act_out"], 1)
                    act.wait_ge(S["routed_mm"], item + 2)
                    tokens().then_inc(S["xe_act"], 1)
                    act.activation(spread[:], bank[6][:, 0:T].rearrange("p (t k) -> p t k", t=TT), ACT.Copy).then_inc(S["spread"], 1)
                    act.wait_ge(S["y_half"], item + 1)
                    act.activation(y_sb[:, 0:512], bank[2][:], ACT.Copy).then_inc(S["y_sb"], 1)
                    act.wait_ge(S["y_full"], item * FF_CHUNKS + 2 * FF_CHUNKS)
                    act.activation(y_sb[:, 512:], bank[3][:], ACT.Copy).then_inc(S["y_sb"], 1)

            def rms(n, src):
                if n in (0, 3):
                    act.wait_ge(S["mem_in"], 16 * (1 + n // 3))
                elif n == 1:
                    act.wait_ge(S["ln_x_done"], 2 * DEPTH)
                elif n == 4:
                    act.wait_ge(S["y_read_2"], D_FF_2 // FCH)
                else:
                    act.wait_ge(S["x_done"], 1 + n // 3)
                for tt in range(TT):
                    ins = act.activation(scr[:, tt, 0:D], src[:, tt, :], ACT.Square, accum_out=rs[:, tt:tt + 1])
                ins.then_inc(S["act_step"], 1)
                act.wait_ge(S["act_step"], made.next("act_step"))
                act.activation(rs[:, 2:2 + TT], rs[:, 0:TT], ACT.Sqrt, scale=1.0 / D, bias=eps("rms_eps")).then_inc(S["rms_std"], 1)
                act.wait_ge(S["rms_std"], made.next("rms_std"))

            def copy_tokens(l, dst, n_panels, n0):
                for j in range(n_panels):
                    n = n0 + j
                    act.wait_ge(S["attn_proj"], l * PANELS_ATTN[0] + n + 1)
                    act.activation(dst[:, :, j * PC:(j + 1) * PC], bank[4 + (l * PANELS_ATTN[0] + n) % 2][:].rearrange("p (t c) -> p t c", t=TT),
                                   ACT.Copy).then_inc(S["attn_read"], 1)
                    act.wait_ge(S["attn_read"], made.next("attn_read"))
                    for i, h in enumerate(head_sets(l)):
                        if max(h[5], 2) == n:
                            head_std(l, i)

            def head_std(l, i):
                at, size = set_stats(l, i)
                act.wait_ge(S["rms_ss"], l * N_SETS[0] + i + 1)
                act.activation(rs[:, at:at + size], rs[:, at:at + size], ACT.Sqrt, scale=1.0 / HEAD, bias=eps("rms_eps")).then_inc(S["qk_std"], 1)
                act.wait_ge(S["qk_std"], made.next("qk_std"))

            def attention_act(l):
                n_turn = 4 + 4 * l
                rms(3 * l, o_tm)
                copy_xT(n_turn, f"mem_norm{l}")
                copy_tokens(l, mem_kv, 2, 0)
                act.wait_ge(S["rms_x"], 3 * l + 1)
                rms(3 * l + 1, x_tm)
                if l == 0:
                    copy_xT(n_turn + 1, "attn_norm0")
                    copy_tokens(l, proj, 9, 2)
                    act.activation(coef[:], proj[:, :, 2176:2212].rearrange("p t (h b) -> p b h t", b=3), ACT.Sigmoid).then_inc(S["nsa_gates"], 1)
                    act.wait_ge(S["nsa_gates"], made.next("nsa_gates"))
                else:
                    copy_xT(n_turn + 1, "kv_norm")
                    copy_tokens(l, proj, 4, 2)
                    copy_xT(n_turn + 2, "attn_norm1")
                    copy_tokens(l, proj[:, :, 4 * PC:], 7, 6)
                head_std(l, N_SETS[l] - 1)
                n0 = 0 if l == 0 else BANKS_T[0]
                for n in range(BANKS_T[l]):
                    if (n0 + n) % 2:
                        act.wait_ge(S["turnq_mm"], n0 + n + 1)
                        act.activation(qkT[:, 2 * n:2 * n + 2, :], bank[n % 4][:].rearrange("p (i t) -> p i t", i=2), ACT.Copy).then_inc(S["turnq_act"], 1)
                        act.wait_ge(S["turnq_act"], made.next("turnq_act"))
                if l == 0:
                    for kv in range(2):
                        act.wait_ge(S["cmp_h_mm"], kv + 1)
                        for hb in range(2):
                            ins = act.activation(cmp_h[:, kv, hb, :], bank[4 + 2 * kv + hb][:, 0:NSA_G * N_CMP], ACT.Gelu_apprx_tanh,
                                                 bias=c1("cmp_b1", 2 * kv + hb))
                        ins.then_inc(S["cmp_h"], 1)
                        act.wait_ge(S["cmp_h"], made.next("cmp_h"))
                    act.wait_ge(S["cmp_kv"], 1)
                    act.activation(rs[0:N_CMP, 4:4 + NSA_G], rs[0:N_CMP, 4:4 + NSA_G], ACT.Sqrt, scale=1.0 / HEAD,
                                   bias=eps("rms_eps")[0:N_CMP]).then_inc(S["cmp_k_std"], 1)
                    act.wait_ge(S["cmp_k_std"], made.next("cmp_k_std"))
                    act.wait_ge(S["cmp_s"], 1)
                    act.activation(cmp_s[:, :, :, 0:N_CMP], cmp_s[:, :, :, 0:N_CMP], ACT.Exp, scale=SCALE).then_inc(S["cmp_e"], 1)
                    act.wait_ge(S["cmp_e"], made.next("cmp_e"))
                    for h in range(NSA_HEADS):
                        act.wait_ge(S["cmp_pT_mm"], h + 1)
                        if h >= 2:
                            act.wait_ge(S["cmp_pv_mm"], h - 1)
                        b = h % 2
                        act.activation(cmp_pT[0:N_CMP, 2 * b:2 * b + 2, :], bank[4 + b][0:N_CMP, 0:T].rearrange("p (t q) -> p t q", t=TT),
                                       ACT.Copy).then_inc(S["cmp_pT"], 1)
                        act.wait_ge(S["cmp_pT"], made.next("cmp_pT"))
                n0 = 0 if l == 0 else len(units(0))
                todo = units(l)

                def exps(n):
                    kind, h, tile = todo[n]
                    u = n0 + n
                    act.wait_ge(S["score_max"], u + 1)
                    if u >= 4:
                        act.wait_ge(S["pT_mm"], u - 3)
                    if u >= 8:
                        act.wait_ge(S["pv_read"], u - 7)
                    for tt in range(TT):
                        if kind == "dil":
                            a, w, at = 0, 3 * P * (tile + 1), 0
                        elif kind == "mem":
                            a, w, at = tt * T, T, tt
                        else:
                            a, w, at = tt * P, P * (tt + 1), tt
                        if kind == "dil" and tt:
                            break
                        e = p_sb[:, u % 4, a:a + w]
                        src = bank[2 * (u % 2)][:, a:a + w] if kind == "mem" else e
                        ins = act.activation(e, src, ACT.Exp, scale=SCALE, bias=unit_stat(u, "neg")[:, at:at + 1],
                                             accum_out=unit_stat(u, "sum")[:, at:at + 1])
                    ins.then_inc(S["score_exp"], 1)
                    act.wait_ge(S["score_exp"], made.next("score_exp"))

                def turned(n):
                    kind, h, tile = todo[n]
                    u = n0 + n
                    s = u % 2
                    act.wait_ge(S["pT_mm"], u + 1)
                    if u >= 2:
                        act.wait_ge(S["pv_mm"], u - 1)
                    w = len(blocks_of(kind, tile)) * P
                    act.activation(pT_sb[:, s, 0:w], bank[4 + s][:, 0:w], ACT.Copy).then_inc(S["pT"], 1)
                    act.wait_ge(S["pT"], made.next("pT"))

                for n in range(len(todo) + 2):
                    if n < len(todo):
                        exps(n)
                    if n >= 2:
                        turned(n - 2)
                n_turn = 6 if l == 0 else 11
                copy_xT(n_turn)
                rms(3 * l + 2, x_tm)
                copy_xT(n_turn + 1, f"mlp_norm{l}")
                mlp_act("mlp", D_FF_2 // FCH, l * (D_FF_2 // FCH), 3)

            act.wait_ge(S["consts_in"], 16)
            for l in range(DEPTH):
                mixer_act(l)
                ln_std(2 * l)
                copy_xT(2 * l + 1, f"ln1_g{l}", f"ln1_b{l}")
                if l == 0:
                    mlp_act("ffn", FF_CHUNKS, 0, 2)
                else:
                    act.wait_ge(S["router_w"], 1)
                    p = rt[:, 2, 0:TT * N_EXPERTS]
                    act.activation(p, p, ACT.Exp).then_inc(S["router_exp"], 1)
                    act.wait_ge(S["router_exp"], made.next("router_exp"))
                    moe_act()
                ln_std(2 * l + 1)
            for l in range(DEPTH):
                attention_act(l)

        @block.vector
        def _(dve):
            made = Made()
            tt_, ts_, stt, copy = dve.tensor_tensor, dve.tensor_scalar, dve.scalar_tensor_tensor, dve.tensor_copy

            def pair(b):
                return bank[b][:].rearrange("p (m t) -> p m t", m=2)

            def copy_xT(n, gain=None, bias=None):
                for i, b in enumerate((0, 2)):
                    dve.wait_ge(S["x_turned"], 4 * n + b + 1)
                    if gain is None:
                        ins = copy(xT[:, 2 * b:2 * b + 2, :], pair(b))
                    else:
                        for kk_ in range(2):
                            ins = ts_(xT[:, 2 * b + kk_, :], bank[b][:, kk_ * T:(kk_ + 1) * T], c1(gain, 2 * b + kk_),
                                      *((None, ALU.mult) if bias is None else (c1(bias, 2 * b + kk_), ALU.mult, ALU.add)))
                    ins.then_inc(S["xT_dve"], 1)
                    dve.wait_ge(S["xT_dve"], made.next("xT_dve"))

            def depthwise(out, src, name, taps, first, last):
                for j in range(first, last):
                    for n in range(2):
                        ins = stt(out[:, n, :], src[:, n, j:j + T], c1(name, n * taps + j), out[:, n, :], ALU.mult, ALU.add) if j else \
                            ts_(out[:, n, :], src[:, n, 0:T], c1(name, n * taps), None, ALU.mult)
                    ins.then_inc(S["dve_step"], 1)
                    dve.wait_ge(S["dve_step"], made.next("dve_step"))

            def mixer_dve(l):
                dve.memset(state[:], 0.0).then_inc(S["cleared"], 1)
                dve.wait_ge(S["cleared"], made.next("cleared"))
                copy_xT(2 * l, *((f"ln2_g{l - 1}", f"ln2_b{l - 1}") if l else ()))
                if l:
                    ln_gain(2 * l - 1)
                dve.wait_ge(S["proj_read"], 24 * l + CONV_PANELS)
                tt_(u_pad[:, :, CONF_TAPS - 1:], u_pad[:, :, CONF_TAPS - 1:], conf_s[:], ALU.mult)
                tt_(s_pad[:, :, SHORT_TAPS - 1:], s_pad[:, :, SHORT_TAPS - 1:], conv_c[:], ALU.mult).then_inc(S["dve_step"], 1)
                dve.wait_ge(S["dve_step"], made.next("dve_step"))
                if l == 0:
                    dve.wait_ge(S["params_in"], 16 * 3)
                depthwise(conv_c, s_pad, f"short_dw{l}", SHORT_TAPS, 0, SHORT_TAPS)
                tt_(conv_c[:], conv_c[:], gb[:], ALU.mult).then_inc(S["branch_c"], 1)
                per = -(-CONF_TAPS // 7)
                for j in range(7):
                    depthwise(conv, u_pad, f"conf_dw{l}", CONF_TAPS, j * per, min((j + 1) * per, CONF_TAPS))
                    dve.wait_ge(S["proj_read"], 24 * l + CONV_PANELS + j + 1)
                    z = pz[:, j % 2]
                    tt_(tmp[:, 0:2, :], z[:, :, 0:T], z[:, :, 1:], ALU.subtract).then_inc(S["dve_step"], 1)
                    dve.wait_ge(S["dve_step"], made.next("dve_step"))
                    for m in range(2):
                        ins = stt(sh[:, 2 * j + m, :], tmp[:, m, :], c1(f"mu{l}", 2 * j + m), z[:, m, 1:], ALU.mult, ALU.add)
                    ins.then_inc(S["shifted"], 1)
                    dve.wait_ge(S["shifted"], made.next("shifted"))
                for c in range(NC):
                    ins = ts_(kk[:, c, :], k_[:, c, :], c1(f"k_k{l}", c), None, ALU.mult)
                ins.then_inc(S["dve_step"], 1)
                dve.wait_ge(S["dve_step"], made.next("dve_step"))
                tt_(tmp[:], kk[:], kk[:], ALU.mult).then_inc(S["kk_sq"], 1)
                dve.wait_ge(S["kk_sq"], made.next("kk_sq"))
                for n in range(2):
                    ins = ts_(conv[:, n, :], conv[:, n, :], c1(f"conf_dw_b{l}", n), None, ALU.add)
                ins.then_inc(S["conf_conv"], 1)
                dve.wait_ge(S["aaa"], l + 1)
                dve.wait_ge(S["kk_mm"], l + 1)
                for c in range(NC):
                    ins = ts_(tmp[:, c, :], a_[:, c, :], 1.0, c1(f"k_a{l}", c), ALU.subtract, ALU.mult)
                ins.then_inc(S["dve_step"], 1)
                dve.wait_ge(S["dve_step"], made.next("dve_step"))
                stt(k_, tmp[:], 1.0, k_, ALU.add, ALU.mult).then_inc(S["dve_step"], 1)
                dve.wait_ge(S["dve_step"], made.next("dve_step"))
                for c in range(NC):
                    ins = stt(tmp[:, c, :], r_[:, c, :], c1(f"r_k{l}", c), k_[:, c, :], ALU.mult, ALU.mult)
                dve.wait_ge(S["kk_norm"], l + 1)
                norm = vt[:].rearrange("p a (b t) -> p (a b) t", t=T)
                ts_(norm, norm, 1e-12, None, ALU.max).then_inc(S["dve_step"], 1)
                dve.wait_ge(S["dve_step"], made.next("dve_step"))
                dve.reciprocal(norm, norm).then_inc(S["bonus_in"], 1)
                dve.wait_ge(S["bonus_in"], made.next("bonus_in"))
                tt_(kk[:], kk[:], norm, ALU.mult).then_inc(S["dve_step"], 1)
                dve.wait_ge(S["dve_step"], made.next("dve_step"))
                tt_(a_[:], kk[:], a_[:], ALU.mult).then_inc(S["dve_step"], 1)
                dve.wait_ge(S["dve_step"], made.next("dve_step"))
                dve.wait_ge(S["decays"], l + 1)
                for c in range(NC):
                    stt(ar[:, c, :, 0, :], kk[:, c, :].rearrange("p (t k) -> p t k", t=TT), -1.0,
                        p_ex[:, c, :].rearrange("p (t k) -> p t k", t=TT), ALU.mult, ALU.mult)
                    ins = tt_(ar[:, c, :, 1, :], r_[:, c, :].rearrange("p (t k) -> p t k", t=TT),
                              p_in[:, c, :].rearrange("p (t k) -> p t k", t=TT), ALU.mult)
                ins.then_inc(S["dve_step"], 1)
                dve.wait_ge(S["dve_step"], made.next("dve_step"))
                tt_(a_[:], a_[:], p_inv[:], ALU.mult)
                tt_(kk[:], k_, p_inv[:], ALU.mult).then_inc(S["dve_step"], 1)
                dve.wait_ge(S["dve_step"], made.next("dve_step"))
                dve.wait_ge(S["bonus_mm"], l + 1)
                for n in range(2):
                    ins = tt_(tmp[:, 2 * n:2 * n + 2, :], pair(6 + n), v_[:, 2 * n:2 * n + 2, :], ALU.mult)
                ins.then_inc(S["features"], 1)
                dve.wait_ge(S["features"], made.next("features"))
                for n, dst in enumerate((vt, bt, kt)):
                    dve.wait_ge(S["turn_mm"], 6 * l + 2 * n + 1)
                    copy(dst[:, 0, :], bank[2 + 2 * n % 4][:]).then_inc(S["turned_dve"], 1)
                    dve.wait_ge(S["turned_dve"], made.next("turned_dve"))

                for tt in range(TT):
                    for hg in range(2):
                        group = 4 * l + 2 * tt + hg
                        dve.wait_ge(S["unit_mm"], group + 1)
                        if tt and not hg:
                            dve.wait_ge(S["o_mm"], 4 * l + 2)
                        for i in range(4):
                            tt_(unit[:, 4 * hg + i, :, :].rearrange("p m t -> p (m t)"), bank[2 + i][:], unit_mask, ALU.mult)
                        for j in range(2):
                            ins = tt_(a3[:, j::2], bank[6 + j][:, 0:2 * P].rearrange("p (i s) -> p i s", i=2).unsqueeze(2).to_broadcast([P, 2, 3, P]),
                                      inv_mask.unsqueeze(1).to_broadcast([P, 2, 3, P]), ALU.mult)
                        ins.then_inc(S["dve_step"], 1)
                        dve.wait_ge(S["dve_step"], made.next("dve_step"))
                        tt_(xa[:].rearrange("p (i s) -> p i s", i=4), unit[:, 4 * hg:4 * hg + 4, 0, :],
                            ident.unsqueeze(1).to_broadcast([P, 4, P]), ALU.add).then_inc(S["masks"], 1)
                        dve.wait_ge(S["masks"], made.next("masks"))
                        n = 14 * group
                        fin = inv[:, 4 * hg:4 * hg + 4, :].rearrange("p i s -> p (i s)")
                        for count, b, dst, add in ((1, 2, pw[:, 0, :], None), (3, 4, xb[:], xa[:]), (6, 2, xa[:], xb[:]),
                                                   (8, 4, xb[:], xa[:]), (10, 3, pw[:, 2, :], None), (11, 6, xa[:], xb[:]),
                                                   (13, 5, pw[:, 2, :], None), (14, 2, fin, xa[:])):
                            dve.wait_ge(S["inv_mm"], n + count)
                            ins = copy(dst, bank[b][:]) if add is None else tt_(dst, bank[b][:], add, ALU.add)
                            ins.then_inc(S["inv_dve"], 1)
                            dve.wait_ge(S["inv_dve"], made.next("inv_dve"))
                    for half in range(2):
                        q = 4 * l + 2 * tt + half
                        hs = slice(half * CHUNK, (half + 1) * CHUNK)
                        dve.wait_ge(S["rhs_mm"], q + 1)
                        copy(rhs_sb[hs].rearrange("p h v -> p (h v)"), bank[2][hs, :]).then_inc(S["rhs"], 1)
                        dve.wait_ge(S["rhs"], made.next("rhs"))
                        dve.wait_ge(S["u_mm"], q + 1)
                        copy(u_sb[hs].rearrange("p h v -> p (h v)"), bank[3][hs, :]).then_inc(S["u"], 1)
                        dve.wait_ge(S["u"], made.next("u"))
                        if q % 4 < 3:
                            dve.wait_ge(S["state_mm"], q - l + 1)
                            end = (2 * tt + half) * CHUNK + CHUNK - 1
                            for j, hd in enumerate((slice(0, HEAD), slice(HEAD, P))):
                                ins = tt_(state[hd, :, j, :], bank[4][hd, 0:NC * HEAD].rearrange("p (c v) -> p c v", c=NC), state[hd, :, j, :], ALU.add)
                            ins.then_inc(S["dve_step"], 1)
                            dve.wait_ge(S["dve_step"], made.next("dve_step"))
                            for j, hd in enumerate((slice(0, HEAD), slice(HEAD, P))):
                                ins = tt_(state[hd, :, j, :], state[hd, :, j, :], p_in[hd, :, end:end + 1].to_broadcast([HEAD, NC, HEAD]), ALU.mult)
                            ins.then_inc(S["state"], 1)
                            dve.wait_ge(S["state"], made.next("state"))

                dve.wait_ge(S["gn_mean_mm"], l + 1)
                for n in range(2):
                    ins = stt(oT[:, 2 * n:2 * n + 2, :], pair(2 + n), -1.0 / HEAD, oT[:, 2 * n:2 * n + 2, :], ALU.mult, ALU.add)
                ins.then_inc(S["dve_step"], 1)
                dve.wait_ge(S["dve_step"], made.next("dve_step"))
                ot4 = oT[:].rearrange("p c (t k) -> p c t k", t=TT)
                for c in range(NC):
                    ins = tt_(ar[:, c, :, 0, :], ot4[:, c], ot4[:, c], ALU.mult)
                ins.then_inc(S["gn_sq"], 1)
                dve.wait_ge(S["gn_sq"], made.next("gn_sq"))
                dve.wait_ge(S["conf_mean_mm"], l + 1)
                for n in range(2):
                    ins = stt(conv[:, n, :], bank[6][:, 0:T], -1.0 / CONF, conv[:, n, :], ALU.mult, ALU.add)
                ins.then_inc(S["dve_step"], 1)
                dve.wait_ge(S["dve_step"], made.next("dve_step"))
                tt_(conv_sq[:], conv[:], conv[:], ALU.mult).then_inc(S["conf_sq"], 1)
                dve.wait_ge(S["conf_sq"], made.next("conf_sq"))
                dve.wait_ge(S["gn_std"], l + 1)
                dve.reciprocal(kk[:], kk[:]).then_inc(S["dve_step"], 1)
                dve.wait_ge(S["dve_step"], made.next("dve_step"))
                tt_(oT[:], oT[:], kk[:], ALU.mult).then_inc(S["dve_step"], 1)
                dve.wait_ge(S["dve_step"], made.next("dve_step"))
                for c in range(NC):
                    ins = ts_(yT[:, c, :], oT[:, c, :], c1(f"gn_g{l}", c), c1(f"gn_b{l}", c), ALU.mult, ALU.add)
                ins.then_inc(S["dve_step"], 1)
                dve.wait_ge(S["dve_step"], made.next("dve_step"))
                tt_(yT[:], yT[:], tmp[:], ALU.add).then_inc(S["dve_step"], 1)
                dve.wait_ge(S["dve_step"], made.next("dve_step"))
                tt_(yT[:], yT[:], g_[:], ALU.mult).then_inc(S["branch_a"], 1)
                dve.wait_ge(S["branch_a"], made.next("branch_a"))
                dve.wait_ge(S["conf_std"], l + 1)
                dve.reciprocal(conf_s[:, 0, :], conf_s[:, 0, :]).then_inc(S["dve_step"], 1)
                dve.wait_ge(S["dve_step"], made.next("dve_step"))
                for n in range(2):
                    ins = tt_(conv[:, n, :], conv[:, n, :], conf_s[:, 0, :], ALU.mult)
                ins.then_inc(S["branch_b"], 1)
                dve.wait_ge(S["branch_b"], made.next("branch_b"))
                dve.wait_ge(S["proj_read"], 24 * (l + 1))
                for n in range(4):
                    b = 2 + 3 * (n % 2)
                    m = slice(2 * n, 2 * n + 2)
                    dve.wait_ge(S["mix_mm"], 4 * l + n + 1)
                    for part_ in range(3):
                        g = gates[:, 8 * part_ + 2 * n:8 * part_ + 2 * n + 2, :]
                        ins = tt_(g, pair(b + part_), g, ALU.mult)
                    ins.then_inc(S["dve_step"], 1)
                    dve.wait_ge(S["dve_step"], made.next("dve_step"))
                    tt_(mixT[:, m, :], gates[:, m, :], gates[:, 8 + 2 * n:10 + 2 * n, :], ALU.add).then_inc(S["dve_step"], 1)
                    dve.wait_ge(S["dve_step"], made.next("dve_step"))
                    tt_(mixT[:, m, :], mixT[:, m, :], gates[:, 16 + 2 * n:18 + 2 * n, :], ALU.add).then_inc(S["mixed"], 1)
                    dve.wait_ge(S["mixed"], made.next("mixed"))
                dve.wait_ge(S["wout_mm"], l + 1)
                for tt in range(TT):
                    for h in range(2):
                        xs = x_tm[:, tt, h * 512:(h + 1) * 512]
                        ins = stt(xs, xs, ALPHA, bank[2 * tt + h][:], ALU.mult, ALU.add)
                ins.then_inc(S["dve_step"], 1)
                dve.wait_ge(S["dve_step"], made.next("dve_step"))

            def layer_norm(n, src):
                for tt in range(TT):
                    for h in range(2):
                        s = 12 * tt + 6 * h
                        ins = dve.bn_stats(stat[:, s:s + 6], src[:, tt, h * 512:(h + 1) * 512])
                ins.then_inc(S["dve_step"], 1)
                dve.wait_ge(S["dve_step"], made.next("dve_step"))
                for tt in range(TT):
                    ins = dve.bn_aggr(stat[:, 26 + 2 * tt:28 + 2 * tt], stat[:, 12 * tt:12 * tt + 12])
                ins.then_inc(S["ln_x"], 1)
                dve.wait_ge(S["ln_x"], made.next("ln_x"))
                dve.wait_ge(S["ln_std"], n + 1)
                dve.reciprocal(stat[:, 34:34 + TT], stat[:, 32:32 + TT]).then_inc(S["dve_step"], 1)
                dve.wait_ge(S["dve_step"], made.next("dve_step"))
                for tt in range(TT):
                    ins = ts_(x_tm[:, tt, :], src[:, tt, :], stat[:, 26 + 2 * tt:27 + 2 * tt], stat[:, 34 + tt:35 + tt], ALU.subtract, ALU.mult)
                ins.then_inc(S["ln_z"], 1)
                dve.wait_ge(S["ln_z"], made.next("ln_z"))

            def ln_gain(n):
                if n < 3:
                    dve.wait_ge(S["x_turned"], 4 * (n + 2))
                dve.wait_ge(S["ln_rows_in"], 16 * (n + 1))
                tt_(x_tm[:], x_tm[:], ln_row[:, 0, :].unsqueeze(1).to_broadcast([P, TT, D]), ALU.mult).then_inc(S["dve_step"], 1)
                dve.wait_ge(S["dve_step"], made.next("dve_step"))
                tt_(x_tm[:], x_tm[:], ln_row[:, 1, :].unsqueeze(1).to_broadcast([P, TT, D]), ALU.add).then_inc(S["ln_x_done"], 1)
                dve.wait_ge(S["ln_x_done"], made.next("ln_x_done"))

            def scale_x(n):
                dve.wait_ge(S["x_turned"], 4 * (n + 1))
                ts_(x_tm[:], x_tm[:], ALPHA, None, ALU.mult).then_inc(S["dve_step"], 1)
                dve.wait_ge(S["dve_step"], made.next("dve_step"))

            def route():
                dve.wait_ge(S["router_mm"], 1)
                lg, rank, p, mx, sq = rt[:, 0, 0:TT * E], rt[:, 1, 0:TT * E], rt[:, 2, 0:TT * E], rt[:, 3, 0:TT], rt[:, 4:6, :]
                l3, p3 = (t.rearrange("p (t e) -> p t e", t=TT) for t in (lg, p))
                copy(lg, bank[0][:, 0:TT * E]).then_inc(S["dve_step"], 1)
                dve.wait_ge(S["dve_step"], made.next("dve_step"))
                dve.tensor_reduce(mx, l3, AX.X, ALU.max).then_inc(S["dve_step"], 1)
                dve.wait_ge(S["dve_step"], made.next("dve_step"))
                tt_(p3, l3, mx.unsqueeze(2).to_broadcast([P, TT, E]), ALU.subtract).then_inc(S["dve_step"], 1)
                dve.wait_ge(S["dve_step"], made.next("dve_step"))
                earlier = cst[:, CONST["earlier"]].rearrange("p (e f) -> p e f", e=E)
                for tt in range(TT):
                    this = l3[:, tt, :].unsqueeze(2).to_broadcast([P, E, E])
                    other = l3[:, tt, :].unsqueeze(1).to_broadcast([P, E, E])
                    s0, s1 = (sq[:, i, :].rearrange("p (e f) -> p e f", e=E) for i in range(2))
                    tt_(s0, other, this, ALU.is_gt)
                    tt_(s1, other, this, ALU.is_equal).then_inc(S["dve_step"], 1)
                    dve.wait_ge(S["dve_step"], made.next("dve_step"))
                    tt_(s1, s1, earlier, ALU.mult).then_inc(S["dve_step"], 1)
                    dve.wait_ge(S["dve_step"], made.next("dve_step"))
                    tt_(s0, s0, s1, ALU.add).then_inc(S["dve_step"], 1)
                    dve.wait_ge(S["dve_step"], made.next("dve_step"))
                    dve.tensor_reduce(rank[:, tt * E:(tt + 1) * E], s0, AX.X, ALU.add).then_inc(S["dve_step"], 1)
                    dve.wait_ge(S["dve_step"], made.next("dve_step"))
                ts_(rank, rank, 1.5, None, ALU.is_lt).then_inc(S["router_w"], 1)
                dve.wait_ge(S["router_w"], made.next("router_w"))
                dve.wait_ge(S["router_exp"], 1)
                tt_(p, p, rank, ALU.mult).then_inc(S["dve_step"], 1)
                dve.wait_ge(S["dve_step"], made.next("dve_step"))
                dve.tensor_reduce(mx, p3, AX.X, ALU.add).then_inc(S["dve_step"], 1)
                dve.wait_ge(S["dve_step"], made.next("dve_step"))
                dve.reciprocal(mx, mx).then_inc(S["dve_step"], 1)
                dve.wait_ge(S["dve_step"], made.next("dve_step"))
                tt_(moe_w[:], p3, mx.unsqueeze(2).to_broadcast([P, TT, E]), ALU.mult).then_inc(S["dve_step"], 1)
                dve.wait_ge(S["dve_step"], made.next("dve_step"))
                dve.wait_ge(S["counts_mm"], 1)
                n = ITEMS + 1
                copy(moe_pos[:].rearrange("p t e -> p (t e)"), bank[1][:, 0:TT * E])
                count, items, start, end = (tiles[:, i, :] for i in range(4))
                copy(count, bank[1][:, TT * E:(TT + 1) * E]).then_inc(S["dve_step"], 1)
                dve.wait_ge(S["dve_step"], made.next("dve_step"))
                ts_(items, count, CAP + 0.5, 1.0, ALU.is_gt, ALU.add).then_inc(S["dve_step"], 1)
                dve.wait_ge(S["dve_step"], made.next("dve_step"))
                s0 = sq[:, 0, :].rearrange("p (e f) -> p e f", e=E)
                tt_(s0, items.unsqueeze(1).to_broadcast([P, E, E]), earlier, ALU.mult)
                chosen = rank.rearrange("p (t e) -> p t e", t=TT)
                far = rt[:, 0, 0:TT * E].rearrange("p (t e) -> p t e", t=TT)
                ts_(far, chosen, -4.0 * T, 4.0 * T, ALU.mult, ALU.add)
                dve.tensor_reduce(table[:, 0:1], items, AX.X, ALU.add).then_inc(S["dve_step"], 1)
                dve.wait_ge(S["dve_step"], made.next("dve_step"))
                tt_(moe_pos[:], moe_pos[:], far, ALU.add)
                dve.tensor_reduce(start, s0, AX.X, ALU.add).then_inc(S["dve_step"], 1)
                dve.wait_ge(S["dve_step"], made.next("dve_step"))
                tt_(end, start, items, ALU.add).then_inc(S["dve_step"], 1)
                dve.wait_ge(S["dve_step"], made.next("dve_step"))
                count = cst[:, CONST["count"]]
                number = count[:, 0:n].unsqueeze(2).to_broadcast([P, n, E])
                its, late, skip, work = (in_item[:, i, :].rearrange("p (i e) -> p i e", e=E) for i in range(4))
                tt_(its, number, start.unsqueeze(1).to_broadcast([P, n, E]), ALU.is_ge)
                tt_(late, number, end.unsqueeze(1).to_broadcast([P, n, E]), ALU.is_lt)
                tt_(skip, number, start.unsqueeze(1).to_broadcast([P, n, E]), ALU.subtract).then_inc(S["dve_step"], 1)
                dve.wait_ge(S["dve_step"], made.next("dve_step"))
                tt_(its, its, late, ALU.mult).then_inc(S["dve_step"], 1)
                dve.wait_ge(S["dve_step"], made.next("dve_step"))
                tt_(work, its, count[:, 0:E].unsqueeze(1).to_broadcast([P, n, E]), ALU.mult).then_inc(S["dve_step"], 1)
                dve.wait_ge(S["dve_step"], made.next("dve_step"))
                dve.tensor_reduce(table[:, 1:1 + n], work, AX.X, ALU.add).then_inc(S["dve_step"], 1)
                dve.wait_ge(S["dve_step"], made.next("dve_step"))
                copy(table_i[:], table[:]).then_inc(S["items_ready"], 1)
                dve.wait_ge(S["items_ready"], made.next("items_ready"))
                for tt in range(TT):
                    stt(late, skip, -float(CAP), moe_pos[:, tt, :].unsqueeze(1).to_broadcast([P, n, E]), ALU.mult, ALU.add)
                    tt_(work, its, moe_w[:, tt, :].unsqueeze(1).to_broadcast([P, n, E]), ALU.mult).then_inc(S["dve_step"], 1)
                    dve.wait_ge(S["dve_step"], made.next("dve_step"))
                    tt_(late, late, its, ALU.mult)
                    dve.tensor_reduce(item_w[:, tt, :], work, AX.X, ALU.add).then_inc(S["dve_step"], 1)
                    dve.wait_ge(S["dve_step"], made.next("dve_step"))
                    dve.tensor_reduce(item_pos[:, tt, :], late, AX.X, ALU.add).then_inc(S["dve_step"], 1)
                    dve.wait_ge(S["dve_step"], made.next("dve_step"))

            def moe_dve():
                count = cst[:, CONST["count"]]
                n_items = dve.value_load(table_i[0:1, 0:1], min_val=N_EXPERTS, max_val=ITEMS)

                def tokens():
                    return copy(xeT[:, 0:4, :], bank[4][:].rearrange("p (k c) -> p k c", k=4))

                for tt in range(TT):
                    ins = ts_(one_hot[:, tt, :], count, item_pos[:, tt, 0:1], None, ALU.is_equal)
                ins.then_inc(S["one_hot"], 1)
                dve.wait_ge(S["routed_mm"], 1)
                tokens().then_inc(S["xe_dve"], 1)
                ts_(acc[:], x_tm[:], ALPHA, None, ALU.mult).then_inc(S["acc_read"], 1)
                with dve.Fori(0, n_items) as item:
                    for s in range(FF_CHUNKS):
                        dve.wait_ge(S["act_out"], item * FF_CHUNKS + (FF_CHUNKS + s + 1))
                        dve.wait_ge(S["y_full"], item * FF_CHUNKS + (FF_CHUNKS + max(s - 1, 0)))
                        tt_(hT[:, s % 2, :, 0:CAP], gate_s[:, s % 2, :, 0:CAP], bank[s % 2][:, 2 * CAP:].rearrange("p (m c) -> p m c", m=2),
                            ALU.mult).then_inc(S["h_ready"], 1)
                        if s == 2:
                            dve.wait_ge(S["routed_mm"], item + 1)
                            for tt in range(TT):
                                ts_(one_hot[:, tt, :], count, item_pos[:, tt, bass.ds(item + 1, 1)], None, ALU.is_equal)
                                ins = ts_(weighted[:, tt, :], count, item_pos[:, tt, bass.ds(item, 1)], item_w[:, tt, bass.ds(item, 1)],
                                          ALU.is_equal, ALU.mult)
                            ins.then_inc(S["one_hot"], 1)
                    dve.wait_ge(S["routed_mm"], item + 2)
                    tokens().then_inc(S["xe_dve"], 1)
                    dve.wait_ge(S["acc_read"], item + 1)
                    for h in range(2):
                        dve.wait_ge(S["scatter_mm"], 2 * item + (h + 1))
                        for tt in range(TT):
                            a = acc[:, tt, h * 512:(h + 1) * 512]
                            ins = tt_(a, a, bank[4 + 2 * h + tt][:], ALU.add)
                    ins.then_inc(S["acc_read"], 1)
                dve.wait_ge(S["acc_read"], n_items + 1)

            def mlp_dve(kind, n_chunks, base, per_step):
                gated, sems = kind == "ffn", mlp_signals(kind)
                nb = 2 if gated else 3

                def hidden(i, slot, early):
                    dve.wait_ge(sems["out"], i + 1)
                    if not early:
                        dve.wait_ge(sems["y"], i - nb + 1)
                    b = bank[(2 * slot + 1) if gated else slot]
                    tt_(hT[:, slot, :, :], gate_s[:, slot, :, :], b[:].rearrange("p (m t) -> p m t", m=2), ALU.mult).then_inc(sems["h"], 1)

                def add(i):
                    dve.wait_ge(sems["y"], i + 1)
                    if not (isinstance(i, int) and i == 0):
                        dve.wait_ge(sems["read"], i)
                    for tt in range(TT):
                        for h in range(2):
                            xs = x_tm[:, tt, h * 512:(h + 1) * 512]
                            ins = tt_(xs, xs, bank[4 + 2 * tt + h][:], ALU.add)
                    ins.then_inc(sems["read"], 1)

                hidden(base, 0, True)
                lead = nb + (n_chunks - nb) % per_step
                for s in range(1, lead):
                    hidden(base + s, s % nb, s < nb)
                    add(base + s - 1)
                with dve.Fori(0, (n_chunks - lead) // per_step) as turn:
                    for s in range(lead, lead + per_step):
                        hidden(turn * per_step + (base + s), s % nb, False)
                        add(turn * per_step + (base + s - 1))
                add(base + n_chunks - 1)
                dve.wait_ge(sems["read"], base + n_chunks)

            def rms_x(n, src):
                dve.wait_ge(S["rms_std"], n + 1)
                if n:
                    dve.wait_ge(S["x_turned"], 4 * (4, 5, 6, 8, 9, 11)[n])
                dve.reciprocal(rs[:, 4:4 + TT], rs[:, 2:2 + TT]).then_inc(S["dve_step"], 1)
                dve.wait_ge(S["dve_step"], made.next("dve_step"))
                for tt in range(TT):
                    ins = ts_(xn[:, tt, :], src[:, tt, :], rs[:, 4 + tt:5 + tt], None, ALU.mult)
                ins.then_inc(S["rms_x"], 1)
                dve.wait_ge(S["rms_x"], made.next("rms_x"))

            def rotate(dst1, dst2, src, n, cos, sin, parts=slice(0, P)):
                a, b = (scr[parts, i, 0:n * HEAD] for i in range(2))
                w = a.shape[0]
                for t, f in ((a, cos), (b, sin)):
                    ins = tt_(t.rearrange("p (n d e) -> p n d e", d=2, e=32), src.rearrange("p n (d e) -> p n d e", d=2),
                              f.unsqueeze(1).unsqueeze(1).to_broadcast([w, n, 2, 32]), ALU.mult)
                ins.then_inc(S["dve_step"], 1)
                dve.wait_ge(S["dve_step"], made.next("dve_step"))
                a, b = (t.rearrange("p (n e) -> p n e", e=HEAD) for t in (a, b))
                for d, x0, x1, op in ((dst1, a[:, :, 0:32], b[:, :, 32:], ALU.subtract), (dst2, b[:, :, 0:32], a[:, :, 32:], ALU.add)):
                    for dst in d:
                        ins = tt_(dst, x0, x1, op)
                return ins

            def norm_heads(l, first, last):
                sets = head_sets(l)
                base = l * N_SETS[0]

                def squares(i):
                    src, n, panels_ = sets[i][0], sets[i][1], sets[i][5]
                    at, _ = set_stats(l, i)
                    dve.wait_ge(S["attn_read"], l * PANELS_ATTN[0] + panels_)
                    for tt in range(TT):
                        sq = scr[:, tt, 0:n * HEAD]
                        tt_(sq, src[:, tt, :], src[:, tt, :], ALU.mult).then_inc(S["dve_step"], 1)
                        dve.wait_ge(S["dve_step"], made.next("dve_step"))
                        ins = dve.tensor_reduce(rs[:, at + tt * n:at + (tt + 1) * n], sq.rearrange("p (n e) -> p n e", e=HEAD), AX.X, ALU.add)
                    ins.then_inc(S["rms_ss"], 1)
                    dve.wait_ge(S["rms_ss"], made.next("rms_ss"))

                def turn(i):
                    src, n, gain, rotary, place, _ = sets[i]
                    at, size = set_stats(l, i)
                    dve.wait_ge(S["qk_std"], base + i + 1)
                    dve.reciprocal(rs[:, at:at + size], rs[:, at:at + size]).then_inc(S["dve_step"], 1)
                    dve.wait_ge(S["dve_step"], made.next("dve_step"))
                    for tt in range(TT):
                        x3 = src[:, tt, :].rearrange("p (n e) -> p n e", e=HEAD)
                        tt_(x3, x3, rs[:, at + tt * n:at + (tt + 1) * n].unsqueeze(2).to_broadcast([P, n, HEAD]), ALU.mult).then_inc(S["dve_step"], 1)
                        dve.wait_ge(S["dve_step"], made.next("dve_step"))
                        tt_(x3, x3, row[:, gain:gain + HEAD].unsqueeze(1).to_broadcast([P, n, HEAD]), ALU.mult).then_inc(S["dve_step"], 1)
                        dve.wait_ge(S["dve_step"], made.next("dve_step"))
                        if rotary:
                            cos, sin = (atc[:, ATTN[f]].rearrange("p (t e) -> p t e", t=TT)[:, tt, :] for f in ("cos", "sin"))
                            if place is None:
                                d1, d2 = [x3[:, :, 0:32]], [x3[:, :, 32:]]
                            else:
                                d1, d2 = ([twice[:, tt, place:place + n, i, e:e + 32] for i in range(2)] for e in (0, 32))
                            rotate(d1, d2, x3, n, cos, sin).then_inc(S["dve_step"], 1)
                            dve.wait_ge(S["dve_step"], made.next("dve_step"))

                for i in range(first, last):
                    squares(i)
                    turn(i)
                    if l == 0 and i == 2:
                        for tt in range(TT):
                            for j in range(2):
                                copy(twice[:, tt, 6:12, j, :], proj[:, tt, 768:1152].rearrange("p (n e) -> p n e", e=HEAD))

            def compress():
                pos = col[:, COLS["cmp_pos"]].rearrange("p (k l) -> p k l", k=2)
                dve.wait_ge(S["turnq_act"], BANKS_T[0] // 2)
                for kv in range(2):
                    for g in range(NSA_G):
                        item = qkT[:, 12 + 3 * kv + g, :].rearrange("p (a s) -> p a s", s=CMP_STRIDE)
                        for odd in range(2):
                            hd = slice(HEAD * odd, HEAD * (odd + 1))
                            for hi in range(2):
                                ins = tt_(cmp_in[hd, kv, 8 * hi:8 * hi + 8, g, :].rearrange("p l i -> p i l"), item[hd, hi:hi + N_CMP, odd::2],
                                          pos[hd, kv, 8 * hi:8 * hi + 8].unsqueeze(1).to_broadcast([HEAD, N_CMP, 8]), ALU.add)
                ins.then_inc(S["cmp_tb"], 1)
                dve.wait_ge(S["cmp_tb"], made.next("cmp_tb"))
                dve.wait_ge(S["cmp_o_mm"], 1)
                blk = slice(0, N_CMP)
                for kv in range(2):
                    b2 = row[blk, ROWS["cmp_b2"]][:, kv * HEAD:(kv + 1) * HEAD].unsqueeze(1).to_broadcast([N_CMP, NSA_G, HEAD])
                    ins = tt_(cmp_kv[blk, kv, :, :], bank[0][blk, kv * NSA_G * HEAD:(kv + 1) * NSA_G * HEAD].rearrange("p (g e) -> p g e", e=HEAD), b2, ALU.add)
                ins.then_inc(S["dve_step"], 1)
                dve.wait_ge(S["dve_step"], made.next("dve_step"))
                k = cmp_kv[blk, 0, :, :]
                tt_(cmp_dup[blk, :, 0, :], k, k, ALU.mult).then_inc(S["dve_step"], 1)
                dve.wait_ge(S["dve_step"], made.next("dve_step"))
                dve.tensor_reduce(rs[blk, 4:4 + NSA_G], cmp_dup[blk, :, 0, :], AX.X, ALU.add).then_inc(S["cmp_kv"], 1)
                dve.wait_ge(S["cmp_kv"], made.next("cmp_kv"))
                dve.wait_ge(S["cmp_k_std"], 1)
                dve.reciprocal(rs[blk, 4:4 + NSA_G], rs[blk, 4:4 + NSA_G]).then_inc(S["dve_step"], 1)
                dve.wait_ge(S["dve_step"], made.next("dve_step"))
                tt_(k, k, rs[blk, 4:4 + NSA_G].unsqueeze(2).to_broadcast([N_CMP, NSA_G, HEAD]), ALU.mult).then_inc(S["dve_step"], 1)
                dve.wait_ge(S["dve_step"], made.next("dve_step"))
                tt_(k, k, row[blk, ROWS["a_k"]][:, 0:HEAD].unsqueeze(1).to_broadcast([N_CMP, NSA_G, HEAD]), ALU.mult).then_inc(S["dve_step"], 1)
                dve.wait_ge(S["dve_step"], made.next("dve_step"))
                d1, d2 = ([cmp_dup[blk, :, i, e:e + 32] for i in range(2)] for e in (0, 32))
                rotate(d1, d2, k, NSA_G, atc[blk, ATTN["cmp_cos"]], atc[blk, ATTN["cmp_sin"]], blk).then_inc(S["cmp_k_ready"], 1)
                dve.wait_ge(S["cmp_k_ready"], made.next("cmp_k_ready"))
                dve.wait_ge(S["cmp_kT_mm"], 1)
                copy(cmp_kT[:, :, 0:N_CMP], bank[1][:, 0:NSA_G * 16].rearrange("p (g i) -> p g i", g=NSA_G)[:, :, 0:N_CMP]).then_inc(S["cmp_kT"], 1)
                dve.wait_ge(S["cmp_kT"], made.next("cmp_kT"))
                dve.wait_ge(S["cmp_s_mm"], 1)
                s3 = cmp_s[:].rearrange("p h t i -> p (h t) i")[:, :, 0:N_CMP]
                mask = atc[:, ATTN["cmp"]].rearrange("p (t i) -> p t i", t=TT)[:, :, 0:N_CMP]
                for odd in range(2):
                    ins = tt_(cmp_s[:, odd::2, :, 0:N_CMP], bank[2 + odd][:, 0:6 * TT * 16].rearrange("p (h t i) -> p h t i", h=6, t=TT)[:, :, :, 0:N_CMP],
                              mask.unsqueeze(1).to_broadcast([P, 6, TT, N_CMP]), ALU.add)
                ins.then_inc(S["dve_step"], 1)
                dve.wait_ge(S["dve_step"], made.next("dve_step"))
                n = NSA_HEADS * TT
                mx = rs[:, 8:8 + n]
                dve.tensor_reduce(mx, s3, AX.X, ALU.max).then_inc(S["dve_step"], 1)
                dve.wait_ge(S["dve_step"], made.next("dve_step"))
                tt_(s3, s3, mx.unsqueeze(2).to_broadcast([P, n, N_CMP]), ALU.subtract).then_inc(S["cmp_s"], 1)
                dve.wait_ge(S["cmp_s"], made.next("cmp_s"))
                dve.wait_ge(S["cmp_e"], 1)
                dve.wait_ge(S["nsa_gates"], 1)
                dve.tensor_reduce(mx, s3, AX.X, ALU.add).then_inc(S["dve_step"], 1)
                dve.wait_ge(S["dve_step"], made.next("dve_step"))
                dve.reciprocal(mx, mx).then_inc(S["dve_step"], 1)
                dve.wait_ge(S["dve_step"], made.next("dve_step"))
                tt_(mx, mx, coef[:, 0].rearrange("p h t -> p (h t)"), ALU.mult).then_inc(S["dve_step"], 1)
                dve.wait_ge(S["dve_step"], made.next("dve_step"))
                m3 = mx.rearrange("p (h t) -> p h t", t=TT)
                tt_(m3, m3, atc[:, ATTN["cmp_ok"]].unsqueeze(1).to_broadcast([P, NSA_HEADS, TT]), ALU.mult).then_inc(S["dve_step"], 1)
                dve.wait_ge(S["dve_step"], made.next("dve_step"))
                tt_(s3, s3, mx.unsqueeze(2).to_broadcast([P, n, N_CMP]), ALU.mult).then_inc(S["cmp_p"], 1)
                dve.wait_ge(S["cmp_p"], made.next("cmp_p"))
                for h in range(NSA_HEADS):
                    dve.wait_ge(S["cmp_pv_mm"], h + 1)
                    copy(o_tm[:, :, h * HEAD:(h + 1) * HEAD], bank[6 + h % 2][:, 0:TT * HEAD].rearrange("p (t e) -> p t e", t=TT)).then_inc(S["cmp_done"], 1)
                    dve.wait_ge(S["cmp_done"], made.next("cmp_done"))

            def attend(l):
                n0 = 0 if l == 0 else len(units(0))
                todo = units(l)

                def maxima(n):
                    kind, h, tile = todo[n]
                    u = n0 + n
                    s = u % 2
                    p = p_sb[:, u % 4, :]
                    mx, neg = unit_stat(u, "max"), unit_stat(u, "neg")
                    dve.wait_ge(S["score_mm"], u + 1)
                    if u >= 4:
                        dve.wait_ge(S["pT_mm"], u - 3)
                    k = TT
                    if kind == "dil":
                        k, w = 1, 3 * P * (tile + 1)
                        mask = atc[:, ATTN[f"dil{tile}"]]
                        for a in range(0, w, 512):
                            e = min(a + 512, w)
                            ins = tt_(p[:, a:e], bank[2 * s + a // 512][:, 0:e - a], mask[:, a:e], ALU.add)
                        ins.then_inc(S["dve_step"], 1)
                        dve.wait_ge(S["dve_step"], made.next("dve_step"))
                        ins = dve.tensor_reduce(mx[:, 0:1], p[:, 0:w], AX.X, ALU.max)
                    elif kind == "mem":
                        ins = dve.tensor_reduce(mx, bank[2 * s][:].rearrange("p (t k) -> p t k", t=TT), AX.X, ALU.max)
                    else:
                        tt_(p[:, 0:3 * P], bank[2 * s][:, 0:3 * P], causal, ALU.add).then_inc(S["dve_step"], 1)
                        dve.wait_ge(S["dve_step"], made.next("dve_step"))
                        dve.tensor_reduce(mx[:, 0:1], p[:, 0:P], AX.X, ALU.max)
                        ins = dve.tensor_reduce(mx[:, 1:2], p[:, P:3 * P], AX.X, ALU.max)
                    ins.then_inc(S["dve_step"], 1)
                    dve.wait_ge(S["dve_step"], made.next("dve_step"))
                    ts_(neg[:, 0:k], mx[:, 0:k], -SCALE, None, ALU.mult).then_inc(S["score_max"], 1)
                    dve.wait_ge(S["score_max"], made.next("score_max"))

                def finish(n):
                    kind, h, tile = todo[n]
                    u = n0 + n
                    s = u % 2
                    k = 1 if kind == "dil" else TT
                    inv_, scale_ = unit_stat(u, "inv")[:, 0:k], unit_stat(u, "scale")[:, 0:k]
                    dve.wait_ge(S["pv_mm"], u + 1)
                    dve.reciprocal(inv_, unit_stat(u, "sum")[:, 0:k]).then_inc(S["dve_step"], 1)
                    dve.wait_ge(S["dve_step"], made.next("dve_step"))
                    if kind == "dil":
                        ins = ts_(o_tm[:, tile, h * HEAD:(h + 1) * HEAD], bank[6 + s][:, 0:HEAD], inv_, None, ALU.mult)
                    else:
                        pv = bank[6 + s][:, 0:TT * HEAD].rearrange("p (t e) -> p t e", t=TT)
                        base = {"mem": NSA_HEADS * HEAD if l == 0 else SLOTS * HEAD}.get(kind, 0)
                        o = o_tm[:, :, base + h * HEAD:base + (h + 1) * HEAD]
                        if kind == "mem":
                            ins = tt_(o, pv, inv_.unsqueeze(2).to_broadcast([P, TT, HEAD]), ALU.mult)
                        else:
                            tt_(scale_, inv_, coef[:, 1 if kind == "sel" else 2, h, :], ALU.mult).then_inc(S["dve_step"], 1)
                            dve.wait_ge(S["dve_step"], made.next("dve_step"))
                            part_ = scr[:, 0, 0:TT * HEAD].rearrange("p (t e) -> p t e", t=TT)
                            tt_(part_, pv, scale_.unsqueeze(2).to_broadcast([P, TT, HEAD]), ALU.mult).then_inc(S["dve_step"], 1)
                            dve.wait_ge(S["dve_step"], made.next("dve_step"))
                            ins = tt_(o, o, part_, ALU.add)
                    ins.then_inc(S["pv_read"], 1)
                    dve.wait_ge(S["pv_read"], made.next("pv_read"))

                for n in range(len(todo) + 4):
                    if n < len(todo):
                        maxima(n)
                    if n >= 4:
                        finish(n - 4)

            def attention_dve(l):
                n_turn = 4 + 4 * l
                dve.wait_ge(S["params_in"], 16 * 4)
                rms_x(3 * l, o_tm)
                copy_xT(n_turn, f"mem_norm{l}")
                rms_x(3 * l + 1, x_tm)
                if l == 0:
                    copy_xT(n_turn + 1, "attn_norm0")
                    norm_heads(l, 0, 5)
                else:
                    copy_xT(n_turn + 1, "kv_norm")
                    norm_heads(l, 0, 1)
                    copy_xT(n_turn + 2, "attn_norm1")
                    norm_heads(l, 1, 6)
                dve.drain().then_inc(S["qk_ready"], 1)
                n0 = 0 if l == 0 else BANKS_T[0]
                for n in range(BANKS_T[l]):
                    if (n0 + n) % 2 == 0:
                        dve.wait_ge(S["turnq_mm"], n0 + n + 1)
                        copy(qkT[:, 2 * n:2 * n + 2, :], bank[n % 4][:].rearrange("p (i t) -> p i t", i=2)).then_inc(S["turnq_dve"], 1)
                        dve.wait_ge(S["turnq_dve"], made.next("turnq_dve"))
                if l == 0:
                    compress()
                else:
                    dve.memset(o_tm[:, :, (SLOTS + MEM_HEADS) * HEAD:], 0.0).then_inc(S["dve_step"], 1)
                    dve.wait_ge(S["dve_step"], made.next("dve_step"))
                attend(l)
                n_turn = 6 if l == 0 else 11
                copy_xT(n_turn)
                dve.wait_ge(S["proj2_mm"], l + 1)
                for tt in range(TT):
                    for h in range(2):
                        xs = x_tm[:, tt, h * 512:(h + 1) * 512]
                        ins = tt_(xs, xs, bank[2 * tt + h][:], ALU.add)
                ins.then_inc(S["x_done"], 1)
                dve.wait_ge(S["x_done"], made.next("x_done"))
                rms_x(3 * l + 2, x_tm)
                copy_xT(n_turn + 1, f"mlp_norm{l}")
                mlp_dve("mlp", D_FF_2 // FCH, l * (D_FF_2 // FCH), 3)

            dve.memset(u_pad[:, :, 0:CONF_TAPS - 1], 0.0)
            dve.memset(s_pad[:, :, 0:SHORT_TAPS - 1], 0.0)
            dve.memset(u_sb[:], 0.0)
            dve.memset(pz[:, :, :, 0:1], 0.0).then_inc(S["cleared"], 1)
            dve.wait_ge(S["cleared"], made.next("cleared"))
            dve.wait_ge(S["consts_in"], 16)
            for l in range(DEPTH):
                mixer_dve(l)
                layer_norm(2 * l, x_tm)
                copy_xT(2 * l + 1, f"ln1_g{l}", f"ln1_b{l}")
                ln_gain(2 * l)
                if l == 0:
                    scale_x(2 * l + 1)
                    mlp_dve("ffn", FF_CHUNKS, 0, 2)
                    layer_norm(2 * l + 1, x_tm)
                else:
                    route()
                    moe_dve()
                    layer_norm(2 * l + 1, acc)
                    ln_gain(2 * l + 1)
            for l in range(DEPTH):
                attention_dve(l)

        @block.gpsimd
        def _(pool):
            for dst, src in ((col, cols), (mid, mids)):
                pool.dma_start(dst[:], src).then_inc(S["params_in"], 16)
            pool.dma_start(row[:], rows.partition_broadcast(P)).then_inc(S["params_in"], 16)
            for n in range(2 * DEPTH):
                if n:
                    pool.wait_ge(S["ln_x_done"], n)
                pool.dma_start(ln_row[:], ln_rows[n].partition_broadcast(P)).then_inc(S["ln_rows_in"], 16)
            pool.wait_ge(S["ln_x_done"], 2 * DEPTH)
            pool.dma_start(atc[:], attn_consts).then_inc(S["params_in"], 16)
            for l in range(DEPTH):
                if l:
                    pool.wait_ge(S["proj2_mm"], l)
                pool.dma_start(o_tm[:], mem.rearrange("(t p) d -> p t d", p=P)).then_inc(S["mem_in"], 16)


def lay_out(i):
    def f(name):
        return np.asarray(i[name], np.float32)

    def blocks(v):
        return v.reshape(-1, P).T

    def col_panel(w, n):
        c = w[:, n * PC:(n + 1) * PC]
        if c.shape[1] < PC:
            c = np.pad(c, ((0, 0), (0, PC - c.shape[1])))
        return c.reshape(KB, P, PC).transpose(1, 0, 2)

    def row_panel(w, n):
        return w[n * PR * P:(n + 1) * PR * P].reshape(PR, P, D).transpose(1, 0, 2)

    per = D_FF // FCH
    branch_out = [np.concatenate([f(n)[l] for n in ("rwkv_w_o", "conf_w_o", "short_w_o")]) for l in range(DEPTH)]
    w_in, w_out, mem_kv = f("w_in"), f("w_out"), f("w_mem_kv_2")
    ffn = [f("ffn_w_gate"), f("ffn_w_up"), f("ffn_w_down")]
    moe = [f("moe_w_gate")[0], f("moe_w_up")[0], f("moe_w_down")[0]]
    a_in, a_out, kv, b_in, b_out = f("a_w_in_2")[0], f("a_w_out_2")[0], f("w_kv_shared_2"), f("b_w_in_2")[0], f("b_w_out_2")[0]
    cmp_w1, up, down = f("a_cmp_w1_2")[0], f("w_up_2"), f("w_down_2")

    def panel(kind, l, n):
        if kind == "w_in":
            return col_panel(w_in[l], n)
        if kind == "mix":
            return col_panel(branch_out[l], n)
        if kind == "w_out":
            return row_panel(w_out[l], n)
        if kind in ("gate", "up", "down"):
            m = ("gate", "up", "down").index(kind)
            w = (moe if l else ffn)[m][n // per]
            return row_panel(w, n % per) if kind == "down" else col_panel(w, n % per)
        if kind == "mem_kv":
            return col_panel(mem_kv[l], n)
        if kind == "cmp":
            return cmp_w1[n // 2].reshape(2, KB, P, CMP_HIDDEN)[n % 2].transpose(1, 0, 2)
        if kind in ("mlp_up", "mlp_down"):
            return col_panel(up[l], n) if kind == "mlp_up" else row_panel(down[l], n)
        w = {"a_in": a_in, "kv": kv, "b_in": b_in, "a_out": a_out, "b_out": b_out}[kind]
        return row_panel(w, n) if kind.endswith("out") else col_panel(w, n)

    weights = np.empty((N_PANELS, P, PANEL), np.float32)
    for n, (kind, l, m) in enumerate(ORDER):
        weights[n] = panel(kind, l, m).reshape(P, PANEL)

    cols = np.zeros((P, COLS.n), np.float32)
    for l in range(DEPTH):
        for name, src in (("mu", "rwkv_mu"), ("a0", "rwkv_a0"), ("k_k", "rwkv_k_k"), ("k_a", "rwkv_k_a"), ("r_k", "rwkv_r_k"),
                          ("gn_g", "rwkv_ln_g"), ("gn_b", "rwkv_ln_b"), ("conf_dw_b", "conf_dw_b"), ("conf_ln_g", "conf_ln_g"),
                          ("conf_ln_b", "conf_ln_b"), ("attn_norm", "attn_norm_2"), ("mlp_norm", "mlp_norm_2"),
                          ("mem_norm", "mem_norm_2"), ("ln1_g", "ln1_g"), ("ln1_b", "ln1_b"), ("ln2_g", "ln2_g"), ("ln2_b", "ln2_b")):
            cols[:, COLS[f"{name}{l}"]] = blocks(f(src)[l].reshape(-1))
        for name in ("conf_dw", "short_dw"):
            w = f(name)[l]
            cols[:, COLS[f"{name}{l}"]] = w.T.reshape(2, P, -1).transpose(1, 0, 2).reshape(P, -1)
    cols[:, COLS["kv_norm"]] = blocks(f("kv_norm_2"))
    cols[:, COLS["cmp_b1"]] = blocks(f("a_cmp_b1_2").reshape(-1))
    cols[:, COLS["cmp_pos"]] = f("a_cmp_pos_2")[0].reshape(2, CMP_BLOCK // 2, P).transpose(2, 0, 1).reshape(P, -1)

    mids = np.zeros((P, MIDS.n), np.float32)
    for l in range(DEPTH):
        mids[:, MIDS[f"w2a2{l}"]] = np.concatenate([f("rwkv_w2")[l], f("rwkv_a2")[l]])
        mids[:, MIDS[f"g2{l}"]] = f("rwkv_g2")[l]
    mids[:, MIDS["router"]] = f("moe_router")[0].reshape(KB, P, N_EXPERTS).transpose(1, 0, 2).reshape(P, -1)
    mids[:, MIDS["cmp_w2"]] = f("a_cmp_w2_2")[0].reshape(2, 2, P, HEAD).transpose(2, 0, 1, 3).reshape(P, -1)

    rows = np.concatenate([f("rwkv_w0").reshape(-1), f("a_q_norm_2").reshape(-1), f("a_k_norm_2").reshape(-1),
                           f("mem_q_norm_2").reshape(-1), f("mem_k_norm_2").reshape(-1), f("a_cmp_b2_2").reshape(-1),
                           f("kv_k_norm_2").reshape(-1), f("b_q_norm_2").reshape(-1)])
    ln_rows = np.stack([np.stack([f(g)[l], f(b)[l]]) for l in range(DEPTH)
                        for g, b in (("ln1_g", "ln1_b"), ("ln2_g", "ln2_b"))])
    consts, attn_consts = shape_constants()
    return {"weights": weights, "consts": consts, "attn_consts": attn_consts, "cols": cols, "mids": mids, "rows": rows,
            "ln_rows": ln_rows, "x": f("x")[0], "mem": f("mem_2")[0]}


def kernel(**inputs):
    import concourse.bacc as bacc
    from concourse.bass_utils import run_bass_kernel_spmd

    arrays = {name: np.ascontiguousarray(a) for name, a in lay_out(inputs).items()}
    nc = bacc.Bacc("TRN2", target_bir_lowering=False, num_devices=1)
    aps = {name: nc.dram_tensor(f"in_{name}", a.shape, F32, kind="ExternalInput").ap() for name, a in arrays.items()}
    out = nc.dram_tensor("out", (T, D), F32, kind="ExternalOutput").ap()
    program(nc, out=out, **aps)
    r = run_bass_kernel_spmd(nc, [{f"in_{name}": a for name, a in arrays.items()}], core_ids=[0])
    return r.results[0]["out"].reshape(1, T, D)
```

```python
from contextlib import ExitStack

import concourse.bass as bass
from concourse import mybir
import numpy as np

F32 = mybir.dt.float32
F32R = mybir.dt.float32r
I32 = mybir.dt.int32
ALU = mybir.AluOpType
ACT = mybir.ActivationFunctionType
AX = mybir.AxisListType

P = 128
D = 1024
T = 256
TT = T // P
KB = D // P
DEPTH = 2
ALPHA = (2.0 * DEPTH) ** 0.25
HEAD = 64

W = 512
RH = W // HEAD
NC = W // P
KAPPA = float(np.exp(-0.5))
CHUNK = 64
CONF = 256
CONF_TAPS = 31
SHORT = 256
SHORT_TAPS = 3
RWKV_BLOCKS = 14
N_EXPERTS = 8
TOP_K = 2
D_FF = 2816
D_FF_2 = 4096
FCH = 256
CAP = 128
ITEMS = N_EXPERTS + (TOP_K * T) // (CAP + 1)
LN_EPS = 1e-5
GN_EPS = 64e-5
RMS_EPS = 1e-6

NSA_HEADS = 12
NSA_G = 3
NSA_R = NSA_HEADS // NSA_G
MEM_HEADS = 4
N_CMP = 15
CMP_BLOCK = 32
CMP_STRIDE = 16
CMP_HIDDEN = 256
DIL = ((128, 1), (512, 4), (2048, 16))
SLOTS = 8
SCALE = HEAD ** -0.5
NEG = -1e30
ROPE_THETA = 10000.0

CMP_STEP = 2

PANEL = 2048
RING = 3
PC = PANEL // KB
PR = PANEL // D


class Fields:

    def __init__(self, *sizes):
        self.at, self.n = {}, 0
        for name, n in sizes:
            self.at[name] = (self.n, n)
            self.n += n

    def __getitem__(self, name):
        a, n = self.at[name]
        return slice(a, a + n)


COLS = Fields(*[(f"{name}{l}", n) for l in range(DEPTH) for name, n in (
    ("mu", RWKV_BLOCKS), ("a0", NC), ("k_k", NC), ("k_a", NC), ("r_k", NC), ("gn_g", NC), ("gn_b", NC),
    ("conf_dw", 2 * CONF_TAPS), ("conf_dw_b", 2), ("conf_ln_g", 2), ("conf_ln_b", 2),
    ("short_dw", 2 * SHORT_TAPS), ("ln1_g", KB), ("ln1_b", KB), ("ln2_g", KB), ("ln2_b", KB),
    ("attn_norm", KB), ("mlp_norm", KB), ("mem_norm", KB))],
    ("kv_norm", KB), ("cmp_b1", 4), ("cmp_pos", 2 * CMP_BLOCK // 2))
MIDS = Fields(*[(f"{name}{l}", W) for l in range(DEPTH) for name in ("w2a2", "g2")],
              ("router", KB * N_EXPERTS), ("cmp_w2", 2 * 2 * HEAD))
ROWS = Fields(("w00", W), ("w01", W), ("a_q", HEAD), ("a_k", 3 * HEAD), ("mem_q0", HEAD), ("mem_q1", HEAD),
              ("mem_k0", HEAD), ("mem_k1", HEAD), ("cmp_b2", 2 * HEAD), ("kv_k", HEAD), ("b_q", 3 * HEAD))
CONST = Fields(("ident", P), ("ones", P), ("heads", P), ("tri", 2 * P), ("unit_mask", 4 * P), ("inv_mask", 3 * P),
               ("earlier", N_EXPERTS * N_EXPERTS),
               ("before", P), ("count", CAP), ("ln_eps", 1), ("gn_eps", 1), ("rms_eps", 1))
ATTN = Fields(("causal", 3 * P), ("dil0", 3 * P), ("dil1", 3 * T), ("cmp", TT * 16), ("cmp_ok", TT),
              ("cos", TT * 32), ("sin", TT * 32), ("cmp_cos", 32), ("cmp_sin", 32))


def shape_constants():
    c = np.zeros((P, CONST.n), np.float32)
    i, j = np.arange(P)[:, None], np.arange(P)[None, :]

    def same(n):
        return i // n == j // n

    c[:, CONST["ident"]] = i == j
    c[:, CONST["ones"]] = 1
    c[:, CONST["heads"]] = same(HEAD)
    up, up_eq, low = same(CHUNK) & (i < j), same(CHUNK) & (i <= j), same(CHUNK) & (i > j)
    c[:, CONST["tri"]] = np.concatenate([up_eq, up], 1)
    c[:, CONST["unit_mask"]] = np.concatenate([up & same(16), up_eq, up, up_eq], 1)
    c[:, CONST["inv_mask"]] = np.concatenate([low & same(16), low & same(32) & ~same(16), low & ~same(32)], 1)
    e = np.arange(N_EXPERTS)
    c[:, CONST["earlier"]] = (e[None, :] < e[:, None]).reshape(1, -1)
    c[:, CONST["before"]] = i < j
    c[:, CONST["count"]] = np.arange(CAP)
    c[:, CONST["ln_eps"]], c[:, CONST["gn_eps"]], c[:, CONST["rms_eps"]] = LN_EPS, GN_EPS, RMS_EPS

    a = np.zeros((P, ATTN.n), np.float32)
    causal = np.where(j <= i, 0, NEG)
    a[:, ATTN["causal"]] = np.concatenate([causal, np.zeros((P, P)), causal], 1)
    t, s = np.arange(T)[:, None], np.arange(T)[None, :]
    dil = [np.where((s <= t) & ((t - s) % d == 0) & (t - s <= w), 0, NEG) for w, d in DIL]
    a[:, ATTN["dil0"]] = np.concatenate([m[:P, :P] for m in dil], 1)
    a[:, ATTN["dil1"]] = np.concatenate([m[P:] for m in dil], 1)
    end = np.arange(N_CMP) * CMP_STRIDE + CMP_BLOCK - 1
    ok = np.zeros((T, 16), bool)
    ok[:, :N_CMP] = end[None, :] <= t
    a[:, ATTN["cmp"]] = np.where(ok, 0, NEG).reshape(TT, P, 16).transpose(1, 0, 2).reshape(P, -1)
    a[:, ATTN["cmp_ok"]] = ok.any(1).reshape(TT, P).T
    freq = ROPE_THETA ** (-np.arange(32, dtype=np.float32) / 32)

    def turns(pos):
        return np.asarray(pos, np.float32)[:, None] * freq.astype(np.float32)[None, :]

    for name, f in (("cos", np.cos), ("sin", np.sin)):
        a[:, ATTN[name]] = f(turns(np.arange(T))).reshape(TT, P, 32).transpose(1, 0, 2).reshape(P, -1)
        a[:N_CMP, ATTN["cmp_" + name]] = f(turns(end))
    return c, a


def chunk_panels(n, parts):
    order = []
    for step in range(n + 1):
        if step < n:
            order += [(p, step) for p in parts[:-1]]
        if step:
            order.append((parts[-1], step - 1))
    return order


IN_ORDER = [*range(7, 12), *range(7), *range(12, 24)]
CONV_PANELS = 5
EARLY_GATES = 3
GROUP_FILL = (2, 1, 1, 1, 1, 1, 1, 0, 0)
CHUNK_FILL = (1, 1, 0)


def gates_done(tt, n, step, in_chunk):
    whole = 2 * sum(GROUP_FILL) + 2 * sum(CHUNK_FILL)
    done = tt * whole + (2 * sum(GROUP_FILL) + n * sum(CHUNK_FILL) + sum(CHUNK_FILL[:step + 1]) if in_chunk else
                         n * sum(GROUP_FILL) + sum(GROUP_FILL[:step + 1]))
    return EARLY_GATES + done // 4
MEM_PANELS = 2


def panel_order():
    order = []
    for l in range(DEPTH):
        order += [("w_in", l, n) for n in IN_ORDER] + [("mix", l, n) for n in range(4)]
        order += [("w_out", l, n) for n in range(4)]
        for e in range(N_EXPERTS if l else 1):
            order += [(p, l, e * (D_FF // FCH) + n) for p, n in chunk_panels(D_FF // FCH, ("gate", "up", "down"))]
    order += [("mem_kv", l, n) for l in range(DEPTH) for n in range(MEM_PANELS)]
    for l in range(DEPTH):
        if l == 0:
            order += [("a_in", 0, n) for n in range(9)] + [("cmp", 0, n) for n in range(4)]
            order += [("a_out", 0, n) for n in range(4)]
        else:
            order += [("kv", 1, n) for n in range(4)] + [("b_in", 1, n) for n in range(7)]
            order += [("b_out", 1, n) for n in range(3)]
        order += [(p, l, n) for p, n in chunk_panels(D_FF_2 // FCH, ("mlp_up", "mlp_down"))]
    return order


ORDER = panel_order()
N_PANELS = len(ORDER)
FF_CHUNKS = D_FF // FCH
PER_ITEM = 3 * FF_CHUNKS
BEFORE_FFN = ORDER.index(("gate", 0, 0))
BEFORE_MOE = ORDER.index(("gate", 1, 0))
MOE_SLOTS = [(BEFORE_MOE + i) % RING for i in range(RING)] + [RING + i for i in range(RING)]
AFTER_MOE = BEFORE_MOE + N_EXPERTS * PER_ITEM


class Made:

    def __init__(self):
        self.count = {}

    def next(self, name):
        self.count[name] = self.count.get(name, 0) + 1
        return self.count[name]


class PanelReader:

    def __init__(self, pe, ring, landed, used):
        self.pe, self.ring, self.landed, self.used = pe, ring, landed, used
        self.n, self.first, self.give_back = 0, 0, False

    def take(self, turn=0, per_turn=0):
        slot, fill = (self.first + self.n) % RING, self.n // RING + 1
        self.pe.wait_ge(self.landed[slot], (turn * (per_turn // RING) + fill) * 16)
        self.held = self.ring[:, self.step(), :]
        return self.held

    def step(self):
        slot = (self.first + self.n) % RING
        self.give_back = self.n > 0
        self.n += 1
        return slot

    def skip(self, n):
        assert n % RING == 0
        self.n += n

    def restart(self, landed, used, ins):
        ins.then_inc(self.used, 1)
        self.first, self.landed, self.used = (self.n + self.first) % RING, landed, used
        self.n, self.give_back = 0, False

    def mm(self, out, lhsT, rhs, start, stop):
        ins = self.pe.matmul(out, lhsT, rhs, start=start, stop=stop)
        if self.give_back:
            ins.then_inc(self.used, 1)
            self.give_back = False
        return ins


SIGNALS = """
panel_used_2 consts_in params_in ln_rows_in mem_in x_in out_stored panel_used cleared
dve_step act_step 
x_turned xT_dve xT_act
proj_out proj_read shifted 
lora_in lora_z lora_a lora_g decay_in aaa gate_lora
cum_mm decays kk_sq kk_mm kk_norm features bonus_in bonus_mm
turn_mm turned_dve turned_act unit_mm masks inv_mm inv_dve inv_act rhs_mm rhs u_mm u state_mm state o_mm o_read
gn_mean_mm gn_sq gn_var_mm gn_std branch_a conf_conv conf_mean_mm conf_sq conf_var_mm conf_std branch_b conf_silu branch_c
mix_mm mixed wout_mm ln_x ln_std ln_z ln_x_done
router_mm router_w router_exp gu_full act_out h_ready y_full y_read up_full relu_out h_ready_2 y_full_2 y_read_2
counts_mm items_ready one_hot routed_mm xe_dve xe_act spread split_hi split x_split h_made h_hi e_split_hi e_split e_made e_hi mem_std mem_inv mem_x mem_turned mem_xT y_half y_sb scatter_mm acc_read
rms_ss rms_std rms_x attn_proj attn_read qk_std qk_ready turnq_mm turnq_dve turnq_act
cmp_h_mm cmp_h cmp_o_mm cmp_tb cmp_kv cmp_k_std cmp_k_ready cmp_kT_mm cmp_kT cmp_s_mm cmp_s cmp_e cmp_p cmp_pT_mm cmp_pT cmp_pv_mm cmp_done
score_mm score_max score_exp pT_mm pT pv_mm pv_read proj2_mm x_done nsa_gates
""".split()


def program(nc, weights, consts, attn_consts, cols, mids, rows, ln_rows, x, mem, out):
    ctx = ExitStack()
    with ctx:
        def sb(name, *shape, stack=ctx, dtype=F32):
            return stack.enter_context(nc.sbuf_tensor(name, [P, *shape], dtype))

        S = {name: ctx.enter_context(nc.semaphore(name)) for name in SIGNALS}
        landed = [ctx.enter_context(nc.semaphore(f"panel_landed{i}")) for i in range(RING)]
        landed_2 = [ctx.enter_context(nc.semaphore(f"panel_landed_2_{i}")) for i in range(RING)]
        landed_more = [ctx.enter_context(nc.semaphore(f"panel_landed_more_{i}")) for i in range(RING)]
        bank = [ctx.enter_context(nc.psum_tensor(f"bank{i}", [P, 512], F32)) for i in range(8)]

        def twice_named(name, *shape, stack=ctx):
            with ExitStack() as first:
                plain = sb(name, *shape, stack=first)
            return plain, sb(name + "_lo", *shape, stack=stack, dtype=F32R)

        ring, ring_lo = twice_named("ring", RING, PANEL)
        x_tm = sb("x_tm", TT, D)
        xT, xT_lo = twice_named("xT", KB, T)
        cst = sb("cst", CONST.n)
        col = sb("col", COLS.n)
        mid = sb("mid", MIDS.n)
        row = sb("row", ROWS.n)
        ln_row = sb("ln_row", 2, D)
        stat = sb("stat", 64)
        ident = cst[:, CONST["ident"]]
        ones = cst[:, CONST["ones"]]
        head_sum = cst[:, CONST["heads"]]
        tri = cst[:, CONST["tri"]]
        inv_mask = cst[:, CONST["inv_mask"]].rearrange("p (m s) -> p m s", m=3)
        unit_mask = cst[:, CONST["unit_mask"]]

        def c1(name, n=0):
            a = COLS[name].start + n
            return col[:, a:a + 1]

        def eps(name):
            return cst[:, CONST[name]]

        mixer = ExitStack()
        gates = sb("gates", 24, T, stack=mixer)
        sh = sb("sh", RWKV_BLOCKS, T, stack=mixer)
        conf_s = sb("conf_s", 2, T, stack=mixer)
        conv = sb("conv", 2, T, stack=mixer)
        gb = sb("gb", 2, T, stack=mixer)
        conv_c = sb("conv_c", 2, T, stack=mixer)
        a_ = sb("a_", NC, T, stack=mixer)
        kk = sb("kk", NC, T, stack=mixer)
        tmp = sb("tmp", NC, T, stack=mixer)
        p_in = sb("p_in", NC, T, stack=mixer)
        p_inv = sb("p_inv", NC, T, stack=mixer)
        p_ex = sb("p_ex", NC, T, stack=mixer)
        ar = sb("ar", NC, TT, 2, P, stack=mixer)
        vt = sb("vt", TT, W, stack=mixer)
        bt = sb("bt", TT, W, stack=mixer)
        kt = sb("kt", TT, W, stack=mixer)
        g_ = sb("g_", NC, T, stack=mixer)
        unit = sb("unit", RH, 4, P, stack=mixer)
        inv = sb("inv", RH, P, stack=mixer)
        rhs_sb = sb("rhs_sb", RH, HEAD, stack=mixer)
        state = sb("state", NC, 2, HEAD, stack=mixer)
        sh_flat = sh[:].rearrange("p b t -> p (b t)")
        a3 = sh_flat[:, 0:12 * P].rearrange("p (i m s) -> p i m s", i=4, m=3)
        pw = sh_flat[:, 12 * P:28 * P].rearrange("p (m s) -> p m s", m=4)
        xa = sb("xa", 4 * P, stack=mixer)
        xb = sb("xb", 4 * P, stack=mixer)
        pz = sb("pz", 2, 2, T + 1, stack=mixer)
        u_pad = sb("u_pad", 2, T + CONF_TAPS - 1, stack=mixer)
        s_pad = sb("s_pad", 2, T + SHORT_TAPS - 1, stack=mixer)
        u_sb = sb("u_sb", RH, HEAD, stack=mixer)
        loras = unit[:].rearrange("p h m s -> p (h m s)")[:, 0:2 * T].rearrange("p (a t) -> p a t", a=2)
        r_, k_, v_ = (sh[:, n * NC:(n + 1) * NC, :] for n in range(3))
        oT = p_ex
        sg_tok = kt
        yT = p_in
        mixT = sh[:, 0:KB, :]
        conv_sq = gb
        mixer.close()

        mlp = ExitStack()
        gate_s = sb("gate_s", 3, 2, T, stack=mlp)
        hT, hT_lo = twice_named("hT", 3, 2, T, stack=mlp)
        atc = sb("atc", ATTN.n, stack=mlp)
        mem_kv = sb("mem_kv", DEPTH, TT, 2 * MEM_HEADS * HEAD, stack=mlp)
        split = ExitStack()
        ring_hi = sb("ring_hi", RING, PANEL, stack=split, dtype=F32R)
        xT_hi = sb("xT_hi", KB, T, stack=split, dtype=F32R)
        hT_hi = sb("hT_hi", 3, 2, T, stack=split, dtype=F32R)

        moe = ExitStack()
        E = N_EXPERTS
        rt = sb("rt", 6, E * E, stack=moe)
        moe_w = sb("moe_w", TT, E, stack=moe)
        moe_pos = sb("moe_pos", TT, E, stack=moe)
        tiles = sb("tiles", 4, E, stack=moe)
        in_item = sb("in_item", 4, (ITEMS + 1) * E, stack=moe)
        item_pos = sb("item_pos", TT, ITEMS + 1, stack=moe)
        item_w = sb("item_w", TT, ITEMS + 1, stack=moe)
        table = sb("table", ITEMS + 2, stack=moe)
        table_i = moe.enter_context(nc.sbuf_tensor("table_i", [P, ITEMS + 2], I32))
        one_hot = sb("one_hot", TT, CAP, stack=moe)
        weighted = sb("weighted", TT, CAP, stack=moe)
        spread = sb("spread", TT, P, stack=moe)
        xeT = sb("xeT", KB, CAP, stack=moe)
        ring_more, ring_more_lo = twice_named("ring_more", RING, PANEL, stack=moe)
        y_sb = sb("y_sb", D, stack=moe)
        acc = sb("acc", TT, D, stack=moe)
        moe.close()
        split.close()

        attn = ExitStack()
        xn = sb("xn", TT, D, stack=attn)
        proj = sb("proj", TT, 11 * PC, stack=attn)
        scr = sb("scr", 2, 24 * HEAD, stack=attn)
        o_tm = sb("o_tm", TT, D, stack=attn)
        p_sb = sb("p_sb", 4, 3 * T, stack=attn)
        pT_sb = sb("pT_sb", 2, 512, stack=attn)
        cmp_in = sb("cmp_in", 2, CMP_BLOCK // 2, NSA_G, N_CMP, stack=attn)
        cmp_h = sb("cmp_h", 2, 2, NSA_G * N_CMP, stack=attn)
        cmp_kv = sb("cmp_kv", 2, NSA_G, HEAD, stack=attn)
        cmp_dup = sb("cmp_dup", NSA_G, 2, HEAD, stack=attn)
        cmp_kT = sb("cmp_kT", NSA_G, 16, stack=attn)
        cmp_s = sb("cmp_s", NSA_HEADS, TT, 16, stack=attn)
        cmp_pT = sb("cmp_pT", 4, P, stack=attn)
        rs = sb("rs", 192, stack=attn)
        coef = sb("coef", 3, NSA_HEADS, TT, stack=attn)
        twice = p_sb[:].rearrange("p a b -> p (a b)").rearrange("p (t k d e) -> p t k d e", t=TT, d=2, e=HEAD)
        qkT = sb("qkT", 22, T, stack=attn)
        memT = [qkT[:, 6 + l * KB:6 + (l + 1) * KB, :] for l in range(DEPTH)]
        mem_in = memT[1].rearrange("p (t k) s -> p t (k s)", t=TT)
        mem_sq = xn[:, 0, :]
        attn.close()
        mlp.close()
        causal = atc[:, ATTN["causal"]]
        MEM_Q = {0: 1920, 1: 1536 + 2 * SLOTS * HEAD}
        B_Q0 = 2 * SLOTS * HEAD

        def head_sets(l):
            mq = proj[:, :, MEM_Q[l]:MEM_Q[l] + MEM_HEADS * HEAD]
            mk = mem_kv[:, l, :, 0:MEM_HEADS * HEAD]
            rq, rk = ROWS[f"mem_q{l}"].start, ROWS[f"mem_k{l}"].start
            if l == 0:
                k0, q0 = ROWS["a_k"].start, ROWS["a_q"].start
                return [(mk, 4, rk, False, None, 4), (proj[:, :, 0:768], 12, q0, True, None, 7),
                        (proj[:, :, 1152:1344], 3, k0 + HEAD, True, 0, 10), (proj[:, :, 1536:1728], 3, k0 + 2 * HEAD, True, 3, 11),
                        (mq, 4, rq, False, None, 13)]
            sets = [(proj[:, :, B_Q0 + g * 512:B_Q0 + (g + 1) * 512], SLOTS, ROWS["b_q"].start + g * HEAD, True, None, 6 + 2 * g) for g in range(3)]
            return [(mk, 4, rk, False, None, 0), (proj[:, :, 0:512], SLOTS, ROWS["kv_k"].start, True, None, 2)] + sets + \
                [(mq, 4, rq, False, None, 11)]

        PANELS_ATTN = (13, 11)
        N_SETS = (5, 6)

        def set_stats(l, n):
            sizes = [TT * h[1] for h in head_sets(l)]
            return 8 + sum(sizes[:n]), sizes[n]

        def turn_items(l, tt):
            def pairs(t, a, n):
                return [t[:, tt, a + i * P:a + (i + 1) * P] for i in range(n)]

            if l == 0:
                dup = [twice[:, tt, k, :, :].rearrange("p d e -> p (d e)") for k in range(12)]
                return pairs(proj, 0, 6) + dup + pairs(proj, MEM_Q[0], 2) + pairs(mem_kv[:, l], 0, 2)
            return pairs(proj, B_Q0, 12) + pairs(proj, 0, 4) + pairs(proj, MEM_Q[1], 2) + pairs(mem_kv[:, l], 0, 2)

        N_ITEMS = (22, 20)
        BANKS_T = (11, 10)
        MEM_ITEM = (18, 16)

        def units(l):
            if l == 0:
                u = [(kind, h, None) for h in range(NSA_HEADS) for kind in ("sel", "win")]
            else:
                u = [("dil", s, tt) for s in range(SLOTS) for tt in range(TT)]
            return u + [("mem", h, None) for h in range(MEM_HEADS)]

        def unit_stat(u, name):
            a = 96 + 16 * ("max", "neg", "sum", "inv", "scale").index(name) + 2 * (u % 8)
            return rs[:, a:a + TT]

        def blocks_of(kind, tt):
            if kind == "dil":
                n = tt + 1
                return [([g * n * P + k * P for g in range(3)], tt, k) for k in range(n)]
            if kind == "mem":
                return [([(2 * t + k) * P], t, k) for t in range(TT) for k in range(TT)]
            return [([0], 0, 0), ([P], 1, 0), ([2 * P], 1, 1)]

        def values(l, kind, h, k):
            if kind == "mem":
                return mem_kv[:, l, k, (MEM_HEADS + h) * HEAD:(MEM_HEADS + h + 1) * HEAD]
            a = 512 + h * HEAD if kind == "dil" else {"sel": 1344, "win": 1728}[kind] + h // NSA_R * HEAD
            return proj[:, k, a:a + HEAD]

        def mlp_signals(kind):
            names = ("gu_full", "act_out", "h_ready", "y_full", "y_read") if kind == "ffn" else \
                ("up_full", "relu_out", "h_ready_2", "y_full_2", "y_read_2")
            return dict(zip(("up", "out", "h", "y", "read"), (S[n] for n in names)))

        def moe_panel(k, item):
            slot, fill = MOE_SLOTS[k % len(MOE_SLOTS)], k // len(MOE_SLOTS) + 1
            per_item = len(range(k % len(MOE_SLOTS), PER_ITEM, len(MOE_SLOTS)))
            if slot < RING:
                return ring[:, slot, :], ring_lo[:, slot, :], landed[slot], item * per_item + (len(range(slot, BEFORE_MOE, RING)) + fill)
            return ring_more[:, slot - RING, :], ring_more_lo[:, slot - RING, :], landed_more[slot - RING], item * per_item + fill

        def moe_order(part, chunk):
            return chunk_panels(FF_CHUNKS, (0, 1, 2)).index((part, chunk))

        block = ctx.enter_context(nc.Block())

        @block.sync
        def _(sp):
            sp.dma_start(x_tm[:], x.rearrange("(t p) d -> p t d", p=P)).then_inc(S["x_in"], 16)
            sp.dma_start(cst[:], consts).then_inc(S["consts_in"], 16)
            for i in range(RING):
                sp.dma_start(ring[:, i, :], weights[i]).then_inc(landed[i], 16)
            rounds = BEFORE_MOE // RING - 1
            with sp.Fori(0, rounds) as turn:
                for i in range(RING):
                    sp.wait_ge(S["panel_used"], turn * RING + (i + 1))
                    sp.dma_start(ring[:, i, :], weights[bass.ds(turn * RING + (RING + i), 1)].rearrange("a p n -> p (a n)")
                                 ).then_inc(landed[i], 16)
            for n in range((rounds + 1) * RING, BEFORE_MOE):
                sp.wait_ge(S["panel_used"], n - RING + 1)
                sp.dma_start(ring[:, n % RING, :], weights[n]).then_inc(landed[n % RING], 16)
            sp.wait_ge(S["items_ready"], 1)
            n_items = sp.value_load(table_i[0:1, 0:1], min_val=N_EXPERTS, max_val=ITEMS)
            with sp.Fori(0, n_items) as item:
                expert = sp.value_load(table_i[0:1, bass.ds(item + 1, 1)], min_val=0, max_val=N_EXPERTS - 1)
                for k in range(PER_ITEM):
                    place, _, sem, _ = moe_panel(k, item)
                    back = len(MOE_SLOTS) if k >= len(MOE_SLOTS) else RING if k < RING else 3 * RING
                    sp.wait_ge(S["panel_used"], item * PER_ITEM + (BEFORE_MOE + k - back + 1))
                    sp.dma_start(place, weights[bass.ds(expert * PER_ITEM + (BEFORE_MOE + k), 1)].rearrange("a p n -> p (a n)")
                                 ).then_inc(sem, 16)
            for i in range(RING):
                slot = (BEFORE_MOE + i) % RING
                sp.wait_ge(S["panel_used"], n_items * PER_ITEM + (BEFORE_MOE + i - RING + 1))
                sp.dma_start(ring[:, slot, :], weights[AFTER_MOE + i]).then_inc(landed_2[slot], 16)
            rounds = (N_PANELS - AFTER_MOE) // RING - 1
            with sp.Fori(0, rounds) as turn:
                for i in range(RING):
                    slot = (BEFORE_MOE + i) % RING
                    sp.wait_ge(S["panel_used_2"], turn * RING + (i + 1))
                    sp.dma_start(ring[:, slot, :], weights[bass.ds(turn * RING + (AFTER_MOE + RING + i), 1)]
                                 .rearrange("a p n -> p (a n)")).then_inc(landed_2[slot], 16)
            for n in range((rounds + 1) * RING, N_PANELS - AFTER_MOE):
                slot = (BEFORE_MOE + n) % RING
                sp.wait_ge(S["panel_used_2"], n - RING + 1)
                sp.dma_start(ring[:, slot, :], weights[AFTER_MOE + n]).then_inc(landed_2[slot], 16)
            sp.wait_ge(S["y_read_2"], DEPTH)
            sp.dma_start(out.rearrange("(t p) d -> p t d", p=P), x_tm[:]).then_inc(S["out_stored"], 16)
            sp.wait_ge(S["out_stored"], 16)

        @block.tensor
        def _(pe):
            panels = PanelReader(pe, ring, landed, S["panel_used"])
            mm = panels.mm

            def turn_x(n, src):
                for b in range(4):
                    for kk_ in range(2):
                        for tt in range(TT):
                            f = (2 * b + kk_) * P
                            ins = pe.transpose(bank[b][:, (kk_ * TT + tt) * P:][:, 0:P], src[:, tt, f:f + P], ident)
                    ins.then_inc(S["x_turned"], 1)

            def wait_xT(n):
                pe.wait_ge(S["xT_dve"], 2 * (n + 1))
                pe.wait_ge(S["xT_act"], 2 * (n + 1))

            def project(l, j, quarter):
                n = 24 * l + j
                if quarter == 0:
                    panels.take()
                    if n >= 2:
                        pe.wait_ge(S["proj_read"], n - 1)
                w, m = panels.held, quarter // 2
                for kb in range(quarter % 2 * (KB // 2), (quarter % 2 + 1) * (KB // 2)):
                    ins = mm(bank[n % 2][:, m * T:(m + 1) * T], w[:, kb * PC + m * P:][:, 0:P], xT[:, kb, :],
                             start=(kb == 0), stop=(kb == KB - 1))
                if quarter == 3:
                    ins.then_inc(S["proj_out"], 1)

            def mixer_pe(l):
                quarters = [(j, q) for j in range(12, 24) for q in range(4)]

                def fill(n):
                    for _ in range(min(n, len(quarters))):
                        project(l, *quarters.pop(0))

                wait_xT(2 * l)
                for j in range(12):
                    for q in range(4):
                        project(l, j, q)
                w2a2 = mid[:, MIDS[f"w2a2{l}"]]
                g2 = mid[:, MIDS[f"g2{l}"]]
                if l == 0:
                    pe.wait_ge(S["params_in"], 16 * 3)
                pe.wait_ge(S["lora_in"], l + 1)
                for tt in range(TT):
                    pe.matmul(bank[2 + tt][:], loras[0:HEAD, 0, tt * P:(tt + 1) * P], w2a2[0:HEAD, :], start=True, stop=False)
                    ins = pe.matmul(bank[2 + tt][:], ones[0:1, :], row[0:1, ROWS[f"w0{l}"]], start=False, stop=True)
                ins.then_inc(S["lora_z"], 1)
                for c in range(NC):
                    ins = pe.matmul(bank[4 + c // 2][:, (c % 2) * T:][:, 0:T], w2a2[HEAD:P, c * P:(c + 1) * P], sh[HEAD:P, 12, :],
                                    start=True, stop=True)
                ins.then_inc(S["lora_a"], 1)
                for c in range(NC):
                    ins = pe.matmul(bank[6 + c // 2][:, (c % 2) * T:][:, 0:T], g2[:, c * P:(c + 1) * P], loras[:, 1, :],
                                    start=True, stop=True)
                ins.then_inc(S["lora_g"], 1)
                fill(4)
                pe.wait_ge(S["decay_in"], l + 1)
                pe.wait_ge(S["aaa"], l + 1)
                for c in range(NC):
                    for tt in range(TT):
                        ins = pe.matmul(bank[2 + c][:, tt * T:(tt + 1) * T], sg_tok[:, tt, c * P:(c + 1) * P], tri,
                                        start=True, stop=True)
                ins.then_inc(S["cum_mm"], 1)
                pe.wait_ge(S["kk_sq"], l + 1)
                pe.wait_ge(S["gate_lora"], l + 1)
                for c in range(NC):
                    ins = pe.matmul(bank[6 + c // 2][:, (c % 2) * T:][:, 0:T], head_sum, tmp[:, c, :], start=True, stop=True)
                ins.then_inc(S["kk_mm"], 1)
                fill(8)
                pe.wait_ge(S["bonus_in"], l + 1)
                for c in range(NC):
                    ins = pe.matmul(bank[6 + c // 2][:, (c % 2) * T:][:, 0:T], head_sum, tmp[:, c, :], start=True, stop=True)
                ins.then_inc(S["bonus_mm"], 1)
                pe.wait_ge(S["features"], l + 1)
                pe.wait_ge(S["decays"], l + 1)
                for n, src in enumerate((v_, a_, kk)):
                    for tt in range(TT):
                        b = 2 + (2 * n + tt) % 4
                        if n == 2:
                            pe.wait_ge((S["turned_dve"], S["turned_act"])[tt], 3 * l + 1)
                        for c in range(NC):
                            ins = pe.transpose(bank[b][:, c * P:(c + 1) * P], src[:, c, tt * P:(tt + 1) * P], ident)
                        ins.then_inc(S["turn_mm"], 1)
                pe.wait_ge(S["turned_dve"], 3 * (l + 1))
                pe.wait_ge(S["turned_act"], 3 * (l + 1))
                for tt in range(TT):
                    tok = slice(tt * P, (tt + 1) * P)
                    for hg in range(2):
                        group = 4 * l + 2 * tt + hg
                        if group % 4:
                            pe.wait_ge(S["inv_dve"], 8 * group)
                            pe.wait_ge(S["inv_act"], 6 * group)
                        if tt and not hg:
                            pe.wait_ge(S["state"], 3 * l + 2)
                            pe.wait_ge(S["o_read"], 4 * l + 2)
                        for i in range(4):
                            c, lo = (4 * hg + i) // 2, HEAD * (i % 2)
                            hd = slice(lo, lo + HEAD)
                            pe.matmul(bank[2 + i][:, 0:T], a_[hd, c, tok], ar[hd, c, tt, :, :], start=True, stop=True)
                            pe.matmul(bank[2 + i][:, T:2 * T], kk[hd, c, tok], ar[hd, c, tt, :, :], start=True, stop=True)
                            ins = pe.matmul(bank[6 + i % 2][:, i // 2 * P:][:, 0:P], ar[hd, c, tt, 0, :], a_[hd, c, tok],
                                            start=True, stop=True)
                        ins.then_inc(S["unit_mm"], 1)
                        fill(GROUP_FILL[0])

                        def four(b, lhs, rhs, turn=False):
                            for i in range(4):
                                o = bank[b][:, i * P:(i + 1) * P]
                                if turn:
                                    ins = pe.transpose(o, lhs(i), ident)
                                else:
                                    ins = pe.matmul(o, lhs(i), rhs(i), start=True, stop=True)
                            ins.then_inc(S["inv_mm"], 1)

                        def part(t):
                            return lambda i: t[:, i * P:(i + 1) * P]

                        def n_1(i):
                            return unit[:, 4 * hg + i, 0, :]

                        def a_1(i):
                            return a3[:, i, 0, :]

                        n_2, a_2, n_4, a_4 = (part(pw[:, m, :]) for m in range(4))
                        a_8, x_odd, x_even = part(pw[:, 0, :]), part(xa), part(xb)
                        turned, g_of = a_2, n_4
                        pe.wait_ge(S["masks"], group + 1)
                        four(2, a_1, n_1)
                        four(3, n_1, a_1)
                        fill(GROUP_FILL[1])
                        dve, act = 8 * group, 6 * group
                        pe.wait_ge(S["inv_dve"], dve + 1)
                        pe.wait_ge(S["inv_act"], act + 1)
                        four(4, a_2, x_odd)
                        four(5, a_2, n_2)
                        four(6, n_2, a_2)
                        fill(GROUP_FILL[2])
                        pe.wait_ge(S["inv_dve"], dve + 2)
                        pe.wait_ge(S["inv_act"], act + 3)
                        four(2, a_4, x_even)
                        four(3, n_4, a_4)
                        fill(GROUP_FILL[3])
                        pe.wait_ge(S["inv_dve"], dve + 3)
                        pe.wait_ge(S["inv_act"], act + 4)
                        four(4, a_8, x_odd)
                        fill(GROUP_FILL[4])
                        pe.wait_ge(S["inv_dve"], dve + 4)
                        four(2, x_even, None, turn=True)
                        four(3, lambda i: a3[:, i, 1, :], x_even)
                        fill(GROUP_FILL[5])
                        pe.wait_ge(S["inv_dve"], dve + 5)
                        pe.wait_ge(S["inv_act"], act + 5)
                        four(6, turned, g_of)
                        fill(GROUP_FILL[6])
                        pe.wait_ge(S["inv_dve"], dve + 6)
                        four(4, x_odd, None, turn=True)
                        four(5, lambda i: a3[:, i, 2, :], x_odd)
                        fill(GROUP_FILL[7])
                        pe.wait_ge(S["inv_dve"], dve + 7)
                        pe.wait_ge(S["inv_act"], act + 6)
                        four(2, turned, g_of)
                        fill(GROUP_FILL[8])
                    pe.wait_ge(S["inv_dve"], 8 * (4 * l + 2 * tt + 2))
                    for half in range(2):
                        q = 4 * l + 2 * tt + half
                        hs = slice(half * CHUNK, (half + 1) * CHUNK)
                        if q % 4 == 0:
                            pe.wait_ge(S["cleared"], l + 2)
                        else:
                            pe.wait_ge(S["state"], q - l)
                        for c in range(NC):
                            pe.matmul(bank[2][hs, c * P:(c + 1) * P], ar[:, c, tt, 0, hs], state[:, c, :, :], start=True, stop=False)
                            for h in (2 * c, 2 * c + 1):
                                hv = slice(h * HEAD, (h + 1) * HEAD)
                                ins = pe.matmul(bank[2][hs, hv], unit[:, h, 2, hs], vt[:, tt, hv], start=False, stop=(h % 2 == 1))
                        ins.then_inc(S["rhs_mm"], 1)
                        fill(CHUNK_FILL[0])
                        pe.wait_ge(S["rhs"], q + 1)
                        for h in range(RH):
                            hv = slice(h * HEAD, (h + 1) * HEAD)
                            ins = pe.matmul(bank[3][hs, hv], inv[hs, h, hs], rhs_sb[hs, h, :], start=True, stop=True)
                        ins.then_inc(S["u_mm"], 1)
                        fill(CHUNK_FILL[1])
                        if q:
                            pe.wait_ge(S["o_read"], q)
                        for h in range(RH):
                            c, lo = h // 2, HEAD * (h % 2)
                            hd, hv = slice(lo, lo + HEAD), slice(h * HEAD, (h + 1) * HEAD)
                            o = bank[5][hd, c * CHUNK:(c + 1) * CHUNK]
                            pe.matmul(o, state[:, c, h % 2, :], ar[:, c, tt, 1, hs], start=True, stop=False)
                            pe.matmul(o, vt[:, tt, hv], unit[:, h, 3, hs], start=False, stop=False)
                            if h == 0:
                                pe.wait_ge(S["u"], q + 1)
                            ins = pe.matmul(o, u_sb[:, h, :], unit[:, h, 1, hs], start=False, stop=True)
                        ins.then_inc(S["o_mm"], 1)
                        if q % 4 < 3:
                            for h in range(RH):
                                c, lo = h // 2, HEAD * (h % 2)
                                hv = slice(h * HEAD, (h + 1) * HEAD)
                                o = bank[4][lo:lo + HEAD, c * HEAD:(c + 1) * HEAD]
                                pe.matmul(o, bt[hs, tt, hv], u_sb[hs, h, :], start=True, stop=False)
                                ins = pe.matmul(o, kt[hs, tt, hv], vt[hs, tt, hv], start=False, stop=True)
                            ins.then_inc(S["state_mm"], 1)
                        fill(CHUNK_FILL[2])
                fill(len(quarters))
                pe.wait_ge(S["o_read"], 4 * (l + 1))
                for c in range(NC):
                    ins = pe.matmul(bank[2 + c // 2][:, (c % 2) * T:][:, 0:T], head_sum, oT[:, c, :], start=True, stop=True)
                ins.then_inc(S["gn_mean_mm"], 1)
                pe.wait_ge(S["conf_conv"], l + 1)
                for n in range(2):
                    ins = pe.matmul(bank[6][:, 0:T], ones, conv[:, n, :], start=(n == 0), stop=(n == 1))
                ins.then_inc(S["conf_mean_mm"], 1)
                pe.wait_ge(S["gn_sq"], l + 1)
                for c in range(NC):
                    ins = pe.matmul(bank[4 + c // 2][:, (c % 2) * T:][:, 0:T], head_sum, ar[:, c, :, 0, :], start=True, stop=True)
                ins.then_inc(S["gn_var_mm"], 1)
                pe.wait_ge(S["conf_sq"], l + 1)
                for n in range(2):
                    ins = pe.matmul(bank[7][:, 0:T], ones, conv_sq[:, n, :], start=(n == 0), stop=(n == 1))
                ins.then_inc(S["conf_var_mm"], 1)
                for n in range(4):
                    w = panels.take()
                    b = 2 + 3 * (n % 2)
                    if n == 0:
                        pe.wait_ge(S["branch_c"], l + 1)
                        pe.wait_ge(S["conf_silu"], l + 1)
                        pe.wait_ge(S["branch_a"], l + 1)
                    elif n >= 2:
                        pe.wait_ge(S["mixed"], 4 * l + n - 1)
                    for part_, (k0, k1, src) in enumerate(((0, 4, yT), (4, 6, conf_s), (6, 8, conv_c))):
                        for m in range(2):
                            for kb in range(k0, k1):
                                ins = mm(bank[b + part_][:, m * T:(m + 1) * T], w[:, kb * PC + m * P:][:, 0:P], src[:, kb - k0, :],
                                         start=(kb == k0), stop=(kb == k1 - 1))
                    ins.then_inc(S["mix_mm"], 1)
                pe.wait_ge(S["mixed"], 4 * (l + 1))
                rows_out(4, lambda kb, tt: mixT[:, kb, tt * P:(tt + 1) * P], S["wout_mm"])

            def rows_out(n_panels, lhs, done):
                for n in range(n_panels):
                    w = panels.take()
                    for i in range(PR):
                        kb = n * PR + i
                        for tt in range(TT):
                            for h in range(2):
                                ins = mm(bank[2 * tt + h][:], lhs(kb, tt), w[:, i * D + h * 512:][:, 0:512],
                                         start=(kb == 0), stop=(kb == n_panels * PR - 1))
                ins.then_inc(done, 1)

            def mm3(out, lhsT, rhs, start, stop):
                mm(out, lhsT[0], rhs[0], start=start, stop=False)
                pe.matmul(out, lhsT[0], rhs[1], start=False, stop=False)
                return pe.matmul(out, lhsT[1], rhs[0], start=False, stop=stop)

            def mlp_pe(kind, n_chunks, base, per_step, n_split, n_x):
                gated, sems = kind == "ffn", mlp_signals(kind)
                nb = 2 if gated else 3
                n0 = panels.n

                def split_panel(turn, per_turn):
                    pe.wait_ge(S["split"], turn * per_turn + (n_split + panels.n - n0 + 1))
                    slot = panels.step()
                    return ring_hi[:, slot, :], ring_lo[:, slot, :]

                def first(i, slot, turn=0, per_turn=0, x_waits=False):
                    for g in range(2 if gated else 1):
                        w = split_panel(turn, per_turn)
                        b = bank[(2 * slot + g) if gated else slot]
                        for m in range(2):
                            for kb in range(KB):
                                if x_waits and g == 0 and m == 0 and kb % 2 == 0:
                                    pe.wait_ge(S["x_split"], 4 * n_x + kb // 2 + 1)
                                ins = mm3(b[:, m * T:(m + 1) * T], [t[:, kb * PC + m * P:][:, 0:P] for t in w], (xT_hi[:, kb, :], xT_lo[:, kb, :]),
                                          start=(kb == 0), stop=(kb == KB - 1))
                    ins.then_inc(sems["up"], 1)

                def last(i, slot, turn=0, per_turn=0, start=False, stop=False):
                    w = split_panel(turn, per_turn)
                    pe.wait_ge(sems["h"], i + 1)
                    for m in range(2):
                        for tt in range(TT):
                            h_ = [t[:, slot, m, tt * P:(tt + 1) * P] for t in (hT_hi, hT_lo)]
                            for h in range(2):
                                ins = mm3(bank[4 + 2 * tt + h][:], h_, [t[:, m * D + h * 512:][:, 0:512] for t in w],
                                          start=(start and m == 0), stop=(stop and m == 1))
                    ins.then_inc(sems["y"], 1)

                first(base, 0, x_waits=True)
                lead = 2 + (n_chunks - 2) % per_step
                for s in range(1, lead):
                    first(base + s, s % nb)
                    last(base + s - 1, (s - 1) % nb, start=(s == 1))
                per_turn = per_step * (3 if gated else 2)
                turns = (n_chunks - lead) // per_step
                with pe.Fori(0, turns) as turn:
                    for s in range(lead, lead + per_step):
                        first(turn * per_step + (base + s), s % nb, turn, per_turn)
                        last(turn * per_step + (base + s - 1), (s - 1) % nb, turn, per_turn)
                panels.skip((turns - 1) * per_turn)
                last(base + n_chunks - 1, (n_chunks - 1) % nb, stop=True)

            def moe_pe():
                def first(s, item):
                    for g in range(2):
                        w, _, sem, n = moe_panel(moe_order(g, s), item)
                        pe.wait_ge(sem, n * 16)
                        panels.step()
                        for m in range(2):
                            o = bank[s % 2][:, (2 * g + m) * CAP:][:, 0:CAP]
                            for kb in range(KB):
                                ins = mm(o, w[:, kb * PC + m * P:][:, 0:P], xeT[:, kb, :], start=(kb == 0), stop=(kb == KB - 1))
                    ins.then_inc(S["gu_full"], 1)

                def last(s, item):
                    w = (ring_hi[:, s % 2, :], moe_panel(moe_order(2, s), item)[1])
                    pe.wait_ge(S["e_split"], item * FF_CHUNKS + (s + 1))
                    panels.step()
                    pe.wait_ge(S["h_ready"], item * FF_CHUNKS + (FF_CHUNKS + s + 1))
                    for h in range(2):
                        for m in range(2):
                            ins = mm3(bank[2 + h][:], [t[:, s % 2, m, 0:CAP] for t in (hT_hi, hT_lo)], [t[:, m * D + h * 512:][:, 0:512] for t in w],
                                      start=(s == 0 and m == 0), stop=(s == FF_CHUNKS - 1 and m == 1))
                        if s == FF_CHUNKS - 1 and h == 0:
                            ins.then_inc(S["y_half"], 1)
                    ins.then_inc(S["y_full"], 1)

                def gather():
                    for kb in range(KB):
                        for tt in range(TT):
                            ins = pe.matmul(bank[4 + kb // 4][:, kb % 4 * CAP:][:, 0:CAP], x_tm[:, tt, kb * P:(kb + 1) * P], one_hot[:, tt, :],
                                            start=(tt == 0), stop=(tt == TT - 1))
                    return ins

                pe.wait_ge(S["items_ready"], 1)
                n_items = pe.value_load(table_i[0:1, 0:1], min_val=N_EXPERTS, max_val=ITEMS)
                pe.wait_ge(S["one_hot"], 1)
                pe.wait_ge(S["ln_x_done"], 2 * DEPTH - 1)
                gather().then_inc(S["routed_mm"], 1)
                with pe.Fori(0, n_items) as item:
                    pe.wait_ge(S["xe_dve"], item + 1)
                    pe.wait_ge(S["xe_act"], item + 1)
                    first(0, item)
                    for s in range(1, FF_CHUNKS):
                        first(s, item)
                        last(s - 1, item)
                    pe.wait_ge(S["one_hot"], item + 2)
                    pe.wait_ge(S["acc_read"], item + 1)
                    gather()
                    for tt in range(TT):
                        ins = pe.transpose(bank[6][:, tt * P:(tt + 1) * P], weighted[:, tt, :], ident)
                    ins.then_inc(S["routed_mm"], 1)
                    last(FF_CHUNKS - 1, item)
                    pe.wait_ge(S["xe_dve"], item + 2)
                    pe.wait_ge(S["xe_act"], item + 2)
                    pe.wait_ge(S["spread"], item + 1)
                    for h in range(2):
                        pe.wait_ge(S["y_sb"], 2 * item + (h + 1))
                        for tt in range(TT):
                            ins = pe.matmul(bank[4 + 2 * h + tt][:], spread[:, tt, :], y_sb[:, h * 512:(h + 1) * 512], start=True, stop=True)
                        ins.then_inc(S["scatter_mm"], 1)
                pe.wait_ge(S["acc_read"], n_items + 1)

            def project_tokens(n_panels, n0, src=xT):
                for n in range(n0, n0 + n_panels):
                    w = panels.take()
                    if n >= 2:
                        pe.wait_ge(S["attn_read"], n - 1)
                    for tt in range(TT):
                        for kb in range(KB):
                            ins = mm(bank[4 + n % 2][:, tt * PC:(tt + 1) * PC], src[:, kb, tt * P:(tt + 1) * P],
                                     w[:, kb * PC:(kb + 1) * PC], start=(kb == 0), stop=(kb == KB - 1))
                    ins.then_inc(S["attn_proj"], 1)

            def turn_heads(l):
                n0 = 0 if l == 0 else BANKS_T[0]
                items = [turn_items(l, tt) for tt in range(TT)]
                pe.wait_ge(S["qk_ready"], l + 1)
                for n in range(BANKS_T[l]):
                    if n >= 4:
                        m = n0 + n - 4
                        pe.wait_ge(S["turnq_dve"] if m % 2 == 0 else S["turnq_act"], m // 2 + 1)
                    for i in range(2):
                        for tt in range(TT):
                            ins = pe.transpose(bank[n % 4][:, (2 * i + tt) * P:][:, 0:P], items[tt][2 * n + i], ident)
                    ins.then_inc(S["turnq_mm"], 1)

            def wait_heads(l):
                n = sum(BANKS_T[:l + 1])
                pe.wait_ge(S["turnq_dve"], (n + 1) // 2)
                pe.wait_ge(S["turnq_act"], n // 2)

            def compress(n):
                if 0 <= n < 4:
                    kv, half = n // 2, n % 2
                    if n == 0:
                        pe.wait_ge(S["cmp_tb"], 1)
                    w = panels.take()
                    for hb in range(2):
                        for kb in range(KB):
                            ins = mm(bank[1 + 2 * hb][:, kv * NSA_G * N_CMP:][:, 0:NSA_G * N_CMP], w[:, kb * CMP_HIDDEN + hb * P:][:, 0:P],
                                     cmp_in[:, kv, half * KB + kb, :, :].rearrange("p g i -> p (g i)"),
                                     start=(half == 0 and kb == 0), stop=(half == 1 and kb == KB - 1))
                    if half:
                        ins.then_inc(S["cmp_h_mm"], 1)
                elif n == 5:
                    w2 = mid[:, MIDS["cmp_w2"]].rearrange("p (k h e) -> p k h e", k=2, h=2)
                    pe.wait_ge(S["cmp_h"], 2)
                    for kv in range(2):
                        for g in range(NSA_G):
                            for hb in range(2):
                                ins = pe.matmul(bank[1][0:N_CMP, (kv * NSA_G + g) * HEAD:][:, 0:HEAD], cmp_h[:, kv, hb, g * N_CMP:(g + 1) * N_CMP],
                                                w2[:, kv, hb, :], start=(hb == 0), stop=(hb == 1))
                    ins.then_inc(S["cmp_o_mm"], 1)
                elif n == 9:
                    pe.wait_ge(S["cmp_k_ready"], 1)
                    for g in range(NSA_G):
                        ins = pe.transpose(bank[3][:, g * 16:g * 16 + N_CMP], cmp_dup[0:N_CMP, g, :, :].rearrange("p d e -> p (d e)"),
                                           ident[0:N_CMP, 0:N_CMP])
                    ins.then_inc(S["cmp_kT_mm"], 1)
                elif n == 11:
                    pe.wait_ge(S["cmp_kT"], 1)
                    for h in range(NSA_HEADS):
                        hd = slice(HEAD * (h % 2), HEAD * (h % 2) + HEAD)
                        for tt in range(TT):
                            ins = pe.matmul(bank[1 + 2 * (h % 2)][:, (h // 2 * TT + tt) * 16:][:, 0:N_CMP], qkT[hd, h // 2, tt * P:(tt + 1) * P],
                                            cmp_kT[hd, h // NSA_R, 0:N_CMP], start=True, stop=True)
                    ins.then_inc(S["cmp_s_mm"], 1)
                h = n - 15
                if 0 <= h < NSA_HEADS:
                    pe.wait_ge(S["cmp_p"], 1)
                    if h:
                        pe.wait_ge(S["cmp_pT"], h)
                    for tt in range(TT):
                        ins = pe.transpose(bank[1][0:N_CMP, h % 2 * T + tt * P:][:, 0:P], cmp_s[:, h, tt, 0:N_CMP], ident)
                    ins.then_inc(S["cmp_pT_mm"], 1)
                h = n - 16
                if 0 <= h < NSA_HEADS:
                    pe.wait_ge(S["cmp_pT"], h + 1)
                    if h:
                        pe.wait_ge(S["cmp_done"], h)
                    for tt in range(TT):
                        ins = pe.matmul(bank[3][:, (h % 2 * TT + tt) * HEAD:][:, 0:HEAD], cmp_pT[0:N_CMP, 2 * (h % 2) + tt, :],
                                        cmp_kv[0:N_CMP, 1, h // NSA_R, :], start=True, stop=True)
                    ins.then_inc(S["cmp_pv_mm"], 1)

            def attend(l):
                n0 = 0 if l == 0 else len(units(0))
                todo = units(l)

                def scores(n):
                    kind, h, tile = todo[n]
                    u = n0 + n
                    if u >= 2:
                        pe.wait_ge(S["score_exp"], u - 1)
                    hd = slice(HEAD * (h % 2), HEAD * (h % 2) + HEAD)
                    for tt in (range(TT) if tile is None else (tile,)):
                        tok, n_k = slice(tt * P, (tt + 1) * P), (tt + 1) * P
                        b = 2 * (u % 2)
                        if kind == "dil":
                            for g in range(3):
                                o = bank[b + (g * n_k) // 512][:, g * n_k % 512:][:, 0:n_k]
                                ins = pe.matmul(o, qkT[hd, 4 * g + h // 2, tok], qkT[hd, 12 + h // 2, 0:n_k], start=True, stop=True)
                        elif kind == "mem":
                            ins = pe.matmul(bank[b][:, tt * T:(tt + 1) * T], qkT[hd, MEM_ITEM[l] + h // 2, tok],
                                            qkT[hd, MEM_ITEM[l] + 2 + h // 2, :], start=True, stop=True)
                        else:
                            item = 6 + (0 if kind == "sel" else 3) + h // NSA_R
                            ins = pe.matmul(bank[b][:, tt * P:tt * P + n_k], qkT[hd, h // 2, tok], qkT[hd, item, 0:n_k], start=True, stop=True)
                    ins.then_inc(S["score_mm"], 1)

                def transposed(n):
                    kind, h, tile = todo[n]
                    u = n0 + n
                    pe.wait_ge(S["score_exp"], u + 1)
                    if u >= 2:
                        pe.wait_ge(S["pT"], u - 1)
                    for i, (starts, _, _) in enumerate(blocks_of(kind, tile)):
                        for m, a in enumerate(starts):
                            o = bank[4 + u % 2][:, i * P:(i + 1) * P]
                            if len(starts) == 1:
                                ins = pe.transpose(o, p_sb[:, u % 4, a:a + P], ident)
                            else:
                                ins = pe.matmul(o, p_sb[:, u % 4, a:a + P], ident, start=(m == 0), stop=(m == len(starts) - 1))
                    ins.then_inc(S["pT_mm"], 1)

                def with_values(n):
                    kind, h, tile = todo[n]
                    u = n0 + n
                    pe.wait_ge(S["pT"], u + 1)
                    if u >= 2:
                        pe.wait_ge(S["pv_read"], u - 1)
                    parts = blocks_of(kind, tile)
                    for i, (_, tt, k) in enumerate(parts):
                        at = 0 if tile is not None else tt * HEAD
                        first = i == 0 or parts[i - 1][1] != tt
                        last = i == len(parts) - 1 or parts[i + 1][1] != tt
                        ins = pe.matmul(bank[6 + u % 2][:, at:at + HEAD], pT_sb[:, u % 2, i * P:(i + 1) * P], values(l, kind, h, k), start=first, stop=last)
                    ins.then_inc(S["pv_mm"], 1)

                for n in range(len(todo) + 3):
                    if n < len(todo):
                        scores(n)
                    if 0 <= n - 2 < len(todo):
                        transposed(n - 2)
                    if n >= 3:
                        with_values(n - 3)
                    if l == 0:
                        compress(n - CMP_STEP)

            def attention_pe(l):
                n_turn = 4 + 3 * l
                n_proj = PANELS_ATTN[0] * l
                if l == 0:
                    for m in range(DEPTH):
                        project_tokens(MEM_PANELS, MEM_PANELS * m, memT[m])
                pe.wait_ge(S["rms_x"], 2 * l + 1)
                turn_x(n_turn, xn)
                wait_xT(n_turn)
                if l == 0:
                    project_tokens(9, DEPTH * MEM_PANELS)
                else:
                    project_tokens(4, n_proj)
                    turn_x(n_turn + 1, xn)
                    wait_xT(n_turn + 1)
                    project_tokens(7, n_proj + 4)
                turn_heads(l)
                wait_heads(l)
                attend(l)
                pe.wait_ge(S["cmp_done"], NSA_HEADS)
                n_turn = (5, 9)[l]
                pe.wait_ge(S["pv_read"], sum(len(units(i)) for i in range(l + 1)))
                turn_x(n_turn, o_tm)
                wait_xT(n_turn)
                rows_out((4, 3)[l], lambda kb, tt: xT[:, kb, tt * P:(tt + 1) * P], S["proj2_mm"])
                pe.wait_ge(S["rms_x"], 2 * l + 2)
                turn_x(n_turn + 1, xn)
                mlp_pe("mlp", D_FF_2 // FCH, l * (D_FF_2 // FCH), 3, PER_ITEM + 2 * l * (D_FF_2 // FCH), 1 + l)

            pe.wait_ge(S["consts_in"], 16)
            pe.wait_ge(S["x_in"], 16)
            for l in range(DEPTH):
                if l:
                    pe.wait_ge(S["ln_z"], 2 * l)
                turn_x(2 * l, x_tm)
                mixer_pe(l)
                pe.wait_ge(S["ln_z"], 2 * l + 1)
                turn_x(2 * l + 1, x_tm)
                if l == 0:
                    mlp_pe("ffn", FF_CHUNKS, 0, 2, 0, 0)
                else:
                    wait_xT(2 * l + 1)
                    router = mid[:, MIDS["router"]]
                    for tt in range(TT):
                        for kb in range(KB):
                            ins = pe.matmul(bank[0][:, tt * N_EXPERTS:(tt + 1) * N_EXPERTS], xT[:, kb, tt * P:(tt + 1) * P],
                                            router[:, kb * N_EXPERTS:(kb + 1) * N_EXPERTS], start=(kb == 0), stop=(kb == KB - 1))
                    ins.then_inc(S["router_mm"], 1)
                    pe.wait_ge(S["router_w"], 1)
                    chosen = [rt[:, 1, tt * N_EXPERTS:(tt + 1) * N_EXPERTS] for tt in range(TT)]
                    before = cst[:, CONST["before"]]
                    e = N_EXPERTS
                    pe.matmul(bank[1][:, 0:e], before, chosen[0], start=True, stop=True)
                    pe.matmul(bank[1][:, e:2 * e], ones, chosen[0], start=True, stop=False)
                    pe.matmul(bank[1][:, e:2 * e], before, chosen[1], start=False, stop=True)
                    pe.matmul(bank[1][:, 2 * e:3 * e], ones, chosen[0], start=True, stop=False)
                    ins = pe.matmul(bank[1][:, 2 * e:3 * e], ones, chosen[1], start=False, stop=True)
                    ins.then_inc(S["counts_mm"], 1)
                    pe.wait_ge(S["mem_x"], 1)
                    for f in range(KB):
                        for tt in range(TT):
                            ins = pe.transpose(bank[(2, 3, 6, 7)[f // 2]][:, (f % 2 * TT + tt) * P:][:, 0:P], mem_in[:, tt, f * P:(f + 1) * P], ident)
                    ins.then_inc(S["mem_turned"], 1)
                    pe.wait_ge(S["mem_xT"], 1)
                    moe_pe()
            panels.restart(landed_2, S["panel_used_2"], pe.transpose(bank[0][:, 0:P], ident, ident))
            for l in range(DEPTH):
                attention_pe(l)

        @block.scalar
        def _(act):
            made = Made()

            def copy_xT(n, gain=None, bias=None):
                for i, b in enumerate((1, 3)):
                    act.wait_ge(S["x_turned"], 4 * n + b + 1)
                    for kk_ in range(2):
                        f = 2 * b + kk_
                        ins = act.activation(xT[:, f, :], bank[b][:, kk_ * T:(kk_ + 1) * T], ACT.Copy if bias is None else ACT.Identity,
                                             scale=1.0 if gain is None else c1(gain, f), bias=0.0 if bias is None else c1(bias, f))
                    ins.then_inc(S["xT_act"], 1)
                    act.wait_ge(S["xT_act"], made.next("xT_act"))

            def proj_copy(l, j):
                n = 24 * l + IN_ORDER.index(j)
                act.wait_ge(S["proj_out"], n + 1)
                src = bank[n % 2][:].rearrange("p (m t) -> p m t", m=2)
                if j < 7:
                    if 7 * l + j >= 2:
                        act.wait_ge(S["shifted"], 7 * l + j - 1)
                    else:
                        act.wait_ge(S["cleared"], 1)
                    act.activation(pz[:, j % 2, :, 1:], src, ACT.Copy).then_inc(S["proj_read"], 1)
                    act.wait_ge(S["proj_read"], made.next("proj_read"))
                elif j == 7:
                    act.activation(u_pad[:, :, CONF_TAPS - 1:], src, ACT.Copy).then_inc(S["proj_read"], 1)
                    act.wait_ge(S["proj_read"], made.next("proj_read"))
                elif j == 8:
                    act.activation(conf_s[:], src, ACT.Sigmoid).then_inc(S["proj_read"], 1)
                    act.wait_ge(S["proj_read"], made.next("proj_read"))
                elif j == 9:
                    act.activation(gb[:], src, ACT.Copy).then_inc(S["proj_read"], 1)
                    act.wait_ge(S["proj_read"], made.next("proj_read"))
                elif j == 10:
                    act.activation(s_pad[:, :, SHORT_TAPS - 1:], src, ACT.Copy).then_inc(S["proj_read"], 1)
                    act.wait_ge(S["proj_read"], made.next("proj_read"))
                elif j == 11:
                    act.activation(conv_c[:], src, ACT.Copy).then_inc(S["proj_read"], 1)
                    act.wait_ge(S["proj_read"], made.next("proj_read"))
                else:
                    m = 2 * (j - 12)
                    act.activation(gates[:, m:m + 2, :], src, ACT.Sigmoid).then_inc(S["proj_read"], 1)
                    act.wait_ge(S["proj_read"], made.next("proj_read"))

            def mixer_act(l):
                gate = list(range(12, 24))

                def gate_copy():
                    proj_copy(l, gate.pop(0))

                def gate_copies(n):
                    while gate and 12 - len(gate) < n:
                        gate_copy()

                copy_xT(2 * l, *((f"ln2_g{l - 1}", f"ln2_b{l - 1}") if l else ()))
                for j in IN_ORDER[:12]:
                    proj_copy(l, j)
                act.wait_ge(S["shifted"], 7 * (l + 1))
                act.activation(loras[0:HEAD, 0, :], sh[0:HEAD, 12, :], ACT.Tanh)
                act.activation(loras[:, 1, :], sh[:, 13, :], ACT.Sigmoid).then_inc(S["lora_in"], 1)
                act.wait_ge(S["lora_in"], made.next("lora_in"))
                act.wait_ge(S["lora_z"], l + 1)
                for tt in range(TT):
                    ins = act.activation(sg_tok[:, tt, :], bank[2 + tt][:], ACT.Sigmoid)
                ins.then_inc(S["decay_in"], 1)
                act.wait_ge(S["decay_in"], made.next("decay_in"))
                if l == 0:
                    act.wait_ge(S["params_in"], 16 * 3)
                act.wait_ge(S["lora_a"], l + 1)
                for c in range(NC):
                    ins = act.activation(a_[:, c, :], bank[4 + c // 2][:, (c % 2) * T:][:, 0:T], ACT.Sigmoid, bias=c1(f"a0{l}", c))
                ins.then_inc(S["aaa"], 1)
                act.wait_ge(S["aaa"], made.next("aaa"))
                act.wait_ge(S["lora_g"], l + 1)
                for n in range(2):
                    ins = act.activation(g_[:, 2 * n:2 * n + 2, :], bank[6 + n][:].rearrange("p (m t) -> p m t", m=2), ACT.Copy)
                ins.then_inc(S["gate_lora"], 1)
                act.wait_ge(S["gate_lora"], made.next("gate_lora"))
                gate_copy()
                act.wait_ge(S["cum_mm"], l + 1)
                for c in range(NC):
                    s = bank[2 + c][:].rearrange("p (t m k) -> p m t k", t=TT, m=2)
                    for dst, m, sign in ((p_in, 0, -KAPPA), (p_inv, 0, KAPPA), (p_ex, 1, -KAPPA)):
                        ins = act.activation(dst[:, c, :].rearrange("p (t k) -> p t k", t=TT), s[:, m], ACT.Exp, scale=sign)
                ins.then_inc(S["decays"], 1)
                act.wait_ge(S["decays"], made.next("decays"))
                act.wait_ge(S["kk_mm"], l + 1)
                for n in range(2):
                    ins = act.activation(vt[:, n, :], bank[6 + n][:], ACT.Sqrt)
                ins.then_inc(S["kk_norm"], 1)
                act.wait_ge(S["kk_norm"], made.next("kk_norm"))
                gate_copy()
                gate_copy()
                for n, dst in enumerate((vt, bt, kt)):
                    act.wait_ge(S["turn_mm"], 6 * l + 2 * n + 2)
                    act.activation(dst[:, 1, :], bank[2 + (2 * n + 1) % 4][:], ACT.Copy).then_inc(S["turned_act"], 1)
                    act.wait_ge(S["turned_act"], made.next("turned_act"))
                for tt in range(TT):
                    for hg in range(2):
                        group = 4 * l + 2 * tt + hg
                        gate_copies(gates_done(tt, hg, 0, False))
                        n = 14 * group
                        for count, b, dst, step in ((2, 3, 1, 1), (4, 5, 2, 1), (5, 6, 3, 2), (7, 3, 0, 4), (9, 2, 1, 6), (12, 4, 1, 8)):
                            act.wait_ge(S["inv_mm"], n + count)
                            act.activation(pw[:, dst, :], bank[b][:], ACT.Copy).then_inc(S["inv_act"], 1)
                            act.wait_ge(S["inv_act"], made.next("inv_act"))
                            gate_copies(gates_done(tt, hg, step, False))
                    for half in range(2):
                        q = 4 * l + 2 * tt + half
                        gate_copies(gates_done(tt, half, 1, True))
                        act.wait_ge(S["o_mm"], q + 1)
                        lo = (2 * tt + half) * CHUNK
                        act.activation(oT[:, :, lo:lo + CHUNK], bank[5][:, 0:NC * CHUNK].rearrange("p (c t) -> p c t", c=NC),
                                       ACT.Copy).then_inc(S["o_read"], 1)
                        act.wait_ge(S["o_read"], made.next("o_read"))
                gate_copies(12)
                act.wait_ge(S["gn_var_mm"], l + 1)
                for n in range(2):
                    ins = act.activation(kk[:, 2 * n:2 * n + 2, :], bank[4 + n][:].rearrange("p (m t) -> p m t", m=2), ACT.Sqrt,
                                         scale=1.0 / HEAD, bias=eps("gn_eps"))
                ins.then_inc(S["gn_std"], 1)
                act.wait_ge(S["gn_std"], made.next("gn_std"))
                act.wait_ge(S["conf_var_mm"], l + 1)
                act.activation(conf_s[:, 0, :], bank[7][:, 0:T], ACT.Sqrt, scale=1.0 / CONF, bias=eps("ln_eps")).then_inc(S["conf_std"], 1)
                act.wait_ge(S["conf_std"], made.next("conf_std"))
                act.wait_ge(S["branch_b"], l + 1)
                for n in range(2):
                    ins = act.activation(conf_s[:, n, :], conv[:, n, :], ACT.Silu, scale=c1(f"conf_ln_g{l}", n), bias=c1(f"conf_ln_b{l}", n))
                ins.then_inc(S["conf_silu"], 1)
                act.wait_ge(S["conf_silu"], made.next("conf_silu"))

            def ln_std(n):
                act.wait_ge(S["ln_x"], n + 1)
                act.activation(stat[:, 32:32 + TT], stat[:, 26:26 + 2 * TT].rearrange("p (t s) -> p s t", s=2)[:, 1, :], ACT.Sqrt,
                               bias=eps("ln_eps")).then_inc(S["ln_std"], 1)
                act.wait_ge(S["ln_std"], made.next("ln_std"))

            def mlp_act(kind, n_chunks, base, per_step):
                gated, sems = kind == "ffn", mlp_signals(kind)
                nb = 2 if gated else 3
                func = ACT.Silu if gated else ACT.Relu

                def chunk(i, slot, early):
                    act.wait_ge(sems["up"], i + 1)
                    if not early:
                        act.wait_ge(sems["h"], i - nb + 1)
                    b = bank[2 * slot if gated else slot]
                    act.activation(gate_s[:, slot, :, :], b[:].rearrange("p (m t) -> p m t", m=2), func).then_inc(sems["out"], 1)

                lead = nb + (n_chunks - nb) % per_step
                for s in range(lead):
                    chunk(base + s, s % nb, s < nb)
                with act.Fori(0, (n_chunks - lead) // per_step) as turn:
                    for s in range(lead, lead + per_step):
                        chunk(turn * per_step + (base + s), s % nb, False)

            def moe_act():
                act.wait_ge(S["items_ready"], 1)
                n_items = act.value_load(table_i[0:1, 0:1], min_val=N_EXPERTS, max_val=ITEMS)

                def tokens():
                    return act.activation(xeT[:, 4:8, :], bank[5][:].rearrange("p (k c) -> p k c", k=4), ACT.Copy)

                act.wait_ge(S["routed_mm"], 1)
                tokens().then_inc(S["xe_act"], 1)
                with act.Fori(0, n_items) as item:
                    for s in range(FF_CHUNKS):
                        act.wait_ge(S["gu_full"], item * FF_CHUNKS + (FF_CHUNKS + s + 1))
                        act.wait_ge(S["h_ready"], item * FF_CHUNKS + (FF_CHUNKS + max(s - 1, 0)))
                        act.activation(gate_s[:, s % 2, :, 0:CAP], bank[s % 2][:, 0:2 * CAP].rearrange("p (m c) -> p m c", m=2), ACT.Silu
                                       ).then_inc(S["act_out"], 1)
                    act.wait_ge(S["routed_mm"], item + 2)
                    tokens().then_inc(S["xe_act"], 1)
                    act.activation(spread[:], bank[6][:, 0:T].rearrange("p (t k) -> p t k", t=TT), ACT.Copy).then_inc(S["spread"], 1)
                    act.wait_ge(S["y_half"], item + 1)
                    act.activation(y_sb[:, 0:512], bank[2][:], ACT.Copy).then_inc(S["y_sb"], 1)
                    act.wait_ge(S["y_full"], item * FF_CHUNKS + 2 * FF_CHUNKS)
                    act.activation(y_sb[:, 512:], bank[3][:], ACT.Copy).then_inc(S["y_sb"], 1)

            def rms(n, src):
                if n == 0:
                    act.wait_ge(S["ln_x_done"], 2 * DEPTH)
                elif n == 2:
                    act.wait_ge(S["y_read_2"], 1)
                else:
                    act.wait_ge(S["x_done"], 1 + n // 2)
                for tt in range(TT):
                    ins = act.activation(scr[:, tt, 0:D], src[:, tt, :], ACT.Square, accum_out=rs[:, tt:tt + 1])
                ins.then_inc(S["act_step"], 1)
                act.wait_ge(S["act_step"], made.next("act_step"))
                act.activation(rs[:, 2:2 + TT], rs[:, 0:TT], ACT.Sqrt, scale=1.0 / D, bias=eps("rms_eps")).then_inc(S["rms_std"], 1)
                act.wait_ge(S["rms_std"], made.next("rms_std"))

            def copy_tokens(l, dst, n_panels, n0):
                for j in range(n_panels):
                    n = n0 + j
                    act.wait_ge(S["attn_proj"], l * PANELS_ATTN[0] + n + 1)
                    act.activation(dst[:, :, j * PC:(j + 1) * PC], bank[4 + (l * PANELS_ATTN[0] + n) % 2][:].rearrange("p (t c) -> p t c", t=TT),
                                   ACT.Copy).then_inc(S["attn_read"], 1)
                    act.wait_ge(S["attn_read"], made.next("attn_read"))
                    for i, h in enumerate(head_sets(l)):
                        if h[5] == n:
                            head_std(l, i)

            def head_std(l, i):
                at, size = set_stats(l, i)
                act.wait_ge(S["rms_ss"], l * N_SETS[0] + i + 1)
                act.activation(rs[:, at:at + size], rs[:, at:at + size], ACT.Sqrt, scale=1.0 / HEAD, bias=eps("rms_eps")).then_inc(S["qk_std"], 1)
                act.wait_ge(S["qk_std"], made.next("qk_std"))

            def compress(n):
                if n == 4:
                    for kv in range(2):
                        act.wait_ge(S["cmp_h_mm"], kv + 1)
                        for hb in range(2):
                            ins = act.activation(cmp_h[:, kv, hb, :], bank[1 + 2 * hb][:, kv * NSA_G * N_CMP:][:, 0:NSA_G * N_CMP],
                                                 ACT.Gelu_apprx_tanh, bias=c1("cmp_b1", 2 * kv + hb))
                        ins.then_inc(S["cmp_h"], 1)
                elif n == 7:
                    act.wait_ge(S["cmp_kv"], 1)
                    act.activation(rs[0:N_CMP, 4:4 + NSA_G], rs[0:N_CMP, 4:4 + NSA_G], ACT.Sqrt, scale=1.0 / HEAD,
                                   bias=eps("rms_eps")[0:N_CMP]).then_inc(S["cmp_k_std"], 1)
                elif n == 13:
                    act.wait_ge(S["cmp_s"], 1)
                    act.activation(cmp_s[:, :, :, 0:N_CMP], cmp_s[:, :, :, 0:N_CMP], ACT.Exp, scale=SCALE).then_inc(S["cmp_e"], 1)
                h = n - 15
                if 0 <= h < NSA_HEADS:
                    act.wait_ge(S["cmp_pT_mm"], h + 1)
                    if h >= 2:
                        act.wait_ge(S["cmp_pv_mm"], h - 1)
                    b = h % 2
                    act.activation(cmp_pT[0:N_CMP, 2 * b:2 * b + 2, :], bank[1][0:N_CMP, b * T:(b + 1) * T].rearrange("p (t q) -> p t q", t=TT),
                                   ACT.Copy).then_inc(S["cmp_pT"], 1)

            def attention_act(l):
                n_turn = 4 + 3 * l
                if l == 0:
                    copy_tokens(0, mem_kv[:, 0], MEM_PANELS, 0)
                    rms(0, x_tm)
                    copy_tokens(0, mem_kv[:, 1], MEM_PANELS, MEM_PANELS)
                    copy_xT(n_turn, "attn_norm0")
                    copy_tokens(0, proj, 9, DEPTH * MEM_PANELS)
                    act.activation(coef[:], proj[:, :, 2176:2212].rearrange("p t (h b) -> p b h t", b=3), ACT.Sigmoid).then_inc(S["nsa_gates"], 1)
                    act.wait_ge(S["nsa_gates"], made.next("nsa_gates"))
                else:
                    rms(2, x_tm)
                    copy_xT(n_turn, "kv_norm")
                    copy_tokens(1, proj, 4, 0)
                    copy_xT(n_turn + 1, "attn_norm1")
                    copy_tokens(1, proj[:, :, 4 * PC:], 7, 4)
                head_std(l, N_SETS[l] - 1)
                n0 = 0 if l == 0 else BANKS_T[0]
                for n in range(BANKS_T[l]):
                    if (n0 + n) % 2:
                        act.wait_ge(S["turnq_mm"], n0 + n + 1)
                        act.activation(qkT[:, 2 * n:2 * n + 2, :], bank[n % 4][:].rearrange("p (i t) -> p i t", i=2), ACT.Copy).then_inc(S["turnq_act"], 1)
                        act.wait_ge(S["turnq_act"], made.next("turnq_act"))
                n0 = 0 if l == 0 else len(units(0))
                todo = units(l)

                def exps(n):
                    kind, h, tile = todo[n]
                    u = n0 + n
                    act.wait_ge(S["score_max"], u + 1)
                    if u >= 4:
                        act.wait_ge(S["pT_mm"], u - 3)
                    if u >= 8:
                        act.wait_ge(S["pv_read"], u - 7)
                    for tt in range(TT):
                        if kind == "dil":
                            a, w, at = 0, 3 * P * (tile + 1), 0
                        elif kind == "mem":
                            a, w, at = tt * T, T, tt
                        else:
                            a, w, at = tt * P, P * (tt + 1), tt
                        if kind == "dil" and tt:
                            break
                        e = p_sb[:, u % 4, a:a + w]
                        src = bank[2 * (u % 2)][:, a:a + w] if kind == "mem" else e
                        ins = act.activation(e, src, ACT.Exp, scale=SCALE, bias=unit_stat(u, "neg")[:, at:at + 1],
                                             accum_out=unit_stat(u, "sum")[:, at:at + 1])
                    ins.then_inc(S["score_exp"], 1)
                    act.wait_ge(S["score_exp"], made.next("score_exp"))

                def turned(n):
                    kind, h, tile = todo[n]
                    u = n0 + n
                    s = u % 2
                    act.wait_ge(S["pT_mm"], u + 1)
                    if u >= 2:
                        act.wait_ge(S["pv_mm"], u - 1)
                    w = len(blocks_of(kind, tile)) * P
                    act.activation(pT_sb[:, s, 0:w], bank[4 + s][:, 0:w], ACT.Copy).then_inc(S["pT"], 1)
                    act.wait_ge(S["pT"], made.next("pT"))

                for n in range(len(todo) + 2):
                    if n < len(todo):
                        exps(n)
                    if n >= 2:
                        turned(n - 2)
                    if l == 0:
                        compress(n - CMP_STEP)
                n_turn = (5, 9)[l]
                copy_xT(n_turn)
                rms(2 * l + 1, x_tm)
                copy_xT(n_turn + 1, f"mlp_norm{l}")
                mlp_act("mlp", D_FF_2 // FCH, l * (D_FF_2 // FCH), 3)

            act.wait_ge(S["consts_in"], 16)
            for l in range(DEPTH):
                mixer_act(l)
                ln_std(2 * l)
                copy_xT(2 * l + 1, f"ln1_g{l}", f"ln1_b{l}")
                if l == 0:
                    mlp_act("ffn", FF_CHUNKS, 0, 2)
                else:
                    act.wait_ge(S["mem_in"], 16)
                    for tt in range(TT):
                        act.activation(mem_sq, mem_in[:, tt, :], ACT.Square, accum_out=stat[:, 40 + tt:41 + tt]).then_inc(S["act_step"], 1)
                        act.wait_ge(S["act_step"], made.next("act_step"))
                    act.activation(stat[:, 42:42 + TT], stat[:, 40:40 + TT], ACT.Sqrt, scale=1.0 / D, bias=eps("rms_eps")).then_inc(S["mem_std"], 1)
                    act.wait_ge(S["router_w"], 1)
                    p = rt[:, 2, 0:TT * N_EXPERTS]
                    act.activation(p, p, ACT.Exp).then_inc(S["router_exp"], 1)
                    act.wait_ge(S["mem_inv"], 1)
                    for tt in range(TT):
                        ins = act.activation(mem_in[:, tt, :], mem_in[:, tt, :], ACT.Copy, scale=stat[:, 44 + tt:45 + tt])
                    ins.then_inc(S["mem_x"], 1)
                    act.wait_ge(S["mem_turned"], 1)
                    for m in range(DEPTH):
                        for f in range(KB):
                            ins = act.activation(memT[m][:, f, :], bank[(2, 3, 6, 7)[f // 2]][:, f % 2 * T:][:, 0:T], ACT.Copy,
                                                 scale=c1(f"mem_norm{m}", f))
                    ins.then_inc(S["mem_xT"], 1)
                    moe_act()
                ln_std(2 * l + 1)
            for l in range(DEPTH):
                attention_act(l)

        @block.vector
        def _(dve):
            made = Made()
            tt_, ts_, stt, copy = dve.tensor_tensor, dve.tensor_scalar, dve.scalar_tensor_tensor, dve.tensor_copy

            def pair(b):
                return bank[b][:].rearrange("p (m t) -> p m t", m=2)

            def copy_xT(n, gain=None, bias=None):
                for i, b in enumerate((0, 2)):
                    dve.wait_ge(S["x_turned"], 4 * n + b + 1)
                    if gain is None:
                        ins = copy(xT[:, 2 * b:2 * b + 2, :], pair(b))
                    else:
                        for kk_ in range(2):
                            ins = ts_(xT[:, 2 * b + kk_, :], bank[b][:, kk_ * T:(kk_ + 1) * T], c1(gain, 2 * b + kk_),
                                      *((None, ALU.mult) if bias is None else (c1(bias, 2 * b + kk_), ALU.mult, ALU.add)))
                    ins.then_inc(S["xT_dve"], 1)
                    dve.wait_ge(S["xT_dve"], made.next("xT_dve"))

            def depthwise(out, src, name, taps, first, last):
                for j in range(first, last):
                    for n in range(2):
                        ins = stt(out[:, n, :], src[:, n, j:j + T], c1(name, n * taps + j), out[:, n, :], ALU.mult, ALU.add) if j else \
                            ts_(out[:, n, :], src[:, n, 0:T], c1(name, n * taps), None, ALU.mult)
                    ins.then_inc(S["dve_step"], 1)
                    dve.wait_ge(S["dve_step"], made.next("dve_step"))

            def mixer_dve(l):
                dve.memset(state[:], 0.0).then_inc(S["cleared"], 1)
                dve.wait_ge(S["cleared"], made.next("cleared"))
                copy_xT(2 * l, *((f"ln2_g{l - 1}", f"ln2_b{l - 1}") if l else ()))
                if l:
                    ln_gain(2 * l - 1)
                dve.wait_ge(S["proj_read"], 24 * l + CONV_PANELS)
                tt_(u_pad[:, :, CONF_TAPS - 1:], u_pad[:, :, CONF_TAPS - 1:], conf_s[:], ALU.mult)
                tt_(s_pad[:, :, SHORT_TAPS - 1:], s_pad[:, :, SHORT_TAPS - 1:], conv_c[:], ALU.mult).then_inc(S["dve_step"], 1)
                dve.wait_ge(S["dve_step"], made.next("dve_step"))
                if l == 0:
                    dve.wait_ge(S["params_in"], 16 * 3)
                depthwise(conv_c, s_pad, f"short_dw{l}", SHORT_TAPS, 0, SHORT_TAPS)
                tt_(conv_c[:], conv_c[:], gb[:], ALU.mult).then_inc(S["branch_c"], 1)
                per = -(-CONF_TAPS // 7)
                for j in range(7):
                    depthwise(conv, u_pad, f"conf_dw{l}", CONF_TAPS, j * per, min((j + 1) * per, CONF_TAPS))
                    dve.wait_ge(S["proj_read"], 24 * l + CONV_PANELS + j + 1)
                    z = pz[:, j % 2]
                    tt_(tmp[:, 0:2, :], z[:, :, 0:T], z[:, :, 1:], ALU.subtract).then_inc(S["dve_step"], 1)
                    dve.wait_ge(S["dve_step"], made.next("dve_step"))
                    for m in range(2):
                        ins = stt(sh[:, 2 * j + m, :], tmp[:, m, :], c1(f"mu{l}", 2 * j + m), z[:, m, 1:], ALU.mult, ALU.add)
                    ins.then_inc(S["shifted"], 1)
                    dve.wait_ge(S["shifted"], made.next("shifted"))
                for c in range(NC):
                    ins = ts_(kk[:, c, :], k_[:, c, :], c1(f"k_k{l}", c), None, ALU.mult)
                ins.then_inc(S["dve_step"], 1)
                dve.wait_ge(S["dve_step"], made.next("dve_step"))
                tt_(tmp[:], kk[:], kk[:], ALU.mult).then_inc(S["kk_sq"], 1)
                dve.wait_ge(S["kk_sq"], made.next("kk_sq"))
                for n in range(2):
                    ins = ts_(conv[:, n, :], conv[:, n, :], c1(f"conf_dw_b{l}", n), None, ALU.add)
                ins.then_inc(S["conf_conv"], 1)
                dve.wait_ge(S["aaa"], l + 1)
                dve.wait_ge(S["kk_mm"], l + 1)
                for c in range(NC):
                    ins = ts_(tmp[:, c, :], a_[:, c, :], 1.0, c1(f"k_a{l}", c), ALU.subtract, ALU.mult)
                ins.then_inc(S["dve_step"], 1)
                dve.wait_ge(S["dve_step"], made.next("dve_step"))
                stt(k_, tmp[:], 1.0, k_, ALU.add, ALU.mult).then_inc(S["dve_step"], 1)
                dve.wait_ge(S["dve_step"], made.next("dve_step"))
                for c in range(NC):
                    ins = stt(tmp[:, c, :], r_[:, c, :], c1(f"r_k{l}", c), k_[:, c, :], ALU.mult, ALU.mult)
                dve.wait_ge(S["kk_norm"], l + 1)
                norm = vt[:].rearrange("p a (b t) -> p (a b) t", t=T)
                ts_(norm, norm, 1e-12, None, ALU.max).then_inc(S["dve_step"], 1)
                dve.wait_ge(S["dve_step"], made.next("dve_step"))
                dve.reciprocal(norm, norm).then_inc(S["bonus_in"], 1)
                dve.wait_ge(S["bonus_in"], made.next("bonus_in"))
                tt_(kk[:], kk[:], norm, ALU.mult).then_inc(S["dve_step"], 1)
                dve.wait_ge(S["dve_step"], made.next("dve_step"))
                tt_(a_[:], kk[:], a_[:], ALU.mult).then_inc(S["dve_step"], 1)
                dve.wait_ge(S["dve_step"], made.next("dve_step"))
                dve.wait_ge(S["decays"], l + 1)
                for c in range(NC):
                    stt(ar[:, c, :, 0, :], kk[:, c, :].rearrange("p (t k) -> p t k", t=TT), -1.0,
                        p_ex[:, c, :].rearrange("p (t k) -> p t k", t=TT), ALU.mult, ALU.mult)
                    ins = tt_(ar[:, c, :, 1, :], r_[:, c, :].rearrange("p (t k) -> p t k", t=TT),
                              p_in[:, c, :].rearrange("p (t k) -> p t k", t=TT), ALU.mult)
                ins.then_inc(S["dve_step"], 1)
                dve.wait_ge(S["dve_step"], made.next("dve_step"))
                tt_(a_[:], a_[:], p_inv[:], ALU.mult)
                tt_(kk[:], k_, p_inv[:], ALU.mult).then_inc(S["dve_step"], 1)
                dve.wait_ge(S["dve_step"], made.next("dve_step"))
                dve.wait_ge(S["bonus_mm"], l + 1)
                for n in range(2):
                    ins = tt_(tmp[:, 2 * n:2 * n + 2, :], pair(6 + n), v_[:, 2 * n:2 * n + 2, :], ALU.mult)
                ins.then_inc(S["features"], 1)
                dve.wait_ge(S["features"], made.next("features"))
                for n, dst in enumerate((vt, bt, kt)):
                    dve.wait_ge(S["turn_mm"], 6 * l + 2 * n + 1)
                    copy(dst[:, 0, :], bank[2 + 2 * n % 4][:]).then_inc(S["turned_dve"], 1)
                    dve.wait_ge(S["turned_dve"], made.next("turned_dve"))

                for tt in range(TT):
                    for hg in range(2):
                        group = 4 * l + 2 * tt + hg
                        dve.wait_ge(S["unit_mm"], group + 1)
                        if tt and not hg:
                            dve.wait_ge(S["o_mm"], 4 * l + 2)
                        for i in range(4):
                            tt_(unit[:, 4 * hg + i, :, :].rearrange("p m t -> p (m t)"), bank[2 + i][:], unit_mask, ALU.mult)
                        for j in range(2):
                            ins = tt_(a3[:, j::2], bank[6 + j][:, 0:2 * P].rearrange("p (i s) -> p i s", i=2).unsqueeze(2).to_broadcast([P, 2, 3, P]),
                                      inv_mask.unsqueeze(1).to_broadcast([P, 2, 3, P]), ALU.mult)
                        ins.then_inc(S["dve_step"], 1)
                        dve.wait_ge(S["dve_step"], made.next("dve_step"))
                        tt_(xa[:].rearrange("p (i s) -> p i s", i=4), unit[:, 4 * hg:4 * hg + 4, 0, :],
                            ident.unsqueeze(1).to_broadcast([P, 4, P]), ALU.add).then_inc(S["masks"], 1)
                        dve.wait_ge(S["masks"], made.next("masks"))
                        n = 14 * group
                        fin = inv[:, 4 * hg:4 * hg + 4, :].rearrange("p i s -> p (i s)")
                        for count, b, dst, add in ((1, 2, pw[:, 0, :], None), (3, 4, xb[:], xa[:]), (6, 2, xa[:], xb[:]),
                                                   (8, 4, xb[:], xa[:]), (10, 3, pw[:, 2, :], None), (11, 6, xa[:], xb[:]),
                                                   (13, 5, pw[:, 2, :], None), (14, 2, fin, xa[:])):
                            dve.wait_ge(S["inv_mm"], n + count)
                            ins = copy(dst, bank[b][:]) if add is None else tt_(dst, bank[b][:], add, ALU.add)
                            ins.then_inc(S["inv_dve"], 1)
                            dve.wait_ge(S["inv_dve"], made.next("inv_dve"))
                    for half in range(2):
                        q = 4 * l + 2 * tt + half
                        hs = slice(half * CHUNK, (half + 1) * CHUNK)
                        dve.wait_ge(S["rhs_mm"], q + 1)
                        copy(rhs_sb[hs].rearrange("p h v -> p (h v)"), bank[2][hs, :]).then_inc(S["rhs"], 1)
                        dve.wait_ge(S["rhs"], made.next("rhs"))
                        dve.wait_ge(S["u_mm"], q + 1)
                        copy(u_sb[hs].rearrange("p h v -> p (h v)"), bank[3][hs, :]).then_inc(S["u"], 1)
                        dve.wait_ge(S["u"], made.next("u"))
                        if q % 4 < 3:
                            dve.wait_ge(S["state_mm"], q - l + 1)
                            end = (2 * tt + half) * CHUNK + CHUNK - 1
                            for j, hd in enumerate((slice(0, HEAD), slice(HEAD, P))):
                                ins = tt_(state[hd, :, j, :], bank[4][hd, 0:NC * HEAD].rearrange("p (c v) -> p c v", c=NC), state[hd, :, j, :], ALU.add)
                            ins.then_inc(S["dve_step"], 1)
                            dve.wait_ge(S["dve_step"], made.next("dve_step"))
                            for j, hd in enumerate((slice(0, HEAD), slice(HEAD, P))):
                                ins = tt_(state[hd, :, j, :], state[hd, :, j, :], p_in[hd, :, end:end + 1].to_broadcast([HEAD, NC, HEAD]), ALU.mult)
                            ins.then_inc(S["state"], 1)
                            dve.wait_ge(S["state"], made.next("state"))

                dve.wait_ge(S["gn_mean_mm"], l + 1)
                for n in range(2):
                    ins = stt(oT[:, 2 * n:2 * n + 2, :], pair(2 + n), -1.0 / HEAD, oT[:, 2 * n:2 * n + 2, :], ALU.mult, ALU.add)
                ins.then_inc(S["dve_step"], 1)
                dve.wait_ge(S["dve_step"], made.next("dve_step"))
                ot4 = oT[:].rearrange("p c (t k) -> p c t k", t=TT)
                for c in range(NC):
                    ins = tt_(ar[:, c, :, 0, :], ot4[:, c], ot4[:, c], ALU.mult)
                ins.then_inc(S["gn_sq"], 1)
                dve.wait_ge(S["gn_sq"], made.next("gn_sq"))
                dve.wait_ge(S["conf_mean_mm"], l + 1)
                for n in range(2):
                    ins = stt(conv[:, n, :], bank[6][:, 0:T], -1.0 / CONF, conv[:, n, :], ALU.mult, ALU.add)
                ins.then_inc(S["dve_step"], 1)
                dve.wait_ge(S["dve_step"], made.next("dve_step"))
                tt_(conv_sq[:], conv[:], conv[:], ALU.mult).then_inc(S["conf_sq"], 1)
                dve.wait_ge(S["conf_sq"], made.next("conf_sq"))
                dve.wait_ge(S["gn_std"], l + 1)
                dve.reciprocal(kk[:], kk[:]).then_inc(S["dve_step"], 1)
                dve.wait_ge(S["dve_step"], made.next("dve_step"))
                tt_(oT[:], oT[:], kk[:], ALU.mult).then_inc(S["dve_step"], 1)
                dve.wait_ge(S["dve_step"], made.next("dve_step"))
                for c in range(NC):
                    ins = ts_(yT[:, c, :], oT[:, c, :], c1(f"gn_g{l}", c), c1(f"gn_b{l}", c), ALU.mult, ALU.add)
                ins.then_inc(S["dve_step"], 1)
                dve.wait_ge(S["dve_step"], made.next("dve_step"))
                tt_(yT[:], yT[:], tmp[:], ALU.add).then_inc(S["dve_step"], 1)
                dve.wait_ge(S["dve_step"], made.next("dve_step"))
                tt_(yT[:], yT[:], g_[:], ALU.mult).then_inc(S["branch_a"], 1)
                dve.wait_ge(S["branch_a"], made.next("branch_a"))
                dve.wait_ge(S["conf_std"], l + 1)
                dve.reciprocal(conf_s[:, 0, :], conf_s[:, 0, :]).then_inc(S["dve_step"], 1)
                dve.wait_ge(S["dve_step"], made.next("dve_step"))
                for n in range(2):
                    ins = tt_(conv[:, n, :], conv[:, n, :], conf_s[:, 0, :], ALU.mult)
                ins.then_inc(S["branch_b"], 1)
                dve.wait_ge(S["branch_b"], made.next("branch_b"))
                dve.wait_ge(S["proj_read"], 24 * (l + 1))
                for n in range(4):
                    b = 2 + 3 * (n % 2)
                    m = slice(2 * n, 2 * n + 2)
                    dve.wait_ge(S["mix_mm"], 4 * l + n + 1)
                    for part_ in range(3):
                        g = gates[:, 8 * part_ + 2 * n:8 * part_ + 2 * n + 2, :]
                        ins = tt_(g, pair(b + part_), g, ALU.mult)
                    ins.then_inc(S["dve_step"], 1)
                    dve.wait_ge(S["dve_step"], made.next("dve_step"))
                    tt_(mixT[:, m, :], gates[:, m, :], gates[:, 8 + 2 * n:10 + 2 * n, :], ALU.add).then_inc(S["dve_step"], 1)
                    dve.wait_ge(S["dve_step"], made.next("dve_step"))
                    tt_(mixT[:, m, :], mixT[:, m, :], gates[:, 16 + 2 * n:18 + 2 * n, :], ALU.add).then_inc(S["mixed"], 1)
                    dve.wait_ge(S["mixed"], made.next("mixed"))
                dve.wait_ge(S["wout_mm"], l + 1)
                for tt in range(TT):
                    for h in range(2):
                        xs = x_tm[:, tt, h * 512:(h + 1) * 512]
                        ins = stt(xs, xs, ALPHA, bank[2 * tt + h][:], ALU.mult, ALU.add)
                ins.then_inc(S["dve_step"], 1)
                dve.wait_ge(S["dve_step"], made.next("dve_step"))

            def layer_norm(n, src):
                for tt in range(TT):
                    for h in range(2):
                        s = 12 * tt + 6 * h
                        ins = dve.bn_stats(stat[:, s:s + 6], src[:, tt, h * 512:(h + 1) * 512])
                ins.then_inc(S["dve_step"], 1)
                dve.wait_ge(S["dve_step"], made.next("dve_step"))
                for tt in range(TT):
                    ins = dve.bn_aggr(stat[:, 26 + 2 * tt:28 + 2 * tt], stat[:, 12 * tt:12 * tt + 12])
                ins.then_inc(S["ln_x"], 1)
                dve.wait_ge(S["ln_x"], made.next("ln_x"))
                dve.wait_ge(S["ln_std"], n + 1)
                dve.reciprocal(stat[:, 34:34 + TT], stat[:, 32:32 + TT]).then_inc(S["dve_step"], 1)
                dve.wait_ge(S["dve_step"], made.next("dve_step"))
                for tt in range(TT):
                    ins = ts_(x_tm[:, tt, :], src[:, tt, :], stat[:, 26 + 2 * tt:27 + 2 * tt], stat[:, 34 + tt:35 + tt], ALU.subtract, ALU.mult)
                ins.then_inc(S["ln_z"], 1)
                dve.wait_ge(S["ln_z"], made.next("ln_z"))

            def ln_gain(n):
                if n < 3:
                    dve.wait_ge(S["x_turned"], 4 * (n + 2))
                dve.wait_ge(S["ln_rows_in"], 16 * (n + 1))
                tt_(x_tm[:], x_tm[:], ln_row[:, 0, :].unsqueeze(1).to_broadcast([P, TT, D]), ALU.mult).then_inc(S["dve_step"], 1)
                dve.wait_ge(S["dve_step"], made.next("dve_step"))
                tt_(x_tm[:], x_tm[:], ln_row[:, 1, :].unsqueeze(1).to_broadcast([P, TT, D]), ALU.add).then_inc(S["ln_x_done"], 1)
                dve.wait_ge(S["ln_x_done"], made.next("ln_x_done"))

            def route():
                dve.wait_ge(S["router_mm"], 1)
                lg, rank, p, mx, sq = rt[:, 0, 0:TT * E], rt[:, 1, 0:TT * E], rt[:, 2, 0:TT * E], rt[:, 3, 0:TT], rt[:, 4:6, :]
                l3, p3 = (t.rearrange("p (t e) -> p t e", t=TT) for t in (lg, p))
                copy(lg, bank[0][:, 0:TT * E]).then_inc(S["dve_step"], 1)
                dve.wait_ge(S["dve_step"], made.next("dve_step"))
                dve.tensor_reduce(mx, l3, AX.X, ALU.max).then_inc(S["dve_step"], 1)
                dve.wait_ge(S["dve_step"], made.next("dve_step"))
                tt_(p3, l3, mx.unsqueeze(2).to_broadcast([P, TT, E]), ALU.subtract).then_inc(S["dve_step"], 1)
                dve.wait_ge(S["dve_step"], made.next("dve_step"))
                earlier = cst[:, CONST["earlier"]].rearrange("p (e f) -> p e f", e=E)
                for tt in range(TT):
                    this = l3[:, tt, :].unsqueeze(2).to_broadcast([P, E, E])
                    other = l3[:, tt, :].unsqueeze(1).to_broadcast([P, E, E])
                    s0, s1 = (sq[:, i, :].rearrange("p (e f) -> p e f", e=E) for i in range(2))
                    tt_(s0, other, this, ALU.is_gt)
                    tt_(s1, other, this, ALU.is_equal).then_inc(S["dve_step"], 1)
                    dve.wait_ge(S["dve_step"], made.next("dve_step"))
                    tt_(s1, s1, earlier, ALU.mult).then_inc(S["dve_step"], 1)
                    dve.wait_ge(S["dve_step"], made.next("dve_step"))
                    tt_(s0, s0, s1, ALU.add).then_inc(S["dve_step"], 1)
                    dve.wait_ge(S["dve_step"], made.next("dve_step"))
                    dve.tensor_reduce(rank[:, tt * E:(tt + 1) * E], s0, AX.X, ALU.add).then_inc(S["dve_step"], 1)
                    dve.wait_ge(S["dve_step"], made.next("dve_step"))
                ts_(rank, rank, 1.5, None, ALU.is_lt).then_inc(S["router_w"], 1)
                dve.wait_ge(S["mem_std"], 1)
                dve.reciprocal(stat[:, 44:44 + TT], stat[:, 42:42 + TT]).then_inc(S["mem_inv"], 1)
                dve.wait_ge(S["router_w"], made.next("router_w"))
                dve.wait_ge(S["router_exp"], 1)
                tt_(p, p, rank, ALU.mult).then_inc(S["dve_step"], 1)
                dve.wait_ge(S["dve_step"], made.next("dve_step"))
                dve.tensor_reduce(mx, p3, AX.X, ALU.add).then_inc(S["dve_step"], 1)
                dve.wait_ge(S["dve_step"], made.next("dve_step"))
                dve.reciprocal(mx, mx).then_inc(S["dve_step"], 1)
                dve.wait_ge(S["dve_step"], made.next("dve_step"))
                tt_(moe_w[:], p3, mx.unsqueeze(2).to_broadcast([P, TT, E]), ALU.mult).then_inc(S["dve_step"], 1)
                dve.wait_ge(S["dve_step"], made.next("dve_step"))
                dve.wait_ge(S["counts_mm"], 1)
                n = ITEMS + 1
                copy(moe_pos[:].rearrange("p t e -> p (t e)"), bank[1][:, 0:TT * E])
                count, items, start, end = (tiles[:, i, :] for i in range(4))
                copy(count, bank[1][:, TT * E:(TT + 1) * E]).then_inc(S["dve_step"], 1)
                dve.wait_ge(S["dve_step"], made.next("dve_step"))
                ts_(items, count, CAP + 0.5, 1.0, ALU.is_gt, ALU.add).then_inc(S["dve_step"], 1)
                dve.wait_ge(S["dve_step"], made.next("dve_step"))
                s0 = sq[:, 0, :].rearrange("p (e f) -> p e f", e=E)
                tt_(s0, items.unsqueeze(1).to_broadcast([P, E, E]), earlier, ALU.mult)
                chosen = rank.rearrange("p (t e) -> p t e", t=TT)
                far = rt[:, 0, 0:TT * E].rearrange("p (t e) -> p t e", t=TT)
                ts_(far, chosen, -4.0 * T, 4.0 * T, ALU.mult, ALU.add)
                dve.tensor_reduce(table[:, 0:1], items, AX.X, ALU.add).then_inc(S["dve_step"], 1)
                dve.wait_ge(S["dve_step"], made.next("dve_step"))
                tt_(moe_pos[:], moe_pos[:], far, ALU.add)
                dve.tensor_reduce(start, s0, AX.X, ALU.add).then_inc(S["dve_step"], 1)
                dve.wait_ge(S["dve_step"], made.next("dve_step"))
                tt_(end, start, items, ALU.add).then_inc(S["dve_step"], 1)
                dve.wait_ge(S["dve_step"], made.next("dve_step"))
                count = cst[:, CONST["count"]]
                number = count[:, 0:n].unsqueeze(2).to_broadcast([P, n, E])
                its, late, skip, work = (in_item[:, i, :].rearrange("p (i e) -> p i e", e=E) for i in range(4))
                tt_(its, number, start.unsqueeze(1).to_broadcast([P, n, E]), ALU.is_ge)
                tt_(late, number, end.unsqueeze(1).to_broadcast([P, n, E]), ALU.is_lt)
                tt_(skip, number, start.unsqueeze(1).to_broadcast([P, n, E]), ALU.subtract).then_inc(S["dve_step"], 1)
                dve.wait_ge(S["dve_step"], made.next("dve_step"))
                tt_(its, its, late, ALU.mult).then_inc(S["dve_step"], 1)
                dve.wait_ge(S["dve_step"], made.next("dve_step"))
                tt_(work, its, count[:, 0:E].unsqueeze(1).to_broadcast([P, n, E]), ALU.mult).then_inc(S["dve_step"], 1)
                dve.wait_ge(S["dve_step"], made.next("dve_step"))
                dve.tensor_reduce(table[:, 1:1 + n], work, AX.X, ALU.add).then_inc(S["dve_step"], 1)
                dve.wait_ge(S["dve_step"], made.next("dve_step"))
                copy(table_i[:], table[:]).then_inc(S["items_ready"], 1)
                dve.wait_ge(S["items_ready"], made.next("items_ready"))
                for tt in range(TT):
                    stt(late, skip, -float(CAP), moe_pos[:, tt, :].unsqueeze(1).to_broadcast([P, n, E]), ALU.mult, ALU.add)
                    tt_(work, its, moe_w[:, tt, :].unsqueeze(1).to_broadcast([P, n, E]), ALU.mult).then_inc(S["dve_step"], 1)
                    dve.wait_ge(S["dve_step"], made.next("dve_step"))
                    tt_(late, late, its, ALU.mult)
                    dve.tensor_reduce(item_w[:, tt, :], work, AX.X, ALU.add).then_inc(S["dve_step"], 1)
                    dve.wait_ge(S["dve_step"], made.next("dve_step"))
                    dve.tensor_reduce(item_pos[:, tt, :], late, AX.X, ALU.add).then_inc(S["dve_step"], 1)
                    dve.wait_ge(S["dve_step"], made.next("dve_step"))

            def moe_dve():
                count = cst[:, CONST["count"]]
                n_items = dve.value_load(table_i[0:1, 0:1], min_val=N_EXPERTS, max_val=ITEMS)

                def tokens():
                    return copy(xeT[:, 0:4, :], bank[4][:].rearrange("p (k c) -> p k c", k=4))

                def split_down(s, item):
                    w, lo, sem, n = moe_panel(moe_order(2, s), item)
                    dve.wait_ge(sem, n * 16)
                    copy(ring_hi[:, s % 2, :], w).then_inc(S["e_split_hi"], 1)
                    dve.wait_ge(S["e_split_hi"], item * FF_CHUNKS + (s + 1))
                    tt_(lo, w, ring_hi[:, s % 2, :].bitcast(F32), ALU.subtract).then_inc(S["e_split"], 1)

                for tt in range(TT):
                    ins = ts_(one_hot[:, tt, :], count, item_pos[:, tt, 0:1], None, ALU.is_equal)
                ins.then_inc(S["one_hot"], 1)
                dve.wait_ge(S["routed_mm"], 1)
                tokens().then_inc(S["xe_dve"], 1)
                ts_(acc[:], x_tm[:], ALPHA, None, ALU.mult).then_inc(S["acc_read"], 1)
                with dve.Fori(0, n_items) as item:
                    for s in range(FF_CHUNKS):
                        if s:
                            split_down(s - 1, item)
                        dve.wait_ge(S["act_out"], item * FF_CHUNKS + (FF_CHUNKS + s + 1))
                        dve.wait_ge(S["y_full"], item * FF_CHUNKS + (FF_CHUNKS + max(s - 1, 0)))
                        h, hi = hT[:, s % 2, :, 0:CAP], hT_hi[:, s % 2, :, 0:CAP]
                        tt_(h, gate_s[:, s % 2, :, 0:CAP], bank[s % 2][:, 2 * CAP:].rearrange("p (m c) -> p m c", m=2), ALU.mult
                            ).then_inc(S["e_made"], 1)
                        dve.wait_ge(S["e_made"], item * FF_CHUNKS + (s + 1))
                        copy(hi, h).then_inc(S["e_hi"], 1)
                        dve.wait_ge(S["e_hi"], item * FF_CHUNKS + (s + 1))
                        tt_(hT_lo[:, s % 2, :, 0:CAP], h, hi.bitcast(F32), ALU.subtract).then_inc(S["h_ready"], 1)
                        if s == 2:
                            dve.wait_ge(S["routed_mm"], item + 1)
                            for tt in range(TT):
                                ts_(one_hot[:, tt, :], count, item_pos[:, tt, bass.ds(item + 1, 1)], None, ALU.is_equal)
                                ins = ts_(weighted[:, tt, :], count, item_pos[:, tt, bass.ds(item, 1)], item_w[:, tt, bass.ds(item, 1)],
                                          ALU.is_equal, ALU.mult)
                            ins.then_inc(S["one_hot"], 1)
                    split_down(FF_CHUNKS - 1, item)
                    dve.wait_ge(S["routed_mm"], item + 2)
                    tokens().then_inc(S["xe_dve"], 1)
                    dve.wait_ge(S["acc_read"], item + 1)
                    for h in range(2):
                        dve.wait_ge(S["scatter_mm"], 2 * item + (h + 1))
                        for tt in range(TT):
                            a = acc[:, tt, h * 512:(h + 1) * 512]
                            ins = tt_(a, a, bank[4 + 2 * h + tt][:], ALU.add)
                    ins.then_inc(S["acc_read"], 1)
                dve.wait_ge(S["acc_read"], n_items + 1)

            def split_x(n):
                for b in range(4):
                    f = slice(2 * b, 2 * b + 2)
                    if b % 2:
                        dve.wait_ge(S["xT_act"], 2 * n + b // 2 + 1)
                    else:
                        dve.wait_ge(S["xT_dve"], 2 * n + b // 2 + 1)
                    copy(xT_hi[:, f, :], xT[:, f, :]).then_inc(S["dve_step"], 1)
                    dve.wait_ge(S["dve_step"], made.next("dve_step"))
                    tt_(xT_lo[:, f, :], xT[:, f, :], xT_hi[:, f, :].bitcast(F32), ALU.subtract).then_inc(S["x_split"], 1)

            def mlp_dve(kind, l, n_chunks, base, per_step, n_split):
                gated, sems = kind == "ffn", mlp_signals(kind)
                nb, ups = (2, 2) if gated else (3, 1)
                arrived, n0 = (landed, BEFORE_FFN) if gated else (landed_2, ORDER.index(("mlp_up", l, 0)) - AFTER_MOE)
                first_slot = 0 if gated else BEFORE_MOE
                done = [0]

                def split_panel(turn=0, per_turn=0):
                    n = n0 + done[0]
                    slot = (first_slot + n) % RING
                    done[0] += 1
                    dve.wait_ge(arrived[slot], (turn * (per_turn // RING) + (n // RING + 1)) * 16)
                    copy(ring_hi[:, slot, :], ring[:, slot, :]).then_inc(S["split_hi"], 1)
                    dve.wait_ge(S["split_hi"], turn * per_turn + (n_split + done[0]))
                    tt_(ring_lo[:, slot, :], ring[:, slot, :], ring_hi[:, slot, :].bitcast(F32), ALU.subtract).then_inc(S["split"], 1)

                def hidden(i, slot, early):
                    dve.wait_ge(sems["out"], i + 1)
                    if not early:
                        dve.wait_ge(sems["y"], i - nb + 1)
                    b = bank[(2 * slot + 1) if gated else slot]
                    tt_(hT[:, slot, :, :], gate_s[:, slot, :, :], b[:].rearrange("p (m t) -> p m t", m=2), ALU.mult).then_inc(S["h_made"], 1)
                    dve.wait_ge(S["h_made"], i + h_before)
                    copy(hT_hi[:, slot, :, :], hT[:, slot, :, :]).then_inc(S["h_hi"], 1)
                    dve.wait_ge(S["h_hi"], i + h_before)
                    tt_(hT_lo[:, slot, :, :], hT[:, slot, :, :], hT_hi[:, slot, :, :].bitcast(F32), ALU.subtract).then_inc(sems["h"], 1)

                h_before = 1 if gated else FF_CHUNKS + 1
                per_turn = per_step * (ups + 1)

                def step(i, slot, early, turn=0):
                    split_panel(turn, per_turn)
                    hidden(i, slot, early)
                    for _ in range(ups):
                        split_panel(turn, per_turn)

                for _ in range(ups):
                    split_panel()
                steps = n_chunks - 1
                lead = nb + (steps - nb) % per_step
                for s in range(lead):
                    step(base + s, s % nb, s < nb)
                turns = (steps - lead) // per_step
                with dve.Fori(0, turns) as turn:
                    for s in range(lead, lead + per_step):
                        step(turn * per_step + (base + s), s % nb, False, turn)
                done[0] += (turns - 1) * per_turn
                hidden(base + steps, steps % nb, False)
                split_panel()
                dve.wait_ge(sems["y"], base + n_chunks)
                for tt in range(TT):
                    for h in range(2):
                        xs = x_tm[:, tt, h * 512:(h + 1) * 512]
                        ins = stt(xs, xs, ALPHA if gated else 1.0, bank[4 + 2 * tt + h][:], ALU.mult, ALU.add)
                ins.then_inc(sems["read"], 1)
                dve.wait_ge(sems["read"], 1 + l)

            def rms_x(n, src):
                dve.wait_ge(S["rms_std"], n + 1)
                if n:
                    dve.wait_ge(S["x_turned"], 4 * (4, 5, 7, 9)[n])
                dve.reciprocal(rs[:, 4:4 + TT], rs[:, 2:2 + TT]).then_inc(S["dve_step"], 1)
                dve.wait_ge(S["dve_step"], made.next("dve_step"))
                for tt in range(TT):
                    ins = ts_(xn[:, tt, :], src[:, tt, :], rs[:, 4 + tt:5 + tt], None, ALU.mult)
                ins.then_inc(S["rms_x"], 1)
                dve.wait_ge(S["rms_x"], made.next("rms_x"))

            def rotate(dst1, dst2, src, n, cos, sin, parts=slice(0, P)):
                a, b = (scr[parts, i, 0:n * HEAD] for i in range(2))
                w = a.shape[0]
                for t, f in ((a, cos), (b, sin)):
                    ins = tt_(t.rearrange("p (n d e) -> p n d e", d=2, e=32), src.rearrange("p n (d e) -> p n d e", d=2),
                              f.unsqueeze(1).unsqueeze(1).to_broadcast([w, n, 2, 32]), ALU.mult)
                ins.then_inc(S["dve_step"], 1)
                dve.wait_ge(S["dve_step"], made.next("dve_step"))
                a, b = (t.rearrange("p (n e) -> p n e", e=HEAD) for t in (a, b))
                for d, x0, x1, op in ((dst1, a[:, :, 0:32], b[:, :, 32:], ALU.subtract), (dst2, b[:, :, 0:32], a[:, :, 32:], ALU.add)):
                    for dst in d:
                        ins = tt_(dst, x0, x1, op)
                return ins

            def norm_heads(l, first, last):
                sets = head_sets(l)
                base = l * N_SETS[0]

                def squares(i):
                    src, n, panels_ = sets[i][0], sets[i][1], sets[i][5]
                    at, _ = set_stats(l, i)
                    dve.wait_ge(S["attn_read"], l * PANELS_ATTN[0] + panels_)
                    for tt in range(TT):
                        sq = scr[:, tt, 0:n * HEAD]
                        tt_(sq, src[:, tt, :], src[:, tt, :], ALU.mult).then_inc(S["dve_step"], 1)
                        dve.wait_ge(S["dve_step"], made.next("dve_step"))
                        ins = dve.tensor_reduce(rs[:, at + tt * n:at + (tt + 1) * n], sq.rearrange("p (n e) -> p n e", e=HEAD), AX.X, ALU.add)
                    ins.then_inc(S["rms_ss"], 1)
                    dve.wait_ge(S["rms_ss"], made.next("rms_ss"))

                def turn(i):
                    src, n, gain, rotary, place, _ = sets[i]
                    at, size = set_stats(l, i)
                    dve.wait_ge(S["qk_std"], base + i + 1)
                    dve.reciprocal(rs[:, at:at + size], rs[:, at:at + size]).then_inc(S["dve_step"], 1)
                    dve.wait_ge(S["dve_step"], made.next("dve_step"))
                    for tt in range(TT):
                        x3 = src[:, tt, :].rearrange("p (n e) -> p n e", e=HEAD)
                        tt_(x3, x3, rs[:, at + tt * n:at + (tt + 1) * n].unsqueeze(2).to_broadcast([P, n, HEAD]), ALU.mult).then_inc(S["dve_step"], 1)
                        dve.wait_ge(S["dve_step"], made.next("dve_step"))
                        tt_(x3, x3, row[:, gain:gain + HEAD].unsqueeze(1).to_broadcast([P, n, HEAD]), ALU.mult).then_inc(S["dve_step"], 1)
                        dve.wait_ge(S["dve_step"], made.next("dve_step"))
                        if rotary:
                            cos, sin = (atc[:, ATTN[f]].rearrange("p (t e) -> p t e", t=TT)[:, tt, :] for f in ("cos", "sin"))
                            if place is None:
                                d1, d2 = [x3[:, :, 0:32]], [x3[:, :, 32:]]
                            else:
                                d1, d2 = ([twice[:, tt, place:place + n, i, e:e + 32] for i in range(2)] for e in (0, 32))
                            rotate(d1, d2, x3, n, cos, sin).then_inc(S["dve_step"], 1)
                            dve.wait_ge(S["dve_step"], made.next("dve_step"))

                for i in range(first, last):
                    squares(i)
                    turn(i)
                    if l == 0 and i == 2:
                        for tt in range(TT):
                            for j in range(2):
                                copy(twice[:, tt, 6:12, j, :], proj[:, tt, 768:1152].rearrange("p (n e) -> p n e", e=HEAD))

            def compress_in():
                pos = col[:, COLS["cmp_pos"]].rearrange("p (k l) -> p k l", k=2)
                dve.wait_ge(S["turnq_act"], BANKS_T[0] // 2)
                for kv in range(2):
                    for g in range(NSA_G):
                        item = qkT[:, 12 + 3 * kv + g, :].rearrange("p (a s) -> p a s", s=CMP_STRIDE)
                        for odd in range(2):
                            hd = slice(HEAD * odd, HEAD * (odd + 1))
                            for hi in range(2):
                                ins = tt_(cmp_in[hd, kv, 8 * hi:8 * hi + 8, g, :].rearrange("p l i -> p i l"), item[hd, hi:hi + N_CMP, odd::2],
                                          pos[hd, kv, 8 * hi:8 * hi + 8].unsqueeze(1).to_broadcast([HEAD, N_CMP, 8]), ALU.add)
                ins.then_inc(S["cmp_tb"], 1)
                dve.wait_ge(S["cmp_tb"], made.next("cmp_tb"))

            def compress(n):
                if n == -1:
                    compress_in()
                blk = slice(0, N_CMP)
                k = cmp_kv[blk, 0, :, :]
                s3 = cmp_s[:].rearrange("p h t i -> p (h t) i")[:, :, 0:N_CMP]
                n_rows = NSA_HEADS * TT
                mx = rs[:, 8:8 + n_rows]
                if n == 6:
                    dve.wait_ge(S["cmp_o_mm"], 1)
                    for kv in range(2):
                        b2 = row[blk, ROWS["cmp_b2"]][:, kv * HEAD:(kv + 1) * HEAD].unsqueeze(1).to_broadcast([N_CMP, NSA_G, HEAD])
                        ins = tt_(cmp_kv[blk, kv, :, :], bank[1][blk, kv * NSA_G * HEAD:(kv + 1) * NSA_G * HEAD].rearrange("p (g e) -> p g e", e=HEAD), b2, ALU.add)
                    ins.then_inc(S["dve_step"], 1)
                    dve.wait_ge(S["dve_step"], made.next("dve_step"))
                    tt_(cmp_dup[blk, :, 0, :], k, k, ALU.mult).then_inc(S["dve_step"], 1)
                    dve.wait_ge(S["dve_step"], made.next("dve_step"))
                    dve.tensor_reduce(rs[blk, 4:4 + NSA_G], cmp_dup[blk, :, 0, :], AX.X, ALU.add).then_inc(S["cmp_kv"], 1)
                    dve.wait_ge(S["cmp_kv"], made.next("cmp_kv"))
                elif n == 8:
                    dve.wait_ge(S["cmp_k_std"], 1)
                    dve.reciprocal(rs[blk, 4:4 + NSA_G], rs[blk, 4:4 + NSA_G]).then_inc(S["dve_step"], 1)
                    dve.wait_ge(S["dve_step"], made.next("dve_step"))
                    tt_(k, k, rs[blk, 4:4 + NSA_G].unsqueeze(2).to_broadcast([N_CMP, NSA_G, HEAD]), ALU.mult).then_inc(S["dve_step"], 1)
                    dve.wait_ge(S["dve_step"], made.next("dve_step"))
                    tt_(k, k, row[blk, ROWS["a_k"]][:, 0:HEAD].unsqueeze(1).to_broadcast([N_CMP, NSA_G, HEAD]), ALU.mult).then_inc(S["dve_step"], 1)
                    dve.wait_ge(S["dve_step"], made.next("dve_step"))
                    d1, d2 = ([cmp_dup[blk, :, i, e:e + 32] for i in range(2)] for e in (0, 32))
                    rotate(d1, d2, k, NSA_G, atc[blk, ATTN["cmp_cos"]], atc[blk, ATTN["cmp_sin"]], blk).then_inc(S["cmp_k_ready"], 1)
                    dve.wait_ge(S["cmp_k_ready"], made.next("cmp_k_ready"))
                elif n == 10:
                    dve.wait_ge(S["cmp_kT_mm"], 1)
                    copy(cmp_kT[:, :, 0:N_CMP], bank[3][:, 0:NSA_G * 16].rearrange("p (g i) -> p g i", g=NSA_G)[:, :, 0:N_CMP]).then_inc(S["cmp_kT"], 1)
                    dve.wait_ge(S["cmp_kT"], made.next("cmp_kT"))
                elif n == 12:
                    dve.wait_ge(S["cmp_s_mm"], 1)
                    mask = atc[:, ATTN["cmp"]].rearrange("p (t i) -> p t i", t=TT)[:, :, 0:N_CMP]
                    for odd in range(2):
                        ins = tt_(cmp_s[:, odd::2, :, 0:N_CMP], bank[1 + 2 * odd][:, 0:6 * TT * 16].rearrange("p (h t i) -> p h t i", h=6, t=TT)[:, :, :, 0:N_CMP],
                                  mask.unsqueeze(1).to_broadcast([P, 6, TT, N_CMP]), ALU.add)
                    ins.then_inc(S["dve_step"], 1)
                    dve.wait_ge(S["dve_step"], made.next("dve_step"))
                    dve.tensor_reduce(mx, s3, AX.X, ALU.max).then_inc(S["dve_step"], 1)
                    dve.wait_ge(S["dve_step"], made.next("dve_step"))
                    tt_(s3, s3, mx.unsqueeze(2).to_broadcast([P, n_rows, N_CMP]), ALU.subtract).then_inc(S["cmp_s"], 1)
                    dve.wait_ge(S["cmp_s"], made.next("cmp_s"))
                elif n == 14:
                    dve.wait_ge(S["cmp_e"], 1)
                    dve.wait_ge(S["nsa_gates"], 1)
                    dve.tensor_reduce(mx, s3, AX.X, ALU.add).then_inc(S["dve_step"], 1)
                    dve.wait_ge(S["dve_step"], made.next("dve_step"))
                    dve.reciprocal(mx, mx).then_inc(S["dve_step"], 1)
                    dve.wait_ge(S["dve_step"], made.next("dve_step"))
                    tt_(mx, mx, coef[:, 0].rearrange("p h t -> p (h t)"), ALU.mult).then_inc(S["dve_step"], 1)
                    dve.wait_ge(S["dve_step"], made.next("dve_step"))
                    m3 = mx.rearrange("p (h t) -> p h t", t=TT)
                    tt_(m3, m3, atc[:, ATTN["cmp_ok"]].unsqueeze(1).to_broadcast([P, NSA_HEADS, TT]), ALU.mult).then_inc(S["dve_step"], 1)
                    dve.wait_ge(S["dve_step"], made.next("dve_step"))
                    tt_(s3, s3, mx.unsqueeze(2).to_broadcast([P, n_rows, N_CMP]), ALU.mult).then_inc(S["cmp_p"], 1)
                    dve.wait_ge(S["cmp_p"], made.next("cmp_p"))
                h = n - 17
                if 0 <= h < NSA_HEADS:
                    dve.wait_ge(S["cmp_pv_mm"], h + 1)
                    o = o_tm[:, :, h * HEAD:(h + 1) * HEAD]
                    tt_(o, o, bank[3][:, h % 2 * TT * HEAD:][:, 0:TT * HEAD].rearrange("p (t e) -> p t e", t=TT), ALU.add).then_inc(S["cmp_done"], 1)
                    dve.wait_ge(S["cmp_done"], made.next("cmp_done"))

            def attend(l):
                n0 = 0 if l == 0 else len(units(0))
                todo = units(l)

                def maxima(n):
                    kind, h, tile = todo[n]
                    u = n0 + n
                    s = u % 2
                    p = p_sb[:, u % 4, :]
                    mx, neg = unit_stat(u, "max"), unit_stat(u, "neg")
                    dve.wait_ge(S["score_mm"], u + 1)
                    if u >= 4:
                        dve.wait_ge(S["pT_mm"], u - 3)
                    k = TT
                    if kind == "dil":
                        k, w = 1, 3 * P * (tile + 1)
                        mask = atc[:, ATTN[f"dil{tile}"]]
                        for a in range(0, w, 512):
                            e = min(a + 512, w)
                            ins = tt_(p[:, a:e], bank[2 * s + a // 512][:, 0:e - a], mask[:, a:e], ALU.add)
                        ins.then_inc(S["dve_step"], 1)
                        dve.wait_ge(S["dve_step"], made.next("dve_step"))
                        ins = dve.tensor_reduce(mx[:, 0:1], p[:, 0:w], AX.X, ALU.max)
                    elif kind == "mem":
                        ins = dve.tensor_reduce(mx, bank[2 * s][:].rearrange("p (t k) -> p t k", t=TT), AX.X, ALU.max)
                    else:
                        tt_(p[:, 0:3 * P], bank[2 * s][:, 0:3 * P], causal, ALU.add).then_inc(S["dve_step"], 1)
                        dve.wait_ge(S["dve_step"], made.next("dve_step"))
                        dve.tensor_reduce(mx[:, 0:1], p[:, 0:P], AX.X, ALU.max)
                        ins = dve.tensor_reduce(mx[:, 1:2], p[:, P:3 * P], AX.X, ALU.max)
                    ins.then_inc(S["dve_step"], 1)
                    dve.wait_ge(S["dve_step"], made.next("dve_step"))
                    ts_(neg[:, 0:k], mx[:, 0:k], -SCALE, None, ALU.mult).then_inc(S["score_max"], 1)
                    dve.wait_ge(S["score_max"], made.next("score_max"))

                def finish(n):
                    kind, h, tile = todo[n]
                    u = n0 + n
                    s = u % 2
                    k = 1 if kind == "dil" else TT
                    inv_, scale_ = unit_stat(u, "inv")[:, 0:k], unit_stat(u, "scale")[:, 0:k]
                    dve.wait_ge(S["pv_mm"], u + 1)
                    dve.reciprocal(inv_, unit_stat(u, "sum")[:, 0:k]).then_inc(S["dve_step"], 1)
                    dve.wait_ge(S["dve_step"], made.next("dve_step"))
                    if kind == "dil":
                        ins = ts_(o_tm[:, tile, h * HEAD:(h + 1) * HEAD], bank[6 + s][:, 0:HEAD], inv_, None, ALU.mult)
                    else:
                        pv = bank[6 + s][:, 0:TT * HEAD].rearrange("p (t e) -> p t e", t=TT)
                        base = {"mem": NSA_HEADS * HEAD if l == 0 else SLOTS * HEAD}.get(kind, 0)
                        o = o_tm[:, :, base + h * HEAD:base + (h + 1) * HEAD]
                        if kind == "mem":
                            ins = tt_(o, pv, inv_.unsqueeze(2).to_broadcast([P, TT, HEAD]), ALU.mult)
                        else:
                            tt_(scale_, inv_, coef[:, 1 if kind == "sel" else 2, h, :], ALU.mult).then_inc(S["dve_step"], 1)
                            dve.wait_ge(S["dve_step"], made.next("dve_step"))
                            part_ = scr[:, 0, 0:TT * HEAD].rearrange("p (t e) -> p t e", t=TT)
                            tt_(part_, pv, scale_.unsqueeze(2).to_broadcast([P, TT, HEAD]), ALU.mult).then_inc(S["dve_step"], 1)
                            dve.wait_ge(S["dve_step"], made.next("dve_step"))
                            ins = tt_(o, o, part_, ALU.add)
                    ins.then_inc(S["pv_read"], 1)
                    dve.wait_ge(S["pv_read"], made.next("pv_read"))

                for n in range(len(todo) + 4):
                    if l == 0:
                        compress(n - CMP_STEP)
                    if n < len(todo):
                        maxima(n)
                    if n >= 4:
                        finish(n - 4)

            def attention_dve(l):
                n_turn = 4 + 3 * l
                dve.wait_ge(S["params_in"], 16 * 4)
                rms_x(2 * l, x_tm)
                if l == 0:
                    copy_xT(n_turn, "attn_norm0")
                    norm_heads(l, 0, 5)
                else:
                    copy_xT(n_turn, "kv_norm")
                    norm_heads(l, 0, 1)
                    copy_xT(n_turn + 1, "attn_norm1")
                    norm_heads(l, 1, 6)
                dve.drain().then_inc(S["qk_ready"], 1)
                n0 = 0 if l == 0 else BANKS_T[0]
                for n in range(BANKS_T[l]):
                    if (n0 + n) % 2 == 0:
                        dve.wait_ge(S["turnq_mm"], n0 + n + 1)
                        copy(qkT[:, 2 * n:2 * n + 2, :], bank[n % 4][:].rearrange("p (i t) -> p i t", i=2)).then_inc(S["turnq_dve"], 1)
                        dve.wait_ge(S["turnq_dve"], made.next("turnq_dve"))
                if l == 0:
                    dve.memset(o_tm[:, :, 0:NSA_HEADS * HEAD], 0.0)
                else:
                    dve.memset(o_tm[:, :, (SLOTS + MEM_HEADS) * HEAD:], 0.0).then_inc(S["dve_step"], 1)
                    dve.wait_ge(S["dve_step"], made.next("dve_step"))
                attend(l)
                n_turn = (5, 9)[l]
                copy_xT(n_turn)
                dve.wait_ge(S["proj2_mm"], l + 1)
                for tt in range(TT):
                    for h in range(2):
                        xs = x_tm[:, tt, h * 512:(h + 1) * 512]
                        ins = tt_(xs, xs, bank[2 * tt + h][:], ALU.add)
                ins.then_inc(S["x_done"], 1)
                dve.wait_ge(S["x_done"], made.next("x_done"))
                rms_x(2 * l + 1, x_tm)
                copy_xT(n_turn + 1, f"mlp_norm{l}")
                split_x(n_turn + 1)
                mlp_dve("mlp", l, D_FF_2 // FCH, l * (D_FF_2 // FCH), 3, PER_ITEM + 2 * l * (D_FF_2 // FCH))

            dve.memset(u_pad[:, :, 0:CONF_TAPS - 1], 0.0)
            dve.memset(s_pad[:, :, 0:SHORT_TAPS - 1], 0.0)
            dve.memset(u_sb[:], 0.0)
            dve.memset(pz[:, :, :, 0:1], 0.0).then_inc(S["cleared"], 1)
            dve.wait_ge(S["cleared"], made.next("cleared"))
            dve.wait_ge(S["consts_in"], 16)
            for l in range(DEPTH):
                mixer_dve(l)
                layer_norm(2 * l, x_tm)
                copy_xT(2 * l + 1, f"ln1_g{l}", f"ln1_b{l}")
                if l == 0:
                    split_x(1)
                    ln_gain(0)
                    mlp_dve("ffn", 0, FF_CHUNKS, 0, 2, 0)
                    layer_norm(2 * l + 1, x_tm)
                else:
                    ln_gain(2)
                    route()
                    moe_dve()
                    layer_norm(2 * l + 1, acc)
                    ln_gain(2 * l + 1)
            for l in range(DEPTH):
                attention_dve(l)

        @block.gpsimd
        def _(pool):
            for dst, src in ((col, cols), (mid, mids)):
                pool.dma_start(dst[:], src).then_inc(S["params_in"], 16)
            pool.dma_start(row[:], rows.partition_broadcast(P)).then_inc(S["params_in"], 16)
            for n in range(2 * DEPTH):
                if n:
                    pool.wait_ge(S["ln_x_done"], n)
                pool.dma_start(ln_row[:], ln_rows[n].partition_broadcast(P)).then_inc(S["ln_rows_in"], 16)
            pool.dma_start(mem_in, mem.rearrange("(t p) d -> p t d", p=P)).then_inc(S["mem_in"], 16)
            pool.wait_ge(S["ln_x_done"], 2 * DEPTH)
            pool.dma_start(atc[:], attn_consts).then_inc(S["params_in"], 16)


def lay_out(i):
    def f(name):
        return np.asarray(i[name], np.float32)

    def blocks(v):
        return v.reshape(-1, P).T

    def col_panel(w, n):
        c = w[:, n * PC:(n + 1) * PC]
        if c.shape[1] < PC:
            c = np.pad(c, ((0, 0), (0, PC - c.shape[1])))
        return c.reshape(KB, P, PC).transpose(1, 0, 2)

    def row_panel(w, n):
        return w[n * PR * P:(n + 1) * PR * P].reshape(PR, P, D).transpose(1, 0, 2)

    per = D_FF // FCH
    branch_out = [np.concatenate([f(n)[l] for n in ("rwkv_w_o", "conf_w_o", "short_w_o")]) for l in range(DEPTH)]
    w_in, w_out, mem_kv = f("w_in"), f("w_out"), f("w_mem_kv_2")
    ffn = [f("ffn_w_gate"), f("ffn_w_up"), f("ffn_w_down")]
    moe = [f("moe_w_gate")[0], f("moe_w_up")[0], f("moe_w_down")[0]]
    a_in, a_out, kv, b_in, b_out = f("a_w_in_2")[0], f("a_w_out_2")[0], f("w_kv_shared_2"), f("b_w_in_2")[0], f("b_w_out_2")[0]
    cmp_w1, up, down = f("a_cmp_w1_2")[0], f("w_up_2"), f("w_down_2")

    def panel(kind, l, n):
        if kind == "w_in":
            return col_panel(w_in[l], n)
        if kind == "mix":
            return col_panel(branch_out[l], n)
        if kind == "w_out":
            return row_panel(w_out[l], n)
        if kind in ("gate", "up", "down"):
            m = ("gate", "up", "down").index(kind)
            w = (moe if l else ffn)[m][n // per]
            return row_panel(w, n % per) if kind == "down" else col_panel(w, n % per)
        if kind == "mem_kv":
            return col_panel(mem_kv[l], n)
        if kind == "cmp":
            return cmp_w1[n // 2].reshape(2, KB, P, CMP_HIDDEN)[n % 2].transpose(1, 0, 2)
        if kind in ("mlp_up", "mlp_down"):
            return col_panel(up[l], n) if kind == "mlp_up" else row_panel(down[l], n)
        w = {"a_in": a_in, "kv": kv, "b_in": b_in, "a_out": a_out, "b_out": b_out}[kind]
        return row_panel(w, n) if kind.endswith("out") else col_panel(w, n)

    weights = np.empty((N_PANELS, P, PANEL), np.float32)
    for n, (kind, l, m) in enumerate(ORDER):
        weights[n] = panel(kind, l, m).reshape(P, PANEL)

    cols = np.zeros((P, COLS.n), np.float32)
    for l in range(DEPTH):
        for name, src in (("mu", "rwkv_mu"), ("a0", "rwkv_a0"), ("k_k", "rwkv_k_k"), ("k_a", "rwkv_k_a"), ("r_k", "rwkv_r_k"),
                          ("gn_g", "rwkv_ln_g"), ("gn_b", "rwkv_ln_b"), ("conf_dw_b", "conf_dw_b"), ("conf_ln_g", "conf_ln_g"),
                          ("conf_ln_b", "conf_ln_b"), ("attn_norm", "attn_norm_2"), ("mlp_norm", "mlp_norm_2"),
                          ("mem_norm", "mem_norm_2"), ("ln1_g", "ln1_g"), ("ln1_b", "ln1_b"), ("ln2_g", "ln2_g"), ("ln2_b", "ln2_b")):
            cols[:, COLS[f"{name}{l}"]] = blocks(f(src)[l].reshape(-1))
        for name in ("conf_dw", "short_dw"):
            w = f(name)[l]
            cols[:, COLS[f"{name}{l}"]] = w.T.reshape(2, P, -1).transpose(1, 0, 2).reshape(P, -1)
    cols[:, COLS["kv_norm"]] = blocks(f("kv_norm_2"))
    cols[:, COLS["cmp_b1"]] = blocks(f("a_cmp_b1_2").reshape(-1))
    cols[:, COLS["cmp_pos"]] = f("a_cmp_pos_2")[0].reshape(2, CMP_BLOCK // 2, P).transpose(2, 0, 1).reshape(P, -1)

    mids = np.zeros((P, MIDS.n), np.float32)
    for l in range(DEPTH):
        mids[:, MIDS[f"w2a2{l}"]] = np.concatenate([f("rwkv_w2")[l], f("rwkv_a2")[l]])
        mids[:, MIDS[f"g2{l}"]] = f("rwkv_g2")[l]
    mids[:, MIDS["router"]] = f("moe_router")[0].reshape(KB, P, N_EXPERTS).transpose(1, 0, 2).reshape(P, -1)
    mids[:, MIDS["cmp_w2"]] = f("a_cmp_w2_2")[0].reshape(2, 2, P, HEAD).transpose(2, 0, 1, 3).reshape(P, -1)

    rows = np.concatenate([f("rwkv_w0").reshape(-1), f("a_q_norm_2").reshape(-1), f("a_k_norm_2").reshape(-1),
                           f("mem_q_norm_2").reshape(-1), f("mem_k_norm_2").reshape(-1), f("a_cmp_b2_2").reshape(-1),
                           f("kv_k_norm_2").reshape(-1), f("b_q_norm_2").reshape(-1)])
    ln_rows = np.stack([np.stack([f(g)[l], f(b)[l]]) for l in range(DEPTH)
                        for g, b in (("ln1_g", "ln1_b"), ("ln2_g", "ln2_b"))])
    consts, attn_consts = shape_constants()
    return {"weights": weights, "consts": consts, "attn_consts": attn_consts, "cols": cols, "mids": mids, "rows": rows,
            "ln_rows": ln_rows, "x": f("x")[0], "mem": f("mem_2")[0]}


def kernel(**inputs):
    import concourse.bacc as bacc
    from concourse.bass_utils import run_bass_kernel_spmd

    arrays = {name: np.ascontiguousarray(a) for name, a in lay_out(inputs).items()}
    nc = bacc.Bacc("TRN2", target_bir_lowering=False, num_devices=1)
    aps = {name: nc.dram_tensor(f"in_{name}", a.shape, F32, kind="ExternalInput").ap() for name, a in arrays.items()}
    out = nc.dram_tensor("out", (T, D), F32, kind="ExternalOutput").ap()
    program(nc, out=out, **aps)
    r = run_bass_kernel_spmd(nc, [{f"in_{name}": a for name, a in arrays.items()}], core_ids=[0])
    return r.results[0]["out"].reshape(1, T, D)
```
